# Optimizing a Trainium2 kernel written in Bass

```python
import math
import jax, jax.numpy as jnp
from jax import lax
import numpy as np

D_MODEL = 1024
BATCH = 1
SEQ = 256
DEPTH = 2

GRID_W = 64
CTX_LEN = 256
N_EVEN = (DEPTH + 1) // 2
N_ODD = DEPTH // 2
EPS = 1e-6

ROPE_HEAD_DIM = 64
ROPE_FREQS = ROPE_HEAD_DIM // 4
ROPE_BASE = 10000.0

SC_WIDTH = D_MODEL // 2
DA_HEADS = 4
DA_HEAD_DIM = ROPE_HEAD_DIM
DA_V_DIM = 2 * DA_HEAD_DIM
DA_QK_WIDTH = DA_HEADS * 2 * DA_HEAD_DIM
DA_WIDTH = DA_HEADS * DA_V_DIM
Q_BLOCK = 128
EVEN_SPLITS = (SC_WIDTH, 2 * SC_WIDTH, 3 * SC_WIDTH, 3 * SC_WIDTH + DA_QK_WIDTH, 3 * SC_WIDTH + 2 * DA_QK_WIDTH)
EVEN_IN = 3 * SC_WIDTH + 2 * DA_QK_WIDTH + DA_WIDTH
EVEN_OUT = SC_WIDTH + DA_WIDTH

POOL_WINDOWS = (2, 4, 8, 16)
POOL_RADII = tuple(w // 2 for w in POOL_WINDOWS)
POOL_GROUPS = 4
POOL_WIDTH = D_MODEL // 2
POOL_GROUP_DIM = POOL_WIDTH // POOL_GROUPS
RET_HEADS = 4
RET_QK_DIM = ROPE_HEAD_DIM
RET_V_DIM = 2 * RET_QK_DIM
RET_QK_WIDTH = RET_HEADS * RET_QK_DIM
RET_WIDTH = RET_HEADS * RET_V_DIM
RET_CHUNK = 128
ODD_SPLITS = (POOL_WIDTH, POOL_WIDTH + RET_QK_WIDTH, POOL_WIDTH + 2 * RET_QK_WIDTH, POOL_WIDTH + 2 * RET_QK_WIDTH + RET_WIDTH)
ODD_IN = POOL_WIDTH + 2 * RET_QK_WIDTH + 2 * RET_WIDTH
ODD_OUT = POOL_WIDTH + RET_WIDTH

FFN_DIM = 2816


def rms_norm(x, g):
    xf = x.astype(jnp.float32)
    y = xf * lax.rsqrt(jnp.mean(xf * xf, axis=-1, keepdims=True) + EPS)
    return (y * g.astype(jnp.float32)).astype(x.dtype)

def modulate(h, shift, scale):
    return h * (1 + scale) + shift

def dwconv3(x, w):
    xp = jnp.pad(x, ((0, 0), (1, 1), (0, 0)))
    return xp[:, :-2] * w[0] + xp[:, 1:-1] * w[1] + xp[:, 2:] * w[2]

def rope_tables(rows):
    row = jnp.repeat(jnp.arange(rows, dtype=jnp.float32), GRID_W)
    col = jnp.tile(jnp.arange(GRID_W, dtype=jnp.float32), rows)
    inv = ROPE_BASE ** (-jnp.arange(ROPE_FREQS, dtype=jnp.float32) / ROPE_FREQS)
    ang = jnp.stack([row[:, None] * inv, col[:, None] * inv], axis=1)
    return jnp.cos(ang), jnp.sin(ang)

def apply_rope(x, cos, sin):
    shp = x.shape
    xr = x.reshape(*shp[:-1], 2, 2, ROPE_FREQS)
    bc = (shp[1],) + (1,) * (x.ndim - 3) + (2, ROPE_FREQS)
    c = cos.reshape(bc).astype(x.dtype)
    s = sin.reshape(bc).astype(x.dtype)
    x1, x2 = xr[..., 0, :], xr[..., 1, :]
    out = jnp.stack([x1 * c - x2 * s, x1 * s + x2 * c], axis=-2)
    return out.reshape(shp)

def conv_ffn(h, w_up, conv_w, conv_b, w_down):
    a, b = jnp.split(h @ w_up, 2, axis=-1)
    a = dwconv3(a, conv_w) + conv_b
    return (jax.nn.silu(a) * b) @ w_down

def diff_lambda_init(layer_idx):
    return 0.8 - 0.6 * math.exp(-0.3 * layer_idx)

def diff_attend(q, k, v, lam):
    s = jnp.einsum('bhmqd,bhmkd->bhmqk', q, k).astype(jnp.float32) * (DA_HEAD_DIM ** -0.5)
    p = jax.nn.softmax(s, axis=-1)
    p = p[:, :, 0] - lam * p[:, :, 1]
    return jnp.einsum('bhqk,bhkv->bhqv', p.astype(v.dtype), v)

def conv_diff_mixer(h_ctx, h_lat, w_in, w_out, sc_conv_w, q_g, k_g, lq1, lk1, lq2, lk2, subln_g, lam_init, cos, sin):
    f32 = jnp.float32
    lam = (jnp.exp(jnp.sum(lq1.astype(f32) * lk1.astype(f32)))
           - jnp.exp(jnp.sum(lq2.astype(f32) * lk2.astype(f32))) + lam_init)

    def project(h, rotate):
        b_g, c_g, xv, q, k, v = jnp.split(h @ w_in, EVEN_SPLITS, axis=-1)
        B_, N = h.shape[:2]
        q = rms_norm(q.reshape(B_, N, DA_HEADS, 2, DA_HEAD_DIM), q_g)
        k = rms_norm(k.reshape(B_, N, DA_HEADS, 2, DA_HEAD_DIM), k_g)
        if rotate:
            q = apply_rope(q, cos, sin)
            k = apply_rope(k, cos, sin)
        q = q.transpose(0, 2, 3, 1, 4)
        k = k.transpose(0, 2, 3, 1, 4)
        v = v.reshape(B_, N, DA_HEADS, DA_V_DIM).transpose(0, 2, 1, 3)
        return (b_g, c_g, xv), q, k, v

    def finish(gates, o):
        b_g, c_g, xv = gates
        y_conv = b_g * dwconv3(c_g * xv, sc_conv_w)
        B_, _, N, _ = o.shape
        o = rms_norm(o.transpose(0, 2, 1, 3), subln_g) * (1.0 - lam_init)
        return jnp.concatenate([y_conv, o.reshape(B_, N, DA_WIDTH).astype(y_conv.dtype)], axis=-1) @ w_out

    gates_c, qc, kc, vc = project(h_ctx, False)
    gates_l, ql, kl, vl = project(h_lat, True)
    k_all = jnp.concatenate([kl, kc], axis=3)
    v_all = jnp.concatenate([vl, vc], axis=2)
    B_, H, _, N, d = ql.shape
    nb = N // Q_BLOCK
    q_blocks = jnp.moveaxis(ql.reshape(B_, H, 2, nb, Q_BLOCK, d), 3, 0)
    o_blocks = lax.map(lambda qb: diff_attend(qb, k_all, v_all, lam), q_blocks)
    o_lat = jnp.moveaxis(o_blocks, 0, 2).reshape(B_, H, N, DA_V_DIM)
    y_lat = finish(gates_l, o_lat)
    y_ctx = finish(gates_c, diff_attend(qc, kc, vc, lam))
    return y_ctx, y_lat

def multiscale_pool(v, pool_w, pool_scale):
    B_, N, _ = v.shape
    vg = v.reshape(B_, N, POOL_GROUPS, POOL_GROUP_DIM).astype(jnp.float32)
    cs = jnp.concatenate([jnp.zeros_like(vg[:, :1]), jnp.cumsum(vg, axis=1)], axis=1)
    t = jnp.arange(N)[:, None]
    r = jnp.array(POOL_RADII)[None, :]
    lo = jnp.clip(t - r, 0, N)
    hi = jnp.clip(t + r + 1, 0, N)
    g = jnp.arange(POOL_GROUPS)[None, :]
    mean = (cs[:, hi, g] - cs[:, lo, g]) / (hi - lo).astype(jnp.float32)[:, :, None]
    y = (mean - vg).astype(v.dtype)
    y = jnp.einsum('bngc,gcd->bngd', y, pool_w)
    return y.reshape(B_, N, POOL_WIDTH) * pool_scale

def retention_scan(q, k, v, lg, s0):
    B_, H, N, _ = q.shape
    dv = v.shape[-1]
    nc = N // RET_CHUNK

    def chunks(t):
        return jnp.moveaxis(t.reshape(B_, H, nc, RET_CHUNK, t.shape[-1]), 2, 0)

    pos = jnp.arange(RET_CHUNK, dtype=jnp.float32)
    diff = pos[:, None] - pos[None, :]
    intra = jnp.where(diff >= 0, jnp.exp(lg[:, None, None] * jnp.maximum(diff, 0.0)), 0.0)
    q_dec = jnp.exp(lg[:, None] * (pos + 1.0))[None, :, :, None]
    k_dec = jnp.exp(lg[:, None] * (RET_CHUNK - 1.0 - pos))[None, :, :, None]
    c_dec = jnp.exp(lg * RET_CHUNK)[None, :, None, None]

    def step(s, qkv):
        qc, kc, vc = qkv
        att = jnp.einsum('bhid,bhjd->bhij', qc, kc) * intra
        o = jnp.einsum('bhij,bhjv->bhiv', att, vc) + jnp.einsum('bhid,bhdv->bhiv', qc * q_dec, s)
        s = s * c_dec + jnp.einsum('bhjd,bhjv->bhdv', kc * k_dec, vc)
        return s, o

    _, o = lax.scan(step, s0, (chunks(q), chunks(k), chunks(v)))
    return jnp.moveaxis(o, 0, 2).reshape(B_, H, N, dv)

def retention_bidir(q, k, v, lg_f, lg_b, s_f, s_b):
    o_f = retention_scan(q, k, v, lg_f, s_f)
    flip = lambda t: jnp.flip(t, axis=2)
    o_b = flip(retention_scan(flip(q), flip(k), flip(v), lg_b, s_b))
    return o_f + o_b

def context_states(k, v, lg_f, lg_b):
    L = k.shape[2]
    j = jnp.arange(L, dtype=jnp.float32)
    w_f = jnp.exp(lg_f[:, None] * (L - 1.0 - j))
    w_b = jnp.exp(lg_b[:, None] * j)
    s_f = jnp.einsum('bhjd,hj,bhjv->bhdv', k, w_f, v)
    s_b = jnp.einsum('bhjd,hj,bhjv->bhdv', k, w_b, v)
    return s_f, s_b

def pool_retention_mixer(h_ctx, h_lat, w_in, w_out, pool_w, pool_scale, dec_f, dec_b, gn_g, cos, sin, with_ctx):
    f32 = jnp.float32
    lg_f = -jnp.exp(dec_f.astype(f32))
    lg_b = -jnp.exp(dec_b.astype(f32))

    def heads(t, dh):
        B_, N = t.shape[:2]
        return t.reshape(B_, N, RET_HEADS, dh)

    def qkv_heads(q, k, v, rotate):
        q, k, v = heads(q, RET_QK_DIM), heads(k, RET_QK_DIM), heads(v, RET_V_DIM)
        if rotate:
            q = apply_rope(q, cos, sin)
            k = apply_rope(k, cos, sin)
        q = (q.astype(f32) * (RET_QK_DIM ** -0.5)).transpose(0, 2, 1, 3)
        k = k.astype(f32).transpose(0, 2, 1, 3)
        v = v.astype(f32).transpose(0, 2, 1, 3)
        return q, k, v

    def finish(pv, g, o):
        B_, _, N, _ = o.shape
        y_r = rms_norm(o.transpose(0, 2, 1, 3), gn_g).reshape(B_, N, RET_WIDTH).astype(g.dtype) * jax.nn.silu(g)
        y_p = multiscale_pool(pv, pool_w, pool_scale)
        return jnp.concatenate([y_p, y_r], axis=-1) @ w_out

    pv_l, q_l, k_l, v_l, g_l = jnp.split(h_lat @ w_in, ODD_SPLITS, axis=-1)
    ql, kl, vl = qkv_heads(q_l, k_l, v_l, True)
    if with_ctx:
        pv_c, q_c, k_c, v_c, g_c = jnp.split(h_ctx @ w_in, ODD_SPLITS, axis=-1)
        qc, kc, vc = qkv_heads(q_c, k_c, v_c, False)
    else:
        k_c, v_c = jnp.split(h_ctx @ w_in[:, ODD_SPLITS[1]:ODD_SPLITS[3]], [RET_QK_WIDTH], axis=-1)
        kc = heads(k_c, RET_QK_DIM).astype(f32).transpose(0, 2, 1, 3)
        vc = heads(v_c, RET_V_DIM).astype(f32).transpose(0, 2, 1, 3)
    s_f, s_b = context_states(kc, vc, lg_f, lg_b)
    y_lat = finish(pv_l, g_l, retention_bidir(ql, kl, vl, lg_f, lg_b, s_f, s_b))
    y_ctx = None
    if with_ctx:
        zero = jnp.zeros_like(s_f)
        y_ctx = finish(pv_c, g_c, retention_bidir(qc, kc, vc, lg_f, lg_b, zero, zero))
    return y_ctx, y_lat

def first_inputs(seed: int = 0) -> dict:
    key = jax.random.key(seed)
    ks = iter(jax.random.split(key, 40))

    def nrm(shape, scale=1.0):
        return scale * jax.random.normal(next(ks), shape, jnp.float32)

    def gain(shape):
        return 1.0 + nrm(shape, 0.05)

    base_decay = jnp.log(-jnp.log1p(-(2.0 ** (-5.0 - jnp.arange(RET_HEADS, dtype=jnp.float32)))))
    return {
        'x': nrm((BATCH, SEQ, D_MODEL)),
        'c': nrm((BATCH, D_MODEL)),
        'ctx': nrm((BATCH, CTX_LEN, D_MODEL)),
        'c_ctx': nrm((D_MODEL,)),
        'mod_w': nrm((DEPTH, D_MODEL, 6 * D_MODEL), 0.5 * D_MODEL ** -0.5),
        'mod_b': nrm((DEPTH, 6 * D_MODEL), 0.01),
        'norm1_g': gain((DEPTH, D_MODEL)),
        'norm2_g': gain((DEPTH, D_MODEL)),
        'ev_w_in': nrm((N_EVEN, D_MODEL, EVEN_IN), D_MODEL ** -0.5),
        'ev_w_out': nrm((N_EVEN, EVEN_OUT, D_MODEL), EVEN_OUT ** -0.5),
        'sc_conv_w': nrm((N_EVEN, 3, SC_WIDTH), 3 ** -0.5),
        'da_q_norm': gain((N_EVEN, DA_HEAD_DIM)),
        'da_k_norm': gain((N_EVEN, DA_HEAD_DIM)),
        'da_lq1': nrm((N_EVEN, DA_HEAD_DIM), 0.1),
        'da_lk1': nrm((N_EVEN, DA_HEAD_DIM), 0.1),
        'da_lq2': nrm((N_EVEN, DA_HEAD_DIM), 0.1),
        'da_lk2': nrm((N_EVEN, DA_HEAD_DIM), 0.1),
        'da_subln_g': gain((N_EVEN, DA_V_DIM)),
        'od_w_in': nrm((N_ODD, D_MODEL, ODD_IN), D_MODEL ** -0.5),
        'od_w_out': nrm((N_ODD, ODD_OUT, D_MODEL), ODD_OUT ** -0.5),
        'pool_w': nrm((N_ODD, POOL_GROUPS, POOL_GROUP_DIM, POOL_GROUP_DIM), POOL_GROUP_DIM ** -0.5),
        'pool_scale': gain((N_ODD, POOL_WIDTH)),
        'ret_decay_f': base_decay + nrm((N_ODD, RET_HEADS), 0.1),
        'ret_decay_b': base_decay + nrm((N_ODD, RET_HEADS), 0.1),
        'ret_gn_g': gain((N_ODD, RET_V_DIM)),
        'ffn_w_up': nrm((DEPTH, D_MODEL, 2 * FFN_DIM), D_MODEL ** -0.5),
        'ffn_conv_w': nrm((DEPTH, 3, FFN_DIM), 3 ** -0.5),
        'ffn_conv_b': nrm((DEPTH, FFN_DIM), 0.01),
        'ffn_w_down': nrm((DEPTH, FFN_DIM, D_MODEL), FFN_DIM ** -0.5),
    }

def first_block(x, c, ctx, c_ctx, mod_w, mod_b, norm1_g, norm2_g, ev_w_in, ev_w_out, sc_conv_w, da_q_norm, da_k_norm,
              da_lq1, da_lk1, da_lq2, da_lk2, da_subln_g, od_w_in, od_w_out, pool_w, pool_scale, ret_decay_f,
              ret_decay_b, ret_gn_g, ffn_w_up, ffn_conv_w, ffn_conv_b, ffn_w_down):
    ROWS = x.shape[1] // GRID_W
    cos, sin = rope_tables(ROWS)
    silu_c = jax.nn.silu(c)
    silu_cc = jax.nn.silu(c_ctx)
    for i in range(DEPTH):
        last = i == DEPTH - 1
        j = i // 2
        mod_l = (silu_c @ mod_w[i] + mod_b[i])[:, None, :]
        mod_c = silu_cc @ mod_w[i] + mod_b[i]
        sh1, sc1, g1, sh2, sc2, g2 = jnp.split(mod_l, 6, axis=-1)
        sh1c, sc1c, g1c, sh2c, sc2c, g2c = jnp.split(mod_c, 6, axis=-1)
        h_lat = modulate(rms_norm(x, norm1_g[i]), sh1, sc1)
        h_ctx = modulate(rms_norm(ctx, norm1_g[i]), sh1c, sc1c)
        if i % 2 == 0:
            y_ctx, y_lat = conv_diff_mixer(h_ctx, h_lat, ev_w_in[j], ev_w_out[j], sc_conv_w[j], da_q_norm[j],
                                           da_k_norm[j], da_lq1[j], da_lk1[j], da_lq2[j], da_lk2[j],
                                           da_subln_g[j], diff_lambda_init(i), cos, sin)
        else:
            y_ctx, y_lat = pool_retention_mixer(h_ctx, h_lat, od_w_in[j], od_w_out[j], pool_w[j], pool_scale[j],
                                                ret_decay_f[j], ret_decay_b[j], ret_gn_g[j], cos, sin, not last)
        x = x + g1 * y_lat
        x = x + g2 * conv_ffn(modulate(rms_norm(x, norm2_g[i]), sh2, sc2),
                              ffn_w_up[i], ffn_conv_w[i], ffn_conv_b[i], ffn_w_down[i])
        if not last:
            ctx = ctx + g1c * y_ctx
            ctx = ctx + g2c * conv_ffn(modulate(rms_norm(ctx, norm2_g[i]), sh2c, sc2c),
                                       ffn_w_up[i], ffn_conv_w[i], ffn_conv_b[i], ffn_w_down[i])
    return x


DEPTH_2 = 4

N_MIXERS = 3
CHUNK = 64
LN_EPS = 1e-5
RMS_EPS = 1e-6
L2_EPS = 1e-6
DN_ALPHA = (2 * DEPTH_2) ** 0.25
DN_BETA = (8 * DEPTH_2) ** -0.25
D_FF = ((8 * D_MODEL + 3 * 256 - 1) // (3 * 256)) * 256

GDN_DK = 128
GDN_DV = 128
GDN_HEADS = D_MODEL // GDN_DK
GDN_KEY = GDN_HEADS * GDN_DK
GDN_VAL = GDN_HEADS * GDN_DV
GDN_CONV = 4
GDN_QKV = 2 * GDN_KEY + GDN_VAL
GDN_IN = GDN_QKV + GDN_VAL + 2 * GDN_HEADS

HGRN_DK = 128
HGRN_HEADS = D_MODEL // HGRN_DK
HGRN_DV = D_MODEL // HGRN_HEADS
HGRN_IN = 4 * D_MODEL

GLA_HEADS = 4
GLA_KEY = D_MODEL // 2
GLA_DK = GLA_KEY // GLA_HEADS
GLA_VAL = D_MODEL
GLA_DV = GLA_VAL // GLA_HEADS
GLA_RANK = 16
GLA_TAU = 16.0
GLA_IN = 2 * GLA_KEY + 2 * GLA_VAL + GLA_RANK

N_GDN = (DEPTH_2 + 2) // 3
N_HGRN = (DEPTH_2 + 1) // 3
N_GLA = DEPTH_2 // 3


F32 = jnp.float32

def layer_norm(x, g, b):
    xf = x.astype(F32)
    mu = jnp.mean(xf, -1, keepdims=True)
    var = jnp.mean(jnp.square(xf - mu), -1, keepdims=True)
    return ((xf - mu) * lax.rsqrt(var + LN_EPS) * g + b).astype(x.dtype)

def gated_rms_norm(o, gate, w):
    of = o.astype(F32)
    y = of * lax.rsqrt(jnp.mean(of * of, -1, keepdims=True) + RMS_EPS) * w
    return y * jax.nn.silu(gate.astype(F32))

def l2_normalize(t):
    t = t.astype(F32)
    return t * lax.rsqrt(jnp.sum(t * t, -1, keepdims=True) + L2_EPS)

def causal_depthwise_conv(x, w):
    K, C = w.shape
    return lax.conv_general_dilated(
        x, w[:, None, :].astype(x.dtype), window_strides=(1,), padding=[(K - 1, 0)],
        dimension_numbers=('NWC', 'WIO', 'NWC'), feature_group_count=C)

def to_chunks(t):
    B, T, H = t.shape[:3]
    return jnp.moveaxis(t.reshape(B, T // CHUNK, CHUNK, H, *t.shape[3:]), 3, 1)

def from_chunks(t):
    B, H, N, C, d = t.shape
    return jnp.moveaxis(t, 1, 3).reshape(B, N * C, H, d)

def lead(t):
    return jnp.moveaxis(t, 2, 0)

def chunk_gated_delta_rule(q, k, v, beta, g):
    B, T, H, dk = q.shape
    dv = v.shape[-1]
    q, k, v = to_chunks(q.astype(F32)), to_chunks(k.astype(F32)), to_chunks(v.astype(F32))
    beta, g = to_chunks(beta.astype(F32)), to_chunks(g.astype(F32))
    G = jnp.cumsum(g, axis=-1)
    incl = jnp.tril(jnp.ones((CHUNK, CHUNK), bool))
    strict = jnp.tril(jnp.ones((CHUNK, CHUNK), bool), -1)
    decay = jnp.exp(jnp.where(incl, G[..., :, None] - G[..., None, :], -jnp.inf))
    kb = k * beta[..., None]
    L = jnp.where(strict, jnp.einsum('bhncd,bhnsd->bhncs', kb, k) * decay, 0.0)
    rhs = jnp.concatenate([v * beta[..., None], kb * jnp.exp(G)[..., None]], axis=-1)
    sol = lax.linalg.triangular_solve(L + jnp.eye(CHUNK, dtype=F32), rhs, left_side=True, lower=True)
    u, w = sol[..., :dv], sol[..., dv:]
    a_qk = jnp.einsum('bhncd,bhnsd->bhncs', q, k) * decay
    q_dec = q * jnp.exp(G)[..., None]
    G_last = G[..., -1:]
    k_dec = k * jnp.exp(G_last - G)[..., None]
    g_last = jnp.exp(G_last[..., 0])

    def step(S, inp):
        u_c, w_c, a_c, q_c, k_c, gl_c = inp
        v_new = u_c - jnp.einsum('bhcd,bhde->bhce', w_c, S)
        o_c = jnp.einsum('bhcd,bhde->bhce', q_c, S) + jnp.einsum('bhcs,bhse->bhce', a_c, v_new)
        S = S * gl_c[..., None, None] + jnp.einsum('bhcd,bhce->bhde', k_c, v_new)
        return S, o_c

    S0 = jnp.zeros((B, H, dk, dv), F32)
    _, o = lax.scan(step, S0, (lead(u), lead(w), lead(a_qk), lead(q_dec), lead(k_dec), lead(g_last)))
    return from_chunks(jnp.moveaxis(o, 0, 2))

def chunk_gla(q, k, v, g):
    B, T, H, dk = q.shape
    dv = v.shape[-1]
    q, k, v, g = (to_chunks(t.astype(F32)) for t in (q, k, v, g))
    G = jnp.cumsum(g, axis=-2)
    G_last = G[..., -1:, :]
    q_dec = q * jnp.exp(G)
    k_dec = k * jnp.exp(G_last - G)
    g_last = jnp.exp(G_last)
    incl = jnp.tril(jnp.ones((CHUNK, CHUNK), bool))[..., None]

    def step(S, inp):
        q_c, k_c, v_c, G_c, qd_c, kd_c, gl_c = inp
        rel = jnp.exp(jnp.where(incl, G_c[..., :, None, :] - G_c[..., None, :, :], -jnp.inf))
        a = jnp.einsum('bhcd,bhsd,bhcsd->bhcs', q_c, k_c, rel)
        o_c = jnp.einsum('bhcd,bhde->bhce', qd_c, S) + jnp.einsum('bhcs,bhse->bhce', a, v_c)
        S = S * gl_c[..., 0, :, None] + jnp.einsum('bhcd,bhce->bhde', kd_c, v_c)
        return S, o_c

    S0 = jnp.zeros((B, H, dk, dv), F32)
    xs = (lead(q), lead(k), lead(v), lead(G), lead(q_dec), lead(k_dec), lead(g_last))
    _, o = lax.scan(step, S0, xs)
    return from_chunks(jnp.moveaxis(o, 0, 2))

def gated_deltanet(x, w_in, conv_w, a_log, dt_bias, norm_w, w_out):
    B, T, _ = x.shape
    p = x @ w_in
    qkv, z, b, a = jnp.split(p, [GDN_QKV, GDN_QKV + GDN_VAL, GDN_QKV + GDN_VAL + GDN_HEADS], axis=-1)
    qkv = jax.nn.silu(causal_depthwise_conv(qkv, conv_w))
    q, k, v = jnp.split(qkv, [GDN_KEY, 2 * GDN_KEY], axis=-1)
    q = l2_normalize(q.reshape(B, T, GDN_HEADS, GDN_DK)) * (GDN_DK ** -0.5)
    k = l2_normalize(k.reshape(B, T, GDN_HEADS, GDN_DK))
    v = v.reshape(B, T, GDN_HEADS, GDN_DV)
    beta = jax.nn.sigmoid(b.astype(F32))
    g = -jnp.exp(a_log.astype(F32)) * jax.nn.softplus(a.astype(F32) + dt_bias.astype(F32))
    o = chunk_gated_delta_rule(q, k, v, beta, g)
    o = gated_rms_norm(o, z.reshape(B, T, GDN_HEADS, GDN_DV), norm_w.astype(F32))
    return o.reshape(B, T, GDN_VAL).astype(x.dtype) @ w_out

def hgrn2(x, w_in, lb, norm_w, w_out):
    B, T, _ = x.shape
    q, f, i, r = jnp.split(x @ w_in, 4, axis=-1)
    q = jax.nn.silu(q.astype(F32)).reshape(B, T, HGRN_HEADS, HGRN_DK) * (HGRN_DK ** -0.5)
    log_f = jnp.logaddexp(jnp.log(lb), jnp.log1p(-lb) + jax.nn.log_sigmoid(f.astype(F32)))
    k = -jnp.expm1(log_f)
    shp_k = (B, T, HGRN_HEADS, HGRN_DK)
    o = chunk_gla(q, k.reshape(shp_k), i.reshape(B, T, HGRN_HEADS, HGRN_DV), log_f.reshape(shp_k))
    o = gated_rms_norm(o, r.reshape(B, T, HGRN_HEADS, HGRN_DV), norm_w.astype(F32))
    return o.reshape(B, T, D_MODEL).astype(x.dtype) @ w_out

def gla(x, w_in, w_gk2, b_gk, norm_w, w_out):
    B, T, _ = x.shape
    q, k, v, r, gk = jnp.split(x @ w_in, [GLA_KEY, 2 * GLA_KEY, 2 * GLA_KEY + GLA_VAL, 2 * GLA_KEY + 2 * GLA_VAL], axis=-1)
    g = jax.nn.log_sigmoid((gk @ w_gk2 + b_gk).astype(F32)) / GLA_TAU
    shp_k = (B, T, GLA_HEADS, GLA_DK)
    q = q.astype(F32).reshape(shp_k) * (GLA_DK ** -0.5)
    o = chunk_gla(q, k.reshape(shp_k), v.reshape(B, T, GLA_HEADS, GLA_DV), g.reshape(shp_k))
    o = gated_rms_norm(o, r.reshape(B, T, GLA_HEADS, GLA_DV), norm_w.astype(F32))
    return o.reshape(B, T, GLA_VAL).astype(x.dtype) @ w_out

def swiglu(x, w_in, w_down):
    gate, up = jnp.split(x @ w_in, 2, axis=-1)
    return (jax.nn.silu(gate) * up) @ w_down

def second_inputs(seed: int = 0) -> dict:
    key = jax.random.key(seed)
    ks = jax.random.split(key, 22)
    nrm = lambda k, shape, s: jax.random.normal(k, shape, F32) * s
    x = jax.random.normal(ks[0], (BATCH, SEQ, D_MODEL), F32)
    gdn_w_in = nrm(ks[1], (N_GDN, D_MODEL, GDN_IN), D_MODEL ** -0.5)
    gdn_conv_w = nrm(ks[2], (N_GDN, GDN_CONV, GDN_QKV), GDN_CONV ** -0.5)
    gdn_a_log = jnp.log(jax.random.uniform(ks[3], (N_GDN, GDN_HEADS), F32, 1.0, 16.0))
    dt = jnp.exp(jax.random.uniform(ks[4], (N_GDN, GDN_HEADS), F32, math.log(1e-3), math.log(1e-1)))
    gdn_dt_bias = dt + jnp.log(-jnp.expm1(-dt))
    gdn_norm_w = 1.0 + nrm(ks[5], (N_GDN, GDN_DV), 0.02)
    gdn_w_out = nrm(ks[6], (N_GDN, GDN_VAL, D_MODEL), GDN_VAL ** -0.5 * DN_BETA)
    hgrn_w_in = nrm(ks[7], (N_HGRN, D_MODEL, HGRN_IN), D_MODEL ** -0.5)
    hgrn_lb_logits = nrm(ks[8], (DEPTH_2, HGRN_HEADS * HGRN_DK), 0.5)
    hgrn_norm_w = 1.0 + nrm(ks[9], (N_HGRN, HGRN_DV), 0.02)
    hgrn_w_out = nrm(ks[10], (N_HGRN, D_MODEL, D_MODEL), D_MODEL ** -0.5 * DN_BETA)
    gla_w_in = nrm(ks[11], (N_GLA, D_MODEL, GLA_IN), D_MODEL ** -0.5)
    gla_w_gk2 = nrm(ks[12], (N_GLA, GLA_RANK, GLA_KEY), GLA_RANK ** -0.5)
    gla_b_gk = nrm(ks[13], (N_GLA, GLA_KEY), 0.1)
    gla_norm_w = 1.0 + nrm(ks[14], (N_GLA, GLA_DV), 0.02)
    gla_w_out = nrm(ks[15], (N_GLA, GLA_VAL, D_MODEL), GLA_VAL ** -0.5 * DN_BETA)
    mix_ln_g = 1.0 + nrm(ks[16], (DEPTH_2, D_MODEL), 0.02)
    mix_ln_b = nrm(ks[17], (DEPTH_2, D_MODEL), 0.02)
    ffn_w_in = nrm(ks[18], (DEPTH_2, D_MODEL, 2 * D_FF), D_MODEL ** -0.5)
    ffn_w_down = nrm(ks[19], (DEPTH_2, D_FF, D_MODEL), D_FF ** -0.5 * DN_BETA)
    ffn_ln_g = 1.0 + nrm(ks[20], (DEPTH_2, D_MODEL), 0.02)
    ffn_ln_b = nrm(ks[21], (DEPTH_2, D_MODEL), 0.02)
    return {"x": x, "gdn_w_in": gdn_w_in, "gdn_conv_w": gdn_conv_w, "gdn_a_log": gdn_a_log,
            "gdn_dt_bias": gdn_dt_bias, "gdn_norm_w": gdn_norm_w, "gdn_w_out": gdn_w_out,
            "hgrn_w_in": hgrn_w_in, "hgrn_lb_logits": hgrn_lb_logits, "hgrn_norm_w": hgrn_norm_w,
            "hgrn_w_out": hgrn_w_out, "gla_w_in": gla_w_in, "gla_w_gk2": gla_w_gk2, "gla_b_gk": gla_b_gk,
            "gla_norm_w": gla_norm_w, "gla_w_out": gla_w_out, "mix_ln_g": mix_ln_g, "mix_ln_b": mix_ln_b,
            "ffn_w_in": ffn_w_in, "ffn_w_down": ffn_w_down, "ffn_ln_g": ffn_ln_g, "ffn_ln_b": ffn_ln_b}

def second_block(x, gdn_w_in, gdn_conv_w, gdn_a_log, gdn_dt_bias, gdn_norm_w, gdn_w_out,
              hgrn_w_in, hgrn_lb_logits, hgrn_norm_w, hgrn_w_out,
              gla_w_in, gla_w_gk2, gla_b_gk, gla_norm_w, gla_w_out,
              mix_ln_g, mix_ln_b, ffn_w_in, ffn_w_down, ffn_ln_g, ffn_ln_b):
    lb_soft = jax.nn.softmax(hgrn_lb_logits.astype(F32), axis=0)
    lb_all = jnp.cumsum(lb_soft, axis=0) - lb_soft[0]
    for i in range(DEPTH_2):
        kind, j = i % N_MIXERS, i // N_MIXERS
        if kind == 0:
            m = gated_deltanet(x, gdn_w_in[j], gdn_conv_w[j], gdn_a_log[j], gdn_dt_bias[j], gdn_norm_w[j], gdn_w_out[j])
        elif kind == 1:
            m = hgrn2(x, hgrn_w_in[j], lb_all[i], hgrn_norm_w[j], hgrn_w_out[j])
        else:
            m = gla(x, gla_w_in[j], gla_w_gk2[j], gla_b_gk[j], gla_norm_w[j], gla_w_out[j])
        x = layer_norm(DN_ALPHA * x + m, mix_ln_g[i], mix_ln_b[i])
        x = layer_norm(DN_ALPHA * x + swiglu(x, ffn_w_in[i], ffn_w_down[i]), ffn_ln_g[i], ffn_ln_b[i])
    return x


def setup_inputs(seed=0):
    out = dict(first_inputs(seed))
    for name, value in second_inputs(seed + 1).items():
        if name != "x":
            out[name + "_2"] = value
    return out


def reference(
    x, c, ctx, c_ctx, mod_w, mod_b, norm1_g, norm2_g, ev_w_in, ev_w_out, sc_conv_w, da_q_norm,
    da_k_norm, da_lq1, da_lk1, da_lq2, da_lk2, da_subln_g, od_w_in, od_w_out, pool_w,
    pool_scale, ret_decay_f, ret_decay_b, ret_gn_g, ffn_w_up, ffn_conv_w, ffn_conv_b,
    ffn_w_down, gdn_w_in_2, gdn_conv_w_2, gdn_a_log_2, gdn_dt_bias_2, gdn_norm_w_2, gdn_w_out_2,
    hgrn_w_in_2, hgrn_lb_logits_2, hgrn_norm_w_2, hgrn_w_out_2, gla_w_in_2, gla_w_gk2_2,
    gla_b_gk_2, gla_norm_w_2, gla_w_out_2, mix_ln_g_2, mix_ln_b_2, ffn_w_in_2, ffn_w_down_2,
    ffn_ln_g_2, ffn_ln_b_2,
):
    x = first_block(
        x, c, ctx, c_ctx, mod_w, mod_b, norm1_g, norm2_g, ev_w_in, ev_w_out, sc_conv_w,
        da_q_norm, da_k_norm, da_lq1, da_lk1, da_lq2, da_lk2, da_subln_g, od_w_in, od_w_out,
        pool_w, pool_scale, ret_decay_f, ret_decay_b, ret_gn_g, ffn_w_up, ffn_conv_w,
        ffn_conv_b, ffn_w_down,
    )
    return second_block(
        x, gdn_w_in_2, gdn_conv_w_2, gdn_a_log_2, gdn_dt_bias_2, gdn_norm_w_2, gdn_w_out_2,
        hgrn_w_in_2, hgrn_lb_logits_2, hgrn_norm_w_2, hgrn_w_out_2, gla_w_in_2, gla_w_gk2_2,
        gla_b_gk_2, gla_norm_w_2, gla_w_out_2, mix_ln_g_2, mix_ln_b_2, ffn_w_in_2, ffn_w_down_2,
        ffn_ln_g_2, ffn_ln_b_2,
    )


_drawn_inputs = setup_inputs


def setup_inputs(seed=0):
    import zlib

    import numpy as np

    out = dict(_drawn_inputs(seed))
    spreads = {}
    factors = {'da_q_norm': 8.0,
     'da_k_norm': 8.0,
     'da_lq1': 8.0,
     'da_lk1': 8.0,
     'da_lq2': 8.0,
     'da_lk2': 8.0,
     'da_subln_g': 5.304,
     'pool_scale': 5.709,
     'ret_gn_g': 8.0,
     'ffn_conv_b': 8.0,
     'gdn_norm_w_2': 8.0,
     'hgrn_lb_logits_2': 8.0,
     'hgrn_norm_w_2': 8.0,
     'gla_w_gk2_2': 3.185,
     'gla_b_gk_2': 8.0,
     'gla_norm_w_2': 22.282}
    for name, (base, spread) in spreads.items():
        noise = np.random.default_rng([zlib.crc32(name.encode()), seed]).standard_normal(out[name].shape)
        drawn = base * np.exp(spread * noise) if base else spread * noise
        out[name] = __import__('jax').numpy.asarray(drawn.astype(out[name].dtype))
    for name, factor in factors.items():
        out[name] = (out[name] * factor).astype(out[name].dtype)
    return out
```

```python
from collections import deque
from contextlib import ExitStack

import numpy as np

import concourse.bass as bass
from concourse import mybir

P = 128
D = 1024
KT = D // P
F = 2816
FT = F // P
T = 256
CW = 2048
UW = 1024
NRAW = 3
NHL = 5
LEAD = 3
EPS = 1e-6
LN_EPS = 1e-5
DN_ALPHA = 8.0 ** 0.25
LAM_INIT = 0.2

F32 = mybir.dt.float32
F32R = mybir.dt.float32r
BF16 = mybir.dt.bfloat16
U32 = mybir.dt.uint32
ALU = mybir.AluOpType
ACT = mybir.ActivationFunctionType
AX = mybir.AxisListType.X



def weight_chunks():
    out = [("m", 0, i) for i in range(8)]
    qkv = [("w", "ev_qkv", i) for i in range(6)]
    conv = [("w", "ev_conv", i) for i in range(6)]
    m0 = [("m", 0, i) for i in range(8, 20)]
    body = qkv + conv
    for i, w in enumerate(body):
        out.append(w)
        out.append(m0[i])
    out += [("w", "ev_out", i) for i in range(4)]
    later = [("m", 0, i) for i in range(20, 24)] + [("m", 1, i) for i in range(24)]
    for i in range(FT):
        out.append(("w", "up0", i))
        if later:
            out.append(later.pop(0))
    for i in range(FT // 2):
        out.append(("w", "down0", i))
        if later:
            out.append(later.pop(0))
    assert not later
    out += [("w", "od_in", i) for i in range(8)]
    out += [("w", "od_out", i) for i in range(4)]
    out += [("w", "up1", i) for i in range(FT)]
    out += [("w", "down1", i) for i in range(FT // 2)]
    mixers = [[(f"gdn0_{c}", 4) for c in "kqvz"] + [("gdn0_out", 4)],
              [(f"hg_{c}", 4) for c in "fqir"] + [("hg_out", 4)],
              [("gla_q", 2), ("gla_k", 2), ("gla_v", 4), ("gla_r", 4), ("gla_out", 4)],
              [(f"gdn1_{c}", 4) for c in "kqvz"] + [("gdn1_out", 4)]]
    for l in range(4):
        for key, n in mixers[l] + [(f"fin{l}", FT), (f"fdn{l}", FT // 2)]:
            out += [("w", key, i) for i in range(n)]
    return out


CORE = [("ident", 128), ("n1", 16), ("n2", 16), ("modb", 96), ("fcw", 132), ("fcb", 44), ("scw", 12),
        ("psc", 4)]
B1 = [("qg", 64), ("kg", 64), ("lq1", 64), ("lk1", 64), ("lq2", 64), ("lk2", 64), ("subg", 128),
      ("ropec", 128), ("ropes", 128), ("rgn", 128), ("decf", 4), ("decb", 4), ("ramps", 8)]
L1C = [("dist_f", 512), ("dist_b", 512), ("two", 512), ("band", 2048), ("poolw", 512)]

C2 = [("U", 128), ("SL", 128), ("ones", 128), ("mT", 896), ("mL", 896), ("gcw", 192), ("lbl", 32), ("alog", 16),
      ("dtb", 16), ("gnw", 256), ("hgn", 128), ("gln", 256), ("wba", 256), ("wgk", 128), ("wgk2", 512)]


def offsets(fields):
    at, out = 0, {}
    for name, n in fields:
        out[name] = (at, n)
        at += n
    return out, at


class Core:

    def __init__(self, nc, ctx):
        self.nc = nc
        self.ctx = ctx
        self.eng = {"pe": nc.tensor, "v": nc.vector, "a": nc.scalar, "g": nc.gpsimd, "sp": nc.sync}
        self.sem = {e: ctx.enter_context(nc.semaphore("s_" + e)) for e in self.eng}
        self.by_name = {"s_" + e: s for e, s in self.sem.items()}
        self.n = {e: 0 for e in self.eng}
        self.seen = {e: {} for e in self.eng}
        self.ps = [ctx.enter_context(nc.psum_tensor(f"ps{i}", [P, 512], F32)) for i in range(8)]
        self.bfree = [[] for _ in range(8)]
        self.idle = deque(range(8))
        self.bg = deque()
        self.ndma = 0
        self.ntensor = 0

    def dma_sem(self, name):
        s = self.ctx.enter_context(self.nc.semaphore(name))
        self.by_name[name] = s
        return name

    def wait(self, e, w):
        if w is None:
            return
        if isinstance(w, tuple) and len(w) == 2 and isinstance(w[0], str):
            name, val = w
            if self.seen[e].get(name, 0) < val:
                self.eng[e].wait_ge(self.by_name[name], val)
                self.seen[e][name] = val
            return
        for x in w:
            self.wait(e, x)

    def done(self, e, ins):
        self.n[e] += 1
        ins.then_inc(self.sem[e], 1)
        return ("s_" + e, self.n[e])

    def v(self, f, *a, w=(), **kw):
        self.wait("v", w)
        return self.done("v", f(*a, **kw))

    def a(self, f, *a, w=(), **kw):
        self.wait("a", w)
        return self.done("a", f(*a, **kw))

    def g(self, f, *a, w=(), **kw):
        self.wait("g", w)
        return self.done("g", f(*a, **kw))

    def mm(self, out, lhsT, rhs, start, stop, w=(), inc=False):
        self.wait("pe", w)
        ins = self.nc.tensor.matmul(out, lhsT, rhs, start=start, stop=stop)
        return self.done("pe", ins) if inc else None

    def tr(self, out, in_, ident, w=(), inc=False):
        self.wait("pe", w)
        ins = self.nc.tensor.transpose(out, in_, ident)
        return self.done("pe", ins) if inc else None

    def dma(self, e, out, in_, w=()):
        name = self.dma_sem(f"d{self.ndma}")
        self.ndma += 1
        self.wait(e, w)
        self.eng[e].dma_start(out, in_).then_inc(self.by_name[name], 16)
        return (name, 16)

    def last(self):
        return [("s_" + e, self.n[e]) for e in ("pe", "v", "a", "g")]

    def fence(self):
        now = self.last()
        for e in ("pe", "v", "a", "g"):
            self.wait(e, [t for t in now if t[0] != "s_" + e])

    def bank(self):
        b = self.idle.popleft()
        self.wait("pe", self.bfree[b])
        return b

    def close(self, b, toks):
        self.bfree[b] = toks
        self.idle.append(b)

    def tick(self, n=1):
        for _ in range(n):
            while self.bg:
                try:
                    next(self.bg[0])
                    break
                except StopIteration:
                    self.bg.popleft()

    def drain(self):
        while self.bg:
            self.tick()


class Scope:
    def __init__(self, k):
        self.k = k
        self.st = ExitStack()

    def __enter__(self):
        return self

    def sb(self, name, shape, dt=F32):
        self.k.ntensor += 1
        return self.st.enter_context(self.k.nc.sbuf_tensor(f"{name}_{self.k.ntensor}", shape, dt))

    def __exit__(self, *failed):
        if not any(failed):
            self.st.close()
            self.k.fence()


class Stream:

    def __init__(self, k, W, plan):
        self.k, self.W, self.plan, self.on_mod = k, W, plan, None
        nc = k.nc
        self.raw = k.ctx.enter_context(nc.sbuf_tensor("raw", [P, NRAW, CW], F32))
        self.hi = k.ctx.enter_context(nc.sbuf_tensor("whi", [P, NHL, UW], F32R))
        self.lo = k.ctx.enter_context(nc.sbuf_tensor("wlo", [P, NHL, UW], F32R))
        self.sems = [k.dma_sem(f"w{i}") for i in range(NRAW)]
        self.units = []
        for j, (kind, key, i) in enumerate(plan):
            self.units += [(j, 0), (j, 1)] if kind == "w" else [(j, None)]
        self.keys = [plan[j][1] for j, h in self.units if h is not None]
        self.pos = 0
        self.made = 0
        self.tok = {}
        self.freed = {}
        self.nfreed = 0
        self.taken = 0
        for j in range(NRAW):
            self.load(j, ())

    def load(self, j, w):
        if j < len(self.plan):
            s = j % NRAW
            self.k.wait("sp", w)
            self.k.nc.sync.dma_start(self.raw[:, s], self.W[j]).then_inc(self.k.by_name[self.sems[s]], 16)

    def landed(self, j):
        return (self.sems[j % NRAW], 16 * (j // NRAW + 1))

    def pump(self, upto):
        k, nc = self.k, self.k.nc
        while self.pos < len(self.units):
            j, h = self.units[self.pos]
            s = j % NRAW
            if h is None:
                if self.made > upto:
                    break
                t = self.on_mod(self.plan[j], self.raw[:, s], self.landed(j))
                self.load(j + NRAW, t)
            else:
                u = self.made
                if u > upto or u - NHL >= self.nfreed:
                    break
                q = u % NHL
                old = self.freed[u - NHL] if u >= NHL else None
                src = self.raw[:, s, h * UW:(h + 1) * UW]
                ta = k.a(nc.scalar.copy, self.hi[:, q], src, w=[self.landed(j), old])
                tv = k.v(nc.vector.tensor_tensor, self.lo[:, q], src, self.hi[:, q].bitcast(F32),
                         op=ALU.subtract, w=[ta])
                self.tok[u] = [ta, tv]
                if h == 1:
                    self.load(j + NRAW, [ta, tv])
                self.made += 1
            self.pos += 1

    def take(self, key):
        u = self.taken
        assert self.keys[u] == key, (u, self.keys[u], key)
        self.pump(u + LEAD)
        assert self.made > u
        self.taken += 1
        return u

    def parts(self, u):
        return self.hi[:, u % NHL], self.lo[:, u % NHL], self.tok[u]

    def free(self, u, tok):
        assert u == self.nfreed
        self.freed[u] = tok
        self.nfreed += 1
        self.pump(self.taken - 1 + LEAD)


def as3(k, out, xh, xl, wh, wl, first, last, w=(), inc=False):
    k.mm(out, xh, wh, first, False, w=w)
    k.mm(out, xh, wl, False, False)
    return k.mm(out, xl, wh, False, last, inc=inc)


def ws3(k, out, wh, wl, xh, xl, first, last, w=(), inc=False):
    k.mm(out, wh, xh, first, False, w=w)
    k.mm(out, wh, xl, False, False)
    return k.mm(out, wl, xh, False, last, inc=inc)


def ws_tile(k, st, key, H, htok, ntok):
    u = st.take(key)
    wh, wl, wt = st.parts(u)
    b = k.bank()
    out = k.ps[b][:, 0:ntok]
    t = None
    for kt in range(KT):
        c = slice(kt * P, (kt + 1) * P)
        t = ws3(k, out, wh[:, c], wl[:, c], H[0][:, kt, 0:ntok], H[1][:, kt, 0:ntok], kt == 0, kt == KT - 1,
                w=[wt, htok] if kt == 0 else (), inc=kt == KT - 1)
    st.free(u, t)
    return b, t


def as_group(k, st, key, H, htok, tiles, cols=(0, 512), evac=None):
    us = []
    for i in range(KT // 2):
        us.append(st.take(key))
    wts = [st.parts(u) for u in us]
    for n, tile in enumerate(tiles):
        lo, hi = cols[tile] if isinstance(cols, dict) else cols
        b = k.bank()
        out = k.ps[b][:, 0:hi - lo]
        for kt in range(KT):
            wh, wl, wt = wts[kt // 2]
            c = slice((kt % 2) * 512 + lo, (kt % 2) * 512 + hi)
            x = slice(tile * P, (tile + 1) * P)
            t = as3(k, out, H[0][:, kt, x], H[1][:, kt, x], wh[:, c], wl[:, c], kt == 0, kt == KT - 1,
                    w=[wt, htok[tile]], inc=kt == KT - 1 or (n == len(tiles) - 1 and kt % 2 == 1))
            if n == len(tiles) - 1 and kt % 2 == 1:
                st.free(us[kt // 2], t)
        evac(tile, b, t)
        k.tick()


def down(k, st, key, nk, x, xtok, evac):
    bs = [[k.bank(), k.bank()] for _ in range(2)]
    us = {}

    def part(kt, tile):
        wh, wl, wt = st.parts(us[kt])
        xh, xl = x(kt, tile)
        for hf in range(2):
            c = slice(hf * 512, (hf + 1) * 512)
            t = as3(k, k.ps[bs[tile][hf]][:, :], xh, xl, wh[:, c], wl[:, c], kt == 0, kt == nk - 1,
                    w=[wt, xtok(kt)], inc=hf == 1 or kt == nk - 1)
            if kt == nk - 1:
                evac(tile, hf, bs[tile][hf], t)
        return t

    held = 2
    for kt in range(nk - held):
        us[kt] = st.take(key)
        part(kt, 0)
        st.free(us[kt], part(kt, 1))
        k.tick()
    for kt in range(nk - held, nk):
        us[kt] = st.take(key)
        part(kt, 0)
    for kt in range(nk - held, nk):
        st.free(us[kt], part(kt, 1))


def split_bank(k, src, hi, lo, w):
    ta = k.a(k.nc.scalar.copy, hi, src, w=w)
    tv = k.v(k.nc.vector.tensor_tensor, lo, src, hi.bitcast(F32), op=ALU.subtract, w=[ta])
    return ta, tv


def fused_block(nc, W, x_in, ctx_in, c_in, cc_in, core_in, b1_in, l1_in, c2_in, ln_in, mexp_in, out, stop=99):
    with ExitStack() as ctx:
        k = Core(nc, ctx)
        V, A, G = nc.vector, nc.scalar, nc.gpsimd
        plan = weight_chunks()
        CO, ncore = offsets(CORE)
        core = ctx.enter_context(nc.sbuf_tensor("core", [P, ncore], F32))
        xt = ctx.enter_context(nc.sbuf_tensor("xt", [P, 4, D], F32))
        half = ctx.enter_context(nc.sbuf_tensor("half", [P, 64], F32))

        st = Stream(k, W, plan)

        def C(name, i=0, n=None):
            at, size = CO[name]
            return core[:, at + i:at + (i + n if n else size)]

        ident = C("ident")

        def finish(xt, toks):
            k.wait("sp", [k.dma("sp", out[i], xt[:, i], w=toks) for i in range(2)])

        def ffn_up(s, key, H, htok, hh, hl, layer):
            ab = s.sb("ab", [P, 2, T])
            sg = s.sb("sg", [P, 2, T])
            hid = s.sb("hid", [P, 2, T])
            t_ab, t_sg, t_hid = {}, {}, {}
            for f in range(FT):
                i = f % 2
                b, t = ws_tile(k, st, key, H, htok, T)
                ps = k.ps[b][:, 0:T]
                if layer is None:
                    t_sg[f] = k.a(A.activation, sg[:, i], ps, ACT.Silu, w=[t, t_ab.get(f - 2)])
                    k.close(b, [t_sg[f]])
                else:
                    w_ = [C("fcw", layer * 66 + tap * 22 + f, 1) for tap in range(3)]
                    ta = k.a(A.activation, ab[:, i], ps, ACT.Identity, bias=C("fcb", layer * 22 + f, 1), scale=w_[1],
                             w=[t, t_sg.get(f - 2)])
                    tv = k.v(V.scalar_tensor_tensor, ab[:, i, 1:T], ps[:, 0:T - 1], w_[0], ab[:, i, 1:T], ALU.mult,
                             ALU.add, w=[ta])
                    tv = k.v(V.scalar_tensor_tensor, ab[:, i, 0:T - 1], ps[:, 1:T], w_[2], ab[:, i, 0:T - 1], ALU.mult,
                             ALU.add, w=[tv])
                    k.close(b, [tv])
                    t_sg[f] = k.a(A.activation, sg[:, i], ab[:, i], ACT.Silu, w=[tv, t_ab.get(f - 2)])
                k.tick()
                b, t = ws_tile(k, st, key, H, htok, T)
                old = t_hid.get(f - 2)
                t_ab[f] = tv = k.v(V.tensor_tensor, hid[:, i], sg[:, i], k.ps[b][:, 0:T], op=ALU.mult,
                                   w=[t, t_sg[f], old])
                k.close(b, [tv])
                ta = k.a(A.copy, hh[:, f], hid[:, i], w=[tv])
                tv = k.v(V.tensor_tensor, hl[:, f], hid[:, i], hh[:, f].bitcast(F32), op=ALU.subtract, w=[ta])
                t_hid[f] = [ta, tv]
                k.tick()
            k.drain()
            return t_hid

        with Scope(k) as s1:
            BO, nb1 = offsets(B1)
            b1 = s1.sb("b1", [P, nb1])
            silu_c = s1.sb("silu_c", [P, 2, D])
            mod = s1.sb("mod", [P, 2, 2, 48])
            gates = [None]
            junk = s1.sb("junk", [P, 2, D], BF16)
            Hh = s1.sb("Hh", [P, KT, 512], F32R)
            Hl = s1.sb("Hl", [P, KT, 512], F32R)
            H = (Hh, Hl)

            def B(name, i=0, n=None):
                at, size = BO[name]
                return b1[:, at + i:at + (i + n if n else size)]

            d_c = [k.dma("a", silu_c[:, i], src.to_broadcast([P, D])) for i, src in enumerate((c_in, cc_in))]
            d_x = [k.dma("a", xt[:, 2 * j + i], src[i]) for j, src in enumerate((x_in, ctx_in)) for i in range(2)]
            d_core = k.dma("a", core[:, :], core_in)
            d_b1 = k.dma("a", b1[:, :], b1_in)
            t_half = k.v(V.memset, half[:, :], -0.5)
            t_silu = [k.a(A.activation, silu_c[:, i], silu_c[:, i], ACT.Silu, w=[d_c[i]]) for i in range(2)]

            t_mod = {}
            t_junk = []
            need = {0: (6, 6), 1: (6, 2)}

            def on_mod(item, raw, landed):
                _, layer, i = item
                toks = []
                for r in range(2):
                    col = 2 * i + r
                    part = col // 8
                    for who in range(2):
                        if part < need[layer][who]:
                            toks.append(k.v(
                                V.tensor_tensor_reduce, out=junk[:, len(t_junk) % 2], in0=raw[:, r * D:(r + 1) * D],
                                in1=silu_c[:, who], scale=1.0, scalar=0.0, op0=ALU.mult, op1=ALU.add,
                                accum_out=mod[:, layer, who, col:col + 1], w=[landed, t_silu, t_junk[-2:-1]]))
                            t_junk.append(toks[-1])
                    t_mod[layer, part] = toks[-1]
                return toks[-1]

            st.on_mod = on_mod

            def mod_part(layer, part, who):
                cols = mod[:, layer, who, part * 8:part * 8 + 8]
                return k.v(V.tensor_tensor, cols, cols, C("modb", layer * 48 + part * 8, 8), op=ALU.add,
                           w=[t_mod[layer, part], d_core])

            def scale_part(layer, part, who, norm):
                t = mod_part(layer, part, who)
                cols = mod[:, layer, who, part * 8:part * 8 + 8]
                return k.v(V.scalar_tensor_tensor, cols, cols, 1.0, C(norm, layer * 8, 8), ALU.add, ALU.mult,
                           w=[t])

            def norm_mod(s, layer, first, norm, tiles, xtok):
                tA, tS = {}, {}
                for who in sorted({t // 2 for t in tiles}):
                    tA[who] = scale_part(layer, first + 1, who, norm)
                    tS[who] = mod_part(layer, first, who)
                stat = s.sb("stat", [P, 3, 4])
                junka = s.sb("junka", [P, 2, D], BF16)
                xh = s.sb("xhat", [P, 2, D])
                tf = s.sb("tf", [P, 2, D])
                rst = {}
                tsq = {}
                for t in tiles:
                    tsq[t] = ts = k.a(A.activation, junka[:, t % 2], xt[:, t], ACT.Square, accum_out=stat[:, 0, t:t + 1],
                                     w=[xtok[t], tsq.get(t - 2)])
                    te = k.g(G.tensor_scalar, stat[:, 1, t:t + 1], stat[:, 0, t:t + 1], 1.0 / D, EPS, ALU.mult,
                             ALU.add, w=[ts])
                    rst[t] = k.g(G.tensor_tensor, stat[:, 2, t:t + 1], stat[:, 1, t:t + 1], half[:, 0:1],
                                 op=ALU.pow, w=[te, t_half])
                tx, ttr, tsp, ttf = {}, {}, {}, {}
                out = {}

                def scaled(i):
                    t = tiles[i]
                    tx[i] = k.v(V.tensor_scalar, xh[:, i % 2], xt[:, t], stat[:, 2, t:t + 1], None, ALU.mult,
                                w=[rst[t], ttr.get(i - 2)])

                scaled(0)
                for i, t in enumerate(tiles):
                    if i + 1 < len(tiles):
                        scaled(i + 1)
                    bs = [k.bank(), k.bank()]
                    for j in range(KT):
                        tt = k.tr(k.ps[bs[j // 4]][:, (j % 4) * P:(j % 4 + 1) * P], xh[:, i % 2, j * P:(j + 1) * P],
                                  ident, w=[tx[i], d_core], inc=j % 4 == 3)
                        if j == 3:
                            t0 = tt
                    ttr[i] = tt
                    who = t // 2
                    sc = mod[:, layer, who, (first + 1) * 8:(first + 2) * 8]
                    sh = mod[:, layer, who, first * 8:(first + 1) * 8]
                    prev = tsp.get(i - 2, ())
                    for j in range(4):
                        tv = k.v(V.tensor_scalar, tf[:, i % 2, j * P:(j + 1) * P], k.ps[bs[0]][:, j * P:(j + 1) * P],
                                 sc[:, j:j + 1], sh[:, j:j + 1], ALU.mult, ALU.add, w=[t0, tA[who], tS[who], prev])
                    for j in range(4, 8):
                        ta = k.a(A.activation, tf[:, i % 2, j * P:(j + 1) * P],
                                 k.ps[bs[1]][:, (j - 4) * P:(j - 3) * P], ACT.Identity, bias=sh[:, j:j + 1],
                                 scale=sc[:, j:j + 1], w=[tt, tA[who], tS[who], prev])
                    k.close(bs[0], [tv])
                    k.close(bs[1], [ta])
                    cols = slice(t * P, (t + 1) * P)
                    src = tf[:, i % 2].rearrange("p (j c) -> p j c", c=P)
                    th = k.a(A.copy, Hh[:, :, cols], src, w=[tv, ta])
                    tl = k.v(V.tensor_tensor, Hl[:, :, cols], src, Hh[:, :, cols].bitcast(F32), op=ALU.subtract,
                             w=[th, ta])
                    tsp[i] = [th, tl]
                    out[t] = [th, tl]
                return out

            def gate_tiles(layer, part, whos, w):
                toks = {}
                for who in whos:
                    t = mod_part(layer, part, who)
                    cols = mod[:, layer, who, part * 8:part * 8 + 8]
                    last = []
                    for hf in range(2):
                        b = k.bank()
                        for j in range(4):
                            tt = k.mm(k.ps[b][:, j * P:(j + 1) * P],
                                      cols[:, hf * 4 + j:hf * 4 + j + 1].to_broadcast([P, P]), ident, True, True,
                                      w=[t], inc=j == 3)
                        ta = k.a(A.copy, gates[0][:, who, hf * 512:(hf + 1) * 512], k.ps[b][:, :], w=[tt, w])
                        k.close(b, [ta])
                        last.append(ta)
                    toks[who] = last
                return toks

            def add_gated(s, tmp, n, b, tile, cols, tg, t):
                who = tile // 2
                buf = tmp[:, n % 2]
                tv = k.v(V.tensor_tensor, buf, k.ps[b][:, :], gates[0][:, who, cols], op=ALU.mult,
                         w=[t, tg[who], add_gated.free.get(n - 2)])
                k.close(b, [tv])
                tx = k.v(V.tensor_tensor, xt[:, tile, cols], xt[:, tile, cols], buf, op=ALU.add, w=[tv])
                add_gated.free[n] = tx
                return tx

            def gated_down(s, tmp, key, nk, x, xtok, tg):
                toks, cnt = {}, [0]

                def ev(tile, hf, b, t):
                    toks.setdefault(tile, []).append(
                        add_gated(s, tmp, cnt[0], b, tile, slice(hf * 512, (hf + 1) * 512), tg, t))
                    cnt[0] += 1
                down(k, st, key, nk, x, xtok, ev)
                return toks

            st.pump(0)
            with Scope(k) as s:
                kT = s.sb("kT", [P, 4, 512])
                qT = s.sb("qT", [P, 2, 4, 512])
                vt = s.sb("vt", [P, 4, 512])
                yc = s.sb("yc", [P, 4, 512])
                with Scope(k) as sn:
                    t_h = norm_mod(sn, 0, 0, "n1", [0, 1, 2, 3], d_x)
                sa = Scope(k)
                tab = sa.sb("tab", [P, 2, 2, 2, 64])
                lamt = sa.sb("lamt", [P, 8])
                sub = sa.sb("sub", [P, P])
                t_z = [k.v(V.memset, qT[64:128, 0], 0.0), k.v(V.memset, qT[0:64, 1], 0.0)]
                t_tab = {}
                for wi, gain in enumerate(("qg", "kg")):
                    g_ = B(gain).unsqueeze(1).to_broadcast([P, 2, 64])
                    t1 = k.g(G.tensor_tensor, tab[:, wi, 0], B("ropec").rearrange("p (t d) -> p t d", t=2), g_,
                             op=ALU.mult, w=[d_b1])
                    sw = B(gain).rearrange("p (r h f) -> p r h f", r=2, h=2)
                    for hf in range(2):
                        for tl in range(2):
                            t1 = k.g(G.tensor_tensor,
                                     tab[:, wi, 1, tl].rearrange("p (r h f) -> p r h f", r=2, h=2)[:, :, hf],
                                     B("ropes", tl * 64, 64).rearrange("p (r h f) -> p r h f", r=2, h=2)[:, :, hf],
                                     sw[:, :, 1 - hf], op=ALU.mult, w=[d_b1])
                    t_tab[wi] = t1
                prod = sa.sb("prod", [P, 2, 64])
                for i in range(2):
                    tl = k.v(V.tensor_tensor_reduce, out=prod[:, i], in0=B(("lq1", "lq2")[i]),
                             in1=B(("lk1", "lk2")[i]), scale=1.0, scalar=0.0, op0=ALU.mult, op1=ALU.add,
                             accum_out=lamt[:, i:i + 1], w=[d_b1])
                te = k.a(A.activation, lamt[:, 2:4], lamt[:, 0:2], ACT.Exp, w=[tl])
                t1 = k.v(V.tensor_tensor, lamt[:, 4:5], lamt[:, 3:4], lamt[:, 2:3], op=ALU.subtract, w=[te])
                t_lam = k.v(V.tensor_scalar, lamt[:, 5:6], lamt[:, 4:5], -LAM_INIT, None, ALU.add, w=[t1])
                t_sub = k.g(G.tensor_scalar, sub[:, :], B("subg"), 1.0 - LAM_INIT, None, ALU.mult, w=[d_b1])

                raw = sa.sb("raw_qk", [P, 2, 512])
                rot = sa.sb("rot_qk", [P, 2, 512])
                zz = sa.sb("zz_qk", [P, 2, 512])
                sst = sa.sb("sst", [P, 2, 3, 8])
                t_kT, t_qT, t_v = {}, {}, {}
                hist = {"n": 0}
                tr_done, rd_done = {}, {}

                def head_norm(which, tile, b, t):
                    n = hist["n"]
                    hist["n"] += 1
                    i = n % 2
                    old = tr_done.get(n - 2)
                    ta = k.a(A.activation, zz[:, i], k.ps[b][:, :], ACT.Square, w=[t, old, rd_done.get(n - 2)])
                    tr = k.a(A.copy, raw[:, i], k.ps[b][:, :])
                    k.close(b, [tr])
                    tv = k.v(V.tensor_reduce, sst[:, i, 0], zz[:, i].rearrange("p (h d) -> p h d", d=64), axis=AX,
                             op=ALU.add, w=[ta, old])
                    yield
                    tg = k.g(G.tensor_scalar, sst[:, i, 1], sst[:, i, 0], 1.0 / 64, EPS, ALU.mult, ALU.add, w=[tv])
                    tg = k.g(G.tensor_tensor, sst[:, i, 2], sst[:, i, 1], half[:, 0:8], op=ALU.pow, w=[tg])
                    r8 = raw[:, i].rearrange("p (h d) -> p h d", d=64)
                    tn = k.g(G.tensor_tensor, r8, r8, sst[:, i, 2].unsqueeze(2).to_broadcast([P, 8, 64]),
                             op=ALU.mult, w=[tg, tr])
                    yield
                    o8 = rot[:, i].rearrange("p (h d) -> p h d", d=64)
                    if tile < 2:
                        z8 = zz[:, i].rearrange("p (h r y f) -> p h r y f", h=8, r=2, y=2)
                        x8 = raw[:, i].rearrange("p (h r y f) -> p h r y f", h=8, r=2, y=2)
                        s8 = tab[:, which, 1, tile].rearrange("p (r y f) -> p r y f", r=2, y=2)
                        tz = []
                        for hf in range(2):
                            for r in range(2):
                                tz.append(k.v(V.tensor_tensor, z8[:, :, r, hf], x8[:, :, r, 1 - hf],
                                              s8[:, r, hf].unsqueeze(1).to_broadcast([P, 8, 16]), op=ALU.mult,
                                              w=[tn, t_tab[which], tv]))
                        to = k.g(G.tensor_tensor, o8, r8,
                                 tab[:, which, 0, tile].unsqueeze(1).to_broadcast([P, 8, 64]), op=ALU.mult,
                                 w=[tn, old])
                        to = k.v(V.tensor_tensor, rot[:, i], rot[:, i], zz[:, i], op=ALU.add, w=[to, tz])
                        rd_done[n] = to
                    else:
                        to = k.g(G.tensor_tensor, o8, r8,
                                 B(("qg", "kg")[which]).unsqueeze(1).to_broadcast([P, 8, 64]), op=ALU.mult,
                                 w=[tn, old])
                        rd_done[n] = tv
                    yield
                    b = k.bank()
                    for h in range(4):
                        tt = k.tr(k.ps[b][:, h * P:(h + 1) * P], rot[:, i, h * P:(h + 1) * P], ident, w=[to],
                                  inc=h == 3)
                    tr_done[n] = tt
                    cols = slice(tile * P, (tile + 1) * P)
                    src = k.ps[b][:, :].rearrange("p (h c) -> p h c", c=P)
                    if which:
                        te = k.a(A.copy, kT[:, :, cols], src, w=[tt])
                        t_kT[tile] = te
                    else:
                        k.a(A.copy, qT[0:64, 0, :, cols], src[0:64], w=[tt, t_z])
                        te = k.a(A.copy, qT[64:128, 1, :, cols], src[64:128])
                        t_qT[tile] = te
                    k.close(b, [te])
                    yield

                def evac_qk(which):
                    def f(tile, b, t):
                        while hist["n"] >= 2 and hist["n"] - 2 not in tr_done:
                            k.tick()
                        gen = head_norm(which, tile, b, t)
                        next(gen)
                        k.bg.append(gen)
                    return f

                def evac_v(tile, b, t):
                    t_v[tile] = k.a(A.copy, vt[:, tile], k.ps[b][:, :], w=[t])
                    k.close(b, [t_v[tile]])

                order = [0, 1, 2, 3]
                as_group(k, st, "ev_qkv", H, t_h, order, evac=evac_qk(1))
                as_group(k, st, "ev_qkv", H, t_h, order, evac=evac_qk(0))
                as_group(k, st, "ev_qkv", H, t_h, order, evac=evac_v)
                t_y = {}

                pr = sa.sb("pr", [P, 2, 2, 512])
                pT = rot
                sm = sa.sb("sm", [P, 2, 8])
                osq = zz[:, 0]
                ost = sa.sb("ost", [P, 4, 12])
                yr = zz[:, 1]
                hist2 = {"n": 0}
                t_pvd, t_sm, t_yr = {}, {}, {}
                t_cat = {}

                def attention(tile):
                    lat = tile < 2
                    nk = 512 if lat else 256
                    k0 = 0 if lat else 256
                    nb = nk // P
                    kts = [0, 1, 2, 3] if lat else [2, 3]
                    ob = None
                    for h in range(4):
                        n = hist2["n"]
                        hist2["n"] += 1
                        i = n % 2
                        bs = [k.bank(), k.bank()]
                        tm = []
                        for m in range(2):
                            tm.append(k.mm(k.ps[bs[m]][:, 0:nk], qT[:, m, h, tile * P:(tile + 1) * P],
                                           kT[:, h, k0:k0 + nk], True, True,
                                           w=[t_qT[tile], [t_kT[j] for j in kts]], inc=True))
                        yield
                        tp = []
                        for m in range(2):
                            tv = k.v(V.tensor_reduce, sm[:, i, m:m + 1], k.ps[bs[m]][:, 0:nk], axis=AX, op=ALU.max,
                                     w=[tm[m], t_sm.get(n - 2)])
                            tv = k.v(V.tensor_scalar, sm[:, i, 2 + m:3 + m], sm[:, i, m:m + 1], -0.125, None,
                                     ALU.mult, w=[tv])
                            ta = k.a(A.activation, pr[:, i, m, 0:nk], k.ps[bs[m]][:, 0:nk], ACT.Exp,
                                     bias=sm[:, i, 2 + m:3 + m], scale=0.125, accum_out=sm[:, i, 4 + m:5 + m],
                                     w=[tv, t_pvd.get(n - 2)])
                            k.close(bs[m], [ta])
                            tp.append(ta)
                        tv = k.v(V.reciprocal, sm[:, i, 6:8], sm[:, i, 4:6], w=[tp])
                        t2 = k.v(V.tensor_tensor, sm[:, i, 7:8], sm[:, i, 7:8], lamt[:, 5:6], op=ALU.mult,
                                 w=[tv, t_lam])
                        t1 = k.v(V.tensor_scalar, pr[:, i, 0, 0:nk], pr[:, i, 0, 0:nk], sm[:, i, 6:7], None, ALU.mult,
                                 w=[tv])
                        t1 = k.v(V.scalar_tensor_tensor, pr[:, i, 0, 0:nk], pr[:, i, 1, 0:nk], sm[:, i, 7:8],
                                 pr[:, i, 0, 0:nk], ALU.mult, ALU.add, w=[t1, t2])
                        t_sm[n] = t1
                        yield
                        b = k.bank()
                        for j in range(nb):
                            tt = k.tr(k.ps[b][:, j * P:(j + 1) * P], pr[:, i, 0, j * P:(j + 1) * P], ident, w=[t1],
                                      inc=j == nb - 1)
                        t_pvd[n] = tt
                        tc = k.a(A.copy, pT[:, i, 0:nk], k.ps[b][:, 0:nk], w=[tt, t_yr.get((n - 2, "pv")), tr_done[6], tr_done[7]])
                        k.close(b, [tc])
                        yield
                        if ob is None:
                            ob = k.bank()
                        for j in range(nb):
                            to = k.mm(k.ps[ob][:, h * P:(h + 1) * P], pT[:, i, j * P:(j + 1) * P],
                                      vt[:, kts[j], h * P:(h + 1) * P], j == 0, j == nb - 1,
                                      w=[tc, t_v[kts[j]]], inc=j == nb - 1)
                        t_yr[n, "pv"] = to
                        yield
                    ta = k.a(A.activation, osq, k.ps[ob][:, :], ACT.Square, w=[to, t_yr.get("sq"), rd_done[6]])
                    tv = k.v(V.tensor_reduce, ost[:, tile, 0:4], osq.rearrange("p (h d) -> p h d", d=P), axis=AX,
                             op=ALU.add, w=[ta])
                    t_yr["sq"] = tv
                    tg = k.g(G.tensor_scalar, ost[:, tile, 4:8], ost[:, tile, 0:4], 1.0 / P, EPS, ALU.mult, ALU.add,
                             w=[tv])
                    tg = k.g(G.tensor_tensor, ost[:, tile, 8:12], ost[:, tile, 4:8], half[:, 0:4], op=ALU.pow, w=[tg])
                    for h in range(4):
                        tv = k.v(V.scalar_tensor_tensor, yr[:, h * P:(h + 1) * P], k.ps[ob][:, h * P:(h + 1) * P],
                                 ost[:, tile, 8 + h:9 + h], sub[:, :], ALU.mult, ALU.mult,
                                 w=[tg, t_sub, t_yr.get("tr"), rd_done[7]])
                    k.close(ob, [tv])
                    yield
                    b = k.bank()
                    for h in range(4):
                        tt = k.tr(k.ps[b][:, h * P:(h + 1) * P], yr[:, h * P:(h + 1) * P], ident, w=[tv], inc=h == 3)
                    t_yr["tr"] = tt
                    yield
                    cols = slice(tile * P, (tile + 1) * P)
                    t_cat[tile] = k.a(A.copy, qT[:, 0, :, cols], k.ps[b][:, :].rearrange("p (h c) -> p h c", c=P),
                                      w=[tt])
                    k.close(b, [t_cat[tile]])

                t_convpe = [None]
                ub = sa.sb("ub", [P, 2, 2, 258])
                cg = sa.sb("cg", [P, 2, 512])
                t_u0 = k.g(G.memset, ub[:, :, :, :], 0.0)
                t_ycv = {}
                t_cfree = {}

                def conv_tile(i):
                    j = i % 2
                    b, t = ws_tile(k, st, "ev_conv", H, list(t_h.values()), 512)
                    tc = k.a(A.copy, cg[:, j], k.ps[b][:, :], w=[t, t_cfree.get(i - 2)])
                    k.close(b, [tc])
                    k.tick(2)
                    b, t = ws_tile(k, st, "ev_conv", H, list(t_h.values()), 512)
                    tu = k.v(V.tensor_tensor, ub[:, j, :, 1:257], cg[:, j].rearrange("p (s c) -> p s c", s=2),
                             k.ps[b][:, :].rearrange("p (s c) -> p s c", s=2), op=ALU.mult,
                             w=[t, tc, t_u0, t_cfree.get(i - 2)])
                    k.close(b, [tu])
                    k.tick(2)
                    b, t = ws_tile(k, st, "ev_conv", H, list(t_h.values()), 512)
                    t_convpe[0] = t
                    c3 = cg[:, j].rearrange("p (s c) -> p s c", s=2)
                    tv = k.v(V.tensor_scalar, c3, ub[:, j, :, 0:256], C("scw", i, 1), None, ALU.mult, w=[tu, d_core])
                    for tap in (1, 2):
                        tv = k.v(V.scalar_tensor_tensor, c3, ub[:, j, :, tap:tap + 256], C("scw", tap * 4 + i, 1), c3,
                                 ALU.mult, ALU.add, w=[tv])
                    tv = k.v(V.tensor_tensor, yc[:, i], cg[:, j], k.ps[b][:, :], op=ALU.mult, w=[tv, t])
                    k.close(b, [tv])
                    t_ycv[i] = tv
                    t_cfree[i] = tv
                    k.tick(2)

                for tile in range(4):
                    k.bg.append(attention(tile))
                for i in range(4):
                    conv_tile(i)
                t_ch = k.a(A.copy, Hh[:, 0:4], yc[:, :], w=[list(t_ycv.values()), t_convpe[0]])
                t_cl = k.v(V.tensor_tensor, Hl[:, 0:4], yc[:, :], Hh[:, 0:4].bitcast(F32), op=ALU.subtract, w=[t_ch])
                k.drain()
                sa.__exit__()
                gates[0] = s.sb("gates", [P, 2, D])
                tg = gate_tiles(0, 2, (0, 1), None)
                t_rh = k.a(A.copy, Hh[:, 4:8], qT[:, 0], w=list(t_cat.values()))
                t_rl = k.v(V.tensor_tensor, Hl[:, 4:8], qT[:, 0], Hh[:, 4:8].bitcast(F32), op=ALU.subtract, w=[t_rh])
                t_cat = {t: [t_ch, t_cl, t_rh, t_rl] for t in order}
                tmp = s.sb("tmp", [P, 2, 512])
                add_gated.free = {}
                cnt = [0]
                t_x = {}
                for hf in range(2):
                    def ev(tile, b, t, hf=hf):
                        tx = add_gated(s, tmp, cnt[0], b, tile, slice(hf * 512, (hf + 1) * 512), tg, t)
                        cnt[0] += 1
                        t_x.setdefault(tile, []).append(tx)
                    as_group(k, st, "ev_out", H, t_cat, order, evac=ev)
            if stop == 1:
                return finish(xt, k.last())

            def ffn_conv(layer, tiles, keys, t_x, tg_part):
                ntok = len(tiles) * P
                ns = ntok // 256
                t_xn = {}
                with Scope(k) as s:
                    hid = s.sb("hid", [P, FT, ntok])
                    with Scope(k) as sn:
                        t_h = norm_mod(sn, layer, 3, "n2", tiles, t_x)
                    ht = list(t_h.values())
                    ab = s.sb("ab", [P, 2, ntok])
                    sb_ = s.sb("sb", [P, 2, ntok])
                    t_ab, t_sb, t_hid = {}, {}, {}
                    for f in range(FT):
                        i = f % 2
                        b, t = ws_tile(k, st, keys[0], H, ht, ntok)
                        ps3 = k.ps[b][:, 0:ntok].rearrange("p (s c) -> p s c", s=ns)
                        a3 = ab[:, i].rearrange("p (s c) -> p s c", s=ns)
                        w_ = lambda tap: C("fcw", layer * 66 + tap * 22 + f, 1)
                        ta = k.a(A.activation, ab[:, i], k.ps[b][:, 0:ntok], ACT.Identity,
                                 bias=C("fcb", layer * 22 + f, 1), scale=w_(1), w=[t, t_ab.get(f - 2)])
                        tv = k.v(V.scalar_tensor_tensor, a3[:, :, 1:256], ps3[:, :, 0:255], w_(0), a3[:, :, 1:256],
                                 ALU.mult, ALU.add, w=[ta])
                        tv = k.v(V.scalar_tensor_tensor, a3[:, :, 0:255], ps3[:, :, 1:256], w_(2), a3[:, :, 0:255],
                                 ALU.mult, ALU.add, w=[tv])
                        k.close(b, [tv])
                        ta = k.a(A.activation, sb_[:, i], ab[:, i], ACT.Silu, w=[tv, t_sb.get(f - 2)])
                        t_ab[f] = ta
                        k.tick()
                        b, t = ws_tile(k, st, keys[0], H, ht, ntok)
                        t_hid[f] = t_sb[f] = k.v(V.tensor_tensor, hid[:, f], sb_[:, i], k.ps[b][:, 0:ntok], op=ALU.mult,
                                                 w=[t, ta])
                        k.close(b, [t_hid[f]])
                        k.tick()
                    k.drain()
                    gates[0] = s.sb("gates", [P, 2, D])
                    tg = gate_tiles(layer, 5, sorted({t // 2 for t in tiles}), None)
                    tmp = s.sb("tmp2", [P, 2, 512])
                    add_gated.free = {}
                    cnt = 0
                    up_done = k.last()[0]
                    t_hl = {}

                    def halves(n):
                        f = n % FT
                        q = n % KT
                        cols = slice(0, ntok)
                        old = t_hl.get((n - KT, "pe"))
                        ta = k.a(A.copy, Hh[:, q, cols], hid[:, f], w=[t_hid[f], up_done, old])
                        tv = k.v(V.tensor_tensor, Hl[:, q, cols], hid[:, f], Hh[:, q, cols].bitcast(F32),
                                 op=ALU.subtract, w=[ta])
                        t_hl[n] = [ta, tv]

                    for n in range(3):
                        halves(n)
                    for hf in range(2):
                        bs = {t: k.bank() for t in tiles}
                        for f in range(0, FT, 2):
                            u = st.take(keys[1])
                            wh, wl, wt = st.parts(u)
                            for kk in range(2):
                                n = hf * FT + f + kk
                                if n + 3 < 2 * FT:
                                    halves(n + 3)
                                c = slice(kk * 512, (kk + 1) * 512)
                                for i, tile in enumerate(tiles):
                                    xs = slice(i * P, (i + 1) * P)
                                    last = f + kk == FT - 1
                                    t = as3(k, k.ps[bs[tile]][:, :], Hh[:, n % KT, xs], Hl[:, n % KT, xs], wh[:, c],
                                            wl[:, c], f + kk == 0, last, w=[wt, t_hl[n]],
                                            inc=last or i == len(tiles) - 1)
                                    if last:
                                        tx = add_gated(s, tmp, cnt, bs[tile], tile, slice(hf * 512, (hf + 1) * 512),
                                                       tg, t)
                                        cnt += 1
                                        t_xn.setdefault(tile, []).append(tx)
                                t_hl[n, "pe"] = t
                            st.free(u, t)
                            k.tick()
                return t_xn

            t_x = ffn_conv(0, [0, 1, 2, 3], ("up0", "down0"), t_x, 5)
            if stop == 2:
                return finish(xt, k.last())

            with Scope(k) as s:
                LO, nl1 = offsets(L1C)
                l1 = s.sb("l1", [P, nl1])
                d_l1 = k.dma("g", l1[:, :], l1_in, w=k.last())
                cat = s.sb("cat", [P, KT, T])
                with Scope(k) as sn:
                    t_h = norm_mod(sn, 1, 0, "n1", order, t_x)

                def L(name, i=0, n=None):
                    at, size = LO[name]
                    return l1[:, at + i:at + (i + n if n else size)]

                sa = Scope(k)
                lg = sa.sb("lg", [P, 8])
                dec = sa.sb("dec", [P, 4, 2, 4])
                decay = sa.sb("decay", [P, 4, 512])
                two = lambda a: a.rearrange("p (t u) c -> p t (u c)", t=2)
                rawq = at = two(cat[:, 0:4])
                zq = two(cat[:, 4:8])
                qk = sa.sb("qk", [P, 2, 512])
                kc = sa.sb("kc", [P, 2, 256])
                vl = sa.sb("vl", [P, 4, 512])
                gate = xt[:, 2].rearrange("p (t c) -> p t c", t=2)
                pv = xt[:, 3].rearrange("p (t c) -> p t c", t=2)
                qTp = sa.sb("qTp", [P, 4, T])
                kTp = sa.sb("kTp", [P, 2, T])
                qd = sa.sb("qd", [P, 2, 4, P])
                qdT = sa.sb("qdT", [P, 4, T])
                kw = sa.sb("kw", [P, 2, 4, P])
                S = sa.sb("S", [P, 4, P])
                yp = sa.sb("yp", [P, 4, T])
                ost = sa.sb("ost", [P, 2, 12])
                yr = qd.rearrange("p t h c -> p t (h c)")
                dtmp = yp[:, 0:2].rearrange("p t c -> p (t c)")

                t_lg = k.a(A.activation, lg[:, 0:4], B("decf"), ACT.Exp, w=[d_b1])
                t_lg = k.a(A.activation, lg[:, 4:8], B("decb"), ACT.Exp, w=[d_b1])
                t_lg = k.v(V.tensor_scalar, lg[:, :], lg[:, :], -1.0, None, ALU.mult, w=[t_lg])
                tt = []
                for i in range(4):
                    tt.append(k.v(V.tensor_tensor, dec[:, i],
                                  B("ramps", 2 * i, 2).unsqueeze(2).to_broadcast([P, 2, 4]),
                                  lg[:, (i % 2) * 4:(i % 2) * 4 + 4].unsqueeze(1).to_broadcast([P, 2, 4]),
                                  op=ALU.mult, w=[t_lg]))
                t_dec = k.a(A.activation, dec[:, :], dec[:, :], ACT.Exp, w=[tt])
                t_dec8 = k.v(V.tensor_scalar, dec[:, 0:2], dec[:, 0:2], 0.125, None, ALU.mult, w=[t_dec])
                t_decay = {}

                def decays():
                    t2 = None
                    for h in range(4):
                        t1 = k.g(G.tensor_scalar, dtmp, L("dist_f"), lg[:, h:h + 1], None, ALU.mult,
                                 w=[t_lg, d_l1, t2])
                        t2 = k.v(V.scalar_tensor_tensor, decay[:, h], L("dist_b"), lg[:, 4 + h:5 + h], dtmp,
                                 ALU.mult, ALU.add, w=[t1])
                        ta = k.a(A.activation, decay[:, h], decay[:, h], ACT.Exp, w=[t2])
                        t_decay[h] = k.g(G.tensor_tensor, decay[:, h], decay[:, h], L("two"), op=ALU.mult, w=[ta])
                        yield

                k.bg.append(decays())
                t_qk, t_kc, t_v, t_g, t_pv = {}, {}, {}, {}, {}

                def evac_qk(tile, b, t):
                    if tile >= 2:
                        t_kc[tile - 2] = k.a(A.copy, kc[:, tile - 2], k.ps[b][:, 0:256], w=[t])
                        k.close(b, [t_kc[tile - 2]])
                        return
                    tr = k.a(A.copy, rawq[:, tile], k.ps[b][:, :], w=[t])
                    k.close(b, [tr])
                    x8 = rawq[:, tile].rearrange("p (h r y f) -> p h r y f", h=8, r=2, y=2)
                    z8 = zq[:, tile].rearrange("p (h r y f) -> p h r y f", h=8, r=2, y=2)
                    s8 = B("ropes", tile * 64, 64).rearrange("p (r y f) -> p r y f", r=2, y=2)
                    tz = []
                    for hf in range(2):
                        for r in range(2):
                            tz.append(k.v(V.tensor_tensor, z8[:, :, r, hf], x8[:, :, r, 1 - hf],
                                          s8[:, r, hf].unsqueeze(1).to_broadcast([P, 8, 16]), op=ALU.mult, w=[tr]))
                    to = k.g(G.tensor_tensor, qk[:, tile].rearrange("p (h d) -> p h d", d=64),
                             rawq[:, tile].rearrange("p (h d) -> p h d", d=64),
                             B("ropec", tile * 64, 64).unsqueeze(1).to_broadcast([P, 8, 64]), op=ALU.mult, w=[tr])
                    t_qk[tile] = k.v(V.tensor_tensor, qk[:, tile], qk[:, tile], zq[:, tile], op=ALU.add, w=[to, tz])

                def evac_v(tile, b, t):
                    t_v[tile] = k.a(A.copy, vl[:, tile], k.ps[b][:, :], w=[t])
                    k.close(b, [t_v[tile]])

                def evac_g(tile, b, t):
                    ta = k.a(A.activation, gate[:, tile], k.ps[b][:, :], ACT.Silu, w=[t])
                    k.close(b, [ta])
                    g4 = gate[:, tile].rearrange("p (h d) -> p h d", d=P)
                    t_g[tile] = k.g(G.tensor_tensor, g4, g4, B("rgn").unsqueeze(1).to_broadcast([P, 4, P]),
                                    op=ALU.mult, w=[ta])

                def evac_pv(tile, b, t):
                    t_pv[tile] = k.a(A.copy, pv[:, tile], k.ps[b][:, :], w=[t])
                    k.close(b, [t_pv[tile]])

                t_cat = {}

                def retention():
                    t_z = [k.v(V.memset, qTp[64:128, 0:4:2], 0.0), k.v(V.memset, qTp[0:64, 1:4:2], 0.0)]
                    t_qd = {}
                    for tile in range(2):
                        q4 = qk[:, tile, 0:256].rearrange("p (h d) -> p h d", d=64)
                        for i in range(2):
                            t_qd[tile] = k.g(G.tensor_tensor, qd[:, tile, :, i * 64:(i + 1) * 64], q4,
                                             dec[:, i, tile].unsqueeze(2).to_broadcast([P, 4, 64]), op=ALU.mult,
                                             w=[t_qk[tile], t_dec8])
                    yield
                    t_qT, t_kT, t_qdT = {}, {}, {}
                    for tile in range(2):
                        b = k.bank()
                        for j in range(4):
                            tt = k.tr(k.ps[b][:, j * P:(j + 1) * P], qk[:, tile, j * P:(j + 1) * P], ident,
                                      w=[t_qk[tile]], inc=j == 3)
                        c = slice(tile * P, (tile + 1) * P)
                        p4 = k.ps[b][:, :].rearrange("p (j c) -> p j c", c=P)
                        k.a(A.copy, qTp[0:64, 0:4:2, c], p4[0:64, 0:2], w=[tt, t_z])
                        t_qT[tile] = k.a(A.copy, qTp[64:128, 1:4:2, c], p4[64:128, 0:2])
                        t_kT[tile] = k.a(A.copy, kTp[:, :, c], p4[:, 2:4])
                        k.close(b, [t_kT[tile]])
                        yield
                        b = k.bank()
                        for h in range(4):
                            tt = k.tr(k.ps[b][:, h * P:(h + 1) * P], qd[:, tile, h], ident, w=[t_qd[tile]], inc=h == 3)
                        t_qdT[tile] = k.a(A.copy, qdT[:, :, c], k.ps[b][:, :].rearrange("p (j c) -> p j c", c=P),
                                          w=[tt])
                        k.close(b, [t_qdT[tile]])
                        yield
                    t_kw = {}
                    for j in range(2):
                        k4 = kc[:, j].rearrange("p (h d) -> p h d", d=64)
                        for i in range(2):
                            t_kw[j] = k.g(G.tensor_tensor, kw[:, j, :, i * 64:(i + 1) * 64], k4,
                                          dec[:, 2 + i, j].unsqueeze(2).to_broadcast([P, 4, 64]), op=ALU.mult,
                                          w=[t_kc[j], t_dec])
                    yield
                    while len(t_v) < 4:
                        yield
                    yield
                    b = k.bank()
                    for h in range(4):
                        for j in range(2):
                            tt = k.mm(k.ps[b][:, h * P:(h + 1) * P], kw[:, j, h], vl[:, 2 + j, h * P:(h + 1) * P], j == 0,
                                      j == 1, w=[t_kw[j], t_v[2 + j]], inc=h == 3 and j == 1)
                    t_S = k.a(A.copy, S[:, :], k.ps[b][:, :].rearrange("p (h d) -> p h d", d=P), w=[tt])
                    k.close(b, [t_S])
                    yield
                    obs = [k.bank(), k.bank()]
                    t_o = {}

                    def scores(h):
                        b = k.bank()
                        for j in range(2):
                            tt = k.mm(k.ps[b][:, j * T:(j + 1) * T], kTp[:, h // 2, j * P:(j + 1) * P], qTp[:, h], True,
                                      True, w=[list(t_kT.values()), list(t_qT.values())], inc=j == 1)
                        t1 = k.v(V.tensor_tensor, at[:, h % 2], k.ps[b][:, :], decay[:, h], op=ALU.mult,
                                 w=[tt, t_decay[h], t_o.get(h - 2)])
                        k.close(b, [t1])
                        return t1

                    t_at = {0: scores(0)}
                    yield
                    for h in range(4):
                        if h < 3:
                            t_at[h + 1] = scores(h + 1)
                        yield
                        for tile in range(2):
                            out = k.ps[obs[tile]][:, h * P:(h + 1) * P]
                            for j in range(2):
                                k.mm(out, at[:, h % 2, j * T + tile * P:j * T + (tile + 1) * P],
                                     vl[:, j, h * P:(h + 1) * P], j == 0, False, w=[t_at[h], t_v[j]])
                            t_o[h] = k.mm(out, qdT[:, h, tile * P:(tile + 1) * P], S[:, h], False, True,
                                          w=[t_qdT[tile], t_S], inc=True)
                        yield
                    while len(t_g) < 2:
                        yield
                    t_n = {}
                    for tile in range(2):
                        ta = k.a(A.activation, yr[:, tile], k.ps[obs[tile]][:, :], ACT.Square, w=[t_o[3]])
                        tv = k.v(V.tensor_reduce, ost[:, tile, 0:4], yr[:, tile].rearrange("p (h d) -> p h d", d=P),
                                 axis=AX, op=ALU.add, w=[ta])
                        tg = k.g(G.tensor_scalar, ost[:, tile, 4:8], ost[:, tile, 0:4], 1.0 / P, EPS, ALU.mult, ALU.add,
                                 w=[tv])
                        tg = k.g(G.tensor_tensor, ost[:, tile, 8:12], ost[:, tile, 4:8], half[:, 0:4], op=ALU.pow,
                                 w=[tg])
                        yield
                        for h in range(4):
                            c = slice(h * P, (h + 1) * P)
                            tv = k.v(V.scalar_tensor_tensor, yr[:, tile, c], k.ps[obs[tile]][:, c],
                                     ost[:, tile, 8 + h:9 + h], gate[:, tile, c], ALU.mult, ALU.mult,
                                     w=[tg, t_g[tile], tv])
                        k.close(obs[tile], [tv])
                        t_n[tile] = tv
                    yield
                    for tile in range(2):
                        b = k.bank()
                        for h in range(4):
                            tt = k.tr(k.ps[b][:, h * P:(h + 1) * P], yr[:, tile, h * P:(h + 1) * P], ident,
                                      w=[t_n[tile]], inc=h == 3)
                        t_cat[tile] = k.a(A.copy, cat[:, 4:8, tile * P:(tile + 1) * P],
                                          k.ps[b][:, :].rearrange("p (h c) -> p h c", c=P), w=[tt])
                        k.close(b, [t_cat[tile]])
                        yield

                def pooling():
                    t_yp = {}
                    for g in range(0, 4, 2):
                        b = k.bank()
                        for r in range(2):
                            for j in range(2):
                                tt = k.mm(k.ps[b][:, r * T:(r + 1) * T], pv[:, j, (g + r) * P:(g + r + 1) * P],
                                          L("band", ((g + r) * 2 + j) * T, T), j == 0, j == 1, w=[t_pv[j], d_l1],
                                          inc=j == 1 and r == 1)
                        t_yp[g] = k.a(A.copy, yp[:, g:g + 2], k.ps[b][:, :].rearrange("p (r c) -> p r c", c=T), w=[tt])
                        k.close(b, [t_yp[g]])
                    yield
                    for g in range(0, 4, 2):
                        b = k.bank()
                        for r in range(2):
                            tt = k.mm(k.ps[b][:, r * T:(r + 1) * T], L("poolw", (g + r) * P, P), yp[:, g + r], True, True,
                                      w=[t_yp[g]], inc=r == 1)
                        for r in range(2):
                            tv = k.v(V.tensor_scalar, cat[:, g + r], k.ps[b][:, r * T:(r + 1) * T],
                                     C("psc", g + r, 1), None, ALU.mult, w=[tt])
                        k.close(b, [tv])
                        t_cat["p", g] = tv
                    yield

                as_group(k, st, "od_in", H, t_h, order, cols={0: (0, 512), 1: (0, 512), 2: (256, 512), 3: (256, 512)},
                         evac=evac_qk)
                k.bg.append(retention())
                as_group(k, st, "od_in", H, t_h, order, evac=evac_v)
                as_group(k, st, "od_in", H, t_h, [0, 1], evac=evac_g)
                as_group(k, st, "od_in", H, t_h, [0, 1], evac=evac_pv)
                k.bg.append(pooling())
                k.drain()
                done = k.last()[0]
                t_hc = k.a(A.copy, Hh[:, :, 0:T], cat[:, :], w=[list(t_cat.values()), done])
                t_lc = k.v(V.tensor_tensor, Hl[:, :, 0:T], cat[:, :], Hh[:, :, 0:T].bitcast(F32), op=ALU.subtract,
                           w=[t_hc])
                sa.__exit__()
                gates[0] = s.sb("gates", [P, 2, D])
                tg = gate_tiles(1, 2, (0,), None)
                tmp = s.sb("tmp", [P, 2, 512])
                add_gated.free = {}
                t_x = gated_down(s, tmp, "od_out", KT, lambda kt, tile: (Hh[:, kt, tile * P:(tile + 1) * P],
                                                                         Hl[:, kt, tile * P:(tile + 1) * P]),
                                 lambda kt: [t_hc, t_lc], tg)
            if stop == 3:
                return finish(xt, k.last())

            with Scope(k) as s:
                hh = s.sb("hh", [P, FT, T], F32R)
                hl = s.sb("hl", [P, FT, T], F32R)
                with Scope(k) as sn:
                    t_h = norm_mod(sn, 1, 3, "n2", [0, 1], t_x)
                t_hid = ffn_up(s, "up1", H, list(t_h.values()), hh, hl, 1)
                gates[0] = s.sb("gates", [P, 2, D])
                tg = gate_tiles(1, 5, (0,), None)
                tmp = s.sb("tmp", [P, 2, 512])
                add_gated.free = {}
                t_x = gated_down(s, tmp, "down1", FT, lambda kt, tile: (hh[:, kt, tile * P:(tile + 1) * P],
                                                                        hl[:, kt, tile * P:(tile + 1) * P]),
                                 lambda kt: t_hid[kt], tg)
        if stop == 4:
            return finish(xt, k.last())

        with Scope(k) as s2:
            QO, nc2 = offsets(C2)
            c2 = s2.sb("c2", [P, nc2])
            d_c2 = k.dma("g", c2[:, :], c2_in, w=k.last())
            Hh = s2.sb("H2h", [P, KT, T], F32R)
            Hl = s2.sb("H2l", [P, KT, T], F32R)
            H = (Hh, Hl)
            lb = s2.sb("lb", [P, 3, 8])
            cst = s2.sb("cst", [P, 2, 16])
            stat = s2.sb("lnstat", [P, 2, 16])
            lng, lnb = xt[:, 2], xt[:, 3]

            def Q(name, i=0, n=None):
                at, size = QO[name]
                return c2[:, at + i:at + (i + n if n else size)]

            t_cst = [k.v(V.memset, cst[:, 0], 1.0), k.v(V.memset, cst[:, 1], 0.5)]
            one = cst[:, 0, 0:1]

            def into_H(tile, tok):
                toks = []
                for hf in range(2):
                    b = k.bank()
                    for j in range(4):
                        tt = k.tr(k.ps[b][:, j * P:(j + 1) * P], xt[:, tile, (hf * 4 + j) * P:(hf * 4 + j + 1) * P],
                                  ident, w=[tok], inc=j == 3)
                    cols = slice(tile * P, (tile + 1) * P)
                    ts = split_bank(k, k.ps[b][:, :].rearrange("p (j c) -> p j c", c=P), Hh[:, hf * 4:hf * 4 + 4, cols],
                                    Hl[:, hf * 4:hf * 4 + 4, cols], [tt])
                    k.close(b, [ts[1]])
                    toks += ts
                return toks

            def tokens_H(yt, tile, hf, tok, ht):
                b = k.bank()
                for j in range(4):
                    tt = k.tr(k.ps[b][:, j * P:(j + 1) * P], yt[:, tile, (hf * 4 + j) * P:(hf * 4 + j + 1) * P], ident,
                              w=[tok], inc=j == 3)
                cols = slice(tile * P, (tile + 1) * P)
                ts = split_bank(k, k.ps[b][:, :].rearrange("p (j c) -> p j c", c=P), Hh[:, hf * 4:hf * 4 + 4, cols],
                                Hl[:, hf * 4:hf * 4 + 4, cols], [tt])
                k.close(b, [ts[1]])
                ht[tile] = ht.get(tile, []) + list(ts)

            ln_n = [0]
            ln_last = [k.last()]

            def load_ln():
                n = ln_n[0]
                ln_n[0] += 1
                return [k.dma("g", dst, ln_in[n, r:r + 1].to_broadcast([P, D]), w=ln_last[0])
                        for r, dst in enumerate((lng, lnb))]

            def down_ln(key, nk, x, xtok, d_ln):
                tb, out = {}, {}

                def ev(tile, hf, b, t):
                    xr = xt[:, tile, hf * 512:(hf + 1) * 512]
                    tx = k.v(V.scalar_tensor_tensor, xr, xr, DN_ALPHA, k.ps[b][:, :], ALU.mult, ALU.add, w=[t])
                    k.close(b, [tx])
                    tb[tile, hf] = k.v(V.bn_stats, stat[:, tile, hf * 6:hf * 6 + 6], xr, w=[tx])
                    if hf == 0:
                        return
                    ta = k.v(V.bn_aggr, stat[:, tile, 12:14], stat[:, tile, 0:12], w=[tb[tile, 0], tb[tile, 1]])
                    te = k.v(V.tensor_scalar, stat[:, tile, 14:15], stat[:, tile, 13:14], LN_EPS, None, ALU.add, w=[ta])
                    tg = k.g(G.tensor_tensor, stat[:, tile, 15:16], stat[:, tile, 14:15], half[:, 0:1], op=ALU.pow,
                             w=[te])
                    tx = k.v(V.scalar_tensor_tensor, xt[:, tile], xt[:, tile], stat[:, tile, 12:13], lng, ALU.subtract,
                             ALU.mult, w=[ta, d_ln])
                    out[tile] = k.v(V.scalar_tensor_tensor, xt[:, tile], xt[:, tile], stat[:, tile, 15:16], lnb,
                                    ALU.mult, ALU.add, w=[tx, tg, d_ln])
                down(k, st, key, nk, x, xtok, ev)
                ln_last[0] = list(out.values())
                return out

            def x_H(kt, tile):
                c = slice(tile * P, (tile + 1) * P)
                return Hh[:, kt, c], Hl[:, kt, c]

            def norm_out(s, ob, tile, hf, nh, extra, gate, ost, sq, t_o, t_gate, old):
                dv = 512 // nh
                ta = k.a(A.activation, sq, k.ps[ob][:, :], ACT.Square, w=[t_o, old])
                tv = k.v(V.tensor_reduce, ost[:, 0, 0:nh], sq.rearrange("p (h d) -> p h d", d=dv), axis=AX, op=ALU.add,
                         w=[ta])
                if extra is None:
                    tv = k.v(V.tensor_scalar, ost[:, 1, 0:nh], ost[:, 0, 0:nh], 1.0 / dv, P * EPS, ALU.mult, ALU.add,
                             w=[tv])
                else:
                    tv = k.v(V.scalar_tensor_tensor, ost[:, 1, 0:nh], ost[:, 0, 0:nh], 1.0 / dv, extra[0], ALU.mult,
                             ALU.add, w=[tv, extra[1]])
                tg = k.g(G.tensor_tensor, ost[:, 2, 0:nh], ost[:, 1, 0:nh], half[:, 0:nh], op=ALU.pow, w=[tv])
                for h in range(nh):
                    gh = gate[:, tile, hf * 512 + h * dv:hf * 512 + (h + 1) * dv]
                    ty = k.v(V.scalar_tensor_tensor, gh, k.ps[ob][:, h * dv:(h + 1) * dv], ost[:, 2, h:h + 1], gh,
                             ALU.mult, ALU.mult, w=[tg, t_gate])
                k.close(ob, [ty])
                return tv, ty

            def small_proj(s, name, i):
                wh = s.sb("wsh", [P, KT * 16], F32R)
                wl = s.sb("wsl", [P, KT * 16], F32R)
                w = Q(name, i * KT * 16, KT * 16)
                ta = k.a(A.copy, wh[:, :], w, w=[d_c2])
                tv = k.v(V.tensor_tensor, wl[:, :], w, wh[:, :].bitcast(F32), op=ALU.subtract, w=[ta])

                def go(htok):
                    b = k.bank()
                    for kt in range(KT):
                        c = slice(kt * 16, (kt + 1) * 16)
                        t = ws3(k, k.ps[b][0:16, 0:T], wh[:, c], wl[:, c], Hh[:, kt], Hl[:, kt], kt == 0, kt == KT - 1,
                                w=[ta, tv, htok], inc=kt == KT - 1)
                    return b, t
                return go

            with Scope(k) as s:
                m = s.sb("lbm", [P, 12, 8])
                lo_ = lambda i: Q("lbl", i * 8, 8)
                t1 = k.v(V.tensor_tensor, m[:, 0], lo_(0), lo_(2), op=ALU.max, w=[d_c2])
                t1 = k.v(V.tensor_tensor, m[:, 0], m[:, 0], lo_(3), op=ALU.max, w=[t1])
                t2 = k.v(V.tensor_tensor, m[:, 1], m[:, 0], lo_(1), op=ALU.max, w=[t1])
                ts = []
                for n, (j, mx) in enumerate(((0, 0), (2, 0), (3, 0), (1, 1))):
                    ts.append(k.v(V.tensor_tensor, m[:, 2 + n], lo_(j), m[:, mx], op=ALU.subtract, w=[t2]))
                ts.append(k.v(V.tensor_tensor, m[:, 6], m[:, 0], m[:, 1], op=ALU.subtract, w=[t2]))
                ta = k.a(A.activation, m[:, 7:12], m[:, 2:7], ACT.Exp, w=[ts])
                t1 = k.v(V.tensor_tensor, m[:, 7], m[:, 7], m[:, 8], op=ALU.add, w=[ta])
                t1 = k.v(V.tensor_tensor, m[:, 7], m[:, 7], m[:, 9], op=ALU.add, w=[t1])
                t2 = k.v(V.tensor_tensor, m[:, 8], m[:, 7], m[:, 11], op=ALU.mult, w=[t1])
                t2 = k.v(V.tensor_tensor, m[:, 8], m[:, 8], m[:, 10], op=ALU.add, w=[t2])
                ta = k.a(A.activation, m[:, 9:11], m[:, 7:9], ACT.Ln, w=[t2, ta])
                t1 = k.v(V.tensor_tensor, lb[:, 0], m[:, 5], m[:, 10], op=ALU.subtract, w=[ta])
                t2 = k.v(V.tensor_tensor, lb[:, 1], m[:, 6], m[:, 9], op=ALU.add, w=[ta])
                t2 = k.v(V.tensor_tensor, lb[:, 1], lb[:, 1], m[:, 10], op=ALU.subtract, w=[t2])
                t_lb = k.v(V.tensor_tensor, lb[:, 2], lb[:, 1], lb[:, 0], op=ALU.subtract, w=[t1, t2])

            def gdn(j, t_h, d_ln):
                with Scope(k) as s:
                    kf = s.sb("kf", [P, 8, T])
                    qf = s.sb("qf", [P, 8, T])
                    gate = s.sb("gate", [P, 2, D])
                    vf = gate.rearrange("p t (a c) -> p (t a) c", c=T)
                    R = s.sb("R", [P, 2, 8, P])
                    DT = s.sb("DT", [P, 2, 8, P])
                    LT = s.sb("LT", [P, 2, 8, P])
                    X = s.sb("X", [P, 2, 8, P])
                    Y = s.sb("Y", [P, 2, 8, P])
                    Pm = s.sb("Pm", [P, 4, 4, P])
                    S1 = s.sb("S1", [P, 8, P])
                    kd = s.sb("kd", [P, 8, P])
                    EG = s.sb("EG", [P, 8, P])
                    sm = s.sb("gsm", [P, 12, 2, 8])
                    ba = s.sb("ba", [P, T])
                    jk = s.sb("jk", [P, 2, P])
                    sq = s.sb("osq", [P, 512])
                    ost = s.sb("gost", [P, 2, 3, 4])
                    bproj = small_proj(s, "wba", j)
                    htok = list(t_h.values())
                    b, t = bproj(htok)
                    t_ba = k.a(A.copy, ba[0:16, :], k.ps[b][0:16, 0:T], w=[t])
                    k.close(b, [t_ba])
                    T_ = {}

                    def quad(x, c, q):
                        return x[:, c, q * 4:q * 4 + 4]

                    def bq(b):
                        return k.ps[b][:, :].rearrange("p (h c) -> p h c", c=P)

                    def decays():
                        b = k.bank()
                        for c in range(2):
                            tt = k.tr(k.ps[b][:, c * 16:(c + 1) * 16], ba[0:16, c * P:(c + 1) * P], ident[0:16, 0:16],
                                      w=[t_ba], inc=c == 1)
                        p4 = k.ps[b][:, 0:32].rearrange("p (c w h) -> p c w h", c=2, w=2)
                        t1 = k.v(V.tensor_copy, sm[:, 0], p4[:, :, 0], w=[tt])
                        t2 = k.v(V.tensor_tensor, sm[:, 1], p4[:, :, 1],
                                 Q("dtb", j * 8, 8).unsqueeze(1).to_broadcast([P, 2, 8]), op=ALU.add, w=[tt, d_c2])
                        k.close(b, [t2])
                        ta = k.a(A.activation, sm[:, 2:4], sm[:, 0:2], ACT.Abs, w=[t1, t2])
                        ta = k.a(A.activation, sm[:, 2:4], sm[:, 2:4], ACT.Exp, scale=-1.0, w=[ta])
                        t1 = k.v(V.tensor_scalar, sm[:, 4], sm[:, 0], 0.0, None, ALU.min, w=[t1])
                        tb = k.a(A.activation, sm[:, 4], sm[:, 4], ACT.Exp, w=[t1])
                        tc = k.a(A.activation, sm[:, 5, 0], Q("alog", j * 8, 8), ACT.Exp)
                        td = k.a(A.activation, sm[:, 6], sm[:, 3], ACT.Ln, bias=one, w=[ta, t_cst])
                        t1 = k.v(V.tensor_scalar, sm[:, 2], sm[:, 2], 1.0, None, ALU.add, w=[ta])
                        t1 = k.v(V.reciprocal, sm[:, 2], sm[:, 2], w=[t1])
                        T_["beta"] = k.v(V.tensor_tensor, sm[:, 0], sm[:, 4], sm[:, 2], op=ALU.mult, w=[t1, tb])
                        t2 = k.v(V.scalar_tensor_tensor, sm[:, 1], sm[:, 1], 0.0, sm[:, 6], ALU.max, ALU.add, w=[td])
                        tg = k.v(V.scalar_tensor_tensor, sm[:, 1], sm[:, 1], -1.0,
                                 sm[:, 5, 0].unsqueeze(1).to_broadcast([P, 2, 8]), ALU.mult, ALU.mult, w=[t2, tc])
                        yield
                        b = k.bank()
                        tt = k.mm(k.ps[b][:, 0:16], Q("SL"), sm[:, 1].rearrange("p c h -> p (c h)"), True, True,
                                  w=[tg, d_c2], inc=True)
                        T_["eR"] = k.a(A.activation, sm[:, 6].rearrange("p c h -> p (c h)"), k.ps[b][:, 0:16], ACT.Exp,
                                       w=[tt])
                        k.close(b, [T_["eR"]])
                        gu = X
                        for c in range(2):
                            T_["gu", c] = k.g(G.tensor_tensor, gu[:, c], Q("U").unsqueeze(1).to_broadcast([P, 8, P]),
                                              sm[:, 1, c].unsqueeze(2).to_broadcast([P, 8, P]), op=ALU.mult, w=[tg])
                        yield
                        yield
                        for c in range(2):
                            for q in range(2):
                                b = k.bank()
                                tt = k.mm(k.ps[b][:, :], Q("SL"), quad(gu, c, q).rearrange("p h c -> p (h c)"), True,
                                          True, w=[T_["gu", c]], inc=True)
                                ta = k.a(A.activation, quad(DT, c, q), bq(b), ACT.Exp, w=[tt])
                                k.close(b, [ta])
                                T_["DT", c, q] = k.g(G.tensor_tensor, quad(DT, c, q), quad(DT, c, q),
                                                     Q("U").unsqueeze(1).to_broadcast([P, 4, P]), op=ALU.mult, w=[ta])
                            yield
                        for q in range(2):
                            b = k.bank()
                            tt = k.mm(k.ps[b][:, :], Q("ones"), quad(gu, 1, q).rearrange("p h c -> p (h c)"), True, True,
                                      w=[T_["gu", 1]], inc=True)
                            T_["EG", q] = k.a(A.activation, EG[:, q * 4:q * 4 + 4], bq(b), ACT.Exp, w=[tt])
                            k.close(b, [T_["EG", q]])
                        T_["guf"] = tt
                        yield

                    t_cv = {}

                    def conv(which, dst, key):
                        for h in range(8):
                            b, t = ws_tile(k, st, key, H, htok, T)
                            ps = k.ps[b][:, 0:T]
                            w_ = [Q("gcw", (j * 4 + tap) * 24 + which * 8 + h, 1) for tap in range(4)]
                            ta = k.a(A.activation, dst[:, h], ps, ACT.Identity, scale=w_[3], w=[t, T_.get(("dst", which))])
                            for n in (1, 2, 3):
                                ta = k.v(V.scalar_tensor_tensor, dst[:, h, n:T], ps[:, 0:T - n], w_[3 - n],
                                         dst[:, h, n:T], ALU.mult, ALU.add, w=[ta])
                            k.close(b, [ta])
                            t_cv[which, h] = ta
                            k.tick()
                        T_["f", which] = k.a(A.activation, dst[:, :], dst[:, :], ACT.Silu,
                                             w=[t_cv[which, h] for h in range(8)])

                    def inverse():
                        kk = {}
                        for c in range(2):
                            for q in range(2):
                                b = k.bank()
                                for h in range(4):
                                    kh = kf[:, q * 4 + h, c * P:(c + 1) * P]
                                    tt = k.mm(k.ps[b][:, h * P:(h + 1) * P], kh, kh, True, True, w=[T_["f", 1]],
                                              inc=h == 3)
                                kk[c, q] = (b, tt)
                            yield
                        t1 = []
                        for c in range(2):
                            for h in range(8):
                                b, tt = kk[c, h // 4]
                                n = c * 8 + h
                                t1.append(k.v(V.tensor_tensor_reduce, out=jk[:, n % 2],
                                              in0=k.ps[b][:, (h % 4) * P:(h % 4 + 1) * P], in1=ident, scale=1.0,
                                              scalar=0.0, op0=ALU.mult, op1=ALU.add, accum_out=sm[:, 7, c, h:h + 1],
                                              w=[tt, t1[-2:-1]]))
                        t1 = k.v(V.tensor_scalar, sm[:, 7], sm[:, 7], EPS, None, ALU.add, w=t1[-1:])
                        T_["root"] = k.g(G.tensor_tensor, sm[:, 8].rearrange("p c h -> p (c h)"),
                                         sm[:, 7].rearrange("p c h -> p (c h)"), cst[:, 1], op=ALU.pow, w=[t1, t_cst])
                        t1 = k.v(V.reciprocal, sm[:, 9], sm[:, 7], w=[t1])
                        t1 = k.v(V.tensor_tensor, sm[:, 9], sm[:, 9], sm[:, 0], op=ALU.mult, w=[t1, T_["beta"]])
                        T_["w"] = t1
                        tn = k.v(V.tensor_scalar, sm[:, 10], sm[:, 9], -1.0, None, ALU.mult, w=[t1])
                        T_["eRw"] = k.v(V.tensor_tensor, sm[:, 11], sm[:, 9], sm[:, 6], op=ALU.mult, w=[t1, T_["eR"]])
                        yield
                        tY, tX, tP = {}, {}, {}
                        m1 = Q("mT").rearrange("p (l c) -> p l c", c=P)
                        for c in range(2):
                            for q in range(2):
                                b, tt = kk[c, q]
                                for h in range(4):
                                    tl = k.v(V.scalar_tensor_tensor, LT[:, c, q * 4 + h],
                                             k.ps[b][:, h * P:(h + 1) * P], sm[:, 10, c, q * 4 + h:q * 4 + h + 1],
                                             DT[:, c, q * 4 + h], ALU.mult, ALU.mult, w=[tn, T_["DT", c, q]])
                                k.close(b, [tl])
                                T_["LT", c, q] = tl
                                t1 = k.g(G.tensor_tensor, quad(Y, c, q), quad(LT, c, q),
                                         m1[:, 0].unsqueeze(1).to_broadcast([P, 4, P]), op=ALU.mult, w=[tl])
                                tY[c, q] = k.g(G.tensor_tensor, quad(Y, c, q), quad(Y, c, q),
                                               ident.unsqueeze(1).to_broadcast([P, 4, P]), op=ALU.add, w=[t1])
                            yield
                        qs = [(c, q) for c in range(2) for q in range(2)]

                        def flip(src, dst, c, q, w):
                            b = k.bank()
                            for h in range(4):
                                tt = k.tr(k.ps[b][:, h * P:(h + 1) * P], src[:, c, q * 4 + h], ident, w=w, inc=h == 3)
                            ta = k.a(A.copy, quad(dst, c, q), bq(b), w=[tt])
                            k.close(b, [ta])
                            return ta, tt

                        yield
                        for c, q in qs:
                            tX[c, q], _ = flip(Y, X, c, q, [tY[c, q], T_["guf"]])
                        yield
                        mk = Q("mL").rearrange("p (l c) -> p l c", c=P)
                        for lv in range(1, 7):
                            bb = {}
                            for c, q in qs:
                                b = k.bank()
                                for h in range(4):
                                    tt = k.mm(k.ps[b][:, h * P:(h + 1) * P], LT[:, c, q * 4 + h], X[:, c, q * 4 + h],
                                              True, True, w=[tX[c, q], T_["LT", c, q]], inc=h == 3)
                                i = c * 2 + q
                                tP[c, q] = k.v(V.tensor_tensor, Pm[:, i], bq(b),
                                               mk[:, lv].unsqueeze(1).to_broadcast([P, 4, P]), op=ALU.mult, w=[tt])
                                k.close(b, [tP[c, q]])
                            yield
                            for c, q in qs:
                                i = c * 2 + q
                                b = k.bank()
                                for h in range(4):
                                    if lv < 6:
                                        l_, r_ = Y[:, c, q * 4 + h], Pm[:, i, h]
                                    else:
                                        l_, r_ = Pm[:, i, h], Y[:, c, q * 4 + h]
                                    tt = k.mm(k.ps[b][:, h * P:(h + 1) * P], l_, r_, True, True,
                                              w=[tP[c, q], tY[c, q]], inc=h == 3)
                                dst = X if lv < 6 else Y
                                tv = k.v(V.tensor_tensor, quad(dst, c, q), quad(dst, c, q), bq(b), op=ALU.add, w=[tt])
                                k.close(b, [tv])
                                if lv < 6:
                                    tX[c, q] = tv
                                else:
                                    T_["Y", c, q] = tv
                            yield
                            if lv < 6:
                                for c, q in qs:
                                    tY[c, q], _ = flip(X, Y, c, q, [tX[c, q]])
                                yield

                    def queries():
                        for c in range(2):
                            for q in range(2):
                                b = k.bank()
                                for h in range(4):
                                    n = q * 4 + h
                                    tt = k.mm(k.ps[b][:, h * P:(h + 1) * P], kf[:, n, c * P:(c + 1) * P],
                                              qf[:, n, c * P:(c + 1) * P], True, True, w=[T_["f", 0]], inc=h == 3)
                                for h in range(4):
                                    n = q * 4 + h
                                    ta = k.v(V.scalar_tensor_tensor, DT[:, c, n], k.ps[b][:, h * P:(h + 1) * P],
                                             sm[:, 9, c, n:n + 1], DT[:, c, n], ALU.mult, ALU.mult,
                                             w=[tt, T_["w"], T_["LT", c, q]])
                                k.close(b, [ta])
                                T_["AT", c, q] = ta
                            yield
                        kq = {}
                        for w_, src in ((0, qf), (1, kf)):
                            kq[w_] = None
                        q2 = LT.rearrange("p c h t -> p (c h t)").rearrange("p (h t) -> p h t", t=T)
                        T_["q2done"] = k.a(A.activation, q2[:, :], qf[:, :], ACT.Square,
                                           w=[T_["f", 0], T_["Y", 0, 0], T_["Y", 0, 1], T_["Y", 1, 0], T_["Y", 1, 1]])
                        yield
                        for c in range(2):
                            for q in range(2):
                                b = k.bank()
                                for h in range(4):
                                    tt = k.mm(k.ps[b][:, h * P:(h + 1) * P], q2[:, q * 4 + h, c * P:(c + 1) * P],
                                              Q("ones"), True, True, w=[T_["q2done"]], inc=h == 3)
                                tv = k.v(V.tensor_scalar, sm[:, 3, c, q * 4:q * 4 + 4],
                                         bq(b)[:, :, 0], EPS, EPS * P, ALU.add, ALU.mult, w=[tt])
                                k.close(b, [tv])
                                T_["qe", c, q] = tv
                        yield

                    def values():
                        for c in range(2):
                            for q in range(2):
                                b = k.bank()
                                for h in range(4):
                                    tt = k.tr(k.ps[b][:, h * P:(h + 1) * P], vf[:, q * 4 + h, c * P:(c + 1) * P], ident,
                                              w=[T_["f", 2]], inc=h == 3)
                                T_["R", c, q] = k.v(V.tensor_tensor, quad(R, c, q), bq(b),
                                                    sm[:, 8, c, q * 4:q * 4 + 4].unsqueeze(2).to_broadcast([P, 4, P]),
                                                    op=ALU.mult, w=[tt, T_["root"]])
                                k.close(b, [T_["R", c, q]])
                        T_["vT"] = tt
                        yield
                        for q in range(2):
                            b = k.bank()
                            for h in range(4):
                                tt = k.tr(k.ps[b][:, h * P:(h + 1) * P], kf[:, q * 4 + h, 0:P], ident, w=[T_["f", 1]],
                                          inc=h == 3)
                            T_["kd", q] = k.v(V.tensor_tensor, kd[:, q * 4:q * 4 + 4], bq(b),
                                              sm[:, 11, 0, q * 4:q * 4 + 4].unsqueeze(2).to_broadcast([P, 4, P]),
                                              op=ALU.mult, w=[tt, T_["eRw"]])
                            k.close(b, [T_["kd", q]])
                        yield

                    def apply(c, q):
                        b = k.bank()
                        for h in range(4):
                            n = q * 4 + h
                            tt = k.mm(k.ps[b][:, h * P:(h + 1) * P], Y[:, c, n], R[:, c, n], True, True,
                                      w=[T_["Y", c, q], T_["R", c, q]], inc=h == 3)
                        T_["Z", c, q] = k.a(A.copy, quad(R, c, q), bq(b), w=[tt])
                        k.close(b, [T_["Z", c, q]])

                    ht = {}

                    def outputs():
                        for q in range(2):
                            apply(0, q)
                        for q in range(2):
                            e4 = EG[:, q * 4:q * 4 + 4]
                            k4 = kf[:, q * 4:q * 4 + 4, P:T]
                            q4 = qf[:, q * 4:q * 4 + 4, P:T]
                            T_["k1", q] = k.g(G.tensor_tensor, k4, k4, e4, op=ALU.mult,
                                              w=[T_["EG", q], T_["AT", 1, q], T_["kd", q]])
                            T_["q1", q] = k.g(G.tensor_tensor, q4, q4, e4, op=ALU.mult,
                                              w=[T_["EG", q], T_["AT", 1, q], T_["q2done"]])
                        yield
                        for q in range(2):
                            b = k.bank()
                            for h in range(4):
                                n = q * 4 + h
                                tt = k.mm(k.ps[b][:, h * P:(h + 1) * P], kd[:, n], R[:, 0, n], True, True,
                                          w=[T_["kd", q], T_["Z", 0, q]], inc=h == 3)
                            T_["S", q] = k.a(A.copy, S1[:, q * 4:q * 4 + 4], bq(b), w=[tt])
                            k.close(b, [T_["S", q]])
                        yield
                        for q in range(2):
                            b = k.bank()
                            for h in range(4):
                                n = q * 4 + h
                                tt = k.mm(k.ps[b][:, h * P:(h + 1) * P], kf[:, n, P:T], S1[:, n], True, True,
                                          w=[T_["k1", q], T_["S", q]], inc=h == 3)
                            T_["R", 1, q] = k.v(V.tensor_tensor, quad(R, 1, q), quad(R, 1, q), bq(b), op=ALU.subtract,
                                                w=[tt, T_["R", 1, q]])
                            k.close(b, [T_["R", 1, q]])
                        yield
                        to = {}
                        for q in range(2):
                            apply(1, q)
                        for q in range(2):
                            b = k.bank()
                            for h in range(4):
                                n = q * 4 + h
                                tt = k.mm(k.ps[b][:, h * P:(h + 1) * P], DT[:, 0, n], R[:, 0, n], True, True,
                                          w=[T_["AT", 0, q], T_["Z", 0, q]], inc=h == 3)
                            to[0, q] = (b, tt)
                        yield
                        for q in range(2):
                            b = k.bank()
                            for h in range(4):
                                n = q * 4 + h
                                o = k.ps[b][:, h * P:(h + 1) * P]
                                k.mm(o, qf[:, n, P:T], S1[:, n], True, False, w=[T_["q1", q], T_["S", q]])
                                tt = k.mm(o, DT[:, 1, n], R[:, 1, n], False, True, w=[T_["AT", 1, q], T_["Z", 1, q]],
                                          inc=h == 3)
                            to[1, q] = (b, tt)
                        yield
                        ty, old = {}, None
                        n = 0
                        for c in range(2):
                            for q in range(2):
                                b, tt = to[c, q]
                                old, ty[c, q] = norm_out(s, b, c, q, 4, (sm[:, 3, c, q * 4:q * 4 + 4], T_["qe", c, q]),
                                                         gate, ost[:, n % 2], sq[:, :], tt, T_["gate", c, q], old)
                                n += 1
                        yield
                        for c in range(2):
                            for q in range(2):
                                tokens_H(gate, c, q, ty[c, q], ht)
                        yield

                    k.bg.append(decays())
                    conv(1, kf, f"gdn{j}_k")
                    k.bg.append(inverse())
                    conv(0, qf, f"gdn{j}_q")
                    conv(2, vf, f"gdn{j}_v")
                    k.bg.append(values())

                    for hf in range(2):
                        def evac_z(tile, b, t, hf=hf):
                            while "vT" not in T_:
                                k.tick()
                            g_ = gate[:, tile, hf * 512:(hf + 1) * 512]
                            ta = k.a(A.activation, g_, k.ps[b][:, :], ACT.Silu, w=[t, T_["vT"]])
                            k.close(b, [ta])
                            g4 = g_.rearrange("p (h d) -> p h d", d=P)
                            T_["gate", tile, hf] = k.g(G.tensor_tensor, g4, g4,
                                                       Q("gnw", j * P, P).unsqueeze(1).to_broadcast([P, 4, P]),
                                                       op=ALU.mult, w=[ta])
                        as_group(k, st, f"gdn{j}_z", H, t_h, [0, 1], evac=evac_z)
                    k.bg.append(queries())
                    k.bg.append(outputs())
                    k.drain()
                return down_ln(f"gdn{j}_out", KT, x_H, lambda kt: list(ht.values()), d_ln)

            def decayed(s, nh, g, t_g, qf, kf, vt, t_qk, t_v, gate, t_gate, ht):
                dv = D // nh
                NS = 8
                mexp = s.sb("mexp", [P, 12 * P], F32R)
                E = s.sb("E", [P, 2, NS, 2, T])
                AT = s.sb("AT", [P, 2, 4, P])
                AX1 = s.sb("AX1", [P, 2, P])
                sq = s.sb("osq", [P, 512])
                ost = s.sb("ost", [P, 2, 3, 4])
                raw = E[:, 0, 0:3].rearrange("p l h t -> p (l h t)")
                d_m = k.dma("g", raw, mexp_in, w=k.last())
                t_m = k.a(A.copy, mexp[:, :], raw, w=[d_m])
                slots = list(range(4)) + [5, 6, 7]
                masks = Q("mT").rearrange("p (l c) -> p l c", c=P)
                t_free, t_atf, t_axf = {}, {}, {}
                ob, t_o = {}, {}
                state = {"old": None, "n": 0}

                def group(gr):
                    i = gr % 2
                    tE = {}
                    for hh in range(2):
                        h = gr * 2 + hh
                        for tile in range(2):
                            for part in range(2):
                                b = k.bank()
                                c0 = (4 + 4 * tile) * P if part else 0
                                rhs = mexp[:, c0:c0 + 512]
                                k.mm(k.ps[b][:, :], g[0][:, tile, h * P:(h + 1) * P], rhs, True, False,
                                     w=[t_g, t_m])
                                tt = k.mm(k.ps[b][:, :], g[1][:, tile, h * P:(h + 1) * P], rhs, False, True, inc=True)
                                s0 = 4 if part else 0
                                tE[hh, tile, part] = k.a(
                                    A.activation, E[:, i, s0:s0 + 4, hh, tile * P:(tile + 1) * P],
                                    k.ps[b][:, :].rearrange("p (l c) -> p l c", c=P), ACT.Exp,
                                    w=[tt, t_free.get(gr - 2)])
                                k.close(b, [tE[hh, tile, part]])
                            yield
                    tE = list(tE.values())
                    hs = slice(gr * 2, gr * 2 + 2)
                    tq = {}
                    for lv in range(7):
                        bl = 64 >> lv
                        sl = slots[lv]
                        view = lambda a: a.rearrange("p h (n y c) -> p (h n) y c", y=2, c=bl)
                        e_ = view(E[:, i, sl])
                        for y, src in ((0, kf), (1, qf)):
                            x_ = view(src[:, hs])[:, :, y]
                            eng = k.g if lv in (1, 3) else k.v
                            f_ = G.tensor_tensor if lv in (1, 3) else V.tensor_tensor
                            tq[lv, y] = eng(f_, e_[:, :, y], e_[:, :, y], x_, op=ALU.mult, w=[tE, t_qk])
                        if lv % 2:
                            yield
                    tx = [k.v(V.tensor_tensor, E[:, i, 4, :, 0:P], E[:, i, 4, :, 0:P], kf[:, hs, 0:P], op=ALU.mult,
                              w=[tE, t_qk]),
                          k.v(V.tensor_tensor, E[:, i, 4, :, P:T], E[:, i, 4, :, P:T], qf[:, hs, P:T], op=ALU.mult,
                              w=[tE, t_qk])]
                    ta = k.g(G.memset, AT[:, i], 0.0, w=[t_atf.get(gr - 2)])
                    yield
                    for lv in range(8):
                        b = k.bank()
                        for hh in range(2):
                            for tile in range(2):
                                c = slice(tile * P, (tile + 1) * P)
                                if lv < 7:
                                    l_ = r_ = E[:, i, slots[lv], hh, c]
                                    w = [tq[lv, 0], tq[lv, 1]]
                                else:
                                    l_, r_ = kf[:, gr * 2 + hh, c], qf[:, gr * 2 + hh, c]
                                    w = [t_qk]
                                n = hh * 2 + tile
                                tt = k.mm(k.ps[b][:, n * P:(n + 1) * P], l_, r_, True, True, w=w, inc=n == 3)
                        mask = masks[:, 6 - lv] if lv < 7 else ident
                        ta = k.v(V.copy_predicated, AT[:, i],
                                 mask.bitcast(U32).unsqueeze(1).to_broadcast([P, 4, P]),
                                 k.ps[b][:, :].rearrange("p (n c) -> p n c", c=P), w=[tt, ta])
                        k.close(b, [ta])
                        if lv % 2:
                            yield
                    b = k.bank()
                    for hh in range(2):
                        tt = k.mm(k.ps[b][:, hh * P:(hh + 1) * P], E[:, i, 4, hh, 0:P], E[:, i, 4, hh, P:T], True, True,
                                  w=[tx], inc=hh == 1)
                    t_free[gr] = tt
                    tc = k.a(A.copy, AX1[:, :], k.ps[b][:, 0:256].rearrange("p (n c) -> p n c", c=P),
                             w=[tt, t_axf.get(gr - 1)])
                    k.close(b, [tc])
                    yield
                    for tile in range(2):
                        while ("v", tile) not in t_v:
                            yield
                    per = 512 // dv
                    for hh in range(2):
                        h = gr * 2 + hh
                        hf, col = h // per, (h % per) * dv
                        for tile in range(2):
                            if (tile, hf) not in ob:
                                ob[tile, hf] = k.bank()
                            o = k.ps[ob[tile, hf]][:, col:col + dv]
                            vs = slice(h * dv, (h + 1) * dv)
                            tt = k.mm(o, AT[:, i, hh * 2 + tile], vt[:, tile, vs], True, tile == 0, w=[ta, t_v["v", tile]],
                                      inc=tile == 0)
                            if tile:
                                tt = k.mm(o, AX1[:, hh], vt[:, 0, vs], False, True, w=[tc, t_v["v", 0]], inc=True)
                            t_o[tile, hf] = tt
                    t_atf[gr] = t_axf[gr] = tt
                    yield
                    if (gr * 2 + 2) % per == 0:
                        for tile in range(2):
                            while (tile, hf) not in t_gate:
                                yield
                            n = state["n"]
                            state["n"] += 1
                            state["old"], ty = norm_out(s, ob[tile, hf], tile, hf, per, None, gate, ost[:, n % 2],
                                                        sq[:, :], t_o[tile, hf], t_gate[tile, hf], state["old"])
                            state[tile, hf] = ty
                        yield

                def finish_():
                    for hf in range(2):
                        for tile in range(2):
                            tokens_H(gate, tile, hf, state[tile, hf], ht)
                    yield

                for gr in range(nh // 2):
                    k.bg.append(group(gr))
                return finish_

            def heads_ws(key, dst, n, htok):
                toks = []
                for h in range(n):
                    b, t = ws_tile(k, st, key, H, htok, T)
                    ta = k.a(A.copy, dst[:, h], k.ps[b][:, 0:T], w=[t])
                    k.close(b, [ta])
                    toks.append(ta)
                    k.tick()
                return toks

            def values_gates(key_v, key_g, t_h, vt, gate, norm, dv, t_v, t_gate):
                for hf in range(2):
                    def ev(tile, b, t, hf=hf):
                        ta = k.a(A.copy, vt[:, tile, hf * 512:(hf + 1) * 512], k.ps[b][:, :], w=[t])
                        k.close(b, [ta])
                        if hf:
                            t_v["v", tile] = [ta]
                    as_group(k, st, key_v, H, t_h, [0, 1], evac=ev)
                for hf in range(2):
                    def ev(tile, b, t, hf=hf):
                        g_ = gate[:, tile, hf * 512:(hf + 1) * 512]
                        ta = k.a(A.activation, g_, k.ps[b][:, :], ACT.Silu, w=[t])
                        k.close(b, [ta])
                        g4 = g_.rearrange("p (h d) -> p h d", d=dv)
                        t_gate[tile, hf] = k.g(G.tensor_tensor, g4, g4,
                                               norm.unsqueeze(1).to_broadcast([P, 512 // dv, dv]), op=ALU.mult, w=[ta])
                    as_group(k, st, key_g, H, t_h, [0, 1], evac=ev)

            def split_tokens(src, dst, t_src, nh):
                toks = []
                for tile in range(2):
                    for q in range(nh // 4):
                        b = k.bank()
                        for h in range(4):
                            tt = k.tr(k.ps[b][:, h * P:(h + 1) * P], src[:, q * 4 + h, tile * P:(tile + 1) * P], ident,
                                      w=[t_src], inc=h == 3)
                        c = slice(q * 512, (q + 1) * 512)
                        ts = split_bank(k, k.ps[b][:, :], dst[0][:, tile, c], dst[1][:, tile, c], [tt])
                        k.close(b, [ts[1]])
                        toks += ts
                    yield
                return toks

            def hgrn(t_h, d_ln):
                with Scope(k) as s:
                    kf = s.sb("kf", [P, 8, T])
                    qf = s.sb("qf", [P, 8, T])
                    gh = s.sb("gh", [P, 2, D], F32R)
                    gl = s.sb("gl", [P, 2, D], F32R)
                    vt = s.sb("vt", [P, 2, D])
                    gate = s.sb("gate", [P, 2, D])
                    htok = list(t_h.values())
                    t_v, t_gate, ht = {}, {}, {}
                    with Scope(k) as sf:
                        t1_ = sf.sb("t1", [P, 8, T])
                        t2_ = sf.sb("t2", [P, 8, T])
                        t3_ = sf.sb("t3", [P, 8, T])
                        tf = heads_ws("hg_f", kf, 8, htok)
                        done = []

                        def forget():
                            bc = lambda r: lb[:, r].unsqueeze(2).to_broadcast([P, 8, T])
                            ta = k.a(A.activation, t1_[:, :], kf[:, :], ACT.Abs, w=[tf])
                            ta = k.a(A.activation, t1_[:, :], t1_[:, :], ACT.Exp, scale=-1.0, w=[ta])
                            ta = k.a(A.activation, t1_[:, :], t1_[:, :], ACT.Ln, bias=one, w=[ta, t_cst])
                            yield
                            tv = k.v(V.scalar_tensor_tensor, t2_[:, :], kf[:, :], 0.0, t1_[:, :], ALU.min, ALU.subtract,
                                     w=[ta])
                            tk = k.v(V.scalar_tensor_tensor, t3_[:, :], kf[:, :], 0.0, t1_[:, :], ALU.max, ALU.add, w=[ta])
                            tv = k.g(G.tensor_tensor, t2_[:, :], t2_[:, :], bc(2), op=ALU.add, w=[tv, t_lb])
                            yield
                            for h in range(8):
                                tk2 = k.a(A.activation, kf[:, h], t3_[:, h], ACT.Exp, scale=-1.0, bias=lb[:, 1, h:h + 1],
                                          w=[tk, t_lb])
                            ta = k.a(A.activation, t1_[:, :], t2_[:, :], ACT.Abs, w=[tv, tk])
                            ta = k.a(A.activation, t1_[:, :], t1_[:, :], ACT.Exp, scale=-1.0, w=[ta])
                            ta = k.a(A.activation, t1_[:, :], t1_[:, :], ACT.Ln, bias=one, w=[ta])
                            yield
                            tv = k.v(V.scalar_tensor_tensor, t2_[:, :], t2_[:, :], 0.0, t1_[:, :], ALU.max, ALU.add,
                                     w=[ta])
                            tv = k.g(G.tensor_tensor, t2_[:, :], t2_[:, :], bc(0), op=ALU.add, w=[tv, t_lb])
                            yield
                            yield
                            toks = yield from split_tokens(t2_, (gh, gl), tv, 8)
                            done.extend([toks, tk2])

                        k.bg.append(forget())
                        tq = heads_ws("hg_q", qf, 8, htok)
                        k.drain()
                        t_q = k.a(A.activation, qf[:, :], qf[:, :], ACT.Silu, w=[tq])
                    fin = decayed(s, 8, (gh, gl), done[0], qf, kf, vt, [t_q, done[1]], t_v, gate, t_gate, ht)
                    values_gates("hg_i", "hg_r", t_h, vt, gate, Q("hgn"), P, t_v, t_gate)
                    k.bg.append(fin())
                    k.drain()
                return down_ln("hg_out", KT, x_H, lambda kt: list(ht.values()), d_ln)

            def gla(t_h, d_ln):
                with Scope(k) as s:
                    kf = s.sb("kf", [P, 4, T])
                    qf = s.sb("qf", [P, 4, T])
                    gh = s.sb("gh", [P, 2, 512], F32R)
                    gl = s.sb("gl", [P, 2, 512], F32R)
                    vt = s.sb("vt", [P, 2, D])
                    gate = s.sb("gate", [P, 2, D])
                    gk = s.sb("gk", [32, T])
                    p_ = s.sb("p", [P, 2, 512])
                    l_ = s.sb("l", [P, 2, 512])
                    htok = list(t_h.values())
                    t_v, t_gate, ht = {}, {}, {}
                    proj = small_proj(s, "wgk", 0)
                    b, t = proj(htok)
                    t_one = k.v(V.memset, gk[:, :], 1.0)
                    t_gk = k.a(A.copy, gk[0:16, :], k.ps[b][0:16, 0:T], w=[t, t_one])
                    k.close(b, [t_gk])
                    tg = []

                    def forget():
                        for tile in range(2):
                            b = k.bank()
                            t = k.mm(k.ps[b][:, :], gk[0:17, tile * P:(tile + 1) * P], Q("wgk2")[0:17], True, True,
                                     w=[t_gk, d_c2], inc=True)
                            tp = k.a(A.copy, p_[:, tile], k.ps[b][:, :], w=[t])
                            k.close(b, [tp])
                        yield
                        ta = k.a(A.activation, l_[:, :], p_[:, :], ACT.Abs, w=[tp])
                        ta = k.a(A.activation, l_[:, :], l_[:, :], ACT.Exp, scale=-1.0, w=[ta])
                        ta = k.a(A.activation, l_[:, :], l_[:, :], ACT.Ln, bias=one, w=[ta, t_cst])
                        yield
                        tv = k.v(V.scalar_tensor_tensor, l_[:, :], p_[:, :], 0.0, l_[:, :], ALU.min, ALU.subtract, w=[ta])
                        ta = k.a(A.activation, gh[:, :], l_[:, :], ACT.Copy, scale=0.0625, w=[tv])
                        tv = k.v(V.scalar_tensor_tensor, gl[:, :], l_[:, :], 0.0625, gh[:, :].bitcast(F32), ALU.mult,
                                 ALU.subtract, w=[ta])
                        tg.extend([ta, tv])

                    k.bg.append(forget())
                    tq = heads_ws("gla_q", qf, 4, htok)
                    tk = heads_ws("gla_k", kf, 4, htok)
                    k.drain()
                    fin = decayed(s, 4, (gh, gl), tg, qf, kf, vt, [tq, tk], t_v, gate, t_gate, ht)
                    values_gates("gla_v", "gla_r", t_h, vt, gate, Q("gln"), 256, t_v, t_gate)
                    k.bg.append(fin())
                    k.drain()
                return down_ln("gla_out", KT, x_H, lambda kt: list(ht.values()), d_ln)

            def ffn(i, t_h, d_ln):
                with Scope(k) as s:
                    hh = s.sb("hh", [P, FT, T], F32R)
                    hl = s.sb("hl", [P, FT, T], F32R)
                    t_hid = ffn_up(s, f"fin{i}", H, list(t_h.values()), hh, hl, None)
                    return down_ln(f"fdn{i}", FT, lambda kt, tile: (hh[:, kt, tile * P:(tile + 1) * P],
                                                                    hl[:, kt, tile * P:(tile + 1) * P]),
                                   lambda kt: t_hid[kt], d_ln)

            for i in range(4):
                mixer = (lambda a, b: gdn(0, a, b), hgrn, gla, lambda a, b: gdn(1, a, b))[i]
                d_ln = load_ln()
                t_h = {t: into_H(t, t_x[t]) for t in range(2)}
                t_x = mixer(t_h, d_ln)
                if stop == 5 + 2 * i:
                    return finish(xt, k.last())
                d_ln = load_ln()
                t_h = {t: into_H(t, t_x[t]) for t in range(2)}
                t_x = ffn(i, t_h, d_ln)
                if stop == 6 + 2 * i:
                    return finish(xt, k.last())
            return finish(xt, list(t_x.values()))



def ws_units(w):
    kk, n = w.shape
    return w.reshape(KT, P, n // P, P).transpose(2, 1, 0, 3).reshape(n // P, P, KT * P)


def as_units(w, cols):
    kk, n = w.shape
    r = UW // cols
    return w.reshape(kk // P // r, r, P, n // cols, cols).transpose(3, 0, 2, 1, 4).reshape(-1, P, UW)


def pair(a, b):
    return np.stack([a, b], 1).reshape(-1, P, UW)


def pack_weights(inp):
    g = lambda name, i=0: np.asarray(inp[name])[i]
    parts = {}
    ev = g("ev_w_in")
    parts["ev_qkv"] = np.concatenate([as_units(ev[:, c:c + 512], 512) for c in (2048, 1536, 2560)])
    parts["ev_conv"] = np.stack([ws_units(ev[:, 512:1024]), ws_units(ev[:, 1024:1536]), ws_units(ev[:, 0:512])],
                                1).reshape(-1, P, UW)
    parts["ev_out"] = as_units(g("ev_w_out"), 512)
    for i in range(2):
        up = g("ffn_w_up", i)
        parts[f"up{i}"] = pair(ws_units(up[:, :F]), ws_units(up[:, F:]))
    parts["down0"] = as_units(g("ffn_w_down", 0), 512)
    parts["down1"] = as_units(g("ffn_w_down", 1), 1024)
    od = g("od_w_in")
    parts["od_in"] = np.concatenate([as_units(od[:, c:c + 512], 512) for c in (512, 1024, 1536, 0)])
    parts["od_out"] = as_units(g("od_w_out"), 1024)
    for j in range(2):
        gd = g("gdn_w_in_2", j)
        for n, c in (("q", 0), ("k", 1024), ("v", 2048)):
            parts[f"gdn{j}_{n}"] = ws_units(gd[:, c:c + 1024])
        parts[f"gdn{j}_z"] = as_units(gd[:, 3072:4096], 512)
        parts[f"gdn{j}_out"] = as_units(g("gdn_w_out_2", j), 1024)
    hg = g("hgrn_w_in_2")
    parts["hg_q"], parts["hg_f"] = ws_units(hg[:, 0:1024]), ws_units(hg[:, 1024:2048])
    parts["hg_i"], parts["hg_r"] = as_units(hg[:, 2048:3072], 512), as_units(hg[:, 3072:4096], 512)
    parts["hg_out"] = as_units(g("hgrn_w_out_2"), 1024)
    gl = g("gla_w_in_2")
    parts["gla_q"], parts["gla_k"] = ws_units(gl[:, 0:512]), ws_units(gl[:, 512:1024])
    parts["gla_v"], parts["gla_r"] = as_units(gl[:, 1024:2048], 512), as_units(gl[:, 2048:3072], 512)
    parts["gla_out"] = as_units(g("gla_w_out_2"), 1024)
    for i in range(4):
        fi = g("ffn_w_in_2", i)
        parts[f"fin{i}"] = pair(ws_units(fi[:, :F]), ws_units(fi[:, F:]))
        parts[f"fdn{i}"] = as_units(g("ffn_w_down_2", i), 1024)
    mw = np.asarray(inp["mod_w"]).transpose(0, 2, 1).reshape(2, 24, 2, P, D).transpose(0, 1, 3, 2, 4).reshape(2, 24, P, CW)
    chunks = {key: v.reshape(-1, 2, P, UW).transpose(0, 2, 1, 3).reshape(-1, P, CW) for key, v in parts.items()}
    plan = weight_chunks()
    out = np.empty((len(plan), P, CW), np.float32)
    for j, (kind, key, i) in enumerate(plan):
        out[j] = mw[key, i] if kind == "m" else chunks[key][i]
    return out


def feat(a):
    a = np.asarray(a)
    return np.moveaxis(a.reshape(*a.shape[:-1], -1, P), -1, 0).reshape(P, -1)


def rows(a):
    a = np.asarray(a).reshape(1, -1)
    return np.broadcast_to(a, (P, a.shape[1]))


def packed(fields, values):
    return np.ascontiguousarray(np.concatenate(
        [np.asarray(values[n], np.float32).reshape(P, -1) for n, size in fields], 1))


def rope():
    t = np.arange(T)
    inv = np.float32(10000.0) ** (-np.arange(16, dtype=np.float32) / np.float32(16))
    ang = np.stack([(t // 64).astype(np.float32)[:, None] * inv, (t % 64).astype(np.float32)[:, None] * inv], 1)
    c, s = np.cos(ang), np.sin(ang)
    cc = np.stack([c, c], 2).reshape(T, 64)
    ss = np.stack([-s, s], 2).reshape(T, 64)
    lay = lambda a: a.reshape(2, P, 64).transpose(1, 0, 2).reshape(P, 128)
    return lay(cc), lay(ss)


def retention_consts():
    j = np.arange(T)[:, None]
    i = np.arange(T)[None, :]
    lay = lambda a: a.reshape(2, P, T).transpose(1, 0, 2).reshape(P, 512)
    f = np.maximum(i - j, 0)
    b = np.maximum(j - i, 0)
    two = (1.0 + (i == j)) * 0.125
    band = np.zeros((4, T, T))
    for g, r in enumerate((1, 2, 4, 8)):
        lo, hi = np.clip(i - r, 0, T), np.clip(i + r + 1, 0, T)
        band[g] = ((j >= lo) & (j < hi)) / (hi - lo) - (i == j)
    bl = band.reshape(4, 2, P, T).transpose(2, 0, 1, 3).reshape(P, 2048)
    return lay(f), lay(b), lay(two), bl


def kernel(**inputs):
    import concourse.bacc as _bacc
    from concourse import mybir as _mybir
    from concourse.bass_utils import run_bass_kernel_spmd as _run

    f32 = _mybir.dt.float32
    inp = {n: np.asarray(v) for n, v in inputs.items()}
    rc, rs = rope()
    df, db, two, band = retention_consts()
    p = np.arange(P)
    t2 = p[:, None] + np.array([0, P])[None, :]
    ramps = np.concatenate([t2 + 1, T - t2, T - 1 - t2, t2], 1)
    core = packed(CORE, {
        "ident": np.eye(P), "n1": feat(inp["norm1_g"]), "n2": feat(inp["norm2_g"]), "modb": feat(inp["mod_b"]),
        "fcw": feat(inp["ffn_conv_w"]), "fcb": feat(inp["ffn_conv_b"]), "scw": feat(inp["sc_conv_w"]),
        "psc": feat(inp["pool_scale"])})
    b1 = packed(B1, {
        "qg": rows(inp["da_q_norm"]), "kg": rows(inp["da_k_norm"]), "lq1": rows(inp["da_lq1"]),
        "lk1": rows(inp["da_lk1"]), "lq2": rows(inp["da_lq2"]), "lk2": rows(inp["da_lk2"]),
        "subg": rows(inp["da_subln_g"]), "ropec": rc, "ropes": rs, "rgn": rows(inp["ret_gn_g"]),
        "decf": rows(inp["ret_decay_f"]), "decb": rows(inp["ret_decay_b"]), "ramps": ramps})
    l1 = packed(L1C, {"dist_f": df, "dist_b": db, "two": two, "band": band,
                      "poolw": inp["pool_w"][0].transpose(1, 0, 2)})
    i, j = p[:, None], p[None, :]
    levels = [((i // (2 * b) == j // (2 * b)) & (i % (2 * b) < b) & (j % (2 * b) >= b)).astype(np.float32)
              for b in (1, 2, 4, 8, 16, 32, 64)]

    def to_middle(b):
        mid = j // (2 * b) * (2 * b) + b
        return np.where(j % (2 * b) >= b, (i >= mid) & (i <= j), (i > j) & (i < mid))

    low = [to_middle(b) for b in (4, 2, 1)]
    mexp = [to_middle(b) for b in (64, 32, 16, 8)] + [i > j] + low + [i <= j] + low
    wgk2 = np.zeros((P, 512), np.float32)
    wgk2[0:16] = inp["gla_w_gk2_2"][0]
    wgk2[16] = inp["gla_b_gk_2"][0]
    cols16 = lambda w: w.reshape(KT, P, 16).transpose(1, 0, 2).reshape(P, KT * 16)
    c2 = packed(C2, {
        "U": i <= j, "SL": i > j, "ones": np.ones((P, P)), "mT": np.concatenate(levels, 1),
        "mL": np.concatenate([m.T for m in levels], 1), "gcw": feat(inp["gdn_conv_w_2"]),
        "lbl": feat(inp["hgrn_lb_logits_2"]), "alog": rows(inp["gdn_a_log_2"]), "dtb": rows(inp["gdn_dt_bias_2"]),
        "gnw": rows(inp["gdn_norm_w_2"]), "hgn": rows(inp["hgrn_norm_w_2"]), "gln": rows(inp["gla_norm_w_2"]),
        "wba": np.concatenate([cols16(inp["gdn_w_in_2"][n][:, 4096:4112]) for n in range(2)], 1),
        "wgk": cols16(inp["gla_w_in_2"][0][:, 3072:3088]), "wgk2": wgk2})
    ln = np.stack([np.stack([inp["mix_ln_g_2"], inp["mix_ln_b_2"]], 1),
                   np.stack([inp["ffn_ln_g_2"], inp["ffn_ln_b_2"]], 1)], 1).reshape(8, 2, D)
    arrays = {
        "w": pack_weights(inp), "x": inp["x"].reshape(2, P, D), "ctx": inp["ctx"].reshape(2, P, D),
        "c": inp["c"].reshape(1, D), "cc": inp["c_ctx"].reshape(1, D), "core": core, "b1": b1, "l1": l1,
        "c2": c2, "ln": np.ascontiguousarray(ln), "mexp": np.concatenate(mexp, 1).astype(np.float32)}
    nc = _bacc.Bacc("TRN2", target_bir_lowering=False, num_devices=1)
    aps = [nc.dram_tensor("in_" + n, a.shape, f32, kind="ExternalInput").ap() for n, a in arrays.items()]
    out = nc.dram_tensor("out", [2, P, D], f32, kind="ExternalOutput").ap()
    fused_block(nc, *aps, out)
    r = _run(nc, [{"in_" + n: a for n, a in arrays.items()}], core_ids=[0])
    return r.results[0]["out"].reshape(1, T, D)
```

```python
from collections import deque
from contextlib import ExitStack

import numpy as np

import concourse.bass as bass
from concourse import mybir

P = 128
D = 1024
KT = D // P
F = 2816
FT = F // P
T = 256
CW = 2048
UW = 1024
NRAW = 3
NHL = 5
LEAD = 3
HELD = 4
EPS = 1e-6
LN_EPS = 1e-5
DN_ALPHA = 8.0 ** 0.25
LAM_INIT = 0.2

F32 = mybir.dt.float32
F32R = mybir.dt.float32r
BF16 = mybir.dt.bfloat16
U32 = mybir.dt.uint32
ALU = mybir.AluOpType
ACT = mybir.ActivationFunctionType
AX = mybir.AxisListType.X



def weight_chunks():
    out = [("m", 0, i) for i in range(8)]
    qkv = [("w", "ev_qkv", i) for i in range(6)]
    conv = [("w", "ev_conv", i) for i in range(6)]
    m0 = [("m", 0, i) for i in range(8, 20)]
    body = qkv + conv
    for i, w in enumerate(body):
        out.append(w)
        out.append(m0[i])
    out += [("w", "ev_out", i) for i in range(4)]
    later = [("m", 0, i) for i in range(20, 24)] + [("m", 1, i) for i in range(24)]
    for i in range(FT):
        out.append(("w", "up0", i))
        if later:
            out.append(later.pop(0))
    for i in range(FT // 2):
        out.append(("w", "down0", i))
        if later:
            out.append(later.pop(0))
    assert not later
    out += [("w", "od_in", i) for i in range(8)]
    out += [("w", "od_out", i) for i in range(4)]
    out += [("w", "up1", i) for i in range(FT)]
    out += [("w", "down1", i) for i in range(FT // 2)]
    gdn = [("z0", 2), ("k", 4), ("q", 4), ("v", 4), ("z1", 2), ("out", 4)]
    mixers = [[("gdn0_" + c, n) for c, n in gdn],
              [("hg_i0", 2), ("hg_f", 4), ("hg_q", 4), ("hg_i1", 2), ("hg_r", 4), ("hg_out", 4)],
              [("gla_v0", 2), ("gla_q", 2), ("gla_k", 2), ("gla_v1", 2), ("gla_r", 4), ("gla_out", 4)],
              [("gdn1_" + c, n) for c, n in gdn]]
    for l in range(4):
        for key, n in mixers[l] + [(f"fin{l}", FT), (f"fdn{l}", FT // 2)]:
            out += [("w", key, i) for i in range(n)]
    return out


CORE = [("ident", 128), ("n1", 16), ("n2", 16), ("modb", 96), ("fcw", 132), ("fcb", 44), ("scw", 12),
        ("psc", 4)]
B1 = [("qg", 64), ("kg", 64), ("lq1", 64), ("lk1", 64), ("lq2", 64), ("lk2", 64), ("subg", 128),
      ("ropec", 128), ("ropes", 128), ("rgn", 128), ("decf", 4), ("decb", 4), ("ramps", 8)]
L1C = [("dist_f", 512), ("dist_b", 512), ("two", 512), ("band", 2048), ("poolw", 512)]

C2 = [("U", 128), ("SL", 128), ("ones", 128), ("mT", 896), ("mL", 896), ("gcw", 192), ("lbl", 32), ("alog", 16),
      ("dtb", 16), ("gnw", 256), ("hgn", 128), ("gln", 256), ("wba", 256), ("wgk", 128), ("wgk2", 512)]


def offsets(fields):
    at, out = 0, {}
    for name, n in fields:
        out[name] = (at, n)
        at += n
    return out, at



class Ev:

    def __init__(self):
        self.tok = None

    def set(self, tok):
        self.tok = tok


class Bank(Ev):

    def set(self, bank, tok):
        self.bank, self.tok = bank, tok


class Evs(dict):
    def __missing__(self, key):
        self[key] = Ev()
        return self[key]


class Slots:

    def __init__(self, n):
        self.idle = deque((i, ()) for i in range(n))
        self.spare = 0

    def take(self):
        return self.idle.popleft()

    def give(self, i, toks):
        self.idle.append((i, toks))


class Core:

    def __init__(self, nc, ctx):
        self.nc = nc
        self.ctx = ctx
        self.eng = {"pe": nc.tensor, "v": nc.vector, "a": nc.scalar, "g": nc.gpsimd, "sp": nc.sync}
        self.sem = {e: ctx.enter_context(nc.semaphore("s_" + e)) for e in self.eng}
        self.by_name = {"s_" + e: s for e, s in self.sem.items()}
        self.n = {e: 0 for e in self.eng}
        self.seen = {e: {} for e in self.eng}
        self.ps = [ctx.enter_context(nc.psum_tensor(f"ps{i}", [P, 512], F32)) for i in range(8)]
        self.banks = Slots(8)
        self.banks.spare = 1
        self.tasks = []
        self.ndma = 0
        self.ntensor = 0
        self.t = {e: 0.0 for e in self.eng}
        self.t["dma"] = 0.0
        self.clock = 0.0
        self.when = {}


    def flat(self, w):
        if w is None:
            return
        if isinstance(w, Ev):
            assert w.tok is not None
            yield from self.flat(w.tok)
        elif isinstance(w, tuple) and len(w) == 2 and isinstance(w[0], str):
            yield w
        else:
            for x in (w.values() if isinstance(w, dict) else w):
                yield from self.flat(x)

    def wait(self, e, w):
        for name, val in self.flat(w):
            self.t[e] = max(self.t[e], self.when.get((name, val), 0.0))
            if self.seen[e].get(name, 0) < val:
                self.eng[e].wait_ge(self.by_name[name], val)
                self.seen[e][name] = val

    def done(self, e, ins):
        self.n[e] += 1
        ins.then_inc(self.sem[e], 1)
        tok = ("s_" + e, self.n[e])
        self.when[tok] = self.t[e] + 0.12
        return tok

    def size(self, a, kw):
        n = 1
        for x in list(a) + list(kw.values()):
            if isinstance(x, bass.AP):
                m = 1
                for d in x.shape[1:]:
                    m *= d
                n = max(n, m)
        return n

    def v(self, f, *a, w=(), **kw):
        self.wait("v", w)
        self.t["v"] += 0.08 + self.size(a, kw) / 960
        return self.done("v", f(*a, **kw))

    def a(self, f, *a, w=(), **kw):
        self.wait("a", w)
        self.t["a"] += 0.15 + self.size(a, kw) / 1200
        return self.done("a", f(*a, **kw))

    def g(self, f, *a, w=(), **kw):
        self.wait("g", w)
        self.t["g"] += 0.3 + self.size(a, kw) / 470
        return self.done("g", f(*a, **kw))

    def mm(self, out, lhsT, rhs, start, stop, w=(), inc=False):
        self.wait("pe", w)
        n = self.size([out], {})
        self.t["pe"] += max(n, 256) / 2400 if rhs.dtype == F32R else max(n, 128) / 600
        ins = self.nc.tensor.matmul(out, lhsT, rhs, start=start, stop=stop)
        return self.done("pe", ins) if inc else None

    def tr(self, out, in_, ident, w=(), inc=False):
        self.wait("pe", w)
        self.t["pe"] += 0.11
        ins = self.nc.tensor.transpose(out, in_, ident)
        return self.done("pe", ins) if inc else None

    def dma_sem(self, name):
        self.by_name[name] = self.ctx.enter_context(self.nc.semaphore(name))
        return name

    def dma(self, e, out, in_, w=()):
        name = self.dma_sem(f"d{self.ndma}")
        self.ndma += 1
        self.wait(e, w)
        self.eng[e].dma_start(out, in_).then_inc(self.by_name[name], 16)
        self.when[name, 16] = max(self.t[e], self.t["dma"]) + 3.0
        return (name, 16)

    def last(self):
        return [("s_" + e, self.n[e]) for e in ("pe", "v", "a", "g")]

    def fence(self, engines=("pe", "v", "a", "g")):
        now = self.last()
        for e in engines:
            self.wait(e, [t for t in now if t[0] != "s_" + e])


    def bank(self):
        while not self.banks.idle:
            self.force()
        b, toks = self.banks.take()
        self.wait("pe", toks)
        return b

    def close(self, b, toks):
        self.banks.give(b, toks)


    def spawn(self, gen):
        self.tasks.append([gen, ()])
        self.step(self.tasks[-1])

    def step(self, task):
        try:
            task[1] = next(task[0])
        except StopIteration:
            self.tasks.remove(task)

    def ready(self, need):
        at, want = 0.0, {}
        for x in need:
            if isinstance(x, Slots):
                want[id(x)] = want.get(id(x), 0) + 1
                if len(x.idle) < want[id(x)] + x.spare:
                    return None
                x = x.idle[want[id(x)] - 1][1]
            for y in self.unset(x):
                return None
            for tok in self.flat(x):
                at = max(at, self.when.get(tok, 0.0))
        return at

    def unset(self, x):
        if isinstance(x, Ev):
            if x.tok is None:
                yield x
            else:
                yield from self.unset(x.tok)
        elif isinstance(x, (list, tuple)):
            for y in x:
                yield from self.unset(y)

    def poll(self):
        again = True
        while again:
            again = False
            now = max(self.t["pe"], self.clock)
            for task in self.tasks:
                at = self.ready(task[1])
                if at is not None and at <= now:
                    self.step(task)
                    again = True
                    break

    def force(self):
        best = None
        for task in self.tasks:
            at = self.ready(task[1])
            if at is not None and (best is None or at < best[0]):
                best = (at, task)
        assert best is not None, "no task can go on"
        self.clock = max(self.clock, best[0])
        self.step(best[1])

    def until(self, evs):
        while any(True for _ in self.unset(evs)):
            self.poll()
            if any(True for _ in self.unset(evs)):
                self.force()

    def drain(self):
        while self.tasks:
            self.poll()
            if self.tasks:
                self.force()


class Scope:

    def __init__(self, k, fenced=False):
        self.k = k
        self.fenced = fenced
        self.st = ExitStack()

    def __enter__(self):
        return self

    def sb(self, name, shape, dt=F32):
        self.k.ntensor += 1
        return self.st.enter_context(self.k.nc.sbuf_tensor(f"{name}_{self.k.ntensor}", shape, dt))

    def __exit__(self, *failed):
        if not any(failed):
            if not self.fenced:
                self.k.drain()
                self.k.fence()
            self.st.close()


class Stream:

    def __init__(self, k, W, plan):
        self.k, self.W, self.plan, self.on_mod = k, W, plan, None
        nc = k.nc
        self.raw = k.ctx.enter_context(nc.sbuf_tensor("raw", [P, NRAW, CW], F32))
        self.hi = k.ctx.enter_context(nc.sbuf_tensor("whi", [P, NHL, UW], F32R))
        self.lo = k.ctx.enter_context(nc.sbuf_tensor("wlo", [P, NHL, UW], F32R))
        self.sems = [k.dma_sem(f"w{i}") for i in range(NRAW)]
        self.units = []
        for j, (kind, key, i) in enumerate(plan):
            self.units += [(j, 0), (j, 1)] if kind == "w" else [(j, None)]
        self.keys = [plan[j][1] for j, h in self.units if h is not None]
        self.pos = 0
        self.made = 0
        self.tok = {}
        self.freed = {}
        self.nfreed = 0
        self.taken = 0
        for j in range(NRAW):
            self.load(j, ())

    def load(self, j, w):
        if j < len(self.plan):
            k, s = self.k, j % NRAW
            k.wait("sp", w)
            k.nc.sync.dma_start(self.raw[:, s], self.W[j]).then_inc(k.by_name[self.sems[s]], 16)
            k.t["dma"] = max(k.t["dma"], k.t["sp"] + 1.5) + 2.9
            k.when[self.landed(j)] = k.t["dma"] + 0.5

    def landed(self, j):
        return (self.sems[j % NRAW], 16 * (j // NRAW + 1))

    def pump(self, upto, now=None):
        k, nc = self.k, self.k.nc
        while self.pos < len(self.units):
            j, h = self.units[self.pos]
            s = j % NRAW
            u = self.made
            if u > upto or (h is not None and u - NHL >= self.nfreed):
                break
            old = self.freed[u - NHL] if h is not None and u >= NHL else None
            if now is not None and max(k.when[self.landed(j)], k.when.get(old, 0.0)) > now:
                break
            if h is None:
                t = self.on_mod(self.plan[j], self.raw[:, s], self.landed(j))
                self.load(j + NRAW, t)
            else:
                q = u % NHL
                src = self.raw[:, s, h * UW:(h + 1) * UW]
                ta = k.a(nc.scalar.copy, self.hi[:, q], src, w=[self.landed(j), old])
                tv = k.v(nc.vector.tensor_tensor, self.lo[:, q], src, self.hi[:, q].bitcast(F32),
                         op=ALU.subtract, w=[ta])
                self.tok[u] = [ta, tv]
                if h == 1:
                    self.load(j + NRAW, [ta, tv])
                self.made += 1
            self.pos += 1

    def take(self, key):
        u = self.taken
        assert self.keys[u] == key, (u, self.keys[u], key)
        self.poll()
        self.pump(u)
        assert self.made > u
        self.taken += 1
        return u

    def poll(self):
        self.k.poll()
        self.pump(self.taken + LEAD, max(self.k.t["pe"], self.k.clock))

    def parts(self, u):
        return self.hi[:, u % NHL], self.lo[:, u % NHL], self.tok[u]

    def free(self, u, tok):
        assert u == self.nfreed
        self.freed[u] = tok
        self.nfreed += 1


def as3(k, out, xh, xl, wh, wl, first, last, w=(), inc=False):
    k.mm(out, xh, wh, first, False, w=w)
    k.mm(out, xh, wl, False, False)
    return k.mm(out, xl, wh, False, last, inc=inc)


def ws3(k, out, wh, wl, xh, xl, first, last, w=(), inc=False):
    k.mm(out, wh, xh, first, False, w=w)
    k.mm(out, wh, xl, False, False)
    return k.mm(out, wl, xh, False, last, inc=inc)


def ws_tile(k, st, key, H, htok, ntok):
    u = st.take(key)
    k.until(htok)
    wh, wl, wt = st.parts(u)
    b = k.bank()
    out = k.ps[b][:, 0:ntok]
    for kt in range(KT):
        c = slice(kt * P, (kt + 1) * P)
        t = ws3(k, out, wh[:, c], wl[:, c], H[0][:, kt, 0:ntok], H[1][:, kt, 0:ntok], kt == 0, kt == KT - 1,
                w=[wt, htok] if kt == 0 else (), inc=kt == KT - 1)
        if ntok > T and kt == 3:
            st.poll()
    st.free(u, t)
    return b, t


def as_group(k, st, key, H, htok, tiles, cols=(0, 512), evac=None):
    us = [st.take(key) for i in range(KT // 2)]
    wts = [st.parts(u) for u in us]
    for n, tile in enumerate(tiles):
        lo, hi = cols[tile] if isinstance(cols, dict) else cols
        k.until(htok[tile])
        b = k.bank()
        out = k.ps[b][:, 0:hi - lo]
        for kt in range(KT):
            wh, wl, wt = wts[kt // 2]
            c = slice((kt % 2) * 512 + lo, (kt % 2) * 512 + hi)
            x = slice(tile * P, (tile + 1) * P)
            t = as3(k, out, H[0][:, kt, x], H[1][:, kt, x], wh[:, c], wl[:, c], kt == 0, kt == KT - 1,
                    w=[wt, htok[tile]], inc=kt == KT - 1 or (n == len(tiles) - 1 and kt % 2 == 1))
            if kt % 2 == 1:
                if n == len(tiles) - 1:
                    st.free(us[kt // 2], t)
                if kt < KT - 1:
                    st.poll()
        evac(tile, b, t)
        st.poll()


def down(k, st, key, nk, x, xtok, evac, ready=None):
    bs = [[k.bank(), k.bank()] for _ in range(2)]
    us = {}

    def part(kt, tile, hf, inc):
        wh, wl, wt = st.parts(us[kt])
        k.until(xtok(kt, tile))
        xh, xl = x(kt, tile)
        c = slice(hf * 512, (hf + 1) * 512)
        return as3(k, k.ps[bs[tile][hf]][:, :], xh, xl, wh[:, c], wl[:, c], kt == 0, kt == nk - 1,
                   w=[wt, xtok(kt, tile)], inc=inc)

    for kt in range(nk - HELD):
        us[kt] = st.take(key)
        for tile in range(2):
            for hf in range(2):
                t = part(kt, tile, hf, tile == 1 and hf == 1)
        st.free(us[kt], t)
    for tile in range(2):
        for hf in range(2):
            for kt in range(nk - HELD, nk):
                if tile == 0 and hf == 0:
                    us[kt] = st.take(key)
                free = tile == 1 and hf == 1
                t = part(kt, tile, hf, free or kt == nk - 1)
                if free:
                    st.free(us[kt], t)
                    st.poll()
            if tile == 0 and hf == 0 and ready:
                k.until([xtok(kt, i) for kt in range(nk) for i in range(2)])
                ready()
            evac(tile, hf, bs[tile][hf], t)
            st.poll()


def split(k, src, hi, lo, w):
    ta = k.a(k.nc.scalar.copy, hi, src, w=w)
    tv = k.v(k.nc.vector.tensor_tensor, lo, src, hi.bitcast(F32), op=ALU.subtract, w=[ta, w])
    return [ta, tv]


def fused_block(nc, W, x_in, ctx_in, c_in, cc_in, core_in, b1_in, l1_in, c2_in, ln_in, mexp_in, out, stop=99):
    with ExitStack() as ctx:
        k = Core(nc, ctx)
        V, A, G = nc.vector, nc.scalar, nc.gpsimd
        CO, ncore = offsets(CORE)
        core = ctx.enter_context(nc.sbuf_tensor("core", [P, ncore], F32))
        xt = ctx.enter_context(nc.sbuf_tensor("xt", [P, 4, D], F32))
        half = ctx.enter_context(nc.sbuf_tensor("half", [P, 16], F32))
        st = Stream(k, W, weight_chunks())

        def C(name, i=0, n=None):
            at, size = CO[name]
            return core[:, at + i:at + (i + n if n else size)]

        ident = C("ident")

        def finish(xt, toks):
            k.until(toks)
            k.wait("sp", [k.dma("sp", out[i], xt[:, i], w=toks) for i in range(2)])

        def bank4(b, c=P):
            return k.ps[b][:, :].rearrange("p (h c) -> p h c", c=c)

        def flips(b, srcs, w):
            for i, src in enumerate(srcs):
                t = k.tr(k.ps[b][:, i * P:(i + 1) * P], src, ident, w=w, inc=i == len(srcs) - 1)
            return t

        def ffn_up(s, key, H, htok, hh, hl, layer):
            tmp = s.sb("ffn_tmp", [P, 3, 2, T])
            slots = Slots(3)
            hid = Evs()

            def act(f, b, t, second):
                yield [t, slots]
                i, old = slots.take()
                ab, sg = tmp[:, i, 0], tmp[:, i, 1]
                ps = k.ps[b][:, 0:T]
                if layer is None:
                    ts = k.a(A.activation, sg, ps, ACT.Silu, w=[t, old])
                    k.close(b, [ts])
                else:
                    w_ = [C("fcw", layer * 66 + tap * 22 + f, 1) for tap in range(3)]
                    ta = k.a(A.activation, ab, ps, ACT.Identity, bias=C("fcb", layer * 22 + f, 1), scale=w_[1],
                             w=[t, old])
                    yield [ta]
                    tv = k.v(V.scalar_tensor_tensor, ab[:, 1:T], ps[:, 0:T - 1], w_[0], ab[:, 1:T], ALU.mult, ALU.add,
                             w=[ta])
                    yield [tv]
                    tv = k.v(V.scalar_tensor_tensor, ab[:, 0:T - 1], ps[:, 1:T], w_[2], ab[:, 0:T - 1], ALU.mult,
                             ALU.add, w=[tv])
                    k.close(b, [tv])
                    yield [tv]
                    ts = k.a(A.activation, sg, ab, ACT.Silu, w=[tv])
                yield [ts, second]
                b, t = second.bank, second.tok
                tv = k.v(V.tensor_tensor, ab, sg, k.ps[b][:, 0:T], op=ALU.mult, w=[ts, t, old])
                k.close(b, [tv])
                yield [tv]
                ta = k.a(A.copy, hh[:, f], ab, w=[tv])
                yield [ta]
                tv = k.v(V.tensor_tensor, hl[:, f], ab, hh[:, f].bitcast(F32), op=ALU.subtract, w=[ta])
                slots.give(i, [ta, tv])
                hid[f].set([ta, tv])

            for f in range(FT):
                b, t = ws_tile(k, st, key, H, htok, T)
                second = Bank()
                k.spawn(act(f, b, t, second))
                b, t = ws_tile(k, st, key, H, htok, T)
                second.set(b, t)
            return hid

        with Scope(k) as s1:
            BO, nb1 = offsets(B1)
            b1 = s1.sb("b1", [P, nb1])
            silu_c = s1.sb("silu_c", [P, 2, D])
            mod = s1.sb("mod", [P, 2, 2, 48])
            junk = s1.sb("junk", [P, 2, D], BF16)
            Hh = s1.sb("Hh", [P, KT, 512], F32R)
            Hl = s1.sb("Hl", [P, KT, 512], F32R)
            H = (Hh, Hl)
            gates = [None]
            order = [2, 3, 0, 1]

            def B(name, i=0, n=None):
                at, size = BO[name]
                return b1[:, at + i:at + (i + n if n else size)]

            d_c = [k.dma("a", silu_c[:, i], src.to_broadcast([P, D])) for i, src in enumerate((c_in, cc_in))]
            d_x = {2 * j + i: k.dma("a", xt[:, 2 * j + i], src[i]) for j, src in ((1, ctx_in), (0, x_in))
                   for i in range(2)}
            d_core = k.dma("a", core[:, :], core_in)
            d_b1 = k.dma("a", b1[:, :], b1_in)
            t_half = k.v(V.memset, half[:, :], -0.5)
            t_silu = [k.a(A.activation, silu_c[:, i], silu_c[:, i], ACT.Silu, w=[d_c[i]]) for i in range(2)]

            t_mod, t_junk = Evs(), []
            need = {0: (6, 6), 1: (6, 2)}

            def on_mod(item, raw, landed):
                _, layer, i = item
                toks = []
                for r in range(2):
                    col = 2 * i + r
                    part = col // 8
                    for who in range(2):
                        if part < need[layer][who]:
                            toks.append(k.v(
                                V.tensor_tensor_reduce, out=junk[:, len(t_junk) % 2], in0=raw[:, r * D:(r + 1) * D],
                                in1=silu_c[:, who], scale=1.0, scalar=0.0, op0=ALU.mult, op1=ALU.add,
                                accum_out=mod[:, layer, who, col:col + 1], w=[landed, t_silu, t_junk[-2:-1]]))
                            t_junk.append(toks[-1])
                    if col % 8 == 7:
                        t_mod[layer, part].set(toks[-1])
                return toks[-1]

            st.on_mod = on_mod

            def mod_part(layer, part, who):
                cols = mod[:, layer, who, part * 8:part * 8 + 8]
                return k.v(V.tensor_tensor, cols, cols, C("modb", layer * 48 + part * 8, 8), op=ALU.add,
                           w=[t_mod[layer, part], d_core])

            def scale_part(layer, part, who, norm):
                t = mod_part(layer, part, who)
                cols = mod[:, layer, who, part * 8:part * 8 + 8]
                return k.v(V.scalar_tensor_tensor, cols, cols, 1.0, C(norm, layer * 8, 8), ALU.add, ALU.mult,
                           w=[t])

            def norm_mod(s, layer, first, norm, tiles, xtok):
                stat = s.sb("stat", [P, 3, 4])
                junka = s.sb("junka", [P, 2, D], BF16)
                xh = s.sb("xhat", [P, 2, D])
                tf = s.sb("tf", [P, 2, D])
                bufs, sq = Slots(2), Slots(2)
                tA, tS, h = Evs(), Evs(), Evs()

                def columns():
                    yield [t_mod[layer, first], t_mod[layer, first + 1]]
                    for who in sorted({t // 2 for t in tiles}):
                        tA[who].set(scale_part(layer, first + 1, who, norm))
                        tS[who].set(mod_part(layer, first, who))

                def tile_(t):
                    yield [xtok[t], sq]
                    q, old = sq.take()
                    ts = k.a(A.activation, junka[:, q], xt[:, t], ACT.Square, accum_out=stat[:, 0, t:t + 1],
                             w=[xtok[t], old])
                    sq.give(q, [ts])
                    te = k.g(G.tensor_scalar, stat[:, 1, t:t + 1], stat[:, 0, t:t + 1], 1.0 / D, EPS, ALU.mult,
                             ALU.add, w=[ts])
                    tr = k.g(G.tensor_tensor, stat[:, 2, t:t + 1], stat[:, 1, t:t + 1], half[:, 0:1],
                             op=ALU.pow, w=[te, t_half])
                    yield [tr, bufs]
                    i, old = bufs.take()
                    tx = k.v(V.tensor_scalar, xh[:, i], xt[:, t], stat[:, 2, t:t + 1], None, ALU.mult, w=[tr, old])
                    who = t // 2
                    sc = mod[:, layer, who, (first + 1) * 8:(first + 2) * 8]
                    sh = mod[:, layer, who, first * 8:(first + 1) * 8]
                    wm = [tA[who], tS[who]]
                    yield [tx, wm, k.banks]
                    b0 = k.bank()
                    t0 = flips(b0, [xh[:, i, j * P:(j + 1) * P] for j in range(4)], [tx, d_core])
                    yield [t0, k.banks]
                    b1 = k.bank()
                    t1 = flips(b1, [xh[:, i, j * P:(j + 1) * P] for j in range(4, 8)], ())
                    for j in range(4):
                        tv = k.v(V.tensor_scalar, tf[:, i, j * P:(j + 1) * P], k.ps[b0][:, j * P:(j + 1) * P],
                                 sc[:, j:j + 1], sh[:, j:j + 1], ALU.mult, ALU.add, w=[t0, wm, old])
                    k.close(b0, [tv])
                    yield [t1]
                    for j in range(4, 8):
                        ta = k.a(A.activation, tf[:, i, j * P:(j + 1) * P], k.ps[b1][:, (j - 4) * P:(j - 3) * P],
                                 ACT.Identity, bias=sh[:, j:j + 1], scale=sc[:, j:j + 1], w=[t1, wm, old])
                    k.close(b1, [ta])
                    cols = slice(t * P, (t + 1) * P)
                    toks = []
                    for hf, tk in enumerate((tv, ta)):
                        yield [tk]
                        src = tf[:, i, hf * 512:(hf + 1) * 512].rearrange("p (j c) -> p j c", c=P)
                        toks += split(k, src, Hh[:, hf * 4:hf * 4 + 4, cols], Hl[:, hf * 4:hf * 4 + 4, cols], [tk])
                    bufs.give(i, toks)
                    h[t].set(toks)

                k.spawn(columns())
                for t in tiles:
                    k.spawn(tile_(t))
                return h

            def gate_tiles(s, layer, part, whos):
                gates[0] = s.sb("gates", [P, 2, D])
                toks = Evs()

                def rows_(who):
                    yield [t_mod[layer, part]]
                    t = mod_part(layer, part, who)
                    cols = mod[:, layer, who, part * 8:part * 8 + 8]
                    last = []
                    for hf in range(2):
                        yield [t, k.banks]
                        b = k.bank()
                        for j in range(4):
                            tt = k.mm(k.ps[b][:, j * P:(j + 1) * P],
                                      cols[:, hf * 4 + j:hf * 4 + j + 1].to_broadcast([P, P]), ident, True, True,
                                      w=[t], inc=j == 3)
                        yield [tt]
                        ta = k.a(A.copy, gates[0][:, who, hf * 512:(hf + 1) * 512], k.ps[b][:, :], w=[tt])
                        k.close(b, [ta])
                        last.append(ta)
                    toks[who].set(last)

                for who in whos:
                    k.spawn(rows_(who))
                return toks

            def add_gated(s):
                tmp = s.sb("gtmp", [P, 2, 512])
                slots = Slots(2)
                evs = Evs()

                def add(tile, hf, b, t, tg):
                    cols = slice(hf * 512, (hf + 1) * 512)
                    yield [t, tg[tile // 2], slots]
                    i, old = slots.take()
                    tv = k.v(V.tensor_tensor, tmp[:, i], k.ps[b][:, :], gates[0][:, tile // 2, cols], op=ALU.mult,
                             w=[t, tg[tile // 2], old])
                    k.close(b, [tv])
                    yield [tv]
                    tx = k.v(V.tensor_tensor, xt[:, tile, cols], xt[:, tile, cols], tmp[:, i], op=ALU.add, w=[tv])
                    slots.give(i, [tx])
                    evs[tile, hf].set(tx)

                def start(tg):
                    return lambda tile, hf, b, t: k.spawn(add(tile, hf, b, t, tg))
                return start, {t: [evs[t, 0], evs[t, 1]] for t in range(4)}

            def rotated(x8, z8, s8, tn):
                tz = []
                for hf in range(2):
                    for r in range(2):
                        tz.append(k.v(V.tensor_tensor, z8[:, :, r, hf], x8[:, :, r, 1 - hf],
                                      s8[:, r, hf].unsqueeze(1).to_broadcast([P, 8, 16]), op=ALU.mult, w=tn))
                return tz

            quarters = lambda a: a.rearrange("p (h r y f) -> p h r y f", h=8, r=2, y=2)

            st.pump(0)
            with Scope(k) as s:
                kT = s.sb("kT", [P, 4, 512])
                qT = s.sb("qT", [P, 2, 4, 512])
                vt = s.sb("vt", [P, 4, 512])
                yc = s.sb("yc", [P, 4, 512])
                with Scope(k) as sn:
                    t_h = norm_mod(sn, 0, 0, "n1", order, d_x)
                with Scope(k) as sa:
                    tab = sa.sb("tab", [P, 2, 2, 2, 64])
                    lamt = sa.sb("lamt", [P, 8])
                    sub = sa.sb("sub", [P, P])
                    prod = sa.sb("prod", [P, 2, 64])
                    raw = sa.sb("raw_qk", [P, 2, 512])
                    rot = sa.sb("rot_qk", [P, 2, 512])
                    zz = sa.sb("zz_qk", [P, 2, 512])
                    sst = sa.sb("sst", [P, 2, 3, 8])
                    pr = sa.sb("pr", [P, 3, 2, 512])
                    sm = sa.sb("sm", [P, 3, 8])
                    ost = sa.sb("ost", [P, 4, 12])
                    ub = sa.sb("ub", [P, 2, 258])
                    cg = sa.sb("cg", [P, 2, 256])
                    E_ = Evs()

                    def tables():
                        yield [d_b1]
                        t_z = [k.v(V.memset, qT[64:128, 0], 0.0), k.v(V.memset, qT[0:64, 1], 0.0)]
                        E_["z"].set(t_z)
                        for wi, gain in enumerate(("qg", "kg")):
                            g_ = B(gain).unsqueeze(1).to_broadcast([P, 2, 64])
                            t1 = [k.v(V.tensor_tensor, tab[:, wi, 0], B("ropec").rearrange("p (t d) -> p t d", t=2),
                                      g_, op=ALU.mult, w=[d_b1])]
                            half_ = lambda a: a.rearrange("p (r h f) -> p r h f", r=2, h=2)
                            for hf in range(2):
                                for tl in range(2):
                                    t1.append(k.v(V.tensor_tensor, half_(tab[:, wi, 1, tl])[:, :, hf],
                                                  half_(B("ropes", tl * 64, 64))[:, :, hf],
                                                  half_(B(gain))[:, :, 1 - hf], op=ALU.mult, w=[d_b1]))
                            E_["tab", wi].set(t1)
                        for i in range(2):
                            tl = k.v(V.tensor_tensor_reduce, out=prod[:, i], in0=B(("lq1", "lq2")[i]),
                                     in1=B(("lk1", "lk2")[i]), scale=1.0, scalar=0.0, op0=ALU.mult, op1=ALU.add,
                                     accum_out=lamt[:, i:i + 1], w=[d_b1])
                        E_["sub"].set(k.v(V.tensor_scalar, sub[:, :], B("subg"), 1.0 - LAM_INIT, None, ALU.mult,
                                          w=[d_b1]))
                        yield [tl]
                        te = k.a(A.activation, lamt[:, 2:4], lamt[:, 0:2], ACT.Exp, w=[tl])
                        yield [te]
                        t1 = k.v(V.tensor_tensor, lamt[:, 4:5], lamt[:, 3:4], lamt[:, 2:3], op=ALU.subtract, w=[te])
                        E_["lam"].set(k.v(V.tensor_scalar, lamt[:, 5:6], lamt[:, 4:5], -LAM_INIT, None, ALU.add,
                                          w=[t1]))

                    qs = Slots(2)
                    e8 = lambda a: a.rearrange("p (h d) -> p h d", d=64)

                    def head_norm(which, tile, b, t):
                        yield [t, qs]
                        i, old = qs.take()
                        ta = k.a(A.activation, zz[:, i], k.ps[b][:, :], ACT.Square, w=[t, old])
                        tr = k.a(A.copy, raw[:, i], k.ps[b][:, :], w=[old])
                        k.close(b, [tr])
                        yield [ta]
                        tv = k.v(V.tensor_reduce, sst[:, i, 0], e8(zz[:, i]), axis=AX, op=ALU.add, w=[ta, old])
                        tg = k.g(G.tensor_scalar, sst[:, i, 1], sst[:, i, 0], 1.0 / 64, EPS, ALU.mult, ALU.add, w=[tv])
                        tg = k.g(G.tensor_tensor, sst[:, i, 2], sst[:, i, 1], half[:, 0:8], op=ALU.pow, w=[tg])
                        yield [tg, tr]
                        r8, o8 = e8(raw[:, i]), e8(rot[:, i])
                        tn = k.v(V.tensor_tensor, r8, r8, sst[:, i, 2].unsqueeze(2).to_broadcast([P, 8, 64]),
                                 op=ALU.mult, w=[tg, tr])
                        yield [tn, E_["tab", which]]
                        if tile < 2:
                            s8 = tab[:, which, 1, tile].rearrange("p (r y f) -> p r y f", r=2, y=2)
                            tz = rotated(quarters(raw[:, i]), quarters(zz[:, i]), s8, [tn, E_["tab", which], tv])
                            to = k.v(V.tensor_tensor, o8, r8, tab[:, which, 0, tile].unsqueeze(1).to_broadcast(
                                [P, 8, 64]), op=ALU.mult, w=[tn, old])
                            yield [to]
                            to = k.v(V.tensor_tensor, rot[:, i], rot[:, i], zz[:, i], op=ALU.add, w=[to, tz])
                        else:
                            to = k.v(V.tensor_tensor, o8, r8,
                                     B(("qg", "kg")[which]).unsqueeze(1).to_broadcast([P, 8, 64]), op=ALU.mult,
                                     w=[tn, old])
                        yield [to, k.banks]
                        b = k.bank()
                        tt = flips(b, [rot[:, i, h * P:(h + 1) * P] for h in range(4)], [to])
                        qs.give(i, [tt])
                        cols = slice(tile * P, (tile + 1) * P)
                        yield [tt, E_["z"]]
                        if which:
                            te = k.a(A.copy, kT[:, :, cols], bank4(b), w=[tt])
                        else:
                            t0 = k.a(A.copy, qT[0:64, 0, :, cols], bank4(b)[0:64], w=[tt, E_["z"]])
                            te = k.a(A.copy, qT[64:128, 1, :, cols], bank4(b)[64:128])
                        k.close(b, [te])
                        E_["qk"[which], tile].set(te if which else [t0, te])

                    def evac_v(tile, b, t):
                        def f():
                            yield [t]
                            ta = k.a(A.copy, vt[:, tile], k.ps[b][:, :], w=[t])
                            k.close(b, [ta])
                            E_["v", tile].set(ta)
                        k.spawn(f())

                    ps_ = Slots(3)

                    def head(tile, h, ob, prev):
                        lat = tile < 2
                        nk, k0, kts = (512, 0, [0, 1, 2, 3]) if lat else (256, 256, [2, 3])
                        nb = nk // P
                        tk = [E_["k", j] for j in kts]
                        yield [E_["q", tile], tk, ps_, k.banks, k.banks, prev]
                        i, old = ps_.take()
                        bs = [k.bank(), k.bank()]
                        tp = []
                        for m in range(2):
                            tp.append(k.mm(k.ps[bs[m]][:, 0:nk], qT[:, m, h, tile * P:(tile + 1) * P],
                                           kT[:, h, k0:k0 + nk], True, True, w=[E_["q", tile], tk], inc=True))
                        tm = []
                        for m in range(2):
                            yield [tp[m]]
                            tm.append(k.v(V.tensor_reduce, sm[:, i, m:m + 1], k.ps[bs[m]][:, 0:nk], axis=AX,
                                          op=ALU.max, w=[tp[m], old]))
                        yield [tm[1]]
                        tv = k.v(V.tensor_scalar, sm[:, i, 2:4], sm[:, i, 0:2], -0.125, None, ALU.mult, w=[tm])
                        yield [tv, E_["lam"]]
                        for m in range(2):
                            tp[m] = k.a(A.activation, pr[:, i, m, 0:nk], k.ps[bs[m]][:, 0:nk], ACT.Exp,
                                        bias=sm[:, i, 2 + m:3 + m], scale=0.125, accum_out=sm[:, i, 4 + m:5 + m],
                                        w=[tv, old])
                            k.close(bs[m], [tp[m]])
                        yield [tp[1]]
                        tv = k.v(V.reciprocal, sm[:, i, 6:8], sm[:, i, 4:6], w=[tp])
                        yield [tv]
                        t2 = k.v(V.tensor_tensor, sm[:, i, 7:8], sm[:, i, 7:8], lamt[:, 5:6], op=ALU.mult,
                                 w=[tv, E_["lam"]])
                        t1 = k.v(V.tensor_scalar, pr[:, i, 0, 0:nk], pr[:, i, 0, 0:nk], sm[:, i, 6:7], None, ALU.mult,
                                 w=[tv])
                        yield [t1]
                        t1 = k.v(V.scalar_tensor_tensor, pr[:, i, 0, 0:nk], pr[:, i, 1, 0:nk], sm[:, i, 7:8],
                                 pr[:, i, 0, 0:nk], ALU.mult, ALU.add, w=[t1, t2])
                        yield [t1, k.banks]
                        b = k.bank()
                        tt = flips(b, [pr[:, i, 0, j * P:(j + 1) * P] for j in range(nb)], [t1])
                        yield [tt]
                        tc = k.a(A.copy, pr[:, i, 1, 0:nk], k.ps[b][:, 0:nk], w=[tt])
                        k.close(b, [tc])
                        yield [tc, [E_["v", j] for j in kts], E_["ob", tile]]
                        ob = E_["ob", tile].bank
                        for j in range(nb):
                            to = k.mm(k.ps[ob][:, h * P:(h + 1) * P], pr[:, i, 1, j * P:(j + 1) * P],
                                      vt[:, kts[j], h * P:(h + 1) * P], j == 0, j == nb - 1,
                                      w=[tc, E_["v", kts[j]]], inc=j == nb - 1)
                        ps_.give(i, [to])
                        E_["o", tile, h].set(to)

                    def attention(tile):
                        E_["ob", tile] = Bank()
                        yield [E_["q", tile], k.banks, E_["last", tile]]
                        ob = k.bank()
                        E_["ob", tile].set(ob, ())
                        for h in range(4):
                            k.spawn(head(tile, h, ob, ()))
                        to = [E_["o", tile, h] for h in range(4)]
                        yield [to]
                        E_["last", {2: 3, 3: 0, 0: 1, 1: None}[tile]].set(())
                        yield [ps_]
                        i, old = ps_.take()
                        osq, yr = pr[:, i, 0], pr[:, i, 1]
                        ta = k.a(A.activation, osq, k.ps[ob][:, :], ACT.Square, w=[to, old])
                        yield [ta]
                        tv = k.v(V.tensor_reduce, ost[:, tile, 0:4], osq.rearrange("p (h d) -> p h d", d=P), axis=AX,
                                 op=ALU.add, w=[ta])
                        tg = k.g(G.tensor_scalar, ost[:, tile, 4:8], ost[:, tile, 0:4], 1.0 / P, EPS, ALU.mult, ALU.add,
                                 w=[tv])
                        tg = k.g(G.tensor_tensor, ost[:, tile, 8:12], ost[:, tile, 4:8], half[:, 0:4], op=ALU.pow, w=[tg])
                        yield [tg, E_["sub"]]
                        for h in range(4):
                            tv = k.v(V.scalar_tensor_tensor, yr[:, h * P:(h + 1) * P], k.ps[ob][:, h * P:(h + 1) * P],
                                     ost[:, tile, 8 + h:9 + h], sub[:, :], ALU.mult, ALU.mult,
                                     w=[tg, E_["sub"], old])
                        k.close(ob, [tv])
                        yield [tv, k.banks]
                        b = k.bank()
                        tt = flips(b, [yr[:, h * P:(h + 1) * P] for h in range(4)], [tv])
                        ps_.give(i, [tt])
                        yield [tt]
                        cols = slice(tile * P, (tile + 1) * P)
                        E_["y", tile].set(k.a(A.copy, qT[:, 0, :, cols], bank4(b), w=[tt]))
                        k.close(b, [E_["y", tile]])

                    cs = Slots(1)
                    t_u0 = k.v(V.memset, ub[:, :, :], 0.0)
                    seqs = lambda a: a.rearrange("p (s c) -> p s c", s=2)

                    def conv_tile(i, bc, tc, bx, bb):
                        yield [tc, cs]
                        j, old = cs.take()
                        tc = k.a(A.copy, cg[:, :, :], seqs(k.ps[bc][:, :]), w=[tc, old])
                        k.close(bc, [tc])
                        yield [tc, bx]
                        tu = k.v(V.tensor_tensor, ub[:, :, 1:257], cg[:, :, :], seqs(k.ps[bx.bank][:, :]), op=ALU.mult,
                                 w=[bx, tc, t_u0, old])
                        k.close(bx.bank, [tu])
                        yield [tu]
                        tv = k.v(V.tensor_scalar, cg[:, :, :], ub[:, :, 0:256], C("scw", i, 1), None, ALU.mult,
                                 w=[tu, d_core])
                        for tap in (1, 2):
                            yield [tv]
                            tv = k.v(V.scalar_tensor_tensor, cg[:, :, :], ub[:, :, tap:tap + 256],
                                     C("scw", tap * 4 + i, 1), cg[:, :, :], ALU.mult, ALU.add, w=[tv])
                        yield [tv, bb]
                        tv = k.v(V.tensor_tensor, yc[:, i], cg[:, :, :].rearrange("p s c -> p (s c)"),
                                 k.ps[bb.bank][:, :], op=ALU.mult, w=[tv, bb])
                        k.close(bb.bank, [tv])
                        cs.give(j, [tv])
                        E_["yc", i].set(tv)

                    k.spawn(tables())
                    spawn_qk = lambda which: lambda tile, b, t: k.spawn(head_norm(which, tile, b, t))
                    as_group(k, st, "ev_qkv", H, t_h, order, evac=spawn_qk(1))
                    as_group(k, st, "ev_qkv", H, t_h, order, evac=spawn_qk(0))
                    E_["last", 2].set(())
                    for tile in order:
                        k.spawn(attention(tile))
                    as_group(k, st, "ev_qkv", H, t_h, order, evac=evac_v)
                    ht = list(t_h.values())
                    for i in range(4):
                        bc, tc = ws_tile(k, st, "ev_conv", H, ht, 512)
                        bx, bb = Bank(), Bank()
                        k.spawn(conv_tile(i, bc, tc, bx, bb))
                        bx.set(*ws_tile(k, st, "ev_conv", H, ht, 512))
                        b, t_pe = ws_tile(k, st, "ev_conv", H, ht, 512)
                        bb.set(b, t_pe)

                    def cat(src, rows_, need, ev):
                        for tile in order:
                            cols = slice(tile * P, (tile + 1) * P)
                            yield need(tile)
                            ev[tile].set(split(k, src[:, :, cols], Hh[:, rows_, cols], Hl[:, rows_, cols],
                                               [need(tile), t_pe]))
                    t_conv, t_att = Evs(), Evs()
                    k.spawn(cat(yc, slice(0, 4), lambda tile: [E_["yc", i] for i in range(4)], t_conv))
                    k.spawn(cat(qT[:, 0], slice(4, 8), lambda tile: [E_["y", tile]], t_att))
                tg = gate_tiles(s, 0, 2, (0, 1))
                start, t_x = add_gated(s)
                t_cat = {t: [t_conv[t], t_att[t]] for t in order}
                go = start(tg)
                for hf in range(2):
                    as_group(k, st, "ev_out", H, t_cat, order, evac=lambda tile, b, t: go(tile, hf, b, t))
            if stop == 1:
                return finish(xt, k.last())

            with Scope(k) as s:
                hid = s.sb("hid", [P, FT, 512])
                with Scope(k) as sn:
                    t_h = norm_mod(sn, 0, 3, "n2", order, t_x)
                tmp = s.sb("ffn_tmp", [P, 3, 2, 512])
                slots = Slots(3)
                t_hid = Evs()
                seqs = lambda a: a.rearrange("p (s c) -> p s c", s=2)

                def act(f, b, t, second):
                    yield [t, slots]
                    i, old = slots.take()
                    ab, sg = tmp[:, i, 0], tmp[:, i, 1]
                    w_ = [C("fcw", tap * 22 + f, 1) for tap in range(3)]
                    ta = k.a(A.activation, ab, k.ps[b][:, :], ACT.Identity, bias=C("fcb", f, 1), scale=w_[1], w=[t, old])
                    yield [ta]
                    tv = k.v(V.scalar_tensor_tensor, seqs(ab)[:, :, 1:T], seqs(k.ps[b][:, :])[:, :, 0:T - 1], w_[0],
                             seqs(ab)[:, :, 1:T], ALU.mult, ALU.add, w=[ta])
                    yield [tv]
                    tv = k.v(V.scalar_tensor_tensor, seqs(ab)[:, :, 0:T - 1], seqs(k.ps[b][:, :])[:, :, 1:T], w_[2],
                             seqs(ab)[:, :, 0:T - 1], ALU.mult, ALU.add, w=[tv])
                    k.close(b, [tv])
                    yield [tv]
                    ts = k.a(A.activation, sg, ab, ACT.Silu, w=[tv])
                    yield [ts, second]
                    tv = k.v(V.tensor_tensor, hid[:, f], sg, k.ps[second.bank][:, :], op=ALU.mult, w=[ts, second])
                    k.close(second.bank, [tv])
                    slots.give(i, [tv])
                    t_hid[f].set(tv)

                ht = list(t_h.values())
                for f in range(FT):
                    b, t = ws_tile(k, st, "up0", H, ht, 512)
                    second = Bank()
                    k.spawn(act(f, b, t, second))
                    b, t_up = ws_tile(k, st, "up0", H, ht, 512)
                    second.set(b, t_up)
                tg = gate_tiles(s, 0, 5, (0, 1))
                start, t_xn = add_gated(s)
                go = start(tg)
                ring, parts = Slots(KT), Evs()

                def halves():
                    for n in range(2 * FT):
                        yield [t_hid[n % FT], ring]
                        q, old = ring.take()
                        parts[n].set(split(k, hid[:, n % FT], Hh[:, q], Hl[:, q], [t_hid[n % FT], t_up, old]))
                        parts[n].at = q

                k.spawn(halves())
                for hf in range(2):
                    bs = {t: k.bank() for t in order}
                    for f in range(0, FT, 2):
                        u = st.take("down0")
                        wh, wl, wt = st.parts(u)
                        for kk in range(2):
                            n = hf * FT + f + kk
                            k.until(parts[n])
                            q = parts[n].at
                            c = slice(kk * 512, (kk + 1) * 512)
                            last = f + kk == FT - 1
                            for i, tile in enumerate(order):
                                xs = slice(tile * P, (tile + 1) * P)
                                t = as3(k, k.ps[bs[tile]][:, :], Hh[:, q, xs], Hl[:, q, xs], wh[:, c], wl[:, c],
                                        f + kk == 0, last, w=[wt, parts[n]], inc=last or i == 3)
                                if last:
                                    go(tile, hf, bs[tile], t)
                            ring.give(q, [t])
                            st.poll()
                        st.free(u, t)
                t_x = t_xn
            if stop == 2:
                return finish(xt, k.last())

            with Scope(k) as s:
                LO, nl1 = offsets(L1C)
                l1 = s.sb("l1", [P, nl1])
                d_l1 = k.dma("sp", l1[:, :], l1_in, w=k.last())
                cat = s.sb("cat", [P, KT, T])
                with Scope(k) as sn:
                    t_h = norm_mod(sn, 1, 0, "n1", order, t_x)

                def L(name, i=0, n=None):
                    at, size = LO[name]
                    return l1[:, at + i:at + (i + n if n else size)]

                with Scope(k) as sa:
                    lg = sa.sb("lg", [P, 8])
                    dec = sa.sb("dec", [P, 4, 2, 4])
                    decay = sa.sb("decay", [P, 4, 512])
                    two = lambda a: a.rearrange("p (t u) c -> p t (u c)", t=2)
                    rawq = at = two(cat[:, 0:4])
                    zq = two(cat[:, 4:8])
                    gate = xt[:, 2].rearrange("p (t c) -> p t c", t=2)
                    pv = xt[:, 3].rearrange("p (t c) -> p t c", t=2)
                    qk = sa.sb("qk", [P, 2, 512])
                    kc = sa.sb("kc", [P, 2, 256])
                    vl = sa.sb("vl", [P, 4, 512])
                    qTp = sa.sb("qTp", [P, 4, T])
                    kTp = sa.sb("kTp", [P, 2, T])
                    qd = sa.sb("qd", [P, 2, 4, P])
                    qdT = sa.sb("qdT", [P, 4, T])
                    kw = sa.sb("kw", [P, 2, 4, P])
                    S = sa.sb("S", [P, 4, P])
                    yp = sa.sb("yp", [P, 4, T])
                    ost = sa.sb("ost", [P, 2, 12])
                    yr = qd.rearrange("p t h c -> p t (h c)")
                    dtmp = yp[:, 0:2].rearrange("p t c -> p (t c)")
                    E_ = Evs()
                    h4 = lambda a: a.rearrange("p (h d) -> p h d", d=64)

                    def decays():
                        yield [d_b1]
                        t1 = k.a(A.activation, lg[:, 0:4], B("decf"), ACT.Exp, w=[d_b1])
                        t2 = k.a(A.activation, lg[:, 4:8], B("decb"), ACT.Exp, w=[d_b1])
                        yield [t2]
                        tl = k.v(V.tensor_scalar, lg[:, :], lg[:, :], -1.0, None, ALU.mult, w=[t1, t2])
                        yield [tl]
                        tt = []
                        for i in range(4):
                            tt.append(k.v(V.tensor_tensor, dec[:, i],
                                          B("ramps", 2 * i, 2).unsqueeze(2).to_broadcast([P, 2, 4]),
                                          lg[:, (i % 2) * 4:(i % 2) * 4 + 4].unsqueeze(1).to_broadcast([P, 2, 4]),
                                          op=ALU.mult, w=[tl]))
                        yield [tt]
                        ta = k.a(A.activation, dec[:, :], dec[:, :], ACT.Exp, w=[tt])
                        yield [ta]
                        E_["dec8"].set(k.v(V.tensor_scalar, dec[:, 0:2], dec[:, 0:2], 0.125, None, ALU.mult, w=[ta]))
                        E_["dec"].set(ta)
                        t2 = None
                        for h in range(4):
                            yield [d_l1, t2]
                            t1 = k.v(V.tensor_scalar, dtmp, L("dist_f"), lg[:, h:h + 1], None, ALU.mult,
                                     w=[tl, d_l1, t2])
                            yield [t1]
                            t2 = k.v(V.scalar_tensor_tensor, decay[:, h], L("dist_b"), lg[:, 4 + h:5 + h], dtmp,
                                     ALU.mult, ALU.add, w=[t1])
                            yield [t2]
                            ta = k.a(A.activation, decay[:, h], decay[:, h], ACT.Exp, w=[t2])
                            yield [ta]
                            E_["decay", h].set(k.v(V.tensor_tensor, decay[:, h], decay[:, h], L("two"), op=ALU.mult,
                                                   w=[ta]))
                        E_["dtmp"].set(t2)

                    def evac_qk(tile, b, t):
                        yield [t]
                        if tile >= 2:
                            ta = k.a(A.copy, kc[:, tile - 2], k.ps[b][:, 0:256], w=[t])
                            k.close(b, [ta])
                            yield [ta, E_["dec"]]
                            tw = []
                            for i in range(2):
                                tw.append(k.v(V.tensor_tensor, kw[:, tile - 2, :, i * 64:(i + 1) * 64],
                                              h4(kc[:, tile - 2]),
                                              dec[:, 2 + i, tile - 2].unsqueeze(2).to_broadcast([P, 4, 64]),
                                              op=ALU.mult, w=[ta, E_["dec"]]))
                            E_["kw", tile - 2].set(tw)
                            return
                        tr = k.a(A.copy, rawq[:, tile], k.ps[b][:, :], w=[t])
                        k.close(b, [tr])
                        yield [tr]
                        s8 = B("ropes", tile * 64, 64).rearrange("p (r y f) -> p r y f", r=2, y=2)
                        tz = rotated(quarters(rawq[:, tile]), quarters(zq[:, tile]), s8, [tr])
                        to = k.v(V.tensor_tensor, qk[:, tile].rearrange("p (h d) -> p h d", d=64),
                                 rawq[:, tile].rearrange("p (h d) -> p h d", d=64),
                                 B("ropec", tile * 64, 64).unsqueeze(1).to_broadcast([P, 8, 64]), op=ALU.mult, w=[tr])
                        yield [to]
                        to = k.v(V.tensor_tensor, qk[:, tile], qk[:, tile], zq[:, tile], op=ALU.add, w=[to, tz])
                        E_["qk", tile].set(to)
                        yield [to, E_["dec8"], k.banks]
                        b = k.bank()
                        tt = flips(b, [qk[:, tile, j * P:(j + 1) * P] for j in range(4)], [to])
                        td = []
                        for i in range(2):
                            td.append(k.v(V.tensor_tensor, qd[:, tile, :, i * 64:(i + 1) * 64], h4(qk[:, tile, 0:256]),
                                          dec[:, i, tile].unsqueeze(2).to_broadcast([P, 4, 64]), op=ALU.mult,
                                          w=[to, E_["dec8"]]))
                        yield [tt, E_["z"]]
                        c = slice(tile * P, (tile + 1) * P)
                        k.a(A.copy, qTp[0:64, 0:4:2, c], bank4(b)[0:64, 0:2], w=[tt, E_["z"]])
                        k.a(A.copy, qTp[64:128, 1:4:2, c], bank4(b)[64:128, 0:2])
                        ta = k.a(A.copy, kTp[:, :, c], bank4(b)[:, 2:4])
                        k.close(b, [ta])
                        E_["T", tile].set(ta)
                        yield [td, k.banks]
                        b = k.bank()
                        tt = flips(b, [qd[:, tile, h] for h in range(4)], [td])
                        yield [tt]
                        ta = k.a(A.copy, qdT[:, :, c], bank4(b), w=[tt])
                        k.close(b, [ta])
                        E_["qdT", tile].set(ta)

                    def evac_v(tile, b, t):
                        yield [t]
                        ta = k.a(A.copy, vl[:, tile], k.ps[b][:, :], w=[t])
                        k.close(b, [ta])
                        E_["v", tile].set(ta)

                    def evac_g(tile, b, t):
                        yield [t, E_["decay", 3]]
                        ta = k.a(A.activation, gate[:, tile], k.ps[b][:, :], ACT.Silu, w=[t])
                        k.close(b, [ta])
                        yield [ta]
                        g4 = gate[:, tile].rearrange("p (h d) -> p h d", d=P)
                        E_["g", tile].set(k.v(V.tensor_tensor, g4, g4, B("rgn").unsqueeze(1).to_broadcast([P, 4, P]),
                                              op=ALU.mult, w=[ta]))

                    def evac_pv(tile, b, t):
                        yield [t]
                        ta = k.a(A.copy, pv[:, tile], k.ps[b][:, :], w=[t])
                        k.close(b, [ta])
                        E_["pv", tile].set(ta)

                    def states():
                        need = [E_["kw", 0], E_["kw", 1], E_["v", 2], E_["v", 3]]
                        yield [need, k.banks]
                        b = k.bank()
                        for h in range(4):
                            for j in range(2):
                                tt = k.mm(k.ps[b][:, h * P:(h + 1) * P], kw[:, j, h], vl[:, 2 + j, h * P:(h + 1) * P],
                                          j == 0, j == 1, w=need, inc=h == 3 and j == 1)
                        yield [tt]
                        ta = k.a(A.copy, S[:, :], bank4(b), w=[tt])
                        k.close(b, [ta])
                        E_["S"].set(ta)

                    atS = Slots(2)

                    def scores(h, obs):
                        yield [E_["T", 0], E_["T", 1], E_["decay", h], atS, k.banks]
                        i, old = atS.take()
                        b = k.bank()
                        for j in range(2):
                            tt = k.mm(k.ps[b][:, j * T:(j + 1) * T], kTp[:, h // 2, j * P:(j + 1) * P], qTp[:, h], True,
                                      True, w=[E_["T", 0], E_["T", 1]], inc=j == 1)
                        yield [tt]
                        ta = k.v(V.tensor_tensor, at[:, i], k.ps[b][:, :], decay[:, h], op=ALU.mult,
                                 w=[tt, E_["decay", h], old])
                        k.close(b, [ta])
                        for tile in range(2):
                            need = [ta, E_["v", 0], E_["v", 1], E_["S"], E_["qdT", tile], obs[tile]]
                            yield need
                            o = k.ps[obs[tile].bank][:, h * P:(h + 1) * P]
                            for j in range(2):
                                k.mm(o, at[:, i, j * T + tile * P:j * T + (tile + 1) * P], vl[:, j, h * P:(h + 1) * P],
                                     j == 0, False, w=need)
                            to = k.mm(o, qdT[:, h, tile * P:(tile + 1) * P], S[:, h], False, True, inc=True)
                            E_["o", tile, h].set(to)
                        atS.give(i, [to])

                    def outputs(tile, obs):
                        yield [k.banks]
                        ob = k.bank()
                        obs[tile].set(ob, ())
                        to = [E_["o", tile, h] for h in range(4)]
                        yield [to, E_["qdT", 0], E_["qdT", 1]]
                        ta = k.a(A.activation, yr[:, tile], k.ps[ob][:, :], ACT.Square, w=[to, E_["qdT", 0], E_["qdT", 1]])
                        yield [ta]
                        tv = k.v(V.tensor_reduce, ost[:, tile, 0:4], yr[:, tile].rearrange("p (h d) -> p h d", d=P),
                                 axis=AX, op=ALU.add, w=[ta])
                        tg = k.g(G.tensor_scalar, ost[:, tile, 4:8], ost[:, tile, 0:4], 1.0 / P, EPS, ALU.mult, ALU.add,
                                 w=[tv])
                        tg = k.g(G.tensor_tensor, ost[:, tile, 8:12], ost[:, tile, 4:8], half[:, 0:4], op=ALU.pow,
                                 w=[tg])
                        yield [tg, E_["g", tile]]
                        for h in range(4):
                            c = slice(h * P, (h + 1) * P)
                            ty = k.v(V.scalar_tensor_tensor, yr[:, tile, c], k.ps[ob][:, c], ost[:, tile, 8 + h:9 + h],
                                     gate[:, tile, c], ALU.mult, ALU.mult, w=[tg, E_["g", tile], tv])
                        k.close(ob, [ty])
                        yield [ty, k.banks]
                        b = k.bank()
                        tt = flips(b, [yr[:, tile, h * P:(h + 1) * P] for h in range(4)], [ty])
                        yield [tt]
                        ta = k.a(A.copy, cat[:, 4:8, tile * P:(tile + 1) * P], bank4(b), w=[tt])
                        k.close(b, [ta])
                        E_["y", tile].set(ta)

                    def pooling(g):
                        yield [E_["pv", 0], E_["pv", 1], E_["dtmp"], d_l1, k.banks]
                        b = k.bank()
                        for r in range(2):
                            for j in range(2):
                                tt = k.mm(k.ps[b][:, r * T:(r + 1) * T], pv[:, j, (g + r) * P:(g + r + 1) * P],
                                          L("band", ((g + r) * 2 + j) * T, T), j == 0, j == 1,
                                          w=[E_["pv", 0], E_["pv", 1], d_l1], inc=j == 1 and r == 1)
                        yield [tt]
                        ta = k.a(A.copy, yp[:, g:g + 2], bank4(b, T), w=[tt, E_["dtmp"]])
                        k.close(b, [ta])
                        yield [ta, k.banks]
                        b = k.bank()
                        for r in range(2):
                            tt = k.mm(k.ps[b][:, r * T:(r + 1) * T], L("poolw", (g + r) * P, P), yp[:, g + r], True, True,
                                      w=[ta], inc=r == 1)
                        yield [tt, [E_["o", i, h] for i in range(2) for h in range(4)]]
                        for r in range(2):
                            tv = k.v(V.tensor_scalar, cat[:, g + r], k.ps[b][:, r * T:(r + 1) * T], C("psc", g + r, 1),
                                     None, ALU.mult, w=[tt, [E_["o", i, h] for i in range(2) for h in range(4)]])
                        k.close(b, [tv])
                        E_["p", g].set(tv)

                    k.spawn(decays())
                    E_["z"].set([k.v(V.memset, qTp[64:128, 0:4:2], 0.0), k.v(V.memset, qTp[0:64, 1:4:2], 0.0)])
                    ctx_cols = {0: (0, 512), 1: (0, 512), 2: (256, 512), 3: (256, 512)}
                    as_group(k, st, "od_in", H, t_h, order, cols=ctx_cols, evac=lambda *a: k.spawn(evac_qk(*a)))
                    k.spawn(states())
                    as_group(k, st, "od_in", H, t_h, order, evac=lambda *a: k.spawn(evac_v(*a)))
                    obs = [Bank(), Bank()]
                    for tile in range(2):
                        k.spawn(outputs(tile, obs))
                    for h in range(4):
                        k.spawn(scores(h, obs))
                    as_group(k, st, "od_in", H, t_h, [0, 1], evac=lambda *a: k.spawn(evac_g(*a)))
                    as_group(k, st, "od_in", H, t_h, [0, 1], evac=lambda *a: k.spawn(evac_pv(*a)))
                    t_pe = k.last()[0]
                    for g in (0, 2):
                        k.spawn(pooling(g))
                    t_cat = Evs()

                    def join(i, need):
                        yield need
                        t_cat[i].set(split(k, cat[:, 2 * i:2 * i + 2], Hh[:, 2 * i:2 * i + 2, 0:T],
                                           Hl[:, 2 * i:2 * i + 2, 0:T], [need, t_pe]))
                    ys = [E_["y", 0], E_["y", 1]]
                    for i, need in enumerate(([E_["p", 0]], [E_["p", 2]], ys, ys)):
                        k.spawn(join(i, need))
                tg = gate_tiles(s, 1, 2, (0,))
                start, t_x = add_gated(s)

                def x_H(kt, tile):
                    c = slice(tile * P, (tile + 1) * P)
                    return Hh[:, kt, c], Hl[:, kt, c]
                down(k, st, "od_out", KT, x_H, lambda kt, tile: t_cat[kt // 2], start(tg))
            if stop == 3:
                return finish(xt, k.last())

            with Scope(k) as s:
                hh = s.sb("hh", [P, FT, T], F32R)
                hl = s.sb("hl", [P, FT, T], F32R)
                with Scope(k) as sn:
                    t_h = norm_mod(sn, 1, 3, "n2", [0, 1], t_x)
                t_hid = ffn_up(s, "up1", H, [t_h[0], t_h[1]], hh, hl, 1)
                tg = gate_tiles(s, 1, 5, (0,))
                start, t_x = add_gated(s)
                down(k, st, "down1", FT, lambda kt, tile: (hh[:, kt, tile * P:(tile + 1) * P],
                                                           hl[:, kt, tile * P:(tile + 1) * P]),
                     lambda kt, tile: t_hid[kt], start(tg))
        if stop == 4:
            return finish(xt, k.last())

        with Scope(k) as s2:
            QO, nc2 = offsets(C2)
            c2 = s2.sb("c2", [P, nc2])
            d_c2 = k.dma("sp", c2[:, :], c2_in, w=k.last())
            Hh = s2.sb("H2h", [P, KT, T], F32R)
            Hl = s2.sb("H2l", [P, KT, T], F32R)
            H = (Hh, Hl)
            lb = s2.sb("lb", [P, 3, 8])
            lbm = s2.sb("lbm", [P, 12, 8])
            cst = s2.sb("cst", [P, 2, 16])
            stat = s2.sb("lnstat", [P, 2, 16])
            lng, lnb = xt[:, 2], xt[:, 3]
            HF = [slice(0, 512), slice(512, 1024)]

            def Q(name, i=0, n=None):
                at, size = QO[name]
                return c2[:, at + i:at + (i + n if n else size)]

            t_cst = [k.v(V.memset, cst[:, 0], 1.0), k.v(V.memset, cst[:, 1], 0.5)]
            one = cst[:, 0, 0:1]

            def spawn(f):
                return lambda *a: k.spawn(f(*a))

            def to_H(src, tile, hf, need, ev):
                yield [need, k.banks]
                b = k.bank()
                tt = flips(b, [src[:, tile, (hf * 4 + j) * P:(hf * 4 + j + 1) * P] for j in range(4)], [need])
                yield [tt]
                rows_, cols = slice(hf * 4, hf * 4 + 4), slice(tile * P, (tile + 1) * P)
                ta = k.a(A.copy, Hh[:, rows_, cols], bank4(b), w=[tt])
                yield [ta]
                tv = k.v(V.tensor_tensor, Hl[:, rows_, cols], bank4(b), Hh[:, rows_, cols].bitcast(F32),
                         op=ALU.subtract, w=[ta])
                k.close(b, [tv])
                ev[tile, hf].set([ta, tv])

            def by_tile(ev):
                return [[ev[tile, 0], ev[tile, 1]] for tile in range(2)]

            ln_n = [0]
            ln_old = [k.last()]
            d_ln = {}

            def load_ln():
                n = ln_n[0]
                ln_n[0] += 1
                ev = d_ln[n] = Ev()

                def go(old):
                    yield [old]
                    ev.set([k.dma("sp", dst, ln_in[n, r:r + 1].to_broadcast([P, D]), w=old)
                            for r, dst in enumerate((lng, lnb))])
                k.spawn(go(ln_old[0]))
                return ev

            def down_ln(key, nk, x, xtok, d_ln, x_old):
                ht, done = Evs(), Evs()
                banks = {(tile, hf): Bank() for tile in range(2) for hf in range(2)}

                def norm(tile):
                    xr = [xt[:, tile, c] for c in HF]
                    tb = []
                    for hf in range(2):
                        bk = banks[tile, hf]
                        yield [bk]
                        tx = k.v(V.scalar_tensor_tensor, xr[hf], xr[hf], DN_ALPHA, k.ps[bk.bank][:, :], ALU.mult, ALU.add,
                                 w=[bk, x_old[tile]])
                        k.close(bk.bank, [tx])
                        yield [tx]
                        tb.append(k.v(V.bn_stats, stat[:, tile, hf * 6:hf * 6 + 6], xr[hf], w=[tx]))
                    yield [tb]
                    ta = k.v(V.bn_aggr, stat[:, tile, 12:14], stat[:, tile, 0:12], w=tb)
                    yield [ta]
                    te = k.v(V.tensor_scalar, stat[:, tile, 14:15], stat[:, tile, 13:14], LN_EPS, None, ALU.add, w=[ta])
                    tg = k.g(G.tensor_tensor, stat[:, tile, 15:16], stat[:, tile, 14:15], half[:, 0:1], op=ALU.pow,
                             w=[te])
                    yield [d_ln]
                    t1 = [k.v(V.scalar_tensor_tensor, xr[hf], xr[hf], stat[:, tile, 12:13], lng[:, HF[hf]], ALU.subtract,
                              ALU.mult, w=[ta, d_ln]) for hf in range(2)]
                    yield [tg]
                    t2 = []
                    for hf in range(2):
                        t2.append(k.v(V.scalar_tensor_tensor, xr[hf], xr[hf], stat[:, tile, 15:16], lnb[:, HF[hf]],
                                      ALU.mult, ALU.add, w=[t1[hf], tg, d_ln]))
                        k.spawn(to_H(xt, tile, hf, t2[hf], ht))
                    done[tile].set(t2)

                def ready():
                    k.drain()
                    k.fence(("v", "a", "g"))
                    for tile in range(2):
                        k.spawn(norm(tile))

                down(k, st, key, nk, x, xtok, lambda tile, hf, b, t: banks[tile, hf].set(b, t), ready)
                ln_old[0] = [done[0], done[1]]
                return by_tile(ht), [done[0], done[1]]

            def x_H(kt, tile):
                c = slice(tile * P, (tile + 1) * P)
                return Hh[:, kt, c], Hl[:, kt, c]

            def norm_out(bk, tile, hf, nh, extra, gate, ost, sq, t_gate, old, used, ev, proj):
                dv = 512 // nh
                yield [bk, old]
                ps = k.ps[bk.bank]
                for h in range(nh):
                    c = slice(h * dv, (h + 1) * dv)
                    tv = k.a(A.activation, sq[:, c], ps[:, c], ACT.Square, accum_out=ost[:, 0, h:h + 1], w=[bk, old])
                used.set(tv)
                yield [tv, extra[1]]
                if extra[0] is None:
                    tv = k.v(V.tensor_scalar, ost[:, 1, 0:nh], ost[:, 0, 0:nh], 1.0 / dv, P * EPS, ALU.mult, ALU.add,
                             w=[tv])
                else:
                    tv = k.v(V.scalar_tensor_tensor, ost[:, 1, 0:nh], ost[:, 0, 0:nh], 1.0 / dv, extra[0], ALU.mult,
                             ALU.add, w=[tv, extra[1]])
                tg = k.g(G.tensor_tensor, ost[:, 2, 0:nh], ost[:, 1, 0:nh], half[:, 0:nh], op=ALU.pow, w=[tv])
                yield [tg, t_gate]
                for h in range(nh):
                    gh = gate[:, tile, hf * 512 + h * dv:hf * 512 + (h + 1) * dv]
                    ty = k.v(V.scalar_tensor_tensor, gh, ps[:, h * dv:(h + 1) * dv], ost[:, 2, h:h + 1], gh,
                             ALU.mult, ALU.mult, w=[tg, t_gate])
                k.close(bk.bank, [ty])
                k.spawn(to_H(gate, tile, hf, [ty, proj], ev))

            def gates_(s, gate, norm, dv, after):
                ev = Evs()

                def f(hf):
                    def g(tile, b, t):
                        g_ = gate[:, tile, HF[hf]]
                        yield [t]
                        tr = k.a(A.copy, g_, k.ps[b][:, :], w=[t])
                        k.close(b, [tr])
                        yield [tr, after]
                        ta = k.a(A.activation, g_, g_, ACT.Silu, w=[tr])
                        yield [ta]
                        g4 = g_.rearrange("p (h d) -> p h d", d=dv)
                        ev[tile, hf].set(k.v(V.tensor_tensor, g4, g4, norm.unsqueeze(1).to_broadcast([P, 512 // dv, dv]),
                                             op=ALU.mult, w=[ta]))
                    return spawn(g)
                return f, ev

            def small_proj(s, name, i, htok):
                wh = s.sb("wsh", [P, KT * 16], F32R)
                wl = s.sb("wsl", [P, KT * 16], F32R)
                w = Q(name, i * KT * 16, KT * 16)
                ts = split(k, w, wh[:, :], wl[:, :], [d_c2])
                k.until(htok)
                b = k.bank()
                for kt in range(KT):
                    c = slice(kt * 16, (kt + 1) * 16)
                    t = ws3(k, k.ps[b][0:16, 0:T], wh[:, c], wl[:, c], Hh[:, kt], Hl[:, kt], kt == 0, kt == KT - 1,
                            w=[ts, htok], inc=kt == KT - 1)
                return b, t

            t_lb = Ev()

            def bounds():
                m = lbm
                lo_ = lambda i: Q("lbl", i * 8, 8)
                yield [d_c2]
                t1 = k.v(V.tensor_tensor, m[:, 0], lo_(0), lo_(2), op=ALU.max, w=[d_c2])
                t1 = k.v(V.tensor_tensor, m[:, 0], m[:, 0], lo_(3), op=ALU.max, w=[t1])
                t2 = k.v(V.tensor_tensor, m[:, 1], m[:, 0], lo_(1), op=ALU.max, w=[t1])
                ts = []
                for n, (j, mx) in enumerate(((0, 0), (2, 0), (3, 0), (1, 1))):
                    ts.append(k.v(V.tensor_tensor, m[:, 2 + n], lo_(j), m[:, mx], op=ALU.subtract, w=[t2]))
                ts.append(k.v(V.tensor_tensor, m[:, 6], m[:, 0], m[:, 1], op=ALU.subtract, w=[t2]))
                ta = k.a(A.activation, m[:, 7:12], m[:, 2:7], ACT.Exp, w=[ts])
                yield [ta]
                t1 = k.v(V.tensor_tensor, m[:, 7], m[:, 7], m[:, 8], op=ALU.add, w=[ta])
                t1 = k.v(V.tensor_tensor, m[:, 7], m[:, 7], m[:, 9], op=ALU.add, w=[t1])
                t2 = k.v(V.tensor_tensor, m[:, 8], m[:, 7], m[:, 11], op=ALU.mult, w=[t1])
                t2 = k.v(V.tensor_tensor, m[:, 8], m[:, 8], m[:, 10], op=ALU.add, w=[t2])
                ta = k.a(A.activation, m[:, 9:11], m[:, 7:9], ACT.Ln, w=[t2, ta])
                yield [ta]
                t1 = k.v(V.tensor_tensor, lb[:, 0], m[:, 5], m[:, 10], op=ALU.subtract, w=[ta])
                t2 = k.v(V.tensor_tensor, lb[:, 1], m[:, 6], m[:, 9], op=ALU.add, w=[ta])
                t2 = k.v(V.tensor_tensor, lb[:, 1], lb[:, 1], m[:, 10], op=ALU.subtract, w=[t2])
                t_lb.set(k.v(V.tensor_tensor, lb[:, 2], lb[:, 1], lb[:, 0], op=ALU.subtract, w=[t1, t2]))

            def gdn(j, t_h, d_ln, x_old):
                with Scope(k, fenced=True) as s:
                    kf = s.sb("kf", [P, 8, T])
                    qf = s.sb("qf", [P, 8, T])
                    gate = s.sb("gate", [P, 2, D])
                    R = s.sb("R", [P, 2, 8, P])
                    DT = s.sb("DT", [P, 2, 8, P])
                    LT = s.sb("LT", [P, 2, 8, P])
                    X = s.sb("X", [P, 2, 8, P])
                    Y = s.sb("Y", [P, 2, 8, P])
                    Pm = s.sb("Pm", [P, 4, 512])
                    S1 = s.sb("S1", [P, 8, P])
                    kd = s.sb("kd", [P, 8, P])
                    EG = s.sb("EG", [P, 8, P])
                    sm = s.sb("gsm", [P, 12, 2, 8])
                    ba = s.sb("ba", [P, T])
                    jk = s.sb("jk", [P, 2, P])
                    ost = s.sb("gost", [P, 4, 3, 4])
                    vq = [a[:, :, :].rearrange("p a c -> p (a c)").rearrange("p (h t) -> p h t", t=T) for a in (S1, kd)]
                    gu = X
                    E_ = Evs()
                    htok = t_h
                    masksT = Q("mT").rearrange("p (l c) -> p l c", c=P)
                    masksL = Q("mL").rearrange("p (l c) -> p l c", c=P)
                    CQ = [(c, q) for q in range(2) for c in range(2)]

                    def quad(x, c, q):
                        return x[:, c, q * 4:q * 4 + 4]

                    def four(b, lhsT, rhs, w):
                        for h in range(4):
                            t = k.mm(k.ps[b][:, h * P:(h + 1) * P], lhsT(h), rhs(h), True, True, w=w, inc=h == 3)
                        return t

                    def decays(b, t):
                        yield [t]
                        t_ba = k.a(A.copy, ba[0:16, :], k.ps[b][0:16, 0:T], w=[t])
                        k.close(b, [t_ba])
                        yield [t_ba, k.banks]
                        b = k.bank()
                        for c in range(2):
                            tt = k.tr(k.ps[b][:, c * 16:(c + 1) * 16], ba[0:16, c * P:(c + 1) * P], ident[0:16, 0:16],
                                      w=[t_ba], inc=c == 1)
                        yield [tt]
                        p4 = k.ps[b][:, 0:32].rearrange("p (c w h) -> p c w h", c=2, w=2)
                        t1 = k.v(V.tensor_copy, sm[:, 0], p4[:, :, 0], w=[tt])
                        t2 = k.v(V.tensor_tensor, sm[:, 1], p4[:, :, 1],
                                 Q("dtb", j * 8, 8).unsqueeze(1).to_broadcast([P, 2, 8]), op=ALU.add, w=[tt, d_c2])
                        k.close(b, [t2])
                        yield [t1, t2]
                        ta = k.a(A.activation, sm[:, 2:4], sm[:, 0:2], ACT.Abs, w=[t1, t2])
                        ta = k.a(A.activation, sm[:, 2:4], sm[:, 2:4], ACT.Exp, scale=-1.0, w=[ta])
                        t1 = k.v(V.tensor_scalar, sm[:, 4], sm[:, 0], 0.0, None, ALU.min, w=[t1])
                        td = k.a(A.activation, sm[:, 6], sm[:, 3], ACT.Ln, bias=one, w=[ta, t_cst])
                        tb = k.a(A.activation, sm[:, 4], sm[:, 4], ACT.Exp, w=[t1])
                        tc = k.a(A.activation, sm[:, 5, 0], Q("alog", j * 8, 8), ACT.Exp)
                        yield [ta, td]
                        t2 = k.v(V.scalar_tensor_tensor, sm[:, 1], sm[:, 1], 0.0, sm[:, 6], ALU.max, ALU.add, w=[td])
                        t1 = k.v(V.tensor_scalar, sm[:, 2], sm[:, 2], 1.0, None, ALU.add, w=[ta])
                        yield [tc]
                        tg = k.v(V.scalar_tensor_tensor, sm[:, 1], sm[:, 1], -1.0,
                                 sm[:, 5, 0].unsqueeze(1).to_broadcast([P, 2, 8]), ALU.mult, ALU.mult, w=[t2, tc])
                        E_["g"].set(tg)
                        t1 = k.v(V.reciprocal, sm[:, 2], sm[:, 2], w=[t1])
                        E_["beta"].set(k.v(V.tensor_tensor, sm[:, 0], sm[:, 4], sm[:, 2], op=ALU.mult, w=[t1, tb]))
                        for c, q in CQ:
                            k.spawn(decay(c, q))
                        yield [tg, k.banks]
                        b = k.bank()
                        tt = k.mm(k.ps[b][:, 0:16], Q("SL"), sm[:, 1].rearrange("p c h -> p (c h)"), True, True,
                                  w=[tg, d_c2], inc=True)
                        yield [tt]
                        E_["eR"].set(k.a(A.activation, sm[:, 6].rearrange("p c h -> p (c h)"), k.ps[b][:, 0:16], ACT.Exp,
                                         w=[tt, td]))
                        k.close(b, [E_["eR"]])

                    def decay(c, q):
                        tg = E_["g"]
                        yield [tg]
                        tu = k.v(V.tensor_tensor, quad(gu, c, q), Q("U").unsqueeze(1).to_broadcast([P, 4, P]),
                                 sm[:, 1, c, q * 4:q * 4 + 4].unsqueeze(2).to_broadcast([P, 4, P]), op=ALU.mult, w=[tg])
                        yield [tu, k.banks]
                        b = k.bank()
                        tt = k.mm(k.ps[b][:, :], Q("SL"), quad(gu, c, q).rearrange("p h c -> p (h c)"), True, True,
                                  w=[tu], inc=True)
                        yield [tt]
                        ta = k.a(A.activation, quad(DT, c, q), bank4(b), ACT.Exp, w=[tt])
                        k.close(b, [ta])
                        E_["DT", c, q].set(ta)
                        if c:
                            yield [k.banks]
                            b = k.bank()
                            tt = k.mm(k.ps[b][:, :], Q("ones"), quad(gu, 1, q).rearrange("p h c -> p (h c)"), True, True,
                                      w=[tu], inc=True)
                            yield [tt]
                            ta = k.a(A.activation, EG[:, q * 4:q * 4 + 4], bank4(b), ACT.Exp, w=[tt])
                            k.close(b, [ta])
                            E_["EG", q].set(ta)
                        E_["guf", c, q].set(tt)

                    exps = [E_["eR"], E_["EG", 0], E_["EG", 1]] + [E_["DT", c, q] for c, q in CQ]

                    def conv(which, h, b, t, dst, old):
                        yield [t, old]
                        ps = k.ps[b][:, 0:T]
                        w_ = [Q("gcw", (j * 4 + tap) * 24 + which * 8 + h, 1) for tap in range(4)]
                        ta = k.a(A.activation, dst, ps, ACT.Identity, scale=w_[3], w=[t, old, d_c2])
                        for n in (1, 2, 3):
                            yield [ta]
                            ta = k.v(V.scalar_tensor_tensor, dst[:, n:T], ps[:, 0:T - n], w_[3 - n], dst[:, n:T],
                                     ALU.mult, ALU.add, w=[ta])
                        k.close(b, [ta])
                        E_["cv", which, h].set(ta)

                    def silu(which, q, dst):
                        need = [E_["cv", which, q * 4 + h] for h in range(4)]
                        yield [need, exps]
                        E_["f", which, q].set(k.a(A.activation, dst, dst, ACT.Silu, w=need))

                    def convolved(which, key, dst):
                        for h in range(8):
                            b, t = ws_tile(k, st, key, H, htok, T)
                            k.spawn(conv(which, h, b, t, dst[h // 4][:, h % 4], ()))
                            if h % 4 == 3:
                                k.spawn(silu(which, h // 4, dst[h // 4]))
                        return t

                    jks = []

                    def inverse(c, q):
                        kh = lambda h: kf[:, q * 4 + h, c * P:(c + 1) * P]
                        r_ = lambda r: sm[:, r, c, q * 4:q * 4 + 4]
                        lt, x_, y_ = quad(LT, c, q), quad(X, c, q), quad(Y, c, q)
                        pm = Pm[:, c * 2 + q].rearrange("p (h c) -> p h c", c=P)
                        tf = E_["f", 1, q]
                        yield [tf, k.banks]
                        b = k.bank()
                        tt = four(b, kh, kh, [tf])
                        yield [tt]
                        for h in range(4):
                            jks.append(k.v(V.tensor_tensor_reduce, out=jk[:, len(jks) % 2],
                                           in0=k.ps[b][:, h * P:(h + 1) * P], in1=ident, scale=1.0, scalar=0.0,
                                           op0=ALU.mult, op1=ALU.add, accum_out=sm[:, 7, c, q * 4 + h:q * 4 + h + 1],
                                           w=[tt, jks[-2:-1]]))
                        t1 = jks[-1]
                        yield [t1, E_["beta"], E_["eR"]]
                        t1 = k.v(V.tensor_scalar, r_(7), r_(7), EPS, None, ALU.add, w=[t1])
                        tr = k.g(G.tensor_tensor, r_(8), r_(7), cst[:, 1, 0:4], op=ALU.pow, w=[t1, t_cst])
                        E_["root", c, q].set(tr)
                        t1 = k.v(V.reciprocal, r_(9), r_(7), w=[t1])
                        t1 = k.v(V.tensor_tensor, r_(9), r_(9), r_(0), op=ALU.mult, w=[t1, E_["beta"]])
                        E_["w", c, q].set(t1)
                        tn = k.v(V.tensor_scalar, r_(10), r_(9), -1.0, None, ALU.mult, w=[t1])
                        E_["eRw", c, q].set(k.v(V.tensor_tensor, r_(11), r_(9), r_(6), op=ALU.mult, w=[t1, E_["eR"]]))
                        td = E_["DT", c, q]
                        yield [tn, td]
                        for h in range(4):
                            tl = k.v(V.scalar_tensor_tensor, lt[:, h], k.ps[b][:, h * P:(h + 1) * P],
                                     sm[:, 10, c, q * 4 + h:q * 4 + h + 1], DT[:, c, q * 4 + h], ALU.mult, ALU.mult,
                                     w=[tn, td])
                        k.close(b, [tl])
                        yield [tl]
                        t1 = k.v(V.tensor_tensor, y_, lt, masksT[:, 0].unsqueeze(1).to_broadcast([P, 4, P]), op=ALU.mult,
                                 w=[tl])
                        E_["DTm", c, q].set(k.g(G.tensor_tensor, quad(DT, c, q), quad(DT, c, q),
                                                Q("U").unsqueeze(1).to_broadcast([P, 4, P]), op=ALU.mult, w=[tl]))
                        yield [t1]
                        tY = k.v(V.tensor_tensor, y_, y_, ident.unsqueeze(1).to_broadcast([P, 4, P]), op=ALU.add, w=[t1])
                        yield [tY, E_["guf", c, q], k.banks]
                        b = k.bank()
                        tt = flips(b, [y_[:, h] for h in range(4)], [tY])
                        yield [tt]
                        tX = k.a(A.copy, x_, bank4(b), w=[tt, E_["guf", c, q]])
                        k.close(b, [tX])
                        for lv in range(1, 7):
                            yield [tX, k.banks]
                            b = k.bank()
                            tt = four(b, lambda h: lt[:, h], lambda h: x_[:, h], [tX, tl])
                            yield [tt]
                            tP = k.v(V.tensor_tensor, pm, bank4(b), masksL[:, lv].unsqueeze(1).to_broadcast([P, 4, P]),
                                     op=ALU.mult, w=[tt])
                            k.close(b, [tP])
                            yield [tP, k.banks]
                            b = k.bank()
                            if lv < 6:
                                tt = four(b, lambda h: y_[:, h], lambda h: pm[:, h], [tP, tY])
                                dst = x_
                            else:
                                E_["LTf", c, q].set(tt)
                                tt = four(b, lambda h: pm[:, h], lambda h: y_[:, h], [tP, tY])
                                dst = y_
                            yield [tt]
                            tv = k.v(V.tensor_tensor, dst, dst, bank4(b), op=ALU.add, w=[tt, tX])
                            k.close(b, [tv])
                            if lv < 6:
                                tX = tv
                                yield [tX, k.banks]
                                b = k.bank()
                                tt = flips(b, [x_[:, h] for h in range(4)], [tX])
                                yield [tt]
                                tY = k.a(A.copy, y_, bank4(b), w=[tt])
                                k.close(b, [tY])
                        E_["Y", c, q].set(tv)

                    def scores(c, q):
                        need = [E_["f", 0, q], E_["f", 1, q]]
                        yield [need, k.banks]
                        cols = slice(c * P, (c + 1) * P)
                        b = k.bank()
                        tt = four(b, lambda h: kf[:, q * 4 + h, cols], lambda h: qf[:, q * 4 + h, cols], need)
                        yield [tt, E_["w", c, q], E_["DTm", c, q]]
                        for h in range(4):
                            n = q * 4 + h
                            ta = k.v(V.scalar_tensor_tensor, DT[:, c, n], k.ps[b][:, h * P:(h + 1) * P],
                                     sm[:, 9, c, n:n + 1], DT[:, c, n], ALU.mult, ALU.mult,
                                     w=[tt, E_["w", c, q], E_["DTm", c, q]])
                        k.close(b, [ta])
                        E_["AT", c, q].set(ta)

                    def squares(c, q):
                        need = [E_["f", 0, q], E_["LTf", c, q]]
                        yield need
                        q2 = quad(LT, c, q)
                        ta = k.a(A.activation, q2, qf[:, q * 4:q * 4 + 4, c * P:(c + 1) * P], ACT.Square, w=need)
                        E_["q2", c, q].set(ta)
                        yield [ta, k.banks]
                        b = k.bank()
                        tt = four(b, lambda h: q2[:, h], lambda h: Q("ones"), [ta])
                        yield [tt]
                        tv = k.v(V.tensor_scalar, sm[:, 3, c, q * 4:q * 4 + 4], bank4(b)[:, :, 0], EPS, EPS * P, ALU.add,
                                 ALU.mult, w=[tt])
                        k.close(b, [tv])
                        E_["qe", c, q].set(tv)

                    def values(c, q):
                        need = [E_["f", 2, q], E_["root", c, q]]
                        yield [need, k.banks]
                        b = k.bank()
                        tt = flips(b, [vq[q][:, h, c * P:(c + 1) * P] for h in range(4)], need)
                        E_["vT", c, q].set(tt)
                        yield [tt]
                        tv = k.v(V.tensor_tensor, quad(R, c, q), bank4(b),
                                 sm[:, 8, c, q * 4:q * 4 + 4].unsqueeze(2).to_broadcast([P, 4, P]), op=ALU.mult,
                                 w=[tt, need])
                        k.close(b, [tv])
                        E_["R", c, q].set(tv)

                    def keys(q):
                        need = [E_["f", 1, q], E_["eRw", 0, q], E_["vT", 0, 1], E_["vT", 1, 1]]
                        yield [need, k.banks]
                        b = k.bank()
                        tt = flips(b, [kf[:, q * 4 + h, 0:P] for h in range(4)], need)
                        yield [tt]
                        tv = k.v(V.tensor_tensor, kd[:, q * 4:q * 4 + 4], bank4(b),
                                 sm[:, 11, 0, q * 4:q * 4 + 4].unsqueeze(2).to_broadcast([P, 4, P]), op=ALU.mult,
                                 w=[tt, need])
                        k.close(b, [tv])
                        E_["kd", q].set(tv)

                    def solved(c, q, t_r):
                        need = [E_["Y", c, q], t_r]
                        yield [need, k.banks]
                        b = k.bank()
                        tt = four(b, lambda h: Y[:, c, q * 4 + h], lambda h: R[:, c, q * 4 + h], need)
                        yield [tt]
                        ta = k.a(A.copy, quad(R, c, q), bank4(b), w=[tt])
                        k.close(b, [ta])
                        E_["Z", c, q].set(ta)

                    def second(q):
                        e4 = EG[:, q * 4:q * 4 + 4]
                        k4 = kf[:, q * 4:q * 4 + 4, P:T]
                        q4 = qf[:, q * 4:q * 4 + 4, P:T]
                        need = [E_["EG", q], E_["AT", 1, q], E_["q2", 1, q]]
                        yield need
                        t_k = k.v(V.tensor_tensor, k4, k4, e4, op=ALU.mult, w=need)
                        E_["q1", q].set(k.v(V.tensor_tensor, q4, q4, e4, op=ALU.mult, w=need))
                        need = [E_["kd", q], E_["Z", 0, q], E_["vT", 0, 0], E_["vT", 1, 0]]
                        yield [need, k.banks]
                        b = k.bank()
                        tt = four(b, lambda h: kd[:, q * 4 + h], lambda h: R[:, 0, q * 4 + h], need)
                        yield [tt]
                        ta = k.a(A.copy, S1[:, q * 4:q * 4 + 4], bank4(b), w=[tt, need])
                        k.close(b, [ta])
                        E_["S", q].set(ta)
                        need = [t_k, ta, E_["R", 1, q]]
                        yield [need, k.banks]
                        b = k.bank()
                        tt = four(b, lambda h: kf[:, q * 4 + h, P:T], lambda h: S1[:, q * 4 + h], need)
                        yield [tt]
                        tv = k.v(V.tensor_tensor, quad(R, 1, q), quad(R, 1, q), bank4(b), op=ALU.subtract, w=[tt, need])
                        k.close(b, [tv])
                        E_["R1", q].set(tv)

                    hn = Evs()

                    def outputs(c, q):
                        need = [E_["AT", c, q], E_["Z", c, q]]
                        if c:
                            need += [E_["q1", q], E_["S", q]]
                        yield [need, k.banks]
                        b = k.bank()
                        for h in range(4):
                            n = q * 4 + h
                            o = k.ps[b][:, h * P:(h + 1) * P]
                            if c:
                                k.mm(o, qf[:, n, P:T], S1[:, n], True, False, w=need)
                            tt = k.mm(o, DT[:, c, n], R[:, c, n], not c, True, w=need, inc=h == 3)
                        bk = Bank()
                        bk.set(b, tt)
                        k.spawn(norm_out(bk, c, q, 4, (sm[:, 3, c, q * 4:q * 4 + 4], E_["qe", c, q]), gate,
                                         ost[:, c * 2 + q], Pm[:, c * 2 + q], t_gate[c, q], E_["Y", c, q], Ev(), hn,
                                         E_["proj"]))

                    gates, t_gate = gates_(s, gate, Q("gnw", j * P, P), P, exps)
                    as_group(k, st, f"gdn{j}_z0", H, t_h, [0, 1], evac=gates(0))
                    k.spawn(decays(*small_proj(s, "wba", j, htok)))
                    for c, q in CQ:
                        k.spawn(inverse(c, q))
                    convolved(1, f"gdn{j}_k", [kf[:, 0:4], kf[:, 4:8]])
                    for c, q in CQ:
                        k.spawn(scores(c, q))
                        k.spawn(squares(c, q))
                    convolved(0, f"gdn{j}_q", [qf[:, 0:4], qf[:, 4:8]])
                    for c, q in CQ:
                        k.spawn(values(c, q))
                    for q in range(2):
                        k.spawn(keys(q))
                    convolved(2, f"gdn{j}_v", vq)
                    for q in range(2):
                        k.spawn(solved(0, q, E_["R", 0, q]))
                        k.spawn(second(q))
                        k.spawn(solved(1, q, E_["R1", q]))
                        k.spawn(outputs(0, q))
                        k.spawn(outputs(1, q))
                    as_group(k, st, f"gdn{j}_z1", H, t_h, [0, 1], evac=gates(1))
                    E_["proj"].set(k.last()[0])
                    return down_ln(f"gdn{j}_out", KT, x_H, lambda kt, tile: hn[tile, kt // 4], d_ln, x_old)

            def decayed(s, nh, g, t_g, qf, kf, vt, t_qk, t_v, gate, t_gate, hn, proj, E, old):
                dv = D // nh
                per = 512 // dv
                mexp = s.sb("mexp", [P, 12 * P], F32R)
                AT = s.sb("AT", [P, 2, 4, P])
                AX1 = s.sb("AX1", [P, 2, 2, P])
                sq = s.sb("osq", [P, 512], BF16)
                ost = s.sb("ost", [P, 4, 3, 4])
                stage = E[:, 0, 0:3].rearrange("p l h t -> p (l h t)")
                slots = list(range(4)) + [5, 6, 7]
                masks = Q("mT").rearrange("p (l c) -> p l c", c=P)
                E_ = Evs()
                d_m = k.dma("sp", stage, mexp_in, w=k.last())

                def constants():
                    yield [d_m]
                    E_["mexp"].set(k.a(A.copy, mexp[:, :], stage, w=[d_m]))

                def exps(gr, hh, tile, part):
                    i, h = gr % 2, gr * 2 + hh
                    tg = t_g(tile, h)
                    free = [E_["free", gr - 2], E_["mexp"], old if gr == 1 else ()]
                    yield [tg, free, k.banks]
                    b = k.bank()
                    c0 = (4 + 4 * tile) * P if part else 0
                    rhs = mexp[:, c0:c0 + 512]
                    k.mm(k.ps[b][:, :], g[0][:, tile, h * P:(h + 1) * P], rhs, True, False, w=[tg, E_["mexp"]])
                    tt = k.mm(k.ps[b][:, :], g[1][:, tile, h * P:(h + 1) * P], rhs, False, True, inc=True)
                    yield [tt]
                    s0 = 4 if part else 0
                    ta = k.a(A.activation, E[:, i, s0:s0 + 4, hh, tile * P:(tile + 1) * P],
                             k.ps[b][:, :].rearrange("p (l c) -> p l c", c=P), ACT.Exp, w=[tt, free])
                    k.close(b, [ta])
                    E_["E", gr, part, hh, tile].set(ta)

                def level(gr, lv, merged):
                    i = gr % 2
                    hs = slice(gr * 2, gr * 2 + 2)
                    need = t_qk(gr)
                    if lv < 7:
                        need = need + [E_["E", gr, lv // 4, hh, tile] for hh in range(2) for tile in range(2)]
                    yield need
                    tq = need
                    if lv < 7:
                        bl, sl = 64 >> lv, slots[lv]
                        view = lambda a: a.rearrange("p h (n y c) -> p (h n) y c", y=2, c=bl)
                        e_ = view(E[:, i, sl])
                        tq = []
                        for y, src in ((0, kf), (1, qf)):
                            tq.append(k.v(V.tensor_tensor, e_[:, :, y], e_[:, :, y], view(src[:, hs])[:, :, y],
                                          op=ALU.mult, w=need))
                    yield [tq, k.banks]
                    b = k.bank()
                    for hh in range(2):
                        for tile in range(2):
                            c = slice(tile * P, (tile + 1) * P)
                            if lv < 7:
                                l_ = r_ = E[:, i, sl, hh, c]
                            else:
                                l_, r_ = kf[:, gr * 2 + hh, c], qf[:, gr * 2 + hh, c]
                            n = hh * 2 + tile
                            tt = k.mm(k.ps[b][:, n * P:(n + 1) * P], l_, r_, True, True, w=tq, inc=n == 3)
                    yield [tt, E_["AT0", gr]]
                    mask = masks[:, 6 - lv] if lv < 7 else ident
                    ta = k.v(V.copy_predicated, AT[:, i], mask.bitcast(U32).unsqueeze(1).to_broadcast([P, 4, P]),
                             bank4(b), w=[tt, E_["AT0", gr], merged[-1:]])
                    k.close(b, [ta])
                    merged.append(ta)
                    E_["gram", gr, lv].set(tt)
                    if len(merged) == 8:
                        E_["AT", gr].set(ta)

                def across(gr):
                    i = gr % 2
                    hs = slice(gr * 2, gr * 2 + 2)
                    need = t_qk(gr) + [E_["E", gr, 1, hh, tile] for hh in range(2) for tile in range(2)]
                    yield need
                    tx = [k.v(V.tensor_tensor, E[:, i, 4, :, 0:P], E[:, i, 4, :, 0:P], kf[:, hs, 0:P], op=ALU.mult,
                              w=need),
                          k.v(V.tensor_tensor, E[:, i, 4, :, P:T], E[:, i, 4, :, P:T], qf[:, hs, P:T], op=ALU.mult,
                              w=need)]
                    yield [tx, k.banks]
                    b = k.bank()
                    for hh in range(2):
                        tt = k.mm(k.ps[b][:, hh * P:(hh + 1) * P], E[:, i, 4, hh, 0:P], E[:, i, 4, hh, P:T], True, True,
                                  w=tx, inc=hh == 1)
                    yield [tt, E_["av", gr - 2]]
                    tc = k.a(A.copy, AX1[:, i], k.ps[b][:, 0:256].rearrange("p (n c) -> p n c", c=P),
                             w=[tt, E_["av", gr - 2]])
                    k.close(b, [tc])
                    E_["AX", gr].set(tc)
                    grams = [E_["gram", gr, lv] for lv in range(8)]
                    yield [grams]
                    E_["free", gr].set([tt, grams])

                def cleared(gr):
                    yield [E_["av", gr - 2]]
                    E_["AT0", gr].set(k.g(G.memset, AT[:, gr % 2], 0.0, w=[E_["av", gr - 2]]))

                ob = {}

                def weighed(gr):
                    i = gr % 2
                    hf = gr * 2 // per
                    need = [E_["AT", gr], E_["AX", gr], t_v[0, hf], t_v[1, hf], E_["av", gr - 1]]
                    first = gr * 2 % per == 0
                    yield [need] + [k.banks] * (2 if first else 0)
                    if first:
                        for tile in range(2):
                            ob[tile, hf] = k.bank()
                    for tile in range(2):
                        for hh in range(2):
                            h = gr * 2 + hh
                            col = (h % per) * dv
                            o = k.ps[ob[tile, hf]][:, col:col + dv]
                            vs = slice(h * dv, (h + 1) * dv)
                            tt = k.mm(o, AT[:, i, hh * 2 + tile], vt[:, tile, vs], True, tile == 0, w=need,
                                      inc=tile == 0)
                            if tile:
                                tt = k.mm(o, AX1[:, i, hh], vt[:, 0, vs], False, True, inc=True)
                        if (gr * 2 + 2) % per == 0:
                            bk = Bank()
                            bk.set(ob[tile, hf], tt)
                            n = hf * 2 + tile
                            k.spawn(norm_out(bk, tile, hf, per, (None, ()), gate, ost[:, n], sq[:, :], t_gate[tile, hf],
                                             E_["sq", n - 1], E_["sq", n], hn, proj))
                    E_["av", gr].set(tt)

                E_["sq", -1].set(())
                for gr in (-2, -1):
                    E_["free", gr].set(())
                    E_["av", gr].set(())
                k.spawn(constants())
                for gr in range(nh // 2):
                    k.spawn(cleared(gr))
                    for part in range(2):
                        for hh in range(2):
                            for tile in range(2):
                                k.spawn(exps(gr, hh, tile, part))
                    merged = []
                    for lv in range(8):
                        k.spawn(level(gr, lv, merged))
                    k.spawn(across(gr))
                    k.spawn(weighed(gr))
                return [E_["E", gr, part, hh, tile] for gr in range(nh // 2) for part in range(2) for hh in range(2)
                        for tile in range(2)]

            def heads_ws(key, n, htok, evac):
                for h in range(n):
                    k.spawn(evac(h, *ws_tile(k, st, key, H, htok, T)))

            def copied(dst, ev):
                def f(h, b, t):
                    yield [t]
                    ta = k.a(A.copy, dst[:, h], k.ps[b][:, 0:T], w=[t])
                    k.close(b, [ta])
                    ev[h].set(ta)
                return f

            def values_(vt, ev):
                def f(hf):
                    def g(tile, b, t):
                        yield [t]
                        ta = k.a(A.copy, vt[:, tile, HF[hf]], k.ps[b][:, :], w=[t])
                        k.close(b, [ta])
                        ev[tile, hf].set(ta)
                    return spawn(g)
                return f

            def hgrn(t_h, d_ln, x_old):
                with Scope(k, fenced=True) as s:
                    kf = s.sb("kf", [P, 8, T])
                    qf = s.sb("qf", [P, 8, T])
                    gh = s.sb("gh", [P, 2, D], F32R)
                    gl = s.sb("gl", [P, 2, D], F32R)
                    vt = s.sb("vt", [P, 2, D])
                    gate = s.sb("gate", [P, 2, D])
                    E = s.sb("E", [P, 2, 8, 2, T])
                    E_, t_f, t_q, t_v, hn = Evs(), Evs(), Evs(), Evs(), Evs()
                    flat = E[:, 1].rearrange("p l h t -> p (l h t)")
                    g_ = gate[:, :, :].rearrange("p t c -> p (t c)")
                    room = [g_[:, 0:1024], g_[:, 1024:2048]] + [flat[:, i * 1024:(i + 1) * 1024] for i in range(4)]
                    room = [a.rearrange("p (h t) -> p h t", t=T) for a in room]
                    bc = lambda r, q: lb[:, r, q * 4:q * 4 + 4].unsqueeze(2).to_broadcast([P, 4, T])

                    def forget(q):
                        f_ = kf[:, q * 4:q * 4 + 4]
                        t1_, t2_, t3_ = room[q * 3:q * 3 + 3]
                        tf = [t_f[q * 4 + h] for h in range(4)]
                        yield [tf]
                        ta = k.a(A.activation, t1_, f_, ACT.Abs, w=[tf])
                        ta = k.a(A.activation, t1_, t1_, ACT.Exp, scale=-1.0, w=[ta])
                        ta = k.a(A.activation, t1_, t1_, ACT.Ln, bias=one, w=[ta, t_cst])
                        yield [ta]
                        tv = k.v(V.scalar_tensor_tensor, t2_, f_, 0.0, t1_, ALU.min, ALU.subtract, w=[ta, tf])
                        tk = k.v(V.scalar_tensor_tensor, t3_, f_, 0.0, t1_, ALU.max, ALU.add, w=[ta, tf])
                        yield [tv, t_lb]
                        tv = k.v(V.tensor_tensor, t2_, t2_, bc(2, q), op=ALU.add, w=[tv, t_lb])
                        yield [tv]
                        ta = k.a(A.activation, t1_, t2_, ACT.Abs, w=[tv, tk])
                        ta = k.a(A.activation, t1_, t1_, ACT.Exp, scale=-1.0, w=[ta])
                        ta = k.a(A.activation, t1_, t1_, ACT.Ln, bias=one, w=[ta])
                        for h in range(4):
                            tk2 = k.a(A.activation, kf[:, q * 4 + h], t3_[:, h], ACT.Exp, scale=-1.0,
                                      bias=lb[:, 1, q * 4 + h:q * 4 + h + 1], w=[tk, t_lb])
                        E_["k", q].set(tk2)
                        yield [ta]
                        tv = k.v(V.scalar_tensor_tensor, t2_, t2_, 0.0, t1_, ALU.max, ALU.add, w=[ta])
                        tv = k.v(V.tensor_tensor, t2_, t2_, bc(0, q), op=ALU.add, w=[tv, t_lb])
                        for tile in range(2):
                            yield [tv, k.banks]
                            b = k.bank()
                            tt = flips(b, [t2_[:, h, tile * P:(tile + 1) * P] for h in range(4)], [tv])
                            yield [tt]
                            ts = split(k, k.ps[b][:, :], gh[:, tile, HF[q]], gl[:, tile, HF[q]], [tt])
                            k.close(b, ts)
                            E_["g", tile, q].set(ts)
                        E_["forget", q].set([ts, tk2])

                    def silu(q):
                        need = [t_q[q * 4 + h] for h in range(4)]
                        yield [need, E_["forget", 0], E_["forget", 1]]
                        E_["q", q].set(k.a(A.activation, qf[:, q * 4:q * 4 + 4], qf[:, q * 4:q * 4 + 4], ACT.Silu, w=need))

                    done = [E_["forget", 0], E_["forget", 1]]
                    v_ = values_(vt, t_v)
                    as_group(k, st, "hg_i0", H, t_h, [0, 1], evac=v_(0))
                    exps = Evs()
                    gates, t_gate = gates_(s, gate, Q("hgn"), P, exps["all"])
                    all_exps = decayed(s, 8, (gh, gl), lambda tile, h: E_["g", tile, h // 4], qf, kf, vt,
                                       lambda gr: [E_["k", gr // 2], E_["q", gr // 2]], t_v, gate, t_gate, hn, E_["proj"], E,
                                       done)
                    exps["all"].set(all_exps)
                    for q in range(2):
                        k.spawn(forget(q))
                    heads_ws("hg_f", 8, t_h, copied(kf, t_f))
                    for q in range(2):
                        k.spawn(silu(q))
                    heads_ws("hg_q", 8, t_h, copied(qf, t_q))
                    as_group(k, st, "hg_i1", H, t_h, [0, 1], evac=v_(1))
                    k.until(done)
                    t_room = done
                    as_group(k, st, "hg_r", H, t_h, [0, 1], evac=gates(0))
                    as_group(k, st, "hg_r", H, t_h, [0, 1], evac=gates(1))
                    E_["proj"].set(k.last()[0])
                    return down_ln("hg_out", KT, x_H, lambda kt, tile: hn[tile, kt // 4], d_ln, x_old)

            def gla(t_h, d_ln, x_old):
                with Scope(k, fenced=True) as s:
                    kf = s.sb("kf", [P, 4, T])
                    qf = s.sb("qf", [P, 4, T])
                    gh = s.sb("gh", [P, 2, 512], F32R)
                    gl = s.sb("gl", [P, 2, 512], F32R)
                    vt = s.sb("vt", [P, 2, D])
                    gate = s.sb("gate", [P, 2, D])
                    gk = s.sb("gk", [32, T])
                    p_ = s.sb("p", [P, 2, 512])
                    l_ = s.sb("l", [P, 2, 512])
                    E = s.sb("E", [P, 2, 8, 2, T])
                    E_, t_q, t_k, t_v, hn = Evs(), Evs(), Evs(), Evs(), Evs()
                    t_one = k.v(V.memset, gk[:, :], 1.0)

                    def low(b, t):
                        yield [t]
                        ta = k.a(A.copy, gk[0:16, :], k.ps[b][0:16, 0:T], w=[t, t_one])
                        k.close(b, [ta])
                        E_["gk"].set(ta)

                    def forget(tile):
                        yield [E_["gk"], k.banks]
                        b = k.bank()
                        t = k.mm(k.ps[b][:, :], gk[0:17, tile * P:(tile + 1) * P], Q("wgk2")[0:17], True, True,
                                 w=[E_["gk"], d_c2], inc=True)
                        yield [t]
                        tp = k.a(A.copy, p_[:, tile], k.ps[b][:, :], w=[t])
                        k.close(b, [tp])
                        ta = k.a(A.activation, l_[:, tile], p_[:, tile], ACT.Abs, w=[tp])
                        ta = k.a(A.activation, l_[:, tile], l_[:, tile], ACT.Exp, scale=-1.0, w=[ta])
                        ta = k.a(A.activation, l_[:, tile], l_[:, tile], ACT.Ln, bias=one, w=[ta, t_cst])
                        yield [ta]
                        tv = k.v(V.scalar_tensor_tensor, l_[:, tile], p_[:, tile], 0.0, l_[:, tile], ALU.min, ALU.subtract,
                                 w=[ta])
                        yield [tv]
                        ta = k.a(A.activation, gh[:, tile], l_[:, tile], ACT.Copy, scale=0.0625, w=[tv])
                        yield [ta]
                        tv = k.v(V.scalar_tensor_tensor, gl[:, tile], l_[:, tile], 0.0625, gh[:, tile].bitcast(F32),
                                 ALU.mult, ALU.subtract, w=[ta])
                        E_["g", tile].set([ta, tv])

                    v_ = values_(vt, t_v)
                    as_group(k, st, "gla_v0", H, t_h, [0, 1], evac=v_(0))
                    exps = Evs()
                    gates, t_gate = gates_(s, gate, Q("gln"), 256, exps["all"])
                    k.spawn(low(*small_proj(s, "wgk", 0, t_h)))
                    for tile in range(2):
                        k.spawn(forget(tile))
                    all_exps = decayed(s, 4, (gh, gl), lambda tile, h: E_["g", tile], qf, kf, vt,
                                       lambda gr: [t_k[gr * 2], t_k[gr * 2 + 1], t_q[gr * 2], t_q[gr * 2 + 1]], t_v, gate,
                                       t_gate, hn, E_["proj"], E, ())
                    exps["all"].set(all_exps)
                    heads_ws("gla_q", 4, t_h, copied(qf, t_q))
                    heads_ws("gla_k", 4, t_h, copied(kf, t_k))
                    as_group(k, st, "gla_v1", H, t_h, [0, 1], evac=v_(1))
                    as_group(k, st, "gla_r", H, t_h, [0, 1], evac=gates(0))
                    as_group(k, st, "gla_r", H, t_h, [0, 1], evac=gates(1))
                    E_["proj"].set(k.last()[0])
                    return down_ln("gla_out", KT, x_H, lambda kt, tile: hn[tile, kt // 4], d_ln, x_old)

            def ffn(i, t_h, d_ln, x_old):
                with Scope(k, fenced=True) as s:
                    hh = s.sb("hh", [P, FT, T], F32R)
                    hl = s.sb("hl", [P, FT, T], F32R)
                    t_hid = ffn_up(s, f"fin{i}", H, t_h, hh, hl, None)
                    return down_ln(f"fdn{i}", FT, lambda kt, tile: (hh[:, kt, tile * P:(tile + 1) * P],
                                                                    hl[:, kt, tile * P:(tile + 1) * P]),
                                   lambda kt, tile: t_hid[kt], d_ln, x_old)

            k.spawn(bounds())
            first = Evs()
            for tile in range(2):
                for hf in range(2):
                    k.spawn(to_H(xt, tile, hf, t_x[tile], first))
            t_h, x_old = by_tile(first), [t_x[0], t_x[1]]
            for i in range(4):
                mixer = (lambda *a: gdn(0, *a), hgrn, gla, lambda *a: gdn(1, *a))[i]
                t_h, x_old = mixer(t_h, load_ln(), x_old)
                if stop == 5 + 2 * i:
                    return finish(xt, x_old)
                t_h, x_old = ffn(i, t_h, load_ln(), x_old)
                if stop == 6 + 2 * i:
                    return finish(xt, x_old)
            return finish(xt, x_old)



def ws_units(w):
    kk, n = w.shape
    return w.reshape(KT, P, n // P, P).transpose(2, 1, 0, 3).reshape(n // P, P, KT * P)


def as_units(w, cols):
    kk, n = w.shape
    r = UW // cols
    return w.reshape(kk // P // r, r, P, n // cols, cols).transpose(3, 0, 2, 1, 4).reshape(-1, P, UW)


def pair(a, b):
    return np.stack([a, b], 1).reshape(-1, P, UW)


def pack_weights(inp):
    g = lambda name, i=0: np.asarray(inp[name])[i]
    parts = {}
    ev = g("ev_w_in")
    parts["ev_qkv"] = np.concatenate([as_units(ev[:, c:c + 512], 512) for c in (2048, 1536, 2560)])
    parts["ev_conv"] = np.stack([ws_units(ev[:, 512:1024]), ws_units(ev[:, 1024:1536]), ws_units(ev[:, 0:512])],
                                1).reshape(-1, P, UW)
    parts["ev_out"] = as_units(g("ev_w_out"), 512)
    for i in range(2):
        up = g("ffn_w_up", i)
        parts[f"up{i}"] = pair(ws_units(up[:, :F]), ws_units(up[:, F:]))
    parts["down0"] = as_units(g("ffn_w_down", 0), 512)
    parts["down1"] = as_units(g("ffn_w_down", 1), 1024)
    od = g("od_w_in")
    parts["od_in"] = np.concatenate([as_units(od[:, c:c + 512], 512) for c in (512, 1024, 1536, 0)])
    parts["od_out"] = as_units(g("od_w_out"), 1024)
    for j in range(2):
        gd = g("gdn_w_in_2", j)
        for n, c in (("q", 0), ("k", 1024), ("v", 2048)):
            parts[f"gdn{j}_{n}"] = ws_units(gd[:, c:c + 1024])
        for hf in range(2):
            parts[f"gdn{j}_z{hf}"] = as_units(gd[:, 3072 + hf * 512:3584 + hf * 512], 512)
        parts[f"gdn{j}_out"] = as_units(g("gdn_w_out_2", j), 1024)
    hg = g("hgrn_w_in_2")
    parts["hg_q"], parts["hg_f"] = ws_units(hg[:, 0:1024]), ws_units(hg[:, 1024:2048])
    parts["hg_r"] = as_units(hg[:, 3072:4096], 512)
    parts["hg_out"] = as_units(g("hgrn_w_out_2"), 1024)
    gl = g("gla_w_in_2")
    parts["gla_q"], parts["gla_k"] = ws_units(gl[:, 0:512]), ws_units(gl[:, 512:1024])
    parts["gla_r"] = as_units(gl[:, 2048:3072], 512)
    for hf in range(2):
        parts[f"hg_i{hf}"] = as_units(hg[:, 2048 + hf * 512:2560 + hf * 512], 512)
        parts[f"gla_v{hf}"] = as_units(gl[:, 1024 + hf * 512:1536 + hf * 512], 512)
    parts["gla_out"] = as_units(g("gla_w_out_2"), 1024)
    for i in range(4):
        fi = g("ffn_w_in_2", i)
        parts[f"fin{i}"] = pair(ws_units(fi[:, :F]), ws_units(fi[:, F:]))
        parts[f"fdn{i}"] = as_units(g("ffn_w_down_2", i), 1024)
    mw = np.asarray(inp["mod_w"]).transpose(0, 2, 1).reshape(2, 24, 2, P, D).transpose(0, 1, 3, 2, 4).reshape(2, 24, P, CW)
    chunks = {key: v.reshape(-1, 2, P, UW).transpose(0, 2, 1, 3).reshape(-1, P, CW) for key, v in parts.items()}
    plan = weight_chunks()
    out = np.empty((len(plan), P, CW), np.float32)
    for j, (kind, key, i) in enumerate(plan):
        out[j] = mw[key, i] if kind == "m" else chunks[key][i]
    return out


def feat(a):
    a = np.asarray(a)
    return np.moveaxis(a.reshape(*a.shape[:-1], -1, P), -1, 0).reshape(P, -1)


def rows(a):
    a = np.asarray(a).reshape(1, -1)
    return np.broadcast_to(a, (P, a.shape[1]))


def packed(fields, values):
    return np.ascontiguousarray(np.concatenate(
        [np.asarray(values[n], np.float32).reshape(P, -1) for n, size in fields], 1))


def rope():
    t = np.arange(T)
    inv = np.float32(10000.0) ** (-np.arange(16, dtype=np.float32) / np.float32(16))
    ang = np.stack([(t // 64).astype(np.float32)[:, None] * inv, (t % 64).astype(np.float32)[:, None] * inv], 1)
    c, s = np.cos(ang), np.sin(ang)
    cc = np.stack([c, c], 2).reshape(T, 64)
    ss = np.stack([-s, s], 2).reshape(T, 64)
    lay = lambda a: a.reshape(2, P, 64).transpose(1, 0, 2).reshape(P, 128)
    return lay(cc), lay(ss)


def retention_consts():
    j = np.arange(T)[:, None]
    i = np.arange(T)[None, :]
    lay = lambda a: a.reshape(2, P, T).transpose(1, 0, 2).reshape(P, 512)
    f = np.maximum(i - j, 0)
    b = np.maximum(j - i, 0)
    two = (1.0 + (i == j)) * 0.125
    band = np.zeros((4, T, T))
    for g, r in enumerate((1, 2, 4, 8)):
        lo, hi = np.clip(i - r, 0, T), np.clip(i + r + 1, 0, T)
        band[g] = ((j >= lo) & (j < hi)) / (hi - lo) - (i == j)
    bl = band.reshape(4, 2, P, T).transpose(2, 0, 1, 3).reshape(P, 2048)
    return lay(f), lay(b), lay(two), bl


def kernel(**inputs):
    import concourse.bacc as _bacc
    from concourse import mybir as _mybir
    from concourse.bass_utils import run_bass_kernel_spmd as _run

    f32 = _mybir.dt.float32
    inp = {n: np.asarray(v) for n, v in inputs.items()}
    rc, rs = rope()
    df, db, two, band = retention_consts()
    p = np.arange(P)
    t2 = p[:, None] + np.array([0, P])[None, :]
    ramps = np.concatenate([t2 + 1, T - t2, T - 1 - t2, t2], 1)
    core = packed(CORE, {
        "ident": np.eye(P), "n1": feat(inp["norm1_g"]), "n2": feat(inp["norm2_g"]), "modb": feat(inp["mod_b"]),
        "fcw": feat(inp["ffn_conv_w"]), "fcb": feat(inp["ffn_conv_b"]), "scw": feat(inp["sc_conv_w"]),
        "psc": feat(inp["pool_scale"])})
    b1 = packed(B1, {
        "qg": rows(inp["da_q_norm"]), "kg": rows(inp["da_k_norm"]), "lq1": rows(inp["da_lq1"]),
        "lk1": rows(inp["da_lk1"]), "lq2": rows(inp["da_lq2"]), "lk2": rows(inp["da_lk2"]),
        "subg": rows(inp["da_subln_g"]), "ropec": rc, "ropes": rs, "rgn": rows(inp["ret_gn_g"]),
        "decf": rows(inp["ret_decay_f"]), "decb": rows(inp["ret_decay_b"]), "ramps": ramps})
    l1 = packed(L1C, {"dist_f": df, "dist_b": db, "two": two, "band": band,
                      "poolw": inp["pool_w"][0].transpose(1, 0, 2)})
    i, j = p[:, None], p[None, :]
    levels = [((i // (2 * b) == j // (2 * b)) & (i % (2 * b) < b) & (j % (2 * b) >= b)).astype(np.float32)
              for b in (1, 2, 4, 8, 16, 32, 64)]

    def to_middle(b):
        mid = j // (2 * b) * (2 * b) + b
        return np.where(j % (2 * b) >= b, (i >= mid) & (i <= j), (i > j) & (i < mid))

    low = [to_middle(b) for b in (4, 2, 1)]
    mexp = [to_middle(b) for b in (64, 32, 16, 8)] + [i > j] + low + [i <= j] + low
    wgk2 = np.zeros((P, 512), np.float32)
    wgk2[0:16] = inp["gla_w_gk2_2"][0]
    wgk2[16] = inp["gla_b_gk_2"][0]
    cols16 = lambda w: w.reshape(KT, P, 16).transpose(1, 0, 2).reshape(P, KT * 16)
    c2 = packed(C2, {
        "U": i <= j, "SL": i > j, "ones": np.ones((P, P)), "mT": np.concatenate(levels, 1),
        "mL": np.concatenate([m.T for m in levels], 1), "gcw": feat(inp["gdn_conv_w_2"]),
        "lbl": feat(inp["hgrn_lb_logits_2"]), "alog": rows(inp["gdn_a_log_2"]), "dtb": rows(inp["gdn_dt_bias_2"]),
        "gnw": rows(inp["gdn_norm_w_2"]), "hgn": rows(inp["hgrn_norm_w_2"]), "gln": rows(inp["gla_norm_w_2"]),
        "wba": np.concatenate([cols16(inp["gdn_w_in_2"][n][:, 4096:4112]) for n in range(2)], 1),
        "wgk": cols16(inp["gla_w_in_2"][0][:, 3072:3088]), "wgk2": wgk2})
    ln = np.stack([np.stack([inp["mix_ln_g_2"], inp["mix_ln_b_2"]], 1),
                   np.stack([inp["ffn_ln_g_2"], inp["ffn_ln_b_2"]], 1)], 1).reshape(8, 2, D)
    arrays = {
        "w": pack_weights(inp), "x": inp["x"].reshape(2, P, D), "ctx": inp["ctx"].reshape(2, P, D),
        "c": inp["c"].reshape(1, D), "cc": inp["c_ctx"].reshape(1, D), "core": core, "b1": b1, "l1": l1,
        "c2": c2, "ln": np.ascontiguousarray(ln), "mexp": np.concatenate(mexp, 1).astype(np.float32)}
    nc = _bacc.Bacc("TRN2", target_bir_lowering=False, num_devices=1)
    aps = [nc.dram_tensor("in_" + n, a.shape, f32, kind="ExternalInput").ap() for n, a in arrays.items()]
    out = nc.dram_tensor("out", [2, P, D], f32, kind="ExternalOutput").ap()
    fused_block(nc, *aps, out)
    r = _run(nc, [{"in_" + n: a for n, a in arrays.items()}], core_ids=[0])
    return r.results[0]["out"].reshape(1, T, D)
```

```python
from collections import deque
from contextlib import ExitStack

import numpy as np

import concourse.bass as bass
from concourse import mybir

P = 128
D = 1024
KT = D // P
F = 2816
FT = F // P
T = 256
CW = 2048
UW = 1024
NS = 8
SLACK = 1.5
SOON = 3
HELD = 5
TAIL = 3
LN_PE = (0, 1)
REST = 0.0
MORE = 2
X3 = 9
TAB = 1
AHEAD = 1
OUT_PE = False
LATE = 0.2
BACK = 3.0
PACE = {"ev_qkv": (1, 1.5, 3.0), "ev_conv": (1, 1.5, 3.0), "ev_out": (1, 1.5, 3.0)}
PACE.update({key: (SOON, SLACK, 1.5) for key in ("hg_i0", "hg_f", "hg_q", "hg_i1", "hg_r")})
PACE.update({f"gdn{j}_{c}": (SOON, 2.0, 2.0) for j in (0, 1) for c in ("z0", "k", "q", "v", "z1")})
EPS = 1e-6
LN_EPS = 1e-5
DN_ALPHA = 8.0 ** 0.25
LAM_INIT = 0.2

F32 = mybir.dt.float32
F32R = mybir.dt.float32r
BF16 = mybir.dt.bfloat16
U32 = mybir.dt.uint32
ALU = mybir.AluOpType
ACT = mybir.ActivationFunctionType
AX = mybir.AxisListType.X



def weight_chunks():
    out = [(kind, 0, i) for i in range(4) for kind in "nm"]
    qkv = [("w", "ev_qkv", i) for i in range(6)]
    conv = [("w", "ev_conv", i) for i in range(6)]
    m0 = [("m", 0, i) for i in range(8, 20)]
    for i, w in enumerate(qkv + conv + [("w", "ev_out", i) for i in range(4)]):
        out.append(w)
        if i >= 2 and m0:
            out.append(m0.pop(0))
    later = [("m", 0, i) for i in range(20, 24)] + [("m", 1, i) for i in range(24)]
    for i in range(FT):
        out.append(("w", "up0", i))
        if later:
            out.append(later.pop(0))
    for i in range(FT // 2):
        out.append(("w", "down0", i))
        if later:
            out.append(later.pop(0))
    assert not later
    out += [("w", "od_in", i) for i in range(8)]
    out += [("w", "od_out", i) for i in range(4)]
    out += [("w", "up1", i) for i in range(FT)]
    out += [("w", "down1", i) for i in range(FT // 2)]
    gdn = [("z0", 2), ("k", 4), ("q", 4), ("v", 4), ("z1", 2), ("out", 4)]
    mixers = [[("gdn0_" + c, n) for c, n in gdn],
              [("hg_i0", 2), ("hg_f", 4), ("hg_q", 4), ("hg_i1", 2), ("hg_r", 4), ("hg_out", 4)],
              [("gla_v0", 2), ("gla_q", 2), ("gla_k", 2), ("gla_v1", 2), ("gla_r", 4), ("gla_out", 4)],
              [("gdn1_" + c, n) for c, n in gdn]]
    for l in range(4):
        for key, n in mixers[l] + [(f"fin{l}", FT), (f"fdn{l}", FT // 2)]:
            out += [("w", key, i) for i in range(n)]
    return out


CORE = [("ident", 128), ("n1", 16), ("n2", 16), ("modb", 96), ("fcw", 132), ("fcb", 44), ("scw", 12),
        ("psc", 4), ("cc", 16)]
B1 = [("qg", 64), ("kg", 64), ("lq1", 64), ("lk1", 64), ("lq2", 64), ("lk2", 64), ("subg", 128),
      ("ropec", 128), ("ropes", 128), ("rgn", 128), ("decf", 4), ("decb", 4), ("ramps", 8)]
L1C = [("dist_f", 512), ("dist_b", 512), ("two", 512), ("band", 2048), ("poolw", 512)]

C2 = [("U", 128), ("SL", 128), ("ones", 128), ("halves", 254), ("turn", 128), ("gcw", 192), ("lbl", 32), ("alog", 16),
      ("dtb", 16), ("gnw", 256), ("hgn", 128), ("gln", 256), ("wba", 256), ("wgk", 128), ("wgk2", 512)]


def offsets(fields):
    at, out = 0, {}
    for name, n in fields:
        out[name] = (at, n)
        at += n
    return out, at



class Ev:

    def __init__(self):
        self.tok = None

    def set(self, tok):
        self.tok = tok


class Bank(Ev):

    def set(self, bank, tok):
        self.bank, self.tok = bank, tok


class Parted(Ev):

    def __init__(self):
        super().__init__()
        self.hi = Ev()


class Evs(dict):
    def __init__(self, kind=Ev):
        super().__init__()
        self.kind = kind

    def __missing__(self, key):
        self[key] = self.kind()
        return self[key]


class Halves(list):
    pass


class Slots:

    def __init__(self, n):
        self.idle = deque((i, ()) for i in range(n))
        self.spare = 0

    def take(self):
        return self.idle.popleft()

    def give(self, i, toks):
        self.idle.append((i, toks))


class Core:

    def __init__(self, nc, ctx):
        self.nc = nc
        self.ctx = ctx
        self.eng = {"pe": nc.tensor, "v": nc.vector, "a": nc.scalar, "g": nc.gpsimd, "sp": nc.sync}
        self.sem = {e: ctx.enter_context(nc.semaphore("s_" + e)) for e in self.eng}
        self.by_name = {"s_" + e: s for e, s in self.sem.items()}
        self.n = {e: 0 for e in self.eng}
        self.seen = {e: {} for e in self.eng}
        self.ps = [ctx.enter_context(nc.psum_tensor(f"ps{i}", [P, 512], F32)) for i in range(8)]
        self.banks = Slots(8)
        self.banks.spare = 1
        self.tasks = []
        self.ndma = 0
        self.ntensor = 0
        self.t = {e: 0.0 for e in self.eng}
        self.t["dma"] = 0.0
        self.clock = 0.0
        self.when = {}
        self.pump = lambda now, soon: None
        self.unsplit = lambda: 0
        self.urgent = 0
        self.soon, self.slack, self.back = SOON, SLACK, BACK
        self.uses = {}


    def flat(self, w):
        if w is None:
            return
        if isinstance(w, Ev):
            assert w.tok is not None
            yield from self.flat(w.tok)
        elif isinstance(w, tuple) and len(w) == 2 and isinstance(w[0], str):
            yield w
        else:
            for x in (w.values() if isinstance(w, dict) else w):
                yield from self.flat(x)

    def wait(self, e, w):
        for name, val in self.flat(w):
            self.t[e] = max(self.t[e], self.when.get((name, val), 0.0))
            if self.seen[e].get(name, 0) < val:
                self.eng[e].wait_ge(self.by_name[name], val)
                self.seen[e][name] = val

    def done(self, e, ins):
        self.n[e] += 1
        ins.then_inc(self.sem[e], 1)
        tok = ("s_" + e, self.n[e])
        self.when[tok] = self.t[e] + LATE
        return tok

    def size(self, a, kw):
        n, ones = 1, 0
        for x in list(a) + list(kw.values()):
            if isinstance(x, bass.AP):
                m = 1
                for d in x.shape[1:]:
                    m *= d
                n = max(n, m)
                ones += m == 1
        return n, ones

    def v(self, f, *a, w=(), **kw):
        self.wait("v", w)
        n, ones = self.size(a, kw)
        self.t["v"] += 0.07 + 0.06 * ones + n / 960
        return self.done("v", f(*a, **kw))

    def a(self, f, *a, w=(), **kw):
        self.wait("a", w)
        n, ones = self.size(a, kw)
        self.t["a"] += 0.08 + 0.09 * ones + n / 1200
        return self.done("a", f(*a, **kw))

    def g(self, f, *a, w=(), **kw):
        self.wait("g", w)
        n, ones = self.size(a, kw)
        self.t["g"] += (0.3 + n / 6 if kw.get("op") == ALU.pow else 0.18 + n / 490)
        return self.done("g", f(*a, **kw))

    def zero(self, out, w=()):
        return self.g(self.nc.gpsimd.memset, out, 0.0, w=[w, ("s_g", self.n["g"])])

    def mm(self, out, lhsT, rhs, start, stop, w=(), inc=False, on=False):
        self.wait("pe", w)
        n = self.size([out], {})[0]
        self.t["pe"] += 0.0025 + (max(n, 256) / 2400 if rhs.dtype == F32R else max(n, 128) / 600)
        ins = self.nc.tensor.matmul(out, lhsT, rhs, start=start, stop=stop, skip_group_check=on)
        return self.done("pe", ins) if inc else None

    def tr(self, out, in_, ident, w=(), inc=False, start=True, stop=True):
        self.wait("pe", w)
        self.t["pe"] += 0.109
        ins = self.nc.tensor.matmul(out, in_, ident, start=start, stop=stop, is_transpose=True)
        return self.done("pe", ins) if inc else None

    def dma_sem(self, name):
        self.by_name[name] = self.ctx.enter_context(self.nc.semaphore(name))
        return name

    def dma(self, e, out, in_, w=()):
        name = self.dma_sem(f"d{self.ndma}")
        self.ndma += 1
        self.wait(e, w)
        self.eng[e].dma_start(out, in_).then_inc(self.by_name[name], 16)
        self.moved(out, (name, 16), self.t[e])
        return (name, 16)

    def moved(self, out, tok, at):
        n = 4 / 360e3
        for d in out.shape:
            n *= d
        self.t["dma"] = max(self.t["dma"], at + 1.5) + n
        self.when[tok] = self.t["dma"] + 0.5

    def last(self):
        return [("s_" + e, self.n[e]) for e in ("pe", "v", "a", "g")]

    def fence(self, engines=("pe", "v", "a", "g")):
        now = self.last()
        for e in engines:
            self.wait(e, [t for t in now if t[0] != "s_" + e])


    def bank(self):
        while not self.banks.idle:
            self.force()
        b, toks = self.banks.take()
        self.wait("pe", toks)
        return b

    def close(self, b, toks):
        self.banks.give(b, toks)


    def spawn(self, gen, low=0, first=False):
        task = [gen, (), low, 0]
        self.tasks.insert(0 if first else len(self.tasks), task)
        self.step(task)

    def step(self, task):
        key = (task[0].__name__, task[3])
        had = dict(self.n)
        task[3] += 1
        try:
            task[1] = next(task[0])
        except StopIteration:
            self.tasks.remove(task)
        self.uses[key] = [e for e in ("v", "a") if self.n[e] > had[e]]

    def busy(self, task, now):
        return any(self.t[e] > now + self.back for e in self.uses.get((task[0].__name__, task[3]), ()))

    def ready(self, need):
        at, want = 0.0, {}
        for x in need:
            if isinstance(x, Slots):
                want[id(x)] = want.get(id(x), 0) + 1
                if len(x.idle) < want[id(x)] + x.spare:
                    return None
                x = x.idle[want[id(x)] - 1][1]
            for y in self.unset(x):
                return None
            for tok in self.flat(x):
                at = max(at, self.when.get(tok, 0.0))
        return at

    def unset(self, x):
        if isinstance(x, Ev):
            if x.tok is None:
                yield x
            else:
                yield from self.unset(x.tok)
        elif isinstance(x, (list, tuple)):
            for y in x:
                yield from self.unset(y)

    def poll(self):
        again = True
        while again:
            again = False
            now = max(self.t["pe"], self.clock)
            self.pump(now, True)
            for task in sorted(self.tasks, key=lambda task: task[2]):
                at = self.ready(task[1])
                if at is not None and at <= now and not self.busy(task, now) and not (task[2] and (self.t["v"] > now + self.slack or self.unsplit() < task[2])):
                    self.step(task)
                    again = True
                    break
        self.pump(max(self.t["pe"], self.clock), False)

    def force(self):
        best = None
        for task in sorted(self.tasks, key=lambda task: task[2]):
            at = self.ready(task[1])
            if at is not None:
                if task[2]:
                    at = max(at, self.t["v"]) + 1.2
                if best is None or at < best[0]:
                    best = (at, task)
        assert best is not None, "no task can go on"
        self.clock = max(self.clock, best[0] - (1.2 if best[1][2] else 0.0))
        self.step(best[1])

    def until(self, evs):
        while any(True for _ in self.unset(evs)):
            self.poll()
            if any(True for _ in self.unset(evs)):
                self.force()

    def drain(self):
        while any(not task[2] for task in self.tasks):
            self.poll()
            if any(not task[2] for task in self.tasks):
                self.force()


class Scope:

    def __init__(self, k, fenced=False):
        self.k = k
        self.fenced = fenced
        self.st = ExitStack()

    def __enter__(self):
        return self

    def sb(self, name, shape, dt=F32):
        self.k.ntensor += 1
        return self.st.enter_context(self.k.nc.sbuf_tensor(f"{name}_{self.k.ntensor}", shape, dt))

    def both(self, name, shape):
        at = self.k.nc.sbuf_base
        a = self.sb(name, shape, F32R)
        return a, self.k.nc.alloc_sbuf_tensor_at(f"{name}_f_{self.k.ntensor}", shape, F32, offset=at)

    def __exit__(self, *failed):
        if not any(failed):
            if not self.fenced:
                self.k.drain()
                self.k.fence()
            self.st.close()


class Stream:

    def __init__(self, k, W, plan):
        self.k, self.W, self.on_mod = k, W, {}
        at = k.nc.sbuf_base
        self.ring = k.ctx.enter_context(k.nc.sbuf_tensor("ring", [P, NS, 2, UW], F32R))
        self.raw = k.nc.alloc_sbuf_tensor_at("raw", [P, NS, 2, UW], F32, offset=at)
        self.sems = [k.dma_sem(f"w{i}") for i in range(NS)]
        self.items = []
        for j, (kind, key, i) in enumerate(plan):
            self.items += [(j, 0), (j, 1)] if kind == "w" else [(j, None)]
        self.plan = plan
        self.at = [n for n, (j, h) in enumerate(self.items) if h is not None]
        self.keys = [plan[self.items[n][0]][1] for n in self.at]
        self.loaded = 0
        self.freed = {}
        self.issued = Evs()
        self.made = self.taken = 0
        self.tok = {}
        self.load()
        k.pump = self.ahead
        k.unsplit = lambda: self.at[self.made] + 1 if self.made < len(self.at) else len(self.items) + 1

    def landed(self, n):
        return (self.sems[n % NS], 16 * (n // NS + 1))

    def load(self):
        k = self.k
        while self.loaded < len(self.items) and (self.loaded < NS or self.loaded - NS in self.freed):
            n = self.loaded
            j, h = self.items[n]
            k.wait("sp", self.freed.get(n - NS))
            slot = self.raw[:, n % NS]
            if h is None:
                dst, src = slot.rearrange("p h c -> p (h c)"), self.W[j]
            else:
                dst, src = slot[:, 1], self.W[j, :, h * UW:(h + 1) * UW]
            k.nc.sync.dma_start(dst, src).then_inc(k.by_name[self.sems[n % NS]], 16)
            k.moved(dst, self.landed(n), k.t["sp"])
            self.loaded += 1
            self.issued[n].set(())
            if h is None:
                k.spawn(self.other(n), n + 1 if n >= NS else 0)

    def other(self, n):
        yield [self.landed(n)]
        kind, layer, i = self.plan[self.items[n][0]]
        slot = self.raw[:, n % NS].rearrange("p h c -> p (h c)")
        self.freed[n] = yield from self.on_mod[kind](layer, i, slot, self.landed(n))
        self.load()

    def pump(self, upto, now=None, may=True):
        k, nc = self.k, self.k.nc
        while self.made < len(self.at) and self.made <= upto:
            n = self.at[self.made]
            if n >= self.loaded:
                break
            landed = self.landed(n)
            if now is not None:
                soon = self.made <= self.taken + (0 if k.urgent else k.soon)
                rest = k.t["v"] <= now + (REST if k.urgent else k.slack) and (not k.urgent or self.made <= self.taken + MORE)
                if k.when[landed] > now or not (soon or may and rest):
                    break
            hi, lo = self.ring[:, n % NS, 0], self.ring[:, n % NS, 1]
            raw = self.raw[:, n % NS, 1]
            ta = k.a(nc.scalar.copy, hi, raw, w=[landed])
            tv = k.v(nc.vector.tensor_tensor, lo, raw, hi.bitcast(F32), op=ALU.subtract, w=[ta])
            self.tok[self.made] = [ta, tv]
            self.made += 1

    def take(self, key):
        u = self.taken
        assert self.keys[u] == key, (u, self.keys[u], key)
        self.k.soon, self.k.slack, self.k.back = PACE.get(key, (SOON, SLACK, BACK))
        self.k.poll()
        while self.loaded <= self.at[u]:
            self.k.force()
        self.pump(u)
        self.taken += 1
        return u

    def ahead(self, now, soon):
        self.pump(len(self.at), now, not soon)

    def parts(self, u):
        s = self.at[u] % NS
        return self.ring[:, s, 0], self.ring[:, s, 1], self.tok[u]

    def free(self, u, tok):
        self.freed[self.at[u]] = tok
        self.load()


def high(w):
    return w.hi if isinstance(w, Parted) else w


def as2(k, out, xh, wh, wl, first, w=()):
    k.mm(out, xh, wh, first, False, w=w)
    k.mm(out, xh, wl, False, False)


def as3(k, out, xh, xl, wh, wl, first, last, w=(), inc=False):
    as2(k, out, xh, wh, wl, first, w)
    return k.mm(out, xl, wh, False, last, inc=inc)


def ws3(k, out, wh, wl, xh, xl, first, last, w=(), inc=False):
    k.mm(out, wh, xh, first, False, w=w)
    k.mm(out, wh, xl, False, False)
    return k.mm(out, wl, xh, False, last, inc=inc)


def ws_tile(k, st, key, H, htok, ntok):
    k.until(htok)
    u = st.take(key)
    wh, wl, wt = st.parts(u)
    b = k.bank()
    out = k.ps[b][:, 0:ntok]
    for kt in range(KT):
        c = slice(kt * P, (kt + 1) * P)
        t = ws3(k, out, wh[:, c], wl[:, c], H[0][:, kt, 0:ntok], H[1][:, kt, 0:ntok], kt == 0, kt == KT - 1,
                w=[wt, htok] if kt == 0 else (), inc=kt == KT - 1)
        if kt % 2 and kt < KT - 1:
            k.poll()
    st.free(u, t)
    return b, t


def as_group(k, st, key, H, htok, tiles, cols=(0, 512), evac=None):
    us = []
    for n, tile in enumerate(tiles):
        lo, hi = cols[tile] if isinstance(cols, dict) else cols
        need = htok[tile] if isinstance(htok[tile], Halves) else [htok[tile], ()]
        x = slice(tile * P, (tile + 1) * P)
        last = n == len(tiles) - 1

        def weights(kt):
            wh, wl, wt = st.parts(us[kt // 2])
            c = slice((kt % 2) * 512 + lo, (kt % 2) * 512 + hi)
            return wh[:, c], wl[:, c], wt

        def low(kt):
            t = k.mm(out, H[1][:, kt, x], weights(kt)[0], False, kt == KT - 1, w=[need[kt // 4]],
                     inc=kt == KT - 1 or (last and kt % 2 == 1))
            if kt % 2 == 1 and last:
                st.free(us[kt // 2], t)
            return t

        k.until(high(need[0]))
        b = k.bank()
        out = k.ps[b][:, 0:hi - lo]
        for half in range(2):
            apart = isinstance(need[half], Parted)
            k.until(high(need[half]))
            for kt in range(half * 4, half * 4 + 4):
                if n == 0 and kt % 2 == 0:
                    us.append(st.take(key))
                wh, wl, wt = weights(kt)
                as2(k, out, H[0][:, kt, x], wh, wl, kt == 0, [wt, high(need[half])])
                if not apart:
                    t = low(kt)
                if kt < KT - 1:
                    k.poll()
            if apart:
                k.until(need[half])
                for kt in range(half * 4, half * 4 + 4):
                    t = low(kt)
        evac(tile, b, t)
        k.poll()


def down(k, st, key, nk, x, xtok, evac, ready=None):
    bs = [[k.bank(), k.bank()] for _ in range(2)]
    us = {}

    def part(kt, tile, hfs, inc):
        wh, wl, wt = st.parts(us[kt])
        xh, xl = x(kt, tile)
        need = xtok(kt, tile)
        cs = [slice(hf * 512, (hf + 1) * 512) for hf in hfs]
        k.until(high(need))
        for hf, c in zip(hfs, cs):
            as2(k, k.ps[bs[tile][hf]][:, :], xh, wh[:, c], wl[:, c], kt == 0, [wt, high(need)])
        k.until(need)
        for hf, c in zip(hfs, cs):
            t = k.mm(k.ps[bs[tile][hf]][:, :], xl, wh[:, c], False, kt == nk - 1, w=need, inc=inc and hf == hfs[-1])
        return t

    for kt in range(nk - HELD):
        us[kt] = st.take(key)
        for tile in range(2):
            t = part(kt, tile, (0, 1), tile == 1)
            if tile == 0:
                k.poll()
        st.free(us[kt], t)
    def rest(tile, hf, kts, last):
        for kt in kts:
            t = part(kt, tile, (hf,), last or kt == nk - 1)
            if last:
                st.free(us[kt], t)
            k.poll()
        return t

    for kt in range(nk - HELD, nk):
        us[kt] = st.take(key)
        t = part(kt, 0, (0,), kt == nk - 1)
        k.poll()
    if ready:
        k.until([xtok(kt, i) for kt in range(nk) for i in range(2)])
        ready()
    evac(0, 0, bs[0][0], t)
    k.poll()
    t = rest(0, 1, range(nk - HELD, nk), False)
    evac(0, 1, bs[0][1], t)
    k.poll()
    for kt in range(nk - HELD, nk - TAIL):
        for hf in range(2):
            rest(1, hf, [kt], hf == 1)
    for hf in range(2):
        t = rest(1, hf, range(nk - TAIL, nk), hf == 1)
        evac(1, hf, bs[1][hf], t)
        k.poll()


def split(k, src, hi, lo, w, ev=None):
    ta = k.a(k.nc.scalar.copy, hi, src, w=w)
    tv = k.v(k.nc.vector.tensor_tensor, lo, src, hi.bitcast(F32), op=ALU.subtract, w=[ta, w])
    if ev is not None:
        ev.hi.set([ta])
        ev.set([ta, tv])
    return [ta, tv]


def fused_block(nc, W, x_in, ctx_in, core_in, b1_in, l1_in, c2_in, ln_in, mexp_in, out):
    with ExitStack() as ctx:
        k = Core(nc, ctx)
        V, A, G = nc.vector, nc.scalar, nc.gpsimd
        CO, ncore = offsets(CORE)
        core = ctx.enter_context(nc.sbuf_tensor("core", [P, ncore], F32))
        xt = ctx.enter_context(nc.sbuf_tensor("xt", [P, 4, D], F32))
        half = ctx.enter_context(nc.sbuf_tensor("half", [P, 16], F32))
        s0 = ctx.enter_context(Scope(k, fenced=True))
        grows = s0.sb("grows", [P, 2, D])
        gtmp = s0.sb("gtmp", [P, 2, 512])
        Hh, Hh_f = s0.both("Hh", [P, KT, 512])
        Hl, Hl_f = s0.both("Hl", [P, KT, 512])
        H = (Hh, Hl)
        d_core = k.dma("sp", core[:, :], core_in)
        d_ctx = k.dma("sp", xt[:, 2], ctx_in[0])
        st = Stream(k, W, weight_chunks())

        def C(name, i=0, n=None):
            at, size = CO[name]
            return core[:, at + i:at + (i + n if n else size)]

        ident = C("ident")

        def bank4(b, c=P):
            return k.ps[b][:, :].rearrange("p (h c) -> p h c", c=c)

        def flips(b, srcs, w, on=False, by=None):
            for i, src in enumerate(srcs):
                t = k.tr(k.ps[b][:, i * P:(i + 1) * P], src, ident if by is None else by, w=w, inc=i == len(srcs) - 1,
                         start=not on or i == 0, stop=not on or i == len(srcs) - 1)
            return t

        def settle():
            k.drain()
            now = k.last()[1:]
            k.fence(("v", "a", "g"))
            return now

        def urgent(evs):
            def settled():
                yield evs
                k.urgent -= 1
            k.urgent += 1
            k.spawn(settled())

        def to_H(src, tile, hf, need, ev, by_pe=False, by=None):
            yield [need, k.banks]
            b = k.bank()
            tt = flips(b, [src[:, tile, (hf * 4 + j) * P:(hf * 4 + j + 1) * P] for j in range(4)], [need], by_pe, by)
            yield [tt]
            rows_, cols = slice(hf * 4, hf * 4 + 4), slice(tile * P, (tile + 1) * P)
            ta = k.a(A.copy, Hh[:, rows_, cols], bank4(b), w=[tt])
            ev[tile, hf].hi.set([ta])
            yield [ta]
            if by_pe:
                tm = k.mm(bank4(b), minus[:, :], Hh[:, rows_, cols], False, True, w=[ta, t_minus], inc=True, on=True)
                yield [tm]
                tv = k.a(A.copy, Hl[:, rows_, cols], bank4(b), w=[tm])
            else:
                tv = k.v(V.tensor_tensor, Hl[:, rows_, cols], bank4(b), Hh[:, rows_, cols].bitcast(F32),
                         op=ALU.subtract, w=[ta])
            k.close(b, [tv])
            ev[tile, hf].set([ta, tv])

        def by_tile(ev):
            return [Halves([ev[tile, 0], ev[tile, 1]]) for tile in range(2)]

        def part_done(bk, tok):
            bk.share.append(tok)
            if len(bk.share) == bk.of:
                k.close(bk.bank, bk.share)

        def whole(b, t):
            bk = Bank()
            bk.set(b, t)
            bk.at, bk.of, bk.share = 0, 1, []
            return bk

        def up_first(key, H, htok, tiles, raw):
            ntok = len(tiles) * P
            per = 512 // ntok
            got = Evs()
            banks = [Bank() for f in range(4)]

            def evac(tile, b, t):
                yield [t]
                ta = k.a(A.copy, raw[:, tile], k.ps[b][:, :], w=[t])
                k.close(b, [ta])
                got[tile].set(ta)

            def turn(f):
                need = [got[tile] for tile in tiles]
                yield [need, k.banks]
                b = k.bank()
                share = []
                for i in range(per):
                    for tile in sorted(tiles):
                        c = i * ntok + tile * P
                        t = k.tr(k.ps[b][:, c:c + P], raw[:, tile, (f + i) * P:(f + i + 1) * P], ident, w=need,
                                 inc=i == per - 1 and tile == max(tiles))
                for i in range(per):
                    bk = banks[f + i]
                    bk.at, bk.of, bk.share = i * ntok, per, share
                    bk.set(b, t)

            as_group(k, st, key, H, htok, tiles, evac=lambda *a: k.spawn(evac(*a)))
            for f in range(0, 4, per):
                k.spawn(turn(f))
            return banks

        def ffn_up(s, key, H, htok, hh, hl, place, layer):
            tmp = s.sb("ffn_tmp", [P, 3, 2, T])
            slots = Slots(3)
            hid = Evs(Parted)

            def act(f, first, second):
                yield [first, slots]
                i, old = slots.take()
                ab, sg = tmp[:, i, 0], tmp[:, i, 1]
                ps = k.ps[first.bank][:, first.at:first.at + T]
                if layer is None:
                    ts = k.a(A.activation, sg, ps, ACT.Silu, w=[first, old, first.share])
                    part_done(first, ts)
                else:
                    w_ = [C("fcw", layer * 66 + tap * 22 + f, 1) for tap in range(3)]
                    ta = k.a(A.activation, ab, ps, ACT.Identity, bias=C("fcb", layer * 22 + f, 1), scale=w_[1],
                             w=[first, old, first.share])
                    yield [ta]
                    tv = k.v(V.scalar_tensor_tensor, ab[:, 1:T], ps[:, 0:T - 1], w_[0], ab[:, 1:T], ALU.mult, ALU.add,
                             w=[ta])
                    yield [tv]
                    tv = k.v(V.scalar_tensor_tensor, ab[:, 0:T - 1], ps[:, 1:T], w_[2], ab[:, 0:T - 1], ALU.mult,
                             ALU.add, w=[tv])
                    part_done(first, tv)
                    yield [tv]
                    ts = k.a(A.activation, sg, ab, ACT.Silu, w=[tv])
                yield [ts, second]
                b, t = second.bank, second.tok
                tv = k.v(V.tensor_tensor, ab, sg, k.ps[b][:, 0:T], op=ALU.mult, w=[ts, t, old])
                k.close(b, [tv])
                yield [tv]
                ta = k.a(A.copy, hh[:, f], ab, w=[tv])
                hid[f].hi.set([ta])
                yield [ta]
                tv = k.v(V.tensor_tensor, hl[:, f], ab, hh[:, f].bitcast(F32), op=ALU.subtract, w=[ta])
                slots.give(i, [ta, tv])
                hid[f].set([ta, tv])

            raw = place[:, 10:14].rearrange("p (t u) c -> p t (u c)", t=2)
            firsts = up_first(key, H, htok, [0, 1], raw)
            htok = [htok[0], htok[1]]
            for f in range(FT):
                second = Bank()
                k.spawn(act(f, firsts[f] if f < 4 else whole(*ws_tile(k, st, key, H, htok, T)), second))
                second.set(*ws_tile(k, st, key, H, htok, T))
            return hid


        with Scope(k, fenced=True) as s1:
            at_s1 = nc.sbuf_base
            BO, nb1 = offsets(B1)
            b1 = s1.sb("b1", [P, nb1])
            silu_c = s1.sb("silu_c", [P, 2, D])
            mod = s1.sb("mod", [P, 2, 2, 48])
            stat = s1.sb("stat", [P, 4, 4, 4])
            stats = [0]
            junk = s1.sb("junk", [P, 2, D], BF16)
            sq = s1.sb("sq", [P, 512], BF16)
            t_sq = []
            ccol = s1.sb("ccol", [P, 2, KT])
            mrows = s1.sb("mrows", [2, 2, 512])
            order = [2, 3, 0, 1]

            def B(name, i=0, n=None):
                at, size = BO[name]
                return b1[:, at + i:at + (i + n if n else size)]

            d_x, d_b1 = Evs(), Ev()

            def arrivals(toks, parts):
                yield toks
                for ev, dst, src in parts:
                    ev.set(k.dma("sp", dst, src))
            d_x[2].set(d_ctx)
            k.spawn(arrivals([st.issued[X3]], [(d_x[3], xt[:, 3], ctx_in[1])]))
            k.spawn(arrivals([st.issued[11]], [(d_x[i], xt[:, i], x_in[i]) for i in range(2)] + [(d_b1, b1[:, :], b1_in)]))
            t_half = k.v(V.memset, half[:, :], -0.5)
            t_scol = k.a(A.activation, ccol[:, :], C("cc").rearrange("p (w t) -> p w t", w=2), ACT.Silu, w=[d_core])
            t_silu = Evs()

            def broadcast(who):
                toks = []
                for hf in range(2):
                    yield [t_scol, k.banks]
                    b = k.bank()
                    for j in range(4):
                        tt = k.mm(k.ps[b][:, j * P:(j + 1) * P],
                                  ccol[:, who, hf * 4 + j:hf * 4 + j + 1].to_broadcast([P, P]), ident, True, True,
                                  w=[t_scol], inc=j == 3)
                    yield [tt]
                    ta = k.a(A.copy, silu_c[:, who, hf * 512:(hf + 1) * 512], k.ps[b][:, :], w=[tt])
                    k.close(b, [ta])
                    toks.append(ta)
                t_silu[who].set(toks)

            for who in range(2):
                k.spawn(broadcast(who))

            t_mod, t_junk, t_first = Evs(), [], Ev()
            need = {0: (6, 6), 1: (6, 2)}

            def by_rows(layer, i, raw, landed):
                for who in (1, 0):
                    yield [t_silu[who], t_first if (layer, i, who) == (0, 3, 0) else ()]
                    for r in range(2):
                        col = 2 * i + r
                        part = col // 8
                        if part < need[layer][who]:
                            t = k.v(V.tensor_tensor_reduce, out=junk[:, len(t_junk) % 2], in0=raw[:, r * D:(r + 1) * D],
                                    in1=silu_c[:, who], scale=1.0, scalar=0.0, op0=ALU.mult, op1=ALU.add,
                                    accum_out=mod[:, layer, who, col:col + 1], w=[landed, t_silu[who], t_junk[-2:-1]])
                            t_junk.append(t)
                            if col % 8 == 7:
                                t_mod[layer, part, who].set(t)
                            yield [t]
                return t

            mrow = {g: Bank() for g in range(2)}

            def by_columns(layer, i, raw, landed):
                g, first = i // 2, i % 2 == 0
                if first:
                    yield [k.banks, t_scol]
                    mrow[g].set(k.bank(), ())
                yield [mrow[g]]
                for kt in range(4):
                    t = k.mm(k.ps[mrow[g].bank][0:2, :], ccol[:, :, i % 2 * 4 + kt], raw[:, kt * 512:(kt + 1) * 512],
                             first and kt == 0, not first and kt == 3, w=[landed, t_scol], inc=kt == 3)
                if not first:
                    k.spawn(turned(g, t))
                return t

            def turned(g, t):
                yield [t, d_core]
                ta = k.a(A.copy, mrows[:, g], k.ps[mrow[g].bank][0:2, :], w=[t])
                k.close(mrow[g].bank, [ta])
                yield [ta, k.banks]
                b = k.bank()
                for j in range(4):
                    tt = k.tr(k.ps[b][:, 2 * j:2 * j + 2], mrows[:, g, j * P:(j + 1) * P], ident[0:2, 0:2], w=[ta, d_core],
                              inc=j == 3)
                yield [tt]
                tv = k.v(V.tensor_copy, mod[:, 0, :, 8 + 4 * g:12 + 4 * g],
                         k.ps[b][:, 0:8].rearrange("p (j w) -> p w j", w=2), w=[tt])
                k.close(b, [tv])
                t_mod["half", g].set(tv)

            for who in range(2):
                t_mod[0, 1, who].set([t_mod["half", 0], t_mod["half", 1]])
            st.on_mod = {"m": by_rows, "n": by_columns}

            def mod_part(layer, part, who):
                cols = mod[:, layer, who, part * 8:part * 8 + 8]
                return k.v(V.tensor_tensor, cols, cols, C("modb", layer * 48 + part * 8, 8), op=ALU.add,
                           w=[t_mod[layer, part, who], d_core])

            def scale_part(layer, part, who, norm):
                t = mod_part(layer, part, who)
                cols = mod[:, layer, who, part * 8:part * 8 + 8]
                return k.v(V.scalar_tensor_tensor, cols, cols, 1.0, C(norm, layer * 8, 8), ALU.add, ALU.mult,
                           w=[t])

            def norm_mod(layer, first, norm, tiles, xtok):
                n = stats[0]
                stats[0] += 1
                tA, tS = Evs(), Evs()
                h = {t: Halves([Parted(), Parted()]) for t in tiles}

                def columns():
                    for who in sorted({t // 2 for t in tiles}, reverse=True):
                        yield [t_mod[layer, first, who], t_mod[layer, first + 1, who]]
                        tA[who].set(scale_part(layer, first + 1, who, norm))
                        tS[who].set(mod_part(layer, first, who))

                def tile_(t):
                    cols = slice(t * P, (t + 1) * P)
                    xh, y = Hh_f[:, :, cols], Hl_f[:, :, cols]
                    x = xt[:, t].rearrange("p (j c) -> p j c", c=P)
                    r_ = lambda r: stat[:, n, r, t:t + 1]
                    for hf in range(2):
                        yield [xtok[t][hf], t_first if n == 0 and t not in tiles[:AHEAD] else ()]
                        ts = k.a(A.activation, sq[:, :], xt[:, t, hf * 512:(hf + 1) * 512], ACT.Square,
                                 accum_out=r_(2 * hf), w=[xtok[t][hf], t_sq])
                        t_sq[:] = [ts]
                        te = k.g(G.tensor_scalar, r_(1), r_(2 * hf), 1.0 / D, r_(1) if hf else EPS, ALU.mult, ALU.add,
                                 w=[ts, te if hf else ()])
                    tr = k.g(G.tensor_tensor, r_(3), r_(1), half[:, 0:1], op=ALU.pow, w=[te, t_half])
                    yield [tr]
                    who = t // 2
                    sc = mod[:, layer, who, (first + 1) * 8:(first + 2) * 8]
                    sh = mod[:, layer, who, first * 8:(first + 1) * 8]
                    wm = [tA[who], tS[who]]
                    hurry = n == 0 and t == tiles[1]
                    k.urgent += hurry
                    tx = k.v(V.tensor_scalar, xh, x, r_(3), None, ALU.mult, w=[tr])
                    yield [tx, d_core, k.banks, k.banks]
                    b0, b1 = k.bank(), k.bank()
                    t0 = flips(b0, [xh[:, j] for j in (0, 1, 4, 5)], [tx, d_core])
                    t1 = flips(b1, [xh[:, j] for j in (2, 3, 6, 7)], ())
                    yield [t0, wm]

                    def by_v(hf):
                        for j in range(2):
                            kt, at = hf * 4 + j, (hf * 2 + j) * P
                            tk = k.v(V.tensor_scalar, y[:, kt], k.ps[b0][:, at:at + P], sc[:, kt:kt + 1], sh[:, kt:kt + 1],
                                     ALU.mult, ALU.add, w=[t0, wm])
                        return tk

                    def by_a(hf):
                        for j in range(2):
                            kt, at = hf * 4 + 2 + j, (hf * 2 + j) * P
                            tk = k.a(A.activation, y[:, kt], k.ps[b1][:, at:at + P], ACT.Identity, bias=sh[:, kt:kt + 1],
                                     scale=sc[:, kt:kt + 1], w=[t1, wm])
                        return tk

                    tv = [by_v(0), by_v(1)]
                    k.close(b0, [tv[1]])
                    for hf in range(2):
                        ta = by_a(hf)
                        yield [tv[hf], ta]
                        rows_ = slice(hf * 4, hf * 4 + 4)
                        split(k, y[:, rows_], Hh[:, rows_, cols], Hl[:, rows_, cols], [tv[hf], ta], h[t][hf])
                    k.close(b1, [ta])
                    k.urgent -= hurry
                    if n == 0 and t == tiles[0]:
                        t_first.set(())

                for t in reversed(tiles):
                    k.spawn(tile_(t), first=True)
                k.spawn(columns(), first=True)
                return h

            gate_way = nc.dram_tensor("gate_way", [2, 2, 2, 8, P], F32).ap()

            def gate_tiles(layer, part, whos, old):
                toks = Evs()

                def rows_(who):
                    yield [t_mod[layer, part, who], old]
                    t = mod_part(layer, part, who)
                    row = grows[0:8, who, 0:P]
                    yield [t, k.banks]
                    b = k.bank()
                    tt = k.tr(k.ps[b][0:8, 0:P], mod[:, layer, who, part * 8:part * 8 + 8], ident, w=[t, d_core], inc=True)
                    yield [tt]
                    ta = k.a(A.copy, row, k.ps[b][0:8, 0:P], w=[tt, old])
                    k.close(b, [ta])
                    yield [ta]
                    way = gate_way[layer, part // 3, who]
                    there = k.dma("sp", way, row, w=[ta])
                    yield [there]
                    toks[who].set(k.dma("sp", grows[:, who], way.rearrange("(o j) c -> o (j c)", o=1).to_broadcast([P, D]),
                                        w=[there]))

                for who in whos:
                    k.spawn(rows_(who))
                return toks

            def add_gated():
                slots = Slots(2)
                evs = Evs()

                def add(tile, hf, b, t, tg):
                    cols = slice(hf * 512, (hf + 1) * 512)
                    yield [t, tg[tile // 2], slots]
                    i, old = slots.take()
                    tv = k.v(V.tensor_tensor, gtmp[:, i], k.ps[b][:, :], grows[:, tile // 2, cols], op=ALU.mult,
                             w=[t, tg[tile // 2], old])
                    k.close(b, [tv])
                    yield [tv]
                    tx = k.v(V.tensor_tensor, xt[:, tile, cols], xt[:, tile, cols], gtmp[:, i], op=ALU.add, w=[tv])
                    slots.give(i, [tx])
                    evs[tile, hf].set(tx)

                def start(tg):
                    return lambda tile, hf, b, t: k.spawn(add(tile, hf, b, t, tg))
                return start, {t: [evs[t, 0], evs[t, 1]] for t in range(4)}

            def rotated(x8, z8, s8, tn):
                tz = []
                for hf in range(2):
                    for r in range(2):
                        tz.append(k.v(V.tensor_tensor, z8[:, :, r, hf], x8[:, :, r, 1 - hf],
                                      s8[:, r, hf].unsqueeze(1).to_broadcast([P, 8, 16]), op=ALU.mult, w=tn))
                return tz

            quarters = lambda a: a.rearrange("p (h r y f) -> p h r y f", h=8, r=2, y=2)

            with Scope(k, fenced=True) as s:
                kT = s.sb("kT", [P, 4, 512])
                qT = s.sb("qT", [P, 2, 4, 512])
                vt = s.sb("vt", [P, 4, 512])
                yc = s.sb("yc", [P, 4, 512])
                t_h = norm_mod(0, 0, "n1", order, {t: [d_x[t], d_x[t]] for t in order})
                urgent([t_h[order[0]]])
                tab = s.sb("tab", [P, 2, 2, 2, 64])
                lamt = s.sb("lamt", [P, 8])
                sub = s.sb("sub", [P, P])
                prod = s.sb("prod", [P, 2, 64])
                raw, rot = (grows[:, i].rearrange("p (t c) -> p t c", t=2) for i in range(2))
                zz = gtmp
                sst = s.sb("sst", [P, 2, 3, 8])
                pr = s.sb("pr", [P, 3, 2, 512])
                sm = s.sb("sm", [P, 3, 8])
                ost = s.sb("ost", [P, 4, 16])
                ub = s.sb("ub", [P, 2, 258])
                cg = s.sb("cg", [P, 2, 256])
                E_ = Evs()

                def tables():
                    yield [d_b1, t_h[order[TAB]]]
                    for wi, gain in enumerate(("qg", "kg")):
                        g_ = B(gain).unsqueeze(1).to_broadcast([P, 2, 64])
                        t1 = [k.v(V.tensor_tensor, tab[:, wi, 0], B("ropec").rearrange("p (t d) -> p t d", t=2),
                                  g_, op=ALU.mult, w=[d_b1])]
                        half_ = lambda a: a.rearrange("p (r h f) -> p r h f", r=2, h=2)
                        for hf in range(2):
                            for tl in range(2):
                                t1.append(k.v(V.tensor_tensor, half_(tab[:, wi, 1, tl])[:, :, hf],
                                              half_(B("ropes", tl * 64, 64))[:, :, hf],
                                              half_(B(gain))[:, :, 1 - hf], op=ALU.mult, w=[d_b1]))
                        E_["tab", wi].set(t1)
                    for i in range(2):
                        tl = k.v(V.tensor_tensor_reduce, out=prod[:, i], in0=B(("lq1", "lq2")[i]),
                                 in1=B(("lk1", "lk2")[i]), scale=1.0, scalar=0.0, op0=ALU.mult, op1=ALU.add,
                                 accum_out=lamt[:, i:i + 1], w=[d_b1])
                    E_["sub"].set(k.v(V.tensor_scalar, sub[:, :], B("subg"), 1.0 - LAM_INIT, None, ALU.mult,
                                      w=[d_b1]))
                    yield [tl]
                    te = k.a(A.activation, lamt[:, 2:4], lamt[:, 0:2], ACT.Exp, w=[tl])
                    yield [te]
                    t1 = k.v(V.tensor_tensor, lamt[:, 4:5], lamt[:, 3:4], lamt[:, 2:3], op=ALU.subtract, w=[te])
                    E_["lam"].set(k.v(V.tensor_scalar, lamt[:, 5:6], lamt[:, 4:5], -LAM_INIT, None, ALU.add,
                                      w=[t1]))

                qs = Slots(2)
                e8 = lambda a: a.rearrange("p (h d) -> p h d", d=64)

                def head_norm(which, tile, b, t):
                    yield [t, qs]
                    i, old = qs.take()
                    ta = k.a(A.activation, zz[:, i], k.ps[b][:, :], ACT.Square, w=[t, old])
                    tr = k.a(A.copy, raw[:, i], k.ps[b][:, :], w=[old])
                    k.close(b, [tr])
                    yield [ta]
                    tv = k.v(V.tensor_reduce, sst[:, i, 0], e8(zz[:, i]), axis=AX, op=ALU.add, w=[ta, old])
                    tg = k.g(G.tensor_scalar, sst[:, i, 1], sst[:, i, 0], 1.0 / 64, EPS, ALU.mult, ALU.add, w=[tv])
                    tg = k.g(G.tensor_tensor, sst[:, i, 2], sst[:, i, 1], half[:, 0:8], op=ALU.pow, w=[tg])
                    yield [tg, tr]
                    r8, o8 = e8(raw[:, i]), e8(rot[:, i])
                    tn = k.v(V.tensor_tensor, r8, r8, sst[:, i, 2].unsqueeze(2).to_broadcast([P, 8, 64]),
                             op=ALU.mult, w=[tg, tr])
                    yield [tn, E_["tab", which]]
                    if tile < 2:
                        s8 = tab[:, which, 1, tile].rearrange("p (r y f) -> p r y f", r=2, y=2)
                        tz = rotated(quarters(raw[:, i]), quarters(zz[:, i]), s8, [tn, E_["tab", which], tv])
                        to = k.v(V.tensor_tensor, o8, r8, tab[:, which, 0, tile].unsqueeze(1).to_broadcast(
                            [P, 8, 64]), op=ALU.mult, w=[tn, old])
                        yield [to]
                        to = k.v(V.tensor_tensor, rot[:, i], rot[:, i], zz[:, i], op=ALU.add, w=[to, tz])
                    else:
                        to = k.v(V.tensor_tensor, o8, r8,
                                 B(("qg", "kg")[which]).unsqueeze(1).to_broadcast([P, 8, 64]), op=ALU.mult,
                                 w=[tn, old])
                    yield [to, k.banks]
                    b = k.bank()
                    tt = flips(b, [rot[:, i, h * P:(h + 1) * P] for h in range(4)], [to])
                    qs.give(i, [tt])
                    cols = slice(tile * P, (tile + 1) * P)
                    yield [tt, E_["z"]]
                    if which:
                        te = k.a(A.copy, kT[:, :, cols], bank4(b), w=[tt])
                    else:
                        t0 = k.a(A.copy, qT[0:64, 0, :, cols], bank4(b)[0:64], w=[tt, E_["z"]])
                        te = k.a(A.copy, qT[64:128, 1, :, cols], bank4(b)[64:128])
                    k.close(b, [te])
                    E_["qk"[which], tile].set(te if which else [t0, te])

                def evac_v(tile, b, t):
                    def f():
                        yield [t]
                        ta = k.a(A.copy, vt[:, tile], k.ps[b][:, :], w=[t])
                        k.close(b, [ta])
                        E_["v", tile].set(ta)
                    k.spawn(f())

                ps_ = Slots(3)

                def head(tile, h, ob, prev):
                    lat = tile < 2
                    nk, k0, kts = (512, 0, [0, 1, 2, 3]) if lat else (256, 256, [2, 3])
                    nb = nk // P
                    tk = [E_["k", j] for j in kts]
                    yield [E_["q", tile], tk, ps_, k.banks, k.banks, prev]
                    i, old = ps_.take()
                    bs = [k.bank(), k.bank()]
                    tp = []
                    for m in range(2):
                        tp.append(k.mm(k.ps[bs[m]][:, 0:nk], qT[:, m, h, tile * P:(tile + 1) * P],
                                       kT[:, h, k0:k0 + nk], True, True, w=[E_["q", tile], tk], inc=True))
                    tm = []
                    for m in range(2):
                        yield [tp[m]]
                        tm.append(k.v(V.tensor_reduce, sm[:, i, m:m + 1], k.ps[bs[m]][:, 0:nk], axis=AX,
                                      op=ALU.max, w=[tp[m], old]))
                    yield [tm[1]]
                    tv = k.v(V.tensor_scalar, sm[:, i, 2:4], sm[:, i, 0:2], -0.125, None, ALU.mult, w=[tm])
                    yield [tv, E_["lam"]]
                    sums = [ost[:, tile, 12 + h:13 + h], sm[:, i, 4:5]]
                    for m in range(2):
                        tp[m] = k.a(A.activation, pr[:, i, m, 0:nk], k.ps[bs[m]][:, 0:nk], ACT.Exp,
                                    bias=sm[:, i, 2 + m:3 + m], scale=0.125, accum_out=sums[m], w=[tv, old])
                        k.close(bs[m], [tp[m]])
                    yield [tp[1]]
                    tv = k.v(V.reciprocal, sm[:, i, 5:6], sm[:, i, 4:5], w=[tp])
                    yield [tv]
                    t2 = k.v(V.scalar_tensor_tensor, sm[:, i, 6:7], sm[:, i, 5:6], lamt[:, 5:6], sums[0], ALU.mult, ALU.mult,
                             w=[tv, tp, E_["lam"]])
                    yield [t2]
                    t1 = k.v(V.scalar_tensor_tensor, pr[:, i, 0, 0:nk], pr[:, i, 1, 0:nk], sm[:, i, 6:7],
                             pr[:, i, 0, 0:nk], ALU.mult, ALU.add, w=[tp, t2])
                    yield [t1, k.banks]
                    b = k.bank()
                    tt = flips(b, [pr[:, i, 0, j * P:(j + 1) * P] for j in range(nb)], [t1])
                    yield [tt]
                    tc = k.a(A.copy, pr[:, i, 1, 0:nk], k.ps[b][:, 0:nk], w=[tt])
                    k.close(b, [tc])
                    yield [tc, [E_["v", j] for j in kts], E_["ob", tile]]
                    ob = E_["ob", tile].bank
                    for j in range(nb):
                        to = k.mm(k.ps[ob][:, h * P:(h + 1) * P], pr[:, i, 1, j * P:(j + 1) * P],
                                  vt[:, kts[j], h * P:(h + 1) * P], j == 0, j == nb - 1,
                                  w=[tc, E_["v", kts[j]]], inc=j == nb - 1)
                    ps_.give(i, [to])
                    E_["o", tile, h].set(to)

                def attention(tile):
                    E_["ob", tile] = Bank()
                    yield [E_["q", tile], k.banks, E_["last", tile]]
                    ob = k.bank()
                    E_["ob", tile].set(ob, ())
                    for h in range(4):
                        k.spawn(head(tile, h, ob, ()))
                    to = [E_["o", tile, h] for h in range(4)]
                    yield [to]
                    E_["last", {2: 3, 3: 0, 0: 1, 1: None}[tile]].set(())
                    yield [ps_]
                    i, old = ps_.take()
                    osq, yr = pr[:, i, 0], pr[:, i, 1]
                    ta = k.a(A.activation, osq, k.ps[ob][:, :], ACT.Square, w=[to, old])
                    yield [ta]
                    tv = k.v(V.tensor_reduce, ost[:, tile, 0:4], osq.rearrange("p (h d) -> p h d", d=P), axis=AX,
                             op=ALU.add, w=[ta])
                    o_ = lambda n: ost[:, tile, 4 * n:4 * n + 4]
                    tr = k.v(V.scalar_tensor_tensor, o_(1), o_(3), EPS, o_(3), ALU.mult, ALU.mult, w=[to])
                    tv = k.v(V.scalar_tensor_tensor, o_(0), o_(0), 1.0 / P, o_(1), ALU.mult, ALU.add, w=[tv, tr])
                    tg = k.g(G.tensor_tensor, o_(2), o_(0), half[:, 0:4], op=ALU.pow, w=[tv])
                    yield [tg, E_["sub"]]
                    for h in range(4):
                        tv = k.v(V.scalar_tensor_tensor, yr[:, h * P:(h + 1) * P], k.ps[ob][:, h * P:(h + 1) * P],
                                 ost[:, tile, 8 + h:9 + h], sub[:, :], ALU.mult, ALU.mult,
                                 w=[tg, E_["sub"], old])
                    k.close(ob, [tv])
                    yield [tv, k.banks]
                    b = k.bank()
                    tt = flips(b, [yr[:, h * P:(h + 1) * P] for h in range(4)], [tv])
                    ps_.give(i, [tt])
                    yield [tt]
                    cols = slice(tile * P, (tile + 1) * P)
                    E_["y", tile].set(k.a(A.copy, qT[:, 0, :, cols], bank4(b), w=[tt]))
                    k.close(b, [E_["y", tile]])

                cs = Slots(1)
                t_u0 = k.zero(ub[:, :, :])
                seqs = lambda a: a.rearrange("p (s c) -> p s c", s=2)

                def conv_tile(i, bc, tc, bx, bb):
                    yield [tc, cs]
                    j, old = cs.take()
                    tc = k.a(A.copy, cg[:, :, :], seqs(k.ps[bc][:, :]), w=[tc, old])
                    k.close(bc, [tc])
                    yield [tc, bx]
                    tu = k.v(V.tensor_tensor, ub[:, :, 1:257], cg[:, :, :], seqs(k.ps[bx.bank][:, :]), op=ALU.mult,
                             w=[bx, tc, t_u0, old])
                    k.close(bx.bank, [tu])
                    yield [tu]
                    tv = k.v(V.tensor_scalar, cg[:, :, :], ub[:, :, 0:256], C("scw", i, 1), None, ALU.mult,
                             w=[tu, d_core])
                    for tap in (1, 2):
                        yield [tv]
                        tv = k.v(V.scalar_tensor_tensor, cg[:, :, :], ub[:, :, tap:tap + 256],
                                 C("scw", tap * 4 + i, 1), cg[:, :, :], ALU.mult, ALU.add, w=[tv])
                    yield [tv, bb]
                    tv = k.v(V.tensor_tensor, yc[:, i], cg[:, :, :].rearrange("p s c -> p (s c)"),
                             k.ps[bb.bank][:, :], op=ALU.mult, w=[tv, bb])
                    k.close(bb.bank, [tv])
                    cs.give(j, [tv])
                    E_["yc", i].set(tv)

                E_["z"].set(k.zero(qT[:, :]))
                k.spawn(tables())
                spawn_qk = lambda which: lambda tile, b, t: k.spawn(head_norm(which, tile, b, t))
                as_group(k, st, "ev_qkv", H, t_h, order, evac=spawn_qk(1))
                as_group(k, st, "ev_qkv", H, t_h, order, evac=spawn_qk(0))
                E_["last", 2].set(())
                for tile in order:
                    k.spawn(attention(tile))
                as_group(k, st, "ev_qkv", H, t_h, order, evac=evac_v)
                ht = list(t_h.values())
                for i in range(4):
                    bc, tc = ws_tile(k, st, "ev_conv", H, ht, 512)
                    bx, bb = Bank(), Bank()
                    k.spawn(conv_tile(i, bc, tc, bx, bb))
                    bx.set(*ws_tile(k, st, "ev_conv", H, ht, 512))
                    b, t_pe = ws_tile(k, st, "ev_conv", H, ht, 512)
                    bb.set(b, t_pe)

                def cat(src, rows_, need, ev):
                    for tile in order:
                        cols = slice(tile * P, (tile + 1) * P)
                        yield need(tile)
                        split(k, src[:, :, cols], Hh[:, rows_, cols], Hl[:, rows_, cols], [need(tile), t_pe], ev[tile])
                t_conv, t_att = Evs(Parted), Evs(Parted)
                k.spawn(cat(yc, slice(0, 4), lambda tile: [E_["yc", i] for i in range(4)], t_conv))
                k.spawn(cat(qT[:, 0], slice(4, 8), lambda tile: [E_["y", tile]], t_att))
                tg = gate_tiles(0, 2, (0, 1), [E_[n, t] for n in "qk" for t in order])
                start, t_x = add_gated()
                t_cat = {t: Halves([t_conv[t], t_att[t]]) for t in order}
                go = start(tg)
                evac = lambda hf: lambda tile, b, t: go(tile, hf, b, t)
                as_group(k, st, "ev_out", H, t_cat, order, evac=evac(0))
                settle()
                t_h = norm_mod(0, 3, "n2", order, t_x)
                as_group(k, st, "ev_out", H, t_cat, order, evac=evac(1))

            with Scope(k, fenced=True) as s:
                hid = s.sb("hid", [P, FT, 512])
                tmp = s.sb("ffn_tmp", [P, 3, 2, 512])
                slots = Slots(3)
                t_hid = Evs()
                seqs = lambda a: a.rearrange("p (s c) -> p s c", s=2)

                def act(f, first, second):
                    yield [first, slots]
                    i, old = slots.take()
                    ab, sg = tmp[:, i, 0], tmp[:, i, 1]
                    w_ = [C("fcw", tap * 22 + f, 1) for tap in range(3)]
                    b, t = first.bank, first.tok
                    ta = k.a(A.activation, ab, k.ps[b][:, :], ACT.Identity, bias=C("fcb", f, 1), scale=w_[1], w=[t, old])
                    yield [ta]
                    tv = k.v(V.scalar_tensor_tensor, seqs(ab)[:, :, 1:T], seqs(k.ps[b][:, :])[:, :, 0:T - 1], w_[0],
                             seqs(ab)[:, :, 1:T], ALU.mult, ALU.add, w=[ta])
                    yield [tv]
                    tv = k.v(V.scalar_tensor_tensor, seqs(ab)[:, :, 0:T - 1], seqs(k.ps[b][:, :])[:, :, 1:T], w_[2],
                             seqs(ab)[:, :, 0:T - 1], ALU.mult, ALU.add, w=[tv])
                    k.close(b, [tv])
                    yield [tv]
                    ts = k.a(A.activation, sg, ab, ACT.Silu, w=[tv])
                    yield [ts, second]
                    tv = k.v(V.tensor_tensor, hid[:, f], sg, k.ps[second.bank][:, :], op=ALU.mult, w=[ts, second])
                    k.close(second.bank, [tv])
                    slots.give(i, [tv])
                    t_hid[f].set(tv)

                firsts = up_first("up0", H, t_h, order, hid[:, 10:14])
                ht = [t_h[t] for t in order]
                for f in range(FT):
                    second = Bank()
                    k.spawn(act(f, firsts[f] if f < 4 else whole(*ws_tile(k, st, "up0", H, ht, 512)), second))
                    b, t_up = ws_tile(k, st, "up0", H, ht, 512)
                    second.set(b, t_up)
                old = [t_x[t] for t in order]
                tg = gate_tiles(0, 5, (0, 1), old)
                start, t_x = add_gated()
                go = start(tg)
                ring, parts = Slots(KT), Evs()

                def halves():
                    for n in range(2 * FT):
                        yield [t_hid[n % FT], ring]
                        q, old = ring.take()
                        parts[n].set(split(k, hid[:, n % FT], Hh[:, q], Hl[:, q], [t_hid[n % FT], t_up, old]))
                        parts[n].at = q

                k.spawn(halves())
                us = {}

                def part(hf, kt, tile, inc):
                    n = hf * FT + kt
                    if kt % 2 == 0 and tile == order[0]:
                        us[hf, kt // 2] = st.take("down0")
                    wh, wl, wt = st.parts(us[hf, kt // 2])
                    k.until(parts[n])
                    q, c, xs = parts[n].at, slice(kt % 2 * 512, (kt % 2 + 1) * 512), slice(tile * P, (tile + 1) * P)
                    t = as3(k, k.ps[bs[tile]][:, :], Hh[:, q, xs], Hl[:, q, xs], wh[:, c], wl[:, c], kt == 0, kt == FT - 1,
                            w=[wt, parts[n]], inc=inc or kt == FT - 1)
                    if kt == FT - 1:
                        go(tile, hf, bs[tile], t)
                    if tile == order[-1]:
                        ring.give(q, [t])
                        if kt % 2:
                            st.free(us[hf, kt // 2], t)
                    return t

                for hf in range(2):
                    bs = {t: k.bank() for t in order}
                    held = KT if hf else 0
                    for kt in range(FT - held):
                        for tile in order:
                            part(hf, kt, tile, tile == order[-1])
                        k.poll()
                    for tile in order[:4 if held else 0]:
                        for kt in range(FT - held, FT):
                            if tile == order[0] and kt == FT - 1:
                                k.until([parts[2 * FT - 1]])
                                settled = settle()
                                t_h = norm_mod(1, 0, "n1", order, t_x)
                                urgent([t_h[t] for t in order])
                            part(hf, kt, tile, tile == order[-1])
                            k.poll()

            t_old = t_x
            with Scope(k, fenced=True) as s:
                LO, nl1 = offsets(L1C)
                l1 = s.sb("l1", [P, nl1])
                d_l1 = k.dma("sp", l1[:, :], l1_in, w=settled)
                cat = s.sb("cat", [P, KT, T])
                def L(name, i=0, n=None):
                    at, size = LO[name]
                    return l1[:, at + i:at + (i + n if n else size)]

                lg = s.sb("lg", [P, 8])
                dec = s.sb("dec", [P, 4, 2, 4])
                decay = s.sb("decay", [P, 4, 512])
                two = lambda a: a.rearrange("p (t u) c -> p t (u c)", t=2)
                rawq = at = two(cat[:, 0:4])
                zq = two(cat[:, 4:8])
                gate = xt[:, 2].rearrange("p (t c) -> p t c", t=2)
                pv = xt[:, 3].rearrange("p (t c) -> p t c", t=2)
                qk = grows[:, 0].rearrange("p (t c) -> p t c", t=2)
                kw = grows[:, 1].rearrange("p (t h d) -> p t h d", t=2, h=4)
                kc = gtmp[:, 0].rearrange("p (t c) -> p t c", t=2)
                vl = s.sb("vl", [P, 4, 512])
                qTp = s.sb("qTp", [P, 4, T])
                kTp = s.sb("kTp", [P, 2, T])
                qd = s.sb("qd", [P, 2, 4, P])
                qdT = s.sb("qdT", [P, 4, T])
                S = s.sb("S", [P, 4, P])
                yp = s.sb("yp", [P, 4, T])
                ost = s.sb("ost", [P, 2, 12])
                yr = qd.rearrange("p t h c -> p t (h c)")
                dtmp = yp[:, 0:2].rearrange("p t c -> p (t c)")
                E_ = Evs()
                h4 = lambda a: a.rearrange("p (h d) -> p h d", d=64)
                all_h = [t_h[t] for t in order]

                def decays():
                    yield [d_b1, all_h]
                    t1 = k.a(A.activation, lg[:, 0:4], B("decf"), ACT.Exp, w=[d_b1])
                    t2 = k.a(A.activation, lg[:, 4:8], B("decb"), ACT.Exp, w=[d_b1])
                    yield [t2]
                    tl = k.v(V.tensor_scalar, lg[:, :], lg[:, :], -1.0, None, ALU.mult, w=[t1, t2])
                    yield [tl]
                    tt = []
                    for i in range(4):
                        tt.append(k.v(V.tensor_tensor, dec[:, i],
                                      B("ramps", 2 * i, 2).unsqueeze(2).to_broadcast([P, 2, 4]),
                                      lg[:, (i % 2) * 4:(i % 2) * 4 + 4].unsqueeze(1).to_broadcast([P, 2, 4]),
                                      op=ALU.mult, w=[tl]))
                    yield [tt]
                    ta = k.a(A.activation, dec[:, :], dec[:, :], ACT.Exp, w=[tt])
                    yield [ta]
                    E_["dec8"].set(k.v(V.tensor_scalar, dec[:, 0:2], dec[:, 0:2], 0.125, None, ALU.mult, w=[ta]))
                    E_["dec"].set(ta)
                    t2 = None
                    for h in range(4):
                        yield [d_l1, t2]
                        t1 = k.v(V.tensor_scalar, dtmp, L("dist_f"), lg[:, h:h + 1], None, ALU.mult,
                                 w=[tl, d_l1, t2])
                        yield [t1]
                        t2 = k.v(V.scalar_tensor_tensor, decay[:, h], L("dist_b"), lg[:, 4 + h:5 + h], dtmp,
                                 ALU.mult, ALU.add, w=[t1, all_h])
                        yield [t2]
                        ta = k.a(A.activation, decay[:, h], decay[:, h], ACT.Exp, w=[t2])
                        yield [ta]
                        E_["decay", h].set(k.v(V.tensor_tensor, decay[:, h], decay[:, h], L("two"), op=ALU.mult,
                                               w=[ta]))
                    E_["dtmp"].set(t2)

                old = [t_old[t] for t in order]

                def evac_qk(tile, b, t):
                    yield [t, old]
                    if tile >= 2:
                        ta = k.a(A.copy, kc[:, tile - 2], k.ps[b][:, 0:256], w=[t, old])
                        k.close(b, [ta])
                        yield [ta, E_["dec"]]
                        tw = []
                        for i in range(2):
                            tw.append(k.v(V.tensor_tensor, kw[:, tile - 2, :, i * 64:(i + 1) * 64],
                                          h4(kc[:, tile - 2]),
                                          dec[:, 2 + i, tile - 2].unsqueeze(2).to_broadcast([P, 4, 64]),
                                          op=ALU.mult, w=[ta, E_["dec"]]))
                        E_["kw", tile - 2].set(tw)
                        return
                    tr = k.a(A.copy, rawq[:, tile], k.ps[b][:, :], w=[t])
                    k.close(b, [tr])
                    yield [tr]
                    s8 = B("ropes", tile * 64, 64).rearrange("p (r y f) -> p r y f", r=2, y=2)
                    tz = rotated(quarters(rawq[:, tile]), quarters(zq[:, tile]), s8, [tr])
                    to = k.v(V.tensor_tensor, qk[:, tile].rearrange("p (h d) -> p h d", d=64),
                             rawq[:, tile].rearrange("p (h d) -> p h d", d=64),
                             B("ropec", tile * 64, 64).unsqueeze(1).to_broadcast([P, 8, 64]), op=ALU.mult, w=[tr, old])
                    yield [to]
                    to = k.v(V.tensor_tensor, qk[:, tile], qk[:, tile], zq[:, tile], op=ALU.add, w=[to, tz])
                    E_["qk", tile].set(to)
                    yield [to, E_["dec8"], k.banks]
                    b = k.bank()
                    tt = flips(b, [qk[:, tile, j * P:(j + 1) * P] for j in range(4)], [to])
                    td = []
                    for i in range(2):
                        td.append(k.v(V.tensor_tensor, qd[:, tile, :, i * 64:(i + 1) * 64], h4(qk[:, tile, 0:256]),
                                      dec[:, i, tile].unsqueeze(2).to_broadcast([P, 4, 64]), op=ALU.mult,
                                      w=[to, E_["dec8"]]))
                    yield [tt, E_["z"]]
                    c = slice(tile * P, (tile + 1) * P)
                    k.a(A.copy, qTp[0:64, 0:4:2, c], bank4(b)[0:64, 0:2], w=[tt, E_["z"]])
                    k.a(A.copy, qTp[64:128, 1:4:2, c], bank4(b)[64:128, 0:2])
                    ta = k.a(A.copy, kTp[:, :, c], bank4(b)[:, 2:4])
                    k.close(b, [ta])
                    E_["T", tile].set(ta)
                    yield [td, k.banks]
                    b = k.bank()
                    tt = flips(b, [qd[:, tile, h] for h in range(4)], [td])
                    yield [tt]
                    ta = k.a(A.copy, qdT[:, :, c], bank4(b), w=[tt])
                    k.close(b, [ta])
                    E_["qdT", tile].set(ta)

                def evac_v(tile, b, t):
                    yield [t]
                    ta = k.a(A.copy, vl[:, tile], k.ps[b][:, :], w=[t])
                    k.close(b, [ta])
                    E_["v", tile].set(ta)

                def evac_g(tile, b, t):
                    yield [t, E_["decay", 3]]
                    ta = k.a(A.activation, gate[:, tile], k.ps[b][:, :], ACT.Silu, w=[t])
                    k.close(b, [ta])
                    yield [ta]
                    g4 = gate[:, tile].rearrange("p (h d) -> p h d", d=P)
                    E_["g", tile].set(k.v(V.tensor_tensor, g4, g4, B("rgn").unsqueeze(1).to_broadcast([P, 4, P]),
                                          op=ALU.mult, w=[ta]))

                def evac_pv(tile, b, t):
                    yield [t]
                    ta = k.a(A.copy, pv[:, tile], k.ps[b][:, :], w=[t])
                    k.close(b, [ta])
                    E_["pv", tile].set(ta)

                def states():
                    need = [E_["kw", 0], E_["kw", 1], E_["v", 2], E_["v", 3]]
                    yield [need, k.banks]
                    b = k.bank()
                    for h in range(4):
                        for j in range(2):
                            tt = k.mm(k.ps[b][:, h * P:(h + 1) * P], kw[:, j, h], vl[:, 2 + j, h * P:(h + 1) * P],
                                      j == 0, j == 1, w=need, inc=h == 3 and j == 1)
                    yield [tt]
                    ta = k.a(A.copy, S[:, :], bank4(b), w=[tt])
                    k.close(b, [ta])
                    E_["S"].set(ta)

                atS = Slots(2)

                def scores(h, obs):
                    yield [E_["T", 0], E_["T", 1], E_["decay", h], atS, k.banks]
                    i, old = atS.take()
                    b = k.bank()
                    for j in range(2):
                        tt = k.mm(k.ps[b][:, j * T:(j + 1) * T], kTp[:, h // 2, j * P:(j + 1) * P], qTp[:, h], True,
                                  True, w=[E_["T", 0], E_["T", 1]], inc=j == 1)
                    yield [tt]
                    ta = k.v(V.tensor_tensor, at[:, i], k.ps[b][:, :], decay[:, h], op=ALU.mult,
                             w=[tt, E_["decay", h], old])
                    k.close(b, [ta])
                    for tile in range(2):
                        need = [ta, E_["v", 0], E_["v", 1], E_["S"], E_["qdT", tile], obs[tile]]
                        yield need
                        o = k.ps[obs[tile].bank][:, h * P:(h + 1) * P]
                        for j in range(2):
                            k.mm(o, at[:, i, j * T + tile * P:j * T + (tile + 1) * P], vl[:, j, h * P:(h + 1) * P],
                                 j == 0, False, w=need)
                        to = k.mm(o, qdT[:, h, tile * P:(tile + 1) * P], S[:, h], False, True, inc=True)
                        E_["o", tile, h].set(to)
                    atS.give(i, [to])

                def outputs(tile, obs):
                    yield [k.banks]
                    ob = k.bank()
                    obs[tile].set(ob, ())
                    to = [E_["o", tile, h] for h in range(4)]
                    yield [to, E_["qdT", 0], E_["qdT", 1]]
                    ta = k.a(A.activation, yr[:, tile], k.ps[ob][:, :], ACT.Square, w=[to, E_["qdT", 0], E_["qdT", 1]])
                    yield [ta]
                    tv = k.v(V.tensor_reduce, ost[:, tile, 0:4], yr[:, tile].rearrange("p (h d) -> p h d", d=P),
                             axis=AX, op=ALU.add, w=[ta])
                    tg = k.g(G.tensor_scalar, ost[:, tile, 4:8], ost[:, tile, 0:4], 1.0 / P, EPS, ALU.mult, ALU.add,
                             w=[tv])
                    tg = k.g(G.tensor_tensor, ost[:, tile, 8:12], ost[:, tile, 4:8], half[:, 0:4], op=ALU.pow,
                             w=[tg])
                    yield [tg, E_["g", tile]]
                    for h in range(4):
                        c = slice(h * P, (h + 1) * P)
                        ty = k.v(V.scalar_tensor_tensor, yr[:, tile, c], k.ps[ob][:, c], ost[:, tile, 8 + h:9 + h],
                                 gate[:, tile, c], ALU.mult, ALU.mult, w=[tg, E_["g", tile], tv])
                    k.close(ob, [ty])
                    yield [ty, k.banks]
                    b = k.bank()
                    tt = flips(b, [yr[:, tile, h * P:(h + 1) * P] for h in range(4)], [ty])
                    yield [tt]
                    ta = k.a(A.copy, cat[:, 4:8, tile * P:(tile + 1) * P], bank4(b), w=[tt])
                    k.close(b, [ta])
                    E_["y", tile].set(ta)

                def pooling(g):
                    yield [E_["pv", 0], E_["pv", 1], E_["dtmp"], d_l1, k.banks]
                    b = k.bank()
                    for r in range(2):
                        for j in range(2):
                            tt = k.mm(k.ps[b][:, r * T:(r + 1) * T], pv[:, j, (g + r) * P:(g + r + 1) * P],
                                      L("band", ((g + r) * 2 + j) * T, T), j == 0, j == 1,
                                      w=[E_["pv", 0], E_["pv", 1], d_l1], inc=j == 1 and r == 1)
                    yield [tt]
                    ta = k.a(A.copy, yp[:, g:g + 2], bank4(b, T), w=[tt, E_["dtmp"]])
                    k.close(b, [ta])
                    yield [ta, k.banks]
                    b = k.bank()
                    for r in range(2):
                        tt = k.mm(k.ps[b][:, r * T:(r + 1) * T], L("poolw", (g + r) * P, P), yp[:, g + r], True, True,
                                  w=[ta], inc=r == 1)
                    yield [tt, [E_["o", i, h] for i in range(2) for h in range(4)]]
                    for r in range(2):
                        tv = k.v(V.tensor_scalar, cat[:, g + r], k.ps[b][:, r * T:(r + 1) * T], C("psc", g + r, 1),
                                 None, ALU.mult, w=[tt, [E_["o", i, h] for i in range(2) for h in range(4)]])
                    k.close(b, [tv])
                    E_["p", g].set(tv)

                k.spawn(decays())
                E_["z"].set([k.zero(qTp[64:128, 0:4:2]), k.zero(qTp[0:64, 1:4:2])])
                ctx_cols = {0: (0, 512), 1: (0, 512), 2: (256, 512), 3: (256, 512)}
                as_group(k, st, "od_in", H, t_h, order, cols=ctx_cols, evac=lambda *a: k.spawn(evac_qk(*a)))
                k.spawn(states())
                as_group(k, st, "od_in", H, t_h, order, evac=lambda *a: k.spawn(evac_v(*a)))
                obs = [Bank(), Bank()]
                for tile in range(2):
                    k.spawn(outputs(tile, obs))
                for h in range(4):
                    k.spawn(scores(h, obs))
                as_group(k, st, "od_in", H, t_h, [0, 1], evac=lambda *a: k.spawn(evac_g(*a)))
                as_group(k, st, "od_in", H, t_h, [0, 1], evac=lambda *a: k.spawn(evac_pv(*a)))
                t_pe = k.last()[0]
                for g in (0, 2):
                    k.spawn(pooling(g))
                t_cat = Evs()

                def join(i, need):
                    yield need
                    t_cat[i].set(split(k, cat[:, 2 * i:2 * i + 2], Hh[:, 2 * i:2 * i + 2, 0:T],
                                       Hl[:, 2 * i:2 * i + 2, 0:T], [need, t_pe]))
                ys = [E_["y", 0], E_["y", 1]]
                for i, need in enumerate(([E_["p", 0]], [E_["p", 2]], ys, ys)):
                    k.spawn(join(i, need))
                tg = gate_tiles(1, 2, (0,), [E_["S"], [E_[n, t] for n in ("T", "qdT") for t in range(2)]])
                start, t_x = add_gated()
                after = []

                def ready():
                    settle()
                    after.append(norm_mod(1, 3, "n2", [0, 1], t_x))
                    urgent([after[0][t] for t in range(2)])

                def x_H(kt, tile):
                    c = slice(tile * P, (tile + 1) * P)
                    return Hh[:, kt, c], Hl[:, kt, c]
                down(k, st, "od_out", KT, x_H, lambda kt, tile: t_cat[kt // 2], start(tg), ready)
                t_h, = after

            with Scope(k, fenced=True) as s:
                hh, hh_f = s.both("hh", [P, FT, T])
                hl = s.sb("hl", [P, FT, T], F32R)
                t_hid = ffn_up(s, "up1", H, t_h, hh, hl, hh_f, 1)
                tg = gate_tiles(1, 5, (0,), [t_x[t] for t in range(2)])
                start, t_x = add_gated()
                first, d_c2 = Evs(Parted), Ev()
                c2 = nc.alloc_sbuf_tensor_at("c2", [P, offsets(C2)[1]], F32, offset=at_s1)

                def ready():
                    d_c2.set(k.dma("sp", c2[:, :], c2_in, w=settle()))
                    for tile in range(2):
                        for hf in range(2):
                            k.spawn(to_H(xt, tile, hf, [t_x[tile][hf]], first), first=True)
                    urgent([first[tile, hf] for tile in range(2) for hf in range(2)])

                down(k, st, "down1", FT, lambda kt, tile: (hh[:, kt, tile * P:(tile + 1) * P],
                                                           hl[:, kt, tile * P:(tile + 1) * P]),
                     lambda kt, tile: t_hid[kt], start(tg), ready)

        with Scope(k) as s2:
            QO, nc2 = offsets(C2)
            s2.sb("c2_place", [P, nc2])
            lb = s2.sb("lb", [P, 3, 8])
            lbm = s2.sb("lbm", [P, 12, 8])
            cst = s2.sb("cst", [P, 2, 16])
            stat = s2.sb("lnstat", [P, 2, 16])
            minus = s2.sb("minus", [P, P], F32R)
            t_minus = k.a(A.activation, minus[:, :], ident, ACT.Copy, scale=-1.0, w=[d_core])
            lng, lnb = xt[:, 2], xt[:, 3]
            HF = [slice(0, 512), slice(512, 1024)]

            def Q(name, i=0, n=None):
                at, size = QO[name]
                return c2[:, at + i:at + (i + n if n else size)]

            def pair_mask(n, y):
                return Q("halves", 2 * (n - 1) + y * n, n)

            lt_way = nc.dram_tensor("lt_way", [2, 8 * 129 * P], F32).ap()
            xy_way = nc.dram_tensor("xy_way", [2, 2, 8 * 129 * P], F32).ap()
            zeroed = [Ev(), Ev()]
            t_cst = [k.v(V.memset, cst[:, 0], 1.0), k.v(V.memset, cst[:, 1], 0.5)]
            one = cst[:, 0, 0:1]

            def spawn(f):
                return lambda *a: k.spawn(f(*a))

            ln_n = [0]
            ln_old = [k.last()]
            d_ln = {}

            def load_ln():
                n = ln_n[0]
                ln_n[0] += 1
                ev = d_ln[n] = Ev()

                def go(old):
                    yield [old]
                    ev.set([k.dma("sp", dst, ln_in[n, r:r + 1].to_broadcast([P, D]), w=old)
                            for r, dst in enumerate((lng, lnb))])
                k.spawn(go(ln_old[0]))
                return ev

            def down_ln(key, nk, x, xtok, d_ln, x_old, final=None, by=None):
                ht, done = Evs(Parted), Evs()
                banks = {(tile, hf): Bank() for tile in range(2) for hf in range(2)}

                def norm(tile):
                    xr = [xt[:, tile, c] for c in HF]
                    tb = []
                    for hf in range(2):
                        bk = banks[tile, hf]
                        yield [bk]
                        tx = k.v(V.scalar_tensor_tensor, xr[hf], xr[hf], DN_ALPHA, k.ps[bk.bank][:, :], ALU.mult, ALU.add,
                                 w=[bk, x_old[tile]])
                        k.close(bk.bank, [tx])
                        yield [tx]
                        tb.append(k.v(V.bn_stats, stat[:, tile, hf * 6:hf * 6 + 6], xr[hf], w=[tx]))
                    yield [tb]
                    ta = k.v(V.bn_aggr, stat[:, tile, 12:14], stat[:, tile, 0:12], w=tb)
                    yield [ta]
                    te = k.v(V.tensor_scalar, stat[:, tile, 14:15], stat[:, tile, 13:14], LN_EPS, None, ALU.add, w=[ta])
                    tg = k.g(G.tensor_tensor, stat[:, tile, 15:16], stat[:, tile, 14:15], half[:, 0:1], op=ALU.pow,
                             w=[te])
                    yield [d_ln]
                    t2 = []
                    for hf in range(2):
                        t1 = k.v(V.scalar_tensor_tensor, xr[hf], xr[hf], stat[:, tile, 12:13], lng[:, HF[hf]], ALU.subtract,
                                 ALU.mult, w=[ta, d_ln])
                        yield [tg, t1]
                        t2.append(k.v(V.scalar_tensor_tensor, xr[hf], xr[hf], stat[:, tile, 15:16], lnb[:, HF[hf]],
                                      ALU.mult, ALU.add, w=[t1, tg, d_ln]))
                        if final is None:
                            k.spawn(to_H(xt, tile, hf, t2[hf], ht, tile in LN_PE, by if tile else None), first=True)
                        else:
                            final.append(k.dma("sp", out[tile, :, HF[hf]], xr[hf], w=t2[hf]))
                    done[tile].set(t2)

                def ready():
                    settle()
                    for tile in range(2):
                        k.spawn(norm(tile))
                    urgent([done[0], done[1]] if final is not None else [ht[tile, hf] for tile in range(2) for hf in range(2)])

                down(k, st, key, nk, x, xtok, lambda tile, hf, b, t: banks[tile, hf].set(b, t), ready)
                ln_old[0] = [done[0], done[1]]
                if final is not None:
                    k.until([done[0], done[1]])
                    k.wait("sp", final)
                return by_tile(ht), [done[0], done[1]]

            def x_H(kt, tile):
                c = slice(tile * P, (tile + 1) * P)
                return Hh[:, kt, c], Hl[:, kt, c]

            def norm_out(bk, tile, hf, nh, extra, gate, ost, sq, t_gate, old, used, ev, proj, by=None):
                dv = 512 // nh
                yield [bk, old]
                ps = k.ps[bk.bank]
                for h in range(nh):
                    c = slice(h * dv, (h + 1) * dv)
                    tv = k.a(A.activation, sq[:, c], ps[:, c], ACT.Square, accum_out=ost[:, 0, h:h + 1], w=[bk, old])
                used.set(tv)
                yield [tv, extra[1]]
                if extra[0] is None:
                    tv = k.v(V.tensor_scalar, ost[:, 1, 0:nh], ost[:, 0, 0:nh], 1.0 / dv, P * EPS, ALU.mult, ALU.add,
                             w=[tv])
                else:
                    tv = k.v(V.scalar_tensor_tensor, ost[:, 1, 0:nh], ost[:, 0, 0:nh], 1.0 / dv, extra[0], ALU.mult,
                             ALU.add, w=[tv, extra[1]])
                tg = k.g(G.tensor_tensor, ost[:, 2, 0:nh], ost[:, 1, 0:nh], half[:, 0:nh], op=ALU.pow, w=[tv])
                yield [tg, t_gate]
                for h in range(nh):
                    gh = gate[:, tile, hf * 512 + h * dv:hf * 512 + (h + 1) * dv]
                    ty = k.v(V.scalar_tensor_tensor, gh, ps[:, h * dv:(h + 1) * dv], ost[:, 2, h:h + 1], gh,
                             ALU.mult, ALU.mult, w=[tg, t_gate])
                k.close(bk.bank, [ty])
                k.spawn(to_H(gate, tile, hf, [ty, proj], ev, OUT_PE, by if tile else None))

            def gates_(s, gate, norm, dv, after):
                ev = Evs()

                def f(hf):
                    def g(tile, b, t):
                        g_ = gate[:, tile, HF[hf]]
                        yield [t]
                        tr = k.a(A.copy, g_, k.ps[b][:, :], w=[t])
                        k.close(b, [tr])
                        yield [tr, after]
                        ta = k.a(A.activation, g_, g_, ACT.Silu, w=[tr])
                        yield [ta]
                        g4 = g_.rearrange("p (h d) -> p h d", d=dv)
                        ev[tile, hf].set(k.v(V.tensor_tensor, g4, g4, norm.unsqueeze(1).to_broadcast([P, 512 // dv, dv]),
                                             op=ALU.mult, w=[ta]))
                    return spawn(g)
                return f, ev

            def small_w(s, name, i):
                wh = s.sb("wsh", [P, KT * 16], F32R)
                wl = s.sb("wsl", [P, KT * 16], F32R)
                return wh, wl, split(k, Q(name, i * KT * 16, KT * 16), wh[:, :], wl[:, :], [d_c2])

            def small_proj(w, htok):
                wh, wl, ts = w
                k.until(htok)
                b = k.bank()
                for kt in range(KT):
                    c = slice(kt * 16, (kt + 1) * 16)
                    t = ws3(k, k.ps[b][0:16, 0:T], wh[:, c], wl[:, c], Hh[:, kt, 0:T], Hl[:, kt, 0:T], kt == 0, kt == KT - 1,
                            w=[ts, htok], inc=kt == KT - 1)
                return b, t

            t_lb = Ev()

            def bounds():
                m = lbm
                lo_ = lambda i: Q("lbl", i * 8, 8)
                yield [d_c2]
                t1 = k.v(V.tensor_tensor, m[:, 0], lo_(0), lo_(2), op=ALU.max, w=[d_c2])
                t1 = k.v(V.tensor_tensor, m[:, 0], m[:, 0], lo_(3), op=ALU.max, w=[t1])
                t2 = k.v(V.tensor_tensor, m[:, 1], m[:, 0], lo_(1), op=ALU.max, w=[t1])
                ts = []
                for n, (j, mx) in enumerate(((0, 0), (2, 0), (3, 0), (1, 1))):
                    ts.append(k.v(V.tensor_tensor, m[:, 2 + n], lo_(j), m[:, mx], op=ALU.subtract, w=[t2]))
                ts.append(k.v(V.tensor_tensor, m[:, 6], m[:, 0], m[:, 1], op=ALU.subtract, w=[t2]))
                ta = k.a(A.activation, m[:, 7:12], m[:, 2:7], ACT.Exp, w=[ts])
                yield [ta]
                t1 = k.v(V.tensor_tensor, m[:, 7], m[:, 7], m[:, 8], op=ALU.add, w=[ta])
                t1 = k.v(V.tensor_tensor, m[:, 7], m[:, 7], m[:, 9], op=ALU.add, w=[t1])
                t2 = k.v(V.tensor_tensor, m[:, 8], m[:, 7], m[:, 11], op=ALU.mult, w=[t1])
                t2 = k.v(V.tensor_tensor, m[:, 8], m[:, 8], m[:, 10], op=ALU.add, w=[t2])
                ta = k.a(A.activation, m[:, 9:11], m[:, 7:9], ACT.Ln, w=[t2, ta])
                yield [ta]
                t1 = k.v(V.tensor_tensor, lb[:, 0], m[:, 5], m[:, 10], op=ALU.subtract, w=[ta])
                t2 = k.v(V.tensor_tensor, lb[:, 1], m[:, 6], m[:, 9], op=ALU.add, w=[ta])
                t2 = k.v(V.tensor_tensor, lb[:, 1], lb[:, 1], m[:, 10], op=ALU.subtract, w=[t2])
                t_lb.set(k.v(V.tensor_tensor, lb[:, 2], lb[:, 1], lb[:, 0], op=ALU.subtract, w=[t1, t2]))

            def whole_way(a):
                return a.rearrange("(m e) -> m e", m=8)[:, 0:P * P].rearrange("m (r t) -> r m t", t=P)

            def diagonal_way(a):
                return a.rearrange("(b e) -> b e", b=64)[:, 0:16 * P].rearrange("b (i t) -> b i t", t=P)[:, :, 0:16]

            def gdn(j, t_h, d_ln, x_old):
                with Scope(k, fenced=True) as s:
                    kf = Hh_f[:, :, T:2 * T]
                    qf = Hl_f[:, :, T:2 * T]
                    gate = s.sb("gate", [P, 2, D])
                    R = grows[:, :, :].rearrange("p c (h d) -> p c h d", h=8)
                    DT = s.sb("DT", [P, 2, 8, P])
                    LT = s.sb("LT", [P, 2, 8, P])
                    X, Y = (s.sb(n, [P, 2, 8, P]) for n in "XY")
                    Pm = s.sb("Pm", [P, 4, 512])
                    S1 = s.sb("S1", [P, 8, P])
                    kd = s.sb("kd", [P, 8, P])
                    EG = gtmp[:, :, :].rearrange("p c (h d) -> p (c h) d", d=P)
                    sm = s.sb("gsm", [P, 11, 2, 8])
                    ba = s.sb("ba", [P, T])
                    jk = s.sb("jk", [P, 2, P])
                    ost = s.sb("gost", [P, 4, 3, 4])
                    vq = [a[:, :, :].rearrange("p a c -> p (a c)").rearrange("p (h t) -> p h t", t=T) for a in (S1, kd)]
                    gu = Pm[:, :, :].rearrange("p (c q) (h t) -> p c (q h) t", c=2, h=4)
                    dg = s.sb("dg", [P, 272 + 272 + 64 + 512])
                    tap3 = s.sb("taps", [P, 1, 3, T])
                    taps = Slots(1)
                    E_ = Evs()
                    htok = t_h
                    CQ = [(c, q) for q in range(2) for c in range(2)]

                    def quad(x, c, q):
                        return x[:, c, q * 4:q * 4 + 4]

                    def four(b, lhsT, rhs, w):
                        for h in range(4):
                            t = k.mm(k.ps[b][:, h * P:(h + 1) * P], lhsT(h), rhs(h), True, True, w=w, inc=h == 3)
                        return t

                    def scaled(dst, b, by, w):
                        for h in range(4):
                            t = k.a(A.activation, dst[:, h], k.ps[b][:, h * P:(h + 1) * P], ACT.Copy, scale=by[:, h:h + 1], w=w)
                        return t

                    def decays(b, t):
                        yield [t]
                        t_ba = k.a(A.copy, ba[0:16, :], k.ps[b][0:16, 0:T], w=[t])
                        k.close(b, [t_ba])
                        yield [t_ba, k.banks]
                        b = k.bank()
                        for c in range(2):
                            tt = k.tr(k.ps[b][:, c * 16:(c + 1) * 16], ba[0:16, c * P:(c + 1) * P], ident[0:16, 0:16],
                                      w=[t_ba], inc=c == 1)
                        yield [tt]
                        p4 = k.ps[b][:, 0:32].rearrange("p (c w h) -> p c w h", c=2, w=2)
                        t1 = k.v(V.tensor_copy, sm[:, 0], p4[:, :, 0], w=[tt])
                        t2 = k.v(V.tensor_tensor, sm[:, 1], p4[:, :, 1],
                                 Q("dtb", j * 8, 8).unsqueeze(1).to_broadcast([P, 2, 8]), op=ALU.add, w=[tt, d_c2])
                        k.close(b, [t2])
                        yield [t1, t2]
                        ta = k.a(A.activation, sm[:, 2:4], sm[:, 0:2], ACT.Abs, w=[t1, t2])
                        ta = k.a(A.activation, sm[:, 2:4], sm[:, 2:4], ACT.Exp, scale=-1.0, w=[ta])
                        t1 = k.v(V.tensor_scalar, sm[:, 4], sm[:, 0], 0.0, None, ALU.min, w=[t1])
                        td = k.a(A.activation, sm[:, 6], sm[:, 3], ACT.Ln, bias=one, w=[ta, t_cst])
                        tb = k.a(A.activation, sm[:, 4], sm[:, 4], ACT.Exp, w=[t1])
                        tc = k.a(A.activation, sm[:, 5, 0], Q("alog", j * 8, 8), ACT.Exp)
                        yield [ta, td]
                        t2 = k.v(V.scalar_tensor_tensor, sm[:, 1], sm[:, 1], 0.0, sm[:, 6], ALU.max, ALU.add, w=[td])
                        t1 = k.v(V.tensor_scalar, sm[:, 2], sm[:, 2], 1.0, None, ALU.add, w=[ta])
                        yield [tc]
                        tg = k.v(V.scalar_tensor_tensor, sm[:, 1], sm[:, 1], -1.0,
                                 sm[:, 5, 0].unsqueeze(1).to_broadcast([P, 2, 8]), ALU.mult, ALU.mult, w=[t2, tc])
                        E_["g"].set(tg)
                        t1 = k.v(V.reciprocal, sm[:, 2], sm[:, 2], w=[t1])
                        E_["beta"].set(k.v(V.tensor_tensor, sm[:, 0], sm[:, 4], sm[:, 2], op=ALU.mult, w=[t1, tb]))
                        for c, q in reversed(CQ):
                            k.spawn(decay(c, q), first=True)
                        yield [tg, k.banks]
                        b = k.bank()
                        tt = k.mm(k.ps[b][:, 0:16], Q("SL"), sm[:, 1].rearrange("p c h -> p (c h)"), True, True,
                                  w=[tg, d_c2], inc=True)
                        yield [tt]
                        E_["eR"].set(k.a(A.activation, sm[:, 6].rearrange("p c h -> p (c h)"), k.ps[b][:, 0:16], ACT.Exp,
                                         w=[tt, td]))
                        k.close(b, [E_["eR"]])

                    def decay(c, q):
                        tg = E_["g"]
                        yield [tg]
                        tu = k.v(V.tensor_tensor, quad(gu, c, q), Q("U").unsqueeze(1).to_broadcast([P, 4, P]),
                                 sm[:, 1, c, q * 4:q * 4 + 4].unsqueeze(2).to_broadcast([P, 4, P]), op=ALU.mult, w=[tg])
                        yield [tu, k.banks]
                        b = k.bank()
                        tt = k.mm(k.ps[b][:, :], Q("SL"), quad(gu, c, q).rearrange("p h c -> p (h c)"), True, True,
                                  w=[tu], inc=True)
                        yield [tt]
                        ta = k.a(A.activation, quad(DT, c, q), bank4(b), ACT.Exp, w=[tt])
                        k.close(b, [ta])
                        E_["DT", c, q].set(ta)
                        if c:
                            yield [k.banks]
                            b = k.bank()
                            tt = k.mm(k.ps[b][:, :], Q("ones"), quad(gu, 1, q).rearrange("p h c -> p (h c)"), True, True,
                                      w=[tu], inc=True)
                            yield [tt]
                            ta = k.a(A.activation, EG[:, q * 4:q * 4 + 4], bank4(b), ACT.Exp, w=[tt])
                            k.close(b, [ta])
                            E_["EG", q].set(ta)
                        E_["guf", c, q].set(tt)

                    exps = [E_["eR"], E_["EG", 0], E_["EG", 1]] + [E_["DT", c, q] for c, q in CQ]

                    def conv(which, h, b, t, dst, old):
                        yield [t, old]
                        ps = k.ps[b][:, 0:T]
                        w_ = [Q("gcw", (j * 4 + tap) * 24 + which * 8 + h, 1) for tap in range(4)]
                        ta = k.a(A.activation, dst, ps, ACT.Identity, scale=w_[3], w=[t, old, d_c2])
                        for n in (1, 2, 3):
                            yield [ta]
                            ta = k.v(V.scalar_tensor_tensor, dst[:, n:T], ps[:, 0:T - n], w_[3 - n], dst[:, n:T],
                                     ALU.mult, ALU.add, w=[ta])
                        k.close(b, [ta])
                        E_["cv", which, h].set(ta)

                    def conv_g(which, h, b, t, dst):
                        yield [t, taps]
                        i, old = taps.take()
                        ps = k.ps[b][:, 0:T]
                        w_ = [Q("gcw", (j * 4 + tap) * 24 + which * 8 + h, 1) for tap in range(4)]
                        ta = k.a(A.activation, dst, ps, ACT.Identity, scale=w_[3], w=[t, d_c2])
                        tx = [k.a(A.activation, tap3[:, i, n - 1, n:T], ps[:, 0:T - n], ACT.Identity, scale=w_[3 - n], w=[old])
                              for n in (1, 2, 3)]
                        k.close(b, tx)
                        for n in (1, 2, 3):
                            yield [ta, tx]
                            ta = k.g(G.tensor_tensor, dst[:, n:T], dst[:, n:T], tap3[:, i, n - 1, n:T], op=ALU.add, w=[ta, tx])
                        taps.give(i, [ta])
                        E_["cv", which, h].set(ta)

                    def silu(which, q, dst):
                        need = [E_["cv", which, q * 4 + h] for h in range(4)]
                        yield [need, exps]
                        E_["f", which, q].set(k.a(A.activation, dst, dst, ACT.Silu, w=need))

                    def convolved(which, key, dst):
                        for h in range(8):
                            b, t = ws_tile(k, st, key, H, htok, T)
                            if which != 1 and h % 2:
                                k.spawn(conv_g(which, h, b, t, dst[h // 4][:, h % 4]))
                            else:
                                k.spawn(conv(which, h, b, t, dst[h // 4][:, h % 4], ()))
                            if h % 4 == 3:
                                k.spawn(silu(which, h // 4, dst[h // 4]))
                        return t

                    jks = []

                    def inverse(c, q):
                        kh = lambda h: kf[:, q * 4 + h, c * P:(c + 1) * P]
                        r_ = lambda r: sm[:, r, c, q * 4:q * 4 + 4]
                        lt, x_, y_ = quad(LT, c, q), X[:, q, c * 4:c * 4 + 4], Y[:, q, c * 4:c * 4 + 4]
                        pm = Pm[:, c * 2 + q, 0:256].rearrange("p (h c) -> p h c", h=4)
                        tf = E_["f", 1, q]
                        yield [tf, k.banks]
                        b = k.bank()
                        tt = four(b, kh, kh, [tf])
                        yield [tt]
                        for h in range(4):
                            jks.append(k.v(V.tensor_tensor_reduce, out=jk[:, len(jks) % 2],
                                           in0=k.ps[b][:, h * P:(h + 1) * P], in1=ident, scale=1.0, scalar=0.0,
                                           op0=ALU.mult, op1=ALU.add, accum_out=sm[:, 7, c, q * 4 + h:q * 4 + h + 1],
                                           w=[tt, jks[-2:-1]]))
                        t1 = jks[-1]
                        yield [t1, E_["beta"]]
                        t1 = k.v(V.tensor_scalar, r_(7), r_(7), EPS, None, ALU.add, w=[t1])
                        tr = k.g(G.tensor_tensor, r_(8), r_(7), cst[:, 1, 0:4], op=ALU.pow, w=[t1, t_cst])
                        E_["root", c, q].set(tr)
                        t1 = k.v(V.reciprocal, r_(9), r_(7), w=[t1])
                        t1 = k.v(V.tensor_tensor, r_(9), r_(9), r_(0), op=ALU.mult, w=[t1, E_["beta"]])
                        E_["w", c, q].set(t1)
                        tn = k.v(V.tensor_scalar, r_(10), r_(9), -1.0, None, ALU.mult, w=[t1])
                        td = E_["DT", c, q]
                        yield [tn, td]
                        for h in range(4):
                            tl = k.v(V.scalar_tensor_tensor, lt[:, h], k.ps[b][:, h * P:(h + 1) * P],
                                     sm[:, 10, c, q * 4 + h:q * 4 + h + 1], DT[:, c, q * 4 + h], ALU.mult, ALU.mult,
                                     w=[tn, td])
                        k.close(b, [tl])
                        E_["LT", c, q].set(tl)
                        yield [tl]
                        E_["DTm", c, q].set(k.g(G.tensor_tensor, quad(DT, c, q), quad(DT, c, q),
                                                Q("U").unsqueeze(1).to_broadcast([P, 4, P]), op=ALU.mult, w=[tl]))
                        tX, tY = [E_["X", q], E_["guf", c, q]], E_["Y", q]
                        yield [tX]
                        for lv in range(4, 7):
                            bl = 1 << lv
                            side = lambda a, y: a.rearrange("p h (n y c) -> p h n y c", y=2, c=bl)[:, :, :, y]
                            got = lambda b, n=P: k.ps[b][0:n, 0:256].rearrange("p (h n c) -> p h n c", h=4, c=bl)
                            xl = side(x_, 0)
                            pv = pm.rearrange("p h (n c) -> p h n c", c=bl)
                            yield [tX, k.banks]
                            b = k.bank()
                            o = got(b)
                            for h in range(4):
                                tt = k.mm(o[:, h], lt[:, h], xl[:, h], True, True, w=[tX, tl], inc=h == 3)
                            yield [tt]
                            mask = pair_mask(64 // bl, 1)
                            tP = k.v(V.tensor_tensor, pv, o, mask.unsqueeze(1).unsqueeze(3).to_broadcast([P, 4, 64 // bl, bl]),
                                     op=ALU.mult, w=[tt])
                            k.close(b, [tP])
                            yield [tP, k.banks]
                            b = k.bank()
                            if lv < 6:
                                o, dst = got(b), xl
                                ops = [(y_[:, h], pv[:, h]) for h in range(4)]
                            else:
                                E_["LTf", c, q].set(tt)
                                o, dst = got(b, 64), side(y_[0:64], 1)
                                ops = [(pm[:, h], side(y_, 1)[:, h]) for h in range(4)]
                            for h in range(4):
                                tt = k.mm(o[:, h], *ops[h], True, True, w=[tP, tY], inc=h == 3)
                            yield [tt]
                            tv = k.v(V.tensor_tensor, dst, dst, o, op=ALU.add, w=[tt, tX])
                            k.close(b, [tv])
                            if lv < 6:
                                tX = tv
                                yield [tX, k.banks]
                                b = k.bank()
                                tt = flips(b, [x_[:, h] for h in range(4)], [tX])
                                yield [tt]
                                tY = k.a(A.copy, y_, bank4(b), w=[tt])
                                k.close(b, [tY])
                        E_["Y", c, q].set(tv)

                    def zeroing(q, old):
                        yield [old]
                        tz = k.zero(X[:, q], w=old)
                        yield [tz]
                        zeroed[q].set([k.dma("a", whole_way(xy_way[q, n]), X[:, q], w=[tz]) for n in range(2)])

                    def diagonals(q):
                        mine = slice(q * 64, q * 64 + 64)
                        blk, x16, half_, prod = (dg[mine, a:b] for a, b in ((0, 272), (272, 544), (544, 608), (608, 1120)))
                        xyd = prod.rearrange("p (w i j) -> p w i j", w=2, i=16)
                        heads = slice(q * 4, q * 4 + 4)
                        lts = [E_["LT", c, q] for c in range(2)]
                        t1 = k.v(V.memset, x16, 0.0)
                        yield [t1]
                        t1 = k.v(V.memset, x16.rearrange("p (i e) -> p i e", e=17)[:, :, 0], 1.0, w=[t1])
                        yield lts
                        way = whole_way(lt_way[q])
                        there = [k.dma("a", way[:, c * 4:c * 4 + 4], LT[:, c, heads], w=lts) for c in range(2)]
                        yield [there]
                        back = k.dma("a", blk[:, 0:256].rearrange("p (i j) -> p i j", j=16), diagonal_way(lt_way[q]),
                                     w=[there])
                        yield [t1, back]

                        def sub(a, at, b):
                            return a.rearrange("p (g e) -> p g e", e=34 * b)[:, :, at:at + 16 * b].rearrange(
                                "p g (r c) -> p g r c", c=16)[:, :, :, 0:b]

                        t1 = k.v(V.tensor_copy, sub(x16, 16, 1), sub(blk, 1, 1), w=[t1, back])
                        turn = lambda a: a.rearrange("p g r k -> p g k r")
                        hf = half_[:, 0:16].rearrange("p (g r c) -> p g r c", g=4, r=2)
                        pr = [prod[:, n * 16:n * 16 + 16].rearrange("p (g r c) -> p g r c", g=4, r=2) for n in (0, 1)]
                        for l_, r_, dst in ((turn(sub(blk, 2, 2)), sub(x16, 0, 2), hf), (sub(x16, 34, 2), hf, sub(x16, 32, 2))):
                            yield [t1]
                            t2 = [k.v(V.tensor_tensor, pr[n], l_[:, :, :, n].unsqueeze(3).to_broadcast([64, 4, 2, 2]),
                                      r_[:, :, n, :].unsqueeze(2).to_broadcast([64, 4, 2, 2]), op=ALU.mult, w=[t1])
                                  for n in (0, 1)]
                            t1 = k.v(V.tensor_tensor, dst, pr[0], pr[1], op=ALU.add, w=t2)
                        for b in (4, 8):
                            g = 8 // b
                            four_ = prod[:, 0:g * b ** 3].rearrange("p (g r c k) -> p g r c k", g=g, r=b, c=b)
                            hf = half_[:, 0:g * b * b].rearrange("p (g r c) -> p g r c", g=g, r=b)
                            for l_, r_, dst in ((turn(sub(blk, b, b)), sub(x16, 0, b), hf),
                                                (sub(x16, 17 * b, b), hf, sub(x16, 16 * b, b))):
                                yield [t1]
                                t2 = [k.v(V.tensor_tensor, four_[:, n], l_[:, n].unsqueeze(2).to_broadcast([64, b, b, b]),
                                          r_[:, n].rearrange("p k c -> p c k").unsqueeze(1).to_broadcast([64, b, b, b]),
                                          op=ALU.mult, w=[t1]) for n in range(g)]
                                t1 = [k.v(V.tensor_reduce, dst[:, n], four_[:, n], axis=AX, op=ALU.add, w=t2)
                                      for n in range(g)]
                        yield [t1]
                        m16 = x16[:, 0:256].rearrange("p (i j) -> p i j", j=16)
                        t2 = [k.a(A.copy, xyd[:, 0], m16, w=[t1]),
                              k.v(V.tensor_copy, xyd[:, 1], m16.rearrange("p i j -> p j i"), w=[t1])]
                        there = [k.dma("a", diagonal_way(xy_way[q, n]), xyd[:, n], w=[t, zeroed[q]]) for n, t in enumerate(t2)]
                        for n, (dst, t) in enumerate(zip((X, Y), there)):
                            yield [t]
                            E_["XY"[n], q].set(k.dma("a", dst[:, q], whole_way(xy_way[q, n]), w=[t]))

                    def scores(c, q):
                        need = [E_["f", 0, q], E_["f", 1, q]]
                        yield [need, k.banks]
                        cols = slice(c * P, (c + 1) * P)
                        b = k.bank()
                        tt = four(b, lambda h: kf[:, q * 4 + h, cols], lambda h: qf[:, q * 4 + h, cols], need)
                        yield [tt, E_["DTm", c, q]]
                        ta = k.v(V.tensor_tensor, quad(DT, c, q), quad(DT, c, q), bank4(b), op=ALU.mult,
                                 w=[tt, E_["DTm", c, q]])
                        k.close(b, [ta])
                        E_["AT", c, q].set(ta)

                    def squares(c, q):
                        q2 = Pm[:, c * 2 + q, 256:512].rearrange("p (h c) -> p h c", h=2)
                        tt = [E_["f", 0, q], E_["guf", c, q]]
                        for n in (0, 2):
                            yield [tt]
                            ta = k.a(A.activation, q2, qf[:, q * 4 + n:q * 4 + n + 2, c * P:(c + 1) * P], ACT.Square, w=tt)
                            E_["q2", c, q, n].set(ta)
                            yield [ta, k.banks]
                            b = k.bank()
                            for h in (0, 1):
                                tt = k.mm(k.ps[b][:, h:h + 1], q2[:, h], Q("ones")[:, 0:1], True, True, w=[ta], inc=h == 1)
                            yield [tt]
                            tv = k.v(V.tensor_scalar, sm[:, 3, c, q * 4 + n:q * 4 + n + 2], k.ps[b][:, 0:2], EPS, EPS * P,
                                     ALU.add, ALU.mult, w=[tt])
                            k.close(b, [tv])
                            E_["qe", c, q, n].set(tv)

                    def values(c, q):
                        need = [E_["f", 2, q], E_["root", c, q]]
                        yield [need, k.banks]
                        b = k.bank()
                        tt = flips(b, [vq[q][:, h, c * P:(c + 1) * P] for h in range(4)], need)
                        E_["vT", c, q].set(tt)
                        yield [tt]
                        tv = scaled(quad(R, c, q), b, sm[:, 8, c, q * 4:q * 4 + 4], [tt, need])
                        k.close(b, [tv])
                        E_["R", c, q].set(tv)

                    def keys(q):
                        need = [E_["f", 1, q], E_["eR"], E_["vT", 0, 1], E_["vT", 1, 1]]
                        yield [need, k.banks]
                        b = k.bank()
                        tt = flips(b, [kf[:, q * 4 + h, 0:P] for h in range(4)], need)
                        yield [tt]
                        tv = k.v(V.tensor_tensor, kd[:, q * 4:q * 4 + 4], bank4(b),
                                 sm[:, 6, 0, q * 4:q * 4 + 4].unsqueeze(2).to_broadcast([P, 4, P]), op=ALU.mult,
                                 w=[tt, need])
                        k.close(b, [tv])
                        E_["kd", q].set(tv)

                    def solved(c, q, t_r):
                        need = [E_["Y", c, q], E_["w", c, q], t_r]
                        yield [need, k.banks]
                        b = k.bank()
                        tt = four(b, lambda h: Y[:, q, c * 4 + h], lambda h: R[:, c, q * 4 + h], need)
                        yield [tt]
                        ta = k.v(V.tensor_tensor, quad(R, c, q), bank4(b),
                                 sm[:, 9, c, q * 4:q * 4 + 4].unsqueeze(2).to_broadcast([P, 4, P]), op=ALU.mult,
                                 w=[tt, need])
                        k.close(b, [ta])
                        E_["Z", c, q].set(ta)

                    def second(q):
                        e4 = EG[:, q * 4:q * 4 + 4]
                        k4 = kf[:, q * 4:q * 4 + 4, P:T]
                        q4 = qf[:, q * 4:q * 4 + 4, P:T]
                        need = [E_["EG", q], E_["AT", 1, q], E_["q2", 1, q, 0], E_["q2", 1, q, 2]]
                        yield need
                        t_k = k.v(V.tensor_tensor, k4, k4, e4, op=ALU.mult, w=need)
                        E_["q1", q].set(k.v(V.tensor_tensor, q4, q4, e4, op=ALU.mult, w=need))
                        need = [E_["kd", q], E_["Z", 0, q], E_["vT", 0, 0], E_["vT", 1, 0]]
                        yield [need, k.banks]
                        b = k.bank()
                        tt = four(b, lambda h: kd[:, q * 4 + h], lambda h: R[:, 0, q * 4 + h], need)
                        yield [tt]
                        ta = k.a(A.copy, S1[:, q * 4:q * 4 + 4], bank4(b), w=[tt, need])
                        k.close(b, [ta])
                        E_["S", q].set(ta)
                        need = [t_k, ta, E_["R", 1, q]]
                        yield [need, k.banks]
                        b = k.bank()
                        tt = four(b, lambda h: kf[:, q * 4 + h, P:T], lambda h: S1[:, q * 4 + h], need)
                        yield [tt]
                        tv = k.v(V.tensor_tensor, quad(R, 1, q), quad(R, 1, q), bank4(b), op=ALU.subtract, w=[tt, need])
                        k.close(b, [tv])
                        E_["R1", q].set(tv)

                    hn = Evs(Parted)

                    def outputs(c, q):
                        need = [E_["AT", c, q], E_["Z", c, q]]
                        if c:
                            need += [E_["q1", q], E_["S", q]]
                        yield [need, k.banks]
                        b = k.bank()
                        for h in range(4):
                            n = q * 4 + h
                            o = k.ps[b][:, h * P:(h + 1) * P]
                            if c:
                                k.mm(o, qf[:, n, P:T], S1[:, n], True, False, w=need)
                            tt = k.mm(o, DT[:, c, n], R[:, c, n], not c, True, w=need, inc=h == 3)
                        bk = Bank()
                        bk.set(b, tt)
                        qe = [E_["qe", c, q, n] for n in (0, 2)]
                        k.spawn(norm_out(bk, c, q, 4, (sm[:, 3, c, q * 4:q * 4 + 4], qe), gate,
                                         ost[:, c * 2 + q], Pm[:, c * 2 + q], t_gate[c, q], [E_["Y", c, q], qe], Ev(), hn,
                                         E_["proj"]))

                    gates, t_gate = gates_(s, gate, Q("gnw", j * P, P), P, exps)
                    if j == 0:
                        for q in range(2):
                            k.spawn(zeroing(q, k.last()[:1]))
                    small = small_w(s, "wba", j)
                    as_group(k, st, f"gdn{j}_z0", H, t_h, [0, 1], evac=gates(0))
                    k.spawn(decays(*small_proj(small, htok)), first=True)
                    for q in range(2):
                        k.spawn(diagonals(q))
                    for c, q in CQ:
                        k.spawn(inverse(c, q))
                    convolved(1, f"gdn{j}_k", [kf[:, 0:4], kf[:, 4:8]])
                    for c, q in CQ:
                        k.spawn(scores(c, q))
                        k.spawn(squares(c, q))
                    convolved(0, f"gdn{j}_q", [qf[:, 0:4], qf[:, 4:8]])
                    for c, q in CQ:
                        k.spawn(values(c, q))
                    for q in range(2):
                        k.spawn(keys(q))
                    convolved(2, f"gdn{j}_v", vq)
                    for q in range(2):
                        k.spawn(solved(0, q, E_["R", 0, q]))
                        k.spawn(second(q))
                        k.spawn(solved(1, q, E_["R1", q]))
                        k.spawn(outputs(0, q))
                        k.spawn(outputs(1, q))
                    as_group(k, st, f"gdn{j}_z1", H, t_h, [0, 1], evac=gates(1))
                    E_["proj"].set(k.last()[0])
                    return down_ln(f"gdn{j}_out", KT, x_H, lambda kt, tile: hn[tile, kt // 4], d_ln, x_old)

            def decayed(s, nh, g, t_g, qf, kf, vt, t_qk, t_v, gate, t_gate, hn, proj, E, old):
                dv = D // nh
                per = 512 // dv
                mexp = s.sb("mexp", [P, 16 * P], F32R)
                AT = s.sb("AT", [P, 2, 4, P])
                AX1 = gtmp[:, 0].rearrange("p (i h t) -> p i h t", i=2, h=2)
                sq = s.sb("osq", [P, 512], BF16)
                first_ = CO["n1"][0]
                both = [core[:, first_:first_ + 2 * P].rearrange("p (h c) -> p h c", c=P)]
                both += [gtmp[:, 1, a:a + 2 * P].rearrange("p (h c) -> p h c", c=P) for a in (0, 2 * P)]
                both.append(s.sb("both", [P, 2, P])[:, :])
                keys = Slots(len(both))
                ost = s.sb("ost", [P, 4, 3, 4])
                stage = E[:, 0, 0:4].rearrange("p l h t -> p (l h t)")
                slots = list(range(4)) + [5, 6, 7]
                E_ = Evs()
                d_m = k.dma("sp", stage, mexp_in, w=k.last())

                def constants():
                    yield [d_m]
                    E_["mexp"].set(k.a(A.copy, mexp[:, :], stage, w=[d_m]))

                def exps(gr, hh, tile, part):
                    i, h = gr % 2, gr * 2 + hh
                    tg = t_g(tile, h)
                    free = [E_["free", gr - 2], E_["mexp"], old if gr == 1 else ()]
                    yield [tg, free, k.banks]
                    b = k.bank()
                    c0 = (2 * part + tile) * 4 * P
                    rhs = mexp[:, c0:c0 + 512]
                    k.mm(k.ps[b][:, :], g[0][:, tile, h * P:(h + 1) * P], rhs, True, False, w=[tg, E_["mexp"]])
                    tt = k.mm(k.ps[b][:, :], g[1][:, tile, h * P:(h + 1) * P], rhs, False, True, inc=True)
                    yield [tt]
                    s0 = 4 if part else 0
                    ta = k.a(A.activation, E[:, i, s0:s0 + 4, hh, tile * P:(tile + 1) * P],
                             k.ps[b][:, :].rearrange("p (l c) -> p l c", c=P), ACT.Exp, w=[tt, free])
                    k.close(b, [ta])
                    E_["E", gr, part, hh, tile].set(ta)

                def level(gr, lv, merged):
                    i = gr % 2
                    hs = slice(gr * 2, gr * 2 + 2)
                    need = t_qk(gr)
                    if lv < 7:
                        need = need + [E_["E", gr, lv // 4, hh, tile] for hh in range(2) for tile in range(2)]
                    yield need
                    tq = need
                    if lv < 7:
                        yield [keys]
                        kb, old = keys.take()
                        bl, sl = 64 >> lv, slots[lv]
                        halves = lambda a: a.rearrange("p a (n y c) -> p a n y c", y=2, c=bl)
                        tq = []
                        for tile in range(2):
                            c = slice(tile * P, (tile + 1) * P)
                            e_ = halves(E[:, i, sl, :, c])
                            for y, src, dst in ((tile, kf, halves(both[kb])), (1 - tile, qf, e_)):
                                tq.append(k.v(V.tensor_tensor, dst[:, :, :, y], e_[:, :, :, y],
                                              halves(src[:, hs, c])[:, :, :, y], op=ALU.mult, w=[need, old]))
                    yield [tq, k.banks]
                    b = k.bank()
                    if lv < 7:
                        for hh in range(2):
                            e_ = E[:, i, sl, hh]
                            queries = bass.AP(tensor=e_.tensor, offset=e_.offset + bl,
                                              ap=[list(e_.ap)[0], [P - bl, 2], [2 * bl, 64 // bl], [1, bl]])
                            o = k.ps[b][:, hh * P:(hh + 1) * P].rearrange("p (t n c) -> p t n c", t=2, c=bl)
                            tt = k.mm(o, both[kb][:, hh], queries, True, True, w=tq, inc=hh == 1)
                        keys.give(kb, [tt])
                        got = k.ps[b][:, 0:256].rearrange("p (a t n c) -> p t a n c", a=2, t=2, c=bl)
                        ops = [(halves(AT[:, i, tile:4:2])[:, :, :, 1 - tile],
                                pair_mask(1 << lv, tile).bitcast(U32).unsqueeze(1).unsqueeze(3).to_broadcast(
                                    [P, 2, 1 << lv, bl]), got[:, tile]) for tile in range(2)]
                    else:
                        for n in range(4):
                            hh, c = n // 2, slice(n % 2 * P, n % 2 * P + P)
                            tt = k.mm(bank4(b)[:, n], kf[:, gr * 2 + hh, c], qf[:, gr * 2 + hh, c], True, True, w=tq, inc=n == 3)
                        ops = [(AT[:, i], ident.bitcast(U32).unsqueeze(1).to_broadcast([P, 4, P]), bank4(b))]
                    yield [tt, E_["AT0", gr]]
                    ta = [k.v(V.copy_predicated, *op, w=[tt, E_["AT0", gr], merged[-1:]]) for op in ops]
                    k.close(b, ta)
                    merged.append(ta)
                    E_["gram", gr, lv].set(tt)
                    if len(merged) == 8:
                        E_["AT", gr].set(ta)

                def across(gr):
                    i = gr % 2
                    hs = slice(gr * 2, gr * 2 + 2)
                    need = t_qk(gr) + [E_["E", gr, 1, hh, tile] for hh in range(2) for tile in range(2)]
                    yield need
                    tx = [k.v(V.tensor_tensor, E[:, i, 4, :, 0:P], E[:, i, 4, :, 0:P], kf[:, hs, 0:P], op=ALU.mult,
                              w=need),
                          k.v(V.tensor_tensor, E[:, i, 4, :, P:T], E[:, i, 4, :, P:T], qf[:, hs, P:T], op=ALU.mult,
                              w=need)]
                    yield [tx, k.banks]
                    b = k.bank()
                    for hh in range(2):
                        tt = k.mm(k.ps[b][:, hh * P:(hh + 1) * P], E[:, i, 4, hh, 0:P], E[:, i, 4, hh, P:T], True, True,
                                  w=tx, inc=hh == 1)
                    yield [tt, E_["av", gr - 2]]
                    tc = k.a(A.copy, AX1[:, i], k.ps[b][:, 0:256].rearrange("p (n c) -> p n c", c=P),
                             w=[tt, E_["av", gr - 2]])
                    k.close(b, [tc])
                    E_["AX", gr].set(tc)
                    grams = [E_["gram", gr, lv] for lv in range(8)]
                    yield [grams]
                    E_["free", gr].set([tt, grams])

                def cleared(gr):
                    yield [E_["av", gr - 2]]
                    E_["AT0", gr].set(k.zero(AT[:, gr % 2], w=[E_["av", gr - 2]]))

                ob = {}

                def weighed(gr):
                    i = gr % 2
                    hf = gr * 2 // per
                    need = [E_["AT", gr], E_["AX", gr], t_v[0, hf], t_v[1, hf], E_["av", gr - 1]]
                    first = gr * 2 % per == 0
                    yield [need] + [k.banks] * (2 if first else 0)
                    if first:
                        for tile in range(2):
                            ob[tile, hf] = k.bank()
                    for tile in range(2):
                        for hh in range(2):
                            h = gr * 2 + hh
                            col = (h % per) * dv
                            o = k.ps[ob[tile, hf]][:, col:col + dv]
                            vs = slice(h * dv, (h + 1) * dv)
                            tt = k.mm(o, AT[:, i, hh * 2 + tile], vt[:, tile, vs], True, tile == 0, w=need,
                                      inc=tile == 0)
                            if tile:
                                tt = k.mm(o, AX1[:, i, hh], vt[:, 0, vs], False, True, inc=True)
                        if (gr * 2 + 2) % per == 0:
                            bk = Bank()
                            bk.set(ob[tile, hf], tt)
                            n = hf * 2 + tile
                            k.spawn(norm_out(bk, tile, hf, per, (None, ()), gate, ost[:, n], sq[:, :], t_gate[tile, hf],
                                             E_["sq", n - 1], E_["sq", n], hn, proj, Q("turn")))
                    E_["av", gr].set(tt)

                E_["sq", -1].set(())
                for gr in (-2, -1):
                    E_["free", gr].set(())
                    E_["av", gr].set(())
                k.spawn(constants())
                for gr in range(nh // 2):
                    k.spawn(cleared(gr))
                    for part in range(2):
                        for hh in range(2):
                            for tile in range(2):
                                k.spawn(exps(gr, hh, tile, part))
                    merged = []
                    for lv in range(8):
                        k.spawn(level(gr, lv, merged))
                    k.spawn(across(gr))
                    k.spawn(weighed(gr))
                return [E_["E", gr, part, hh, tile] for gr in range(nh // 2) for part in range(2) for hh in range(2)
                        for tile in range(2)]

            def heads_ws(key, n, htok, evac):
                for h in range(n):
                    k.spawn(evac(h, *ws_tile(k, st, key, H, htok, T)))

            def copied(dst, ev):
                def f(h, b, t):
                    yield [t]
                    ta = k.a(A.copy, dst[:, h], k.ps[b][:, 0:T], w=[t])
                    k.close(b, [ta])
                    ev[h].set(ta)
                return f

            def values_(vt, ev):
                def f(hf):
                    def g(tile, b, t):
                        yield [t]
                        ta = k.a(A.copy, vt[:, tile, HF[hf]], k.ps[b][:, :], w=[t])
                        k.close(b, [ta])
                        ev[tile, hf].set(ta)
                    return spawn(g)
                return f

            def hgrn(t_h, d_ln, x_old):
                with Scope(k, fenced=True) as s:
                    kf = Hh_f[:, :, T:2 * T]
                    qf = Hl_f[:, :, T:2 * T]
                    gh = s.sb("gh", [P, 2, D], F32R)
                    gl = s.sb("gl", [P, 2, D], F32R)
                    vt = s.sb("vt", [P, 2, D])
                    gate = grows
                    E = s.sb("E", [P, 2, 8, 2, T])
                    E_, t_f, t_q, t_v, hn = Evs(), Evs(), Evs(), Evs(), Evs(Parted)
                    flat = E[:, 1].rearrange("p l h t -> p (l h t)")
                    g_ = gate[:, :, :].rearrange("p t c -> p (t c)")
                    room = [g_[:, 0:1024], g_[:, 1024:2048]] + [flat[:, i * 1024:(i + 1) * 1024] for i in range(4)]
                    room = [a.rearrange("p (h t) -> p h t", t=T) for a in room]
                    bc = lambda r, q: lb[:, r, q * 4:q * 4 + 4].unsqueeze(2).to_broadcast([P, 4, T])

                    def forget(q):
                        f_ = kf[:, q * 4:q * 4 + 4]
                        t1_, t2_, t3_ = room[q * 3:q * 3 + 3]
                        tf = [t_f[q * 4 + h] for h in range(4)]
                        yield [tf]
                        ta = k.a(A.activation, t1_, f_, ACT.Abs, w=[tf])
                        ta = k.a(A.activation, t1_, t1_, ACT.Exp, scale=-1.0, w=[ta])
                        ta = k.a(A.activation, t1_, t1_, ACT.Ln, bias=one, w=[ta, t_cst])
                        yield [ta]
                        tv = k.v(V.scalar_tensor_tensor, t2_, f_, 0.0, t1_, ALU.min, ALU.subtract, w=[ta, tf])
                        tk = k.v(V.scalar_tensor_tensor, t3_, f_, 0.0, t1_, ALU.max, ALU.add, w=[ta, tf])
                        yield [tv, t_lb]
                        tv = k.v(V.tensor_tensor, t2_, t2_, bc(2, q), op=ALU.add, w=[tv, t_lb])
                        yield [tv]
                        ta = k.a(A.activation, t1_, t2_, ACT.Abs, w=[tv, tk])
                        ta = k.a(A.activation, t1_, t1_, ACT.Exp, scale=-1.0, w=[ta])
                        ta = k.a(A.activation, t1_, t1_, ACT.Ln, bias=one, w=[ta])
                        for h in range(4):
                            tk2 = k.a(A.activation, kf[:, q * 4 + h], t3_[:, h], ACT.Exp, scale=-1.0,
                                      bias=lb[:, 1, q * 4 + h:q * 4 + h + 1], w=[tk, t_lb])
                        E_["k", q].set(tk2)
                        yield [ta]
                        tv = k.v(V.scalar_tensor_tensor, t2_, t2_, 0.0, t1_, ALU.max, ALU.add, w=[ta])
                        tv = k.v(V.tensor_tensor, t2_, t2_, bc(0, q), op=ALU.add, w=[tv, t_lb])
                        for tile in range(2):
                            yield [tv, k.banks]
                            b = k.bank()
                            tt = flips(b, [t2_[:, h, tile * P:(tile + 1) * P] for h in range(4)], [tv])
                            yield [tt]
                            ts = split(k, k.ps[b][:, :], gh[:, tile, HF[q]], gl[:, tile, HF[q]], [tt])
                            k.close(b, ts)
                            E_["g", tile, q].set(ts)
                        E_["forget", q].set([ts, tk2])

                    def silu(q):
                        need = [t_q[q * 4 + h] for h in range(4)]
                        yield [need, E_["forget", 0], E_["forget", 1]]
                        E_["q", q].set(k.a(A.activation, qf[:, q * 4:q * 4 + 4], qf[:, q * 4:q * 4 + 4], ACT.Silu, w=need))

                    done = [E_["forget", 0], E_["forget", 1]]
                    v_ = values_(vt, t_v)
                    as_group(k, st, "hg_i0", H, t_h, [0, 1], evac=v_(0))
                    exps = Evs()
                    gates, t_gate = gates_(s, gate, Q("hgn"), P, exps["all"])
                    all_exps = decayed(s, 8, (gh, gl), lambda tile, h: E_["g", tile, h // 4], qf, kf, vt,
                                       lambda gr: [E_["k", gr // 2], E_["q", gr // 2]], t_v, gate, t_gate, hn, E_["proj"], E,
                                       done)
                    exps["all"].set(all_exps)
                    for q in range(2):
                        k.spawn(forget(q))
                    heads_ws("hg_f", 8, t_h, copied(kf, t_f))
                    for q in range(2):
                        k.spawn(silu(q))
                    heads_ws("hg_q", 8, t_h, copied(qf, t_q))
                    as_group(k, st, "hg_i1", H, t_h, [0, 1], evac=v_(1))
                    k.until(done)
                    t_room = done
                    as_group(k, st, "hg_r", H, t_h, [0, 1], evac=gates(0))
                    as_group(k, st, "hg_r", H, t_h, [0, 1], evac=gates(1))
                    E_["proj"].set(k.last()[0])
                    return down_ln("hg_out", KT, x_H, lambda kt, tile: hn[tile, kt // 4], d_ln, x_old)

            def gla(t_h, d_ln, x_old):
                with Scope(k, fenced=True) as s:
                    kf = Hh_f[:, 0:4, T:2 * T]
                    qf = Hh_f[:, 4:8, T:2 * T]
                    gh = s.sb("gh", [P, 2, 512], F32R)
                    gl = s.sb("gl", [P, 2, 512], F32R)
                    vt = s.sb("vt", [P, 2, D])
                    gate = grows
                    gk = s.sb("gk", [32, T])
                    p_, l_ = (Hl_f[:, i:i + 4, T:2 * T].rearrange("p (t a) c -> p t a c", t=2) for i in (0, 4))
                    twos = lambda a: a.rearrange("p (a c) -> p a c", a=2)
                    E = s.sb("E", [P, 2, 8, 2, T])
                    E_, t_q, t_k, t_v, hn = Evs(), Evs(), Evs(), Evs(), Evs(Parted)
                    t_one = k.v(V.memset, gk[:, :], 1.0)

                    def low(b, t):
                        yield [t]
                        ta = k.a(A.copy, gk[0:16, :], k.ps[b][0:16, 0:T], w=[t, t_one])
                        k.close(b, [ta])
                        E_["gk"].set(ta)

                    def forget(tile):
                        yield [E_["gk"], k.banks]
                        b = k.bank()
                        t = k.mm(k.ps[b][:, :], gk[0:17, tile * P:(tile + 1) * P], Q("wgk2")[0:17], True, True,
                                 w=[E_["gk"], d_c2], inc=True)
                        yield [t]
                        tp = k.a(A.copy, p_[:, tile], twos(k.ps[b][:, :]), w=[t])
                        k.close(b, [tp])
                        ta = k.a(A.activation, l_[:, tile], p_[:, tile], ACT.Abs, w=[tp])
                        ta = k.a(A.activation, l_[:, tile], l_[:, tile], ACT.Exp, scale=-1.0, w=[ta])
                        ta = k.a(A.activation, l_[:, tile], l_[:, tile], ACT.Ln, bias=one, w=[ta, t_cst])
                        yield [ta]
                        tv = k.v(V.scalar_tensor_tensor, l_[:, tile], p_[:, tile], 0.0, l_[:, tile], ALU.min, ALU.subtract,
                                 w=[ta])
                        yield [tv]
                        ta = k.a(A.activation, twos(gh[:, tile]), l_[:, tile], ACT.Copy, scale=0.0625, w=[tv])
                        yield [ta]
                        tv = k.v(V.scalar_tensor_tensor, twos(gl[:, tile]), l_[:, tile], 0.0625, twos(gh[:, tile].bitcast(F32)),
                                 ALU.mult, ALU.subtract, w=[ta])
                        E_["g", tile].set([ta, tv])

                    v_ = values_(vt, t_v)
                    small = small_w(s, "wgk", 0)
                    as_group(k, st, "gla_v0", H, t_h, [0, 1], evac=v_(0))
                    exps = Evs()
                    gates, t_gate = gates_(s, gate, Q("gln"), 256, exps["all"])
                    k.spawn(low(*small_proj(small, t_h)))
                    for tile in range(2):
                        k.spawn(forget(tile))
                    all_exps = decayed(s, 4, (gh, gl), lambda tile, h: E_["g", tile], qf, kf, vt,
                                       lambda gr: [t_k[gr * 2], t_k[gr * 2 + 1], t_q[gr * 2], t_q[gr * 2 + 1]], t_v, gate,
                                       t_gate, hn, E_["proj"], E, ())
                    exps["all"].set(all_exps)
                    heads_ws("gla_q", 4, t_h, copied(qf, t_q))
                    heads_ws("gla_k", 4, t_h, copied(kf, t_k))
                    as_group(k, st, "gla_v1", H, t_h, [0, 1], evac=v_(1))
                    as_group(k, st, "gla_r", H, t_h, [0, 1], evac=gates(0))
                    as_group(k, st, "gla_r", H, t_h, [0, 1], evac=gates(1))
                    E_["proj"].set(k.last()[0])
                    return down_ln("gla_out", KT, x_H, lambda kt, tile: hn[tile, kt // 4], d_ln, x_old)

            def ffn(i, t_h, d_ln, x_old, final=None, by=None):
                with Scope(k, fenced=True) as s:
                    hh, hh_f = s.both("hh", [P, FT, T])
                    hl = s.sb("hl", [P, FT, T], F32R)
                    t_hid = ffn_up(s, f"fin{i}", H, t_h, hh, hl, hh_f, None)
                    return down_ln(f"fdn{i}", FT, lambda kt, tile: (hh[:, kt, tile * P:(tile + 1) * P],
                                                                    hl[:, kt, tile * P:(tile + 1) * P]),
                                   lambda kt, tile: t_hid[kt], d_ln, x_old, final, by)

            k.spawn(bounds())
            t_h, x_old = by_tile(first), [t_x[0], t_x[1]]
            for i in range(4):
                mixer = (lambda *a: gdn(0, *a), hgrn, gla, lambda *a: gdn(1, *a))[i]
                t_h, x_old = mixer(t_h, load_ln(), x_old)
                t_h, x_old = ffn(i, t_h, load_ln(), x_old, [] if i == 3 else None, Q("turn") if i < 2 else None)



def ws_units(w):
    kk, n = w.shape
    return w.reshape(KT, P, n // P, P).transpose(2, 1, 0, 3).reshape(n // P, P, KT * P)


def as_units(w, cols):
    kk, n = w.shape
    r = UW // cols
    return w.reshape(kk // P // r, r, P, n // cols, cols).transpose(3, 0, 2, 1, 4).reshape(-1, P, UW)


def up_units(w):
    a, b = w[:, :F], w[:, F:]
    pairs = np.stack([ws_units(a[:, 512:]), ws_units(b[:, 512:])], 1).reshape(-1, P, UW)
    return np.concatenate([as_units(a[:, :512], 512), ws_units(b[:, :512]), pairs])


def pack_weights(inp):
    g = lambda name, i=0: np.asarray(inp[name])[i]
    parts = {}
    ev = g("ev_w_in")
    parts["ev_qkv"] = np.concatenate([as_units(ev[:, c:c + 512], 512) for c in (2048, 1536, 2560)])
    parts["ev_conv"] = np.stack([ws_units(ev[:, 512:1024]), ws_units(ev[:, 1024:1536]), ws_units(ev[:, 0:512])],
                                1).reshape(-1, P, UW)
    parts["ev_out"] = as_units(g("ev_w_out"), 512)
    for i in range(2):
        up = g("ffn_w_up", i)
        parts[f"up{i}"] = up_units(up)
    parts["down0"] = as_units(g("ffn_w_down", 0), 512)
    parts["down1"] = as_units(g("ffn_w_down", 1), 1024)
    od = g("od_w_in")
    parts["od_in"] = np.concatenate([as_units(od[:, c:c + 512], 512) for c in (512, 1024, 1536, 0)])
    parts["od_out"] = as_units(g("od_w_out"), 1024)
    for j in range(2):
        gd = g("gdn_w_in_2", j)
        for n, c in (("q", 0), ("k", 1024), ("v", 2048)):
            parts[f"gdn{j}_{n}"] = ws_units(gd[:, c:c + 1024])
        for hf in range(2):
            parts[f"gdn{j}_z{hf}"] = as_units(gd[:, 3072 + hf * 512:3584 + hf * 512], 512)
        parts[f"gdn{j}_out"] = as_units(g("gdn_w_out_2", j), 1024)
    hg = g("hgrn_w_in_2")
    parts["hg_q"], parts["hg_f"] = ws_units(hg[:, 0:1024]), ws_units(hg[:, 1024:2048])
    parts["hg_r"] = as_units(hg[:, 3072:4096], 512)
    parts["hg_out"] = as_units(g("hgrn_w_out_2"), 1024)
    gl = g("gla_w_in_2")
    parts["gla_q"], parts["gla_k"] = ws_units(gl[:, 0:512]), ws_units(gl[:, 512:1024])
    parts["gla_r"] = as_units(gl[:, 2048:3072], 512)
    for hf in range(2):
        parts[f"hg_i{hf}"] = as_units(hg[:, 2048 + hf * 512:2560 + hf * 512], 512)
        parts[f"gla_v{hf}"] = as_units(gl[:, 1024 + hf * 512:1536 + hf * 512], 512)
    parts["gla_out"] = as_units(g("gla_w_out_2"), 1024)
    for i in range(4):
        parts[f"fin{i}"] = up_units(g("ffn_w_in_2", i))
        parts[f"fdn{i}"] = as_units(g("ffn_w_down_2", i), 1024)
    mw = np.asarray(inp["mod_w"]).transpose(0, 2, 1).reshape(2, 24, 2, P, D).transpose(0, 1, 3, 2, 4).reshape(2, 24, P, CW)
    chunks = {key: v.reshape(-1, 2, P, UW).transpose(0, 2, 1, 3).reshape(-1, P, CW) for key, v in parts.items()}
    sc = np.asarray(inp["mod_w"])[0, :, D:2 * D].reshape(2, 4, P, 2, 512).transpose(3, 0, 2, 1, 4).reshape(4, P, CW)
    other = {"m": lambda key, i: mw[key, i], "n": lambda key, i: sc[i]}
    plan = weight_chunks()
    out = np.empty((len(plan), P, CW), np.float32)
    for j, (kind, key, i) in enumerate(plan):
        out[j] = chunks[key][i] if kind == "w" else other[kind](key, i)
    return out


def feat(a):
    a = np.asarray(a)
    return np.moveaxis(a.reshape(*a.shape[:-1], -1, P), -1, 0).reshape(P, -1)


def rows(a):
    a = np.asarray(a).reshape(1, -1)
    return np.broadcast_to(a, (P, a.shape[1]))


def packed(fields, values):
    return np.ascontiguousarray(np.concatenate(
        [np.asarray(values[n], np.float32).reshape(P, -1) for n, size in fields], 1))


def rope():
    t = np.arange(T)
    inv = np.float32(10000.0) ** (-np.arange(16, dtype=np.float32) / np.float32(16))
    ang = np.stack([(t // 64).astype(np.float32)[:, None] * inv, (t % 64).astype(np.float32)[:, None] * inv], 1)
    c, s = np.cos(ang), np.sin(ang)
    cc = np.stack([c, c], 2).reshape(T, 64)
    ss = np.stack([-s, s], 2).reshape(T, 64)
    lay = lambda a: a.reshape(2, P, 64).transpose(1, 0, 2).reshape(P, 128)
    return lay(cc), lay(ss)


def retention_consts():
    j = np.arange(T)[:, None]
    i = np.arange(T)[None, :]
    lay = lambda a: a.reshape(2, P, T).transpose(1, 0, 2).reshape(P, 512)
    f = np.maximum(i - j, 0)
    b = np.maximum(j - i, 0)
    two = (1.0 + (i == j)) * 0.125
    band = np.zeros((4, T, T))
    for g, r in enumerate((1, 2, 4, 8)):
        lo, hi = np.clip(i - r, 0, T), np.clip(i + r + 1, 0, T)
        band[g] = ((j >= lo) & (j < hi)) / (hi - lo) - (i == j)
    bl = band.reshape(4, 2, P, T).transpose(2, 0, 1, 3).reshape(P, 2048)
    return lay(f), lay(b), lay(two), bl


def kernel(**inputs):
    import concourse.bacc as _bacc
    from concourse import mybir as _mybir
    from concourse.bass_utils import run_bass_kernel_spmd as _run

    f32 = _mybir.dt.float32
    inp = {n: np.asarray(v) for n, v in inputs.items()}
    rc, rs = rope()
    df, db, two, band = retention_consts()
    p = np.arange(P)
    t2 = p[:, None] + np.array([0, P])[None, :]
    ramps = np.concatenate([t2 + 1, T - t2, T - 1 - t2, t2], 1)
    core = packed(CORE, {
        "ident": np.eye(P), "n1": feat(inp["norm1_g"]), "n2": feat(inp["norm2_g"]), "modb": feat(inp["mod_b"]),
        "fcw": feat(inp["ffn_conv_w"]), "fcb": feat(inp["ffn_conv_b"]), "scw": feat(inp["sc_conv_w"]),
        "psc": feat(inp["pool_scale"]), "cc": feat(np.stack([inp["c"].reshape(D), inp["c_ctx"]]))})
    b1 = packed(B1, {
        "qg": rows(inp["da_q_norm"]), "kg": rows(inp["da_k_norm"]), "lq1": rows(inp["da_lq1"]),
        "lk1": rows(inp["da_lk1"]), "lq2": rows(inp["da_lq2"]), "lk2": rows(inp["da_lk2"]),
        "subg": rows(inp["da_subln_g"]), "ropec": rc, "ropes": rs, "rgn": rows(inp["ret_gn_g"]),
        "decf": rows(inp["ret_decay_f"]), "decb": rows(inp["ret_decay_b"]), "ramps": ramps})
    l1 = packed(L1C, {"dist_f": df, "dist_b": db, "two": two, "band": band,
                      "poolw": inp["pool_w"][0].transpose(1, 0, 2)})
    i, j = p[:, None], p[None, :]
    halves = [(p[:, None] // b == 2 * np.arange(64 // b)[None, :] + y).astype(np.float32)
              for b in (64, 32, 16, 8, 4, 2, 1) for y in (0, 1)]

    def to_middle(b):
        mid = j // (2 * b) * (2 * b) + b
        return np.where(j % (2 * b) >= b, (i >= mid) & (i <= j), (i > j) & (i < mid))

    low = [to_middle(b) for b in (4, 2, 1)]
    high = [to_middle(b) for b in (64, 32, 16, 8)]
    back = lambda ms: [m[::-1, ::-1] for m in ms]
    mexp = high + back(high) + [i > j] + low + back([i <= j] + low)
    wgk2 = np.zeros((P, 512), np.float32)
    wgk2[0:16] = inp["gla_w_gk2_2"][0]
    wgk2[16] = inp["gla_b_gk_2"][0]
    cols16 = lambda w: w.reshape(KT, P, 16).transpose(1, 0, 2).reshape(P, KT * 16)
    c2 = packed(C2, {
        "U": i <= j, "SL": i > j, "ones": np.ones((P, P)), "halves": np.concatenate(halves, 1), "turn": np.eye(P)[::-1],
        "gcw": feat(inp["gdn_conv_w_2"]),
        "lbl": feat(inp["hgrn_lb_logits_2"]), "alog": rows(inp["gdn_a_log_2"]), "dtb": rows(inp["gdn_dt_bias_2"]),
        "gnw": rows(inp["gdn_norm_w_2"]), "hgn": rows(inp["hgrn_norm_w_2"]), "gln": rows(inp["gla_norm_w_2"]),
        "wba": np.concatenate([cols16(inp["gdn_w_in_2"][n][:, 4096:4112]) for n in range(2)], 1),
        "wgk": cols16(inp["gla_w_in_2"][0][:, 3072:3088]), "wgk2": wgk2})
    ln = np.stack([np.stack([inp["mix_ln_g_2"], inp["mix_ln_b_2"]], 1),
                   np.stack([inp["ffn_ln_g_2"], inp["ffn_ln_b_2"]], 1)], 1).reshape(8, 2, D)
    arrays = {
        "w": pack_weights(inp), "x": inp["x"].reshape(2, P, D), "ctx": inp["ctx"].reshape(2, P, D),
        "core": core, "b1": b1, "l1": l1,
        "c2": c2, "ln": np.ascontiguousarray(ln), "mexp": np.concatenate(mexp, 1).astype(np.float32)}
    nc = _bacc.Bacc("TRN2", target_bir_lowering=False, num_devices=1)
    aps = [nc.dram_tensor("in_" + n, a.shape, f32, kind="ExternalInput").ap() for n, a in arrays.items()]
    out = nc.dram_tensor("out", [2, P, D], f32, kind="ExternalOutput").ap()
    fused_block(nc, *aps, out)
    r = _run(nc, [{"in_" + n: a for n, a in arrays.items()}], core_ids=[0])
    return r.results[0]["out"].reshape(1, T, D)
```
